# Optimizing a Trainium2 kernel written in Bass

```python
import jax, jax.numpy as jnp
from jax import lax
import numpy as np
import math

D_MODEL = 1024
BATCH = 1
SEQ = 512
DEPTH = 2

N_MIXERS = 2
EPS = 1e-6

SSM_EXPAND = 2
SSM_D_INNER = SSM_EXPAND * D_MODEL
SSM_HEAD_DIM = 64
SSM_HEADS = SSM_D_INNER // SSM_HEAD_DIM
SSM_GROUPS = 8
SSM_HEADS_PER_GROUP = SSM_HEADS // SSM_GROUPS
SSM_STATE = 128
SSM_CONV = 4
SSM_CHUNK = 128
SSM_BC_DIM = SSM_GROUPS * SSM_STATE
SSM_CONV_DIM = SSM_D_INNER + 2 * SSM_BC_DIM
SSM_IN_DIM = SSM_D_INNER + SSM_CONV_DIM + SSM_HEADS

ATT_HEAD_DIM = 64
ATT_Q_HEADS = D_MODEL // ATT_HEAD_DIM
ATT_KV_HEADS = 4
ATT_GQA = ATT_Q_HEADS // ATT_KV_HEADS
ATT_WIDTH = ATT_Q_HEADS * ATT_HEAD_DIM
ATT_KV_WIDTH = ATT_KV_HEADS * ATT_HEAD_DIM
ATT_IN_DIM = 2 * ATT_WIDTH + 2 * ATT_KV_WIDTH
WINDOW = 128
ATT_BLOCK = 128
ROPE_THETA = 500000.0
ROPE_DIM = ATT_HEAD_DIM // 4

N_SSM_LAYERS = (DEPTH + 1) // 2
N_ATT_LAYERS = DEPTH // 2


def rmsnorm(x, w):
    xf = x.astype(jnp.float32)
    y = xf * lax.rsqrt(jnp.mean(xf * xf, axis=-1, keepdims=True) + EPS)
    return (y * w.astype(jnp.float32)).astype(x.dtype)

def causal_depthwise_conv(u, w, b):
    c = u.shape[-1]
    out = lax.conv_general_dilated(
        u, w[:, None, :].astype(u.dtype), window_strides=(1,),
        padding=((SSM_CONV - 1, 0),), dimension_numbers=('NWC', 'WIO', 'NWC'),
        feature_group_count=c)
    return out + b.astype(u.dtype)

def ssd_chunked(xs, dt, A, Bm, Cm):
    b, L = xs.shape[:2]
    c, l = L // SSM_CHUNK, SSM_CHUNK
    G, R, P, N = SSM_GROUPS, SSM_HEADS_PER_GROUP, SSM_HEAD_DIM, SSM_STATE
    x = (xs * dt[..., None]).reshape(b, c, l, G, R, P)
    a = jnp.moveaxis((dt * A).reshape(b, c, l, G, R), 2, -1)
    a_cs = jnp.cumsum(a, axis=-1)
    Bc = Bm.reshape(b, c, l, G, N)
    Cc = Cm.reshape(b, c, l, G, N)
    causal = jnp.tril(jnp.ones((l, l), dtype=bool))
    seg = a_cs[..., :, None] - a_cs[..., None, :]
    decay = jnp.exp(jnp.where(causal, seg, -jnp.inf))
    cb = jnp.einsum('bclgn,bcsgn->bcgls', Cc, Bc)
    y_diag = jnp.einsum('bcgrls,bcsgrp->bclgrp', cb[:, :, :, None] * decay, x)
    decay_to_end = jnp.exp(a_cs[..., -1:] - a_cs)
    states = jnp.einsum('bclgn,bcgrl,bclgrp->bcgrpn', Bc, decay_to_end, x)
    chunk_decay = jnp.exp(a_cs[..., -1])

    def step(h, inp):
        s, d = inp
        return h * d[..., None, None] + s, h

    h0 = jnp.zeros_like(states[:, 0])
    _, h_in = lax.scan(step, h0, (jnp.moveaxis(states, 1, 0), jnp.moveaxis(chunk_decay, 1, 0)))
    h_in = jnp.moveaxis(h_in, 0, 1)
    y_off = jnp.einsum('bclgn,bcgrpn,bcgrl->bclgrp', Cc, h_in, jnp.exp(a_cs))
    return (y_diag + y_off).reshape(b, L, SSM_HEADS, P)

def mamba2_mixer(h, w_in, conv_w, conv_b, dt_bias, a_log, d_skip, gate_norm, w_out):
    b, L, _ = h.shape
    f32 = jnp.float32
    z, xbc, dt = jnp.split(h @ w_in, [SSM_D_INNER, SSM_D_INNER + SSM_CONV_DIM], axis=-1)
    xbc = jax.nn.silu(causal_depthwise_conv(xbc, conv_w, conv_b))
    xs, Bm, Cm = jnp.split(xbc, [SSM_D_INNER, SSM_D_INNER + SSM_BC_DIM], axis=-1)
    xs = xs.reshape(b, L, SSM_HEADS, SSM_HEAD_DIM).astype(f32)
    Bm = Bm.reshape(b, L, SSM_GROUPS, SSM_STATE).astype(f32)
    Cm = Cm.reshape(b, L, SSM_GROUPS, SSM_STATE).astype(f32)
    dt = jax.nn.softplus(dt.astype(f32) + dt_bias.astype(f32))
    A = -jnp.exp(a_log.astype(f32))
    y = ssd_chunked(xs, dt, A, Bm, Cm) + d_skip.astype(f32)[:, None] * xs
    y = y.reshape(b, L, SSM_D_INNER) * jax.nn.silu(z.astype(f32))
    y = rmsnorm(y, gate_norm)
    return y.astype(h.dtype) @ w_out

def rope_tables(positions):
    inv = ROPE_THETA ** (-jnp.arange(0, ROPE_DIM, 2, dtype=jnp.float32) / ROPE_DIM)
    ang = positions.astype(jnp.float32)[..., None] * inv
    return jnp.cos(ang)[:, :, None, :], jnp.sin(ang)[:, :, None, :]

def apply_partial_rope(t, cos, sin):
    half = ROPE_DIM // 2
    t1, t2, rest = t[..., :half], t[..., half:ROPE_DIM], t[..., ROPE_DIM:]
    return jnp.concatenate([t1 * cos - t2 * sin, t2 * cos + t1 * sin, rest], axis=-1)

def swa_sink_mixer(h, cos, sin, w_in, sinks, w_out):
    b, L, _ = h.shape
    f32 = jnp.float32
    Hk, D, BLK = ATT_KV_HEADS, ATT_HEAD_DIM, ATT_BLOCK
    q, k, v, gate = jnp.split(
        h @ w_in, [ATT_WIDTH, ATT_WIDTH + ATT_KV_WIDTH, ATT_WIDTH + 2 * ATT_KV_WIDTH], axis=-1)
    q = apply_partial_rope(q.reshape(b, L, ATT_Q_HEADS, D).astype(f32), cos, sin)
    k = apply_partial_rope(k.reshape(b, L, Hk, D).astype(f32), cos, sin)
    v = v.reshape(b, L, Hk, D).astype(f32)
    nb = L // BLK
    qb = q.reshape(b, nb, BLK, Hk, ATT_GQA, D)

    def band(t):
        tp = jnp.pad(t, ((0, 0), (BLK, 0), (0, 0), (0, 0))).reshape(b, nb + 1, BLK, Hk, D)
        return jnp.concatenate([tp[:, :-1], tp[:, 1:]], axis=2)

    kb, vb = band(k), band(v)
    s = jnp.einsum('bnikgd,bnjkd->bnkgij', qb, kb) * (D ** -0.5)
    qi = jnp.arange(BLK)[:, None]
    kj = jnp.arange(2 * BLK)[None, :]
    dist = qi + BLK - kj
    blk = jnp.arange(nb)[:, None, None]
    valid = (dist >= 0) & (dist < WINDOW) & ((blk - 1) * BLK + kj >= 0)
    s = jnp.where(valid[None, :, None, None], s, -jnp.inf)
    sink = sinks.astype(f32).reshape(Hk, ATT_GQA)[None, None, :, :, None, None]
    m = jnp.maximum(jnp.max(s, axis=-1, keepdims=True), sink)
    p = jnp.exp(s - m)
    denom = jnp.sum(p, axis=-1, keepdims=True) + jnp.exp(sink - m)
    o = jnp.einsum('bnkgij,bnjkd->bnikgd', p / denom, vb)
    o = o.reshape(b, L, ATT_WIDTH) * jax.nn.silu(gate.astype(f32))
    return o.astype(h.dtype) @ w_out

def first_inputs(seed: int = 0) -> dict:
    key = jax.random.key(seed)
    ks = jax.random.split(key, 16)
    f32 = jnp.float32
    nS, nA = N_SSM_LAYERS, N_ATT_LAYERS
    x = jax.random.normal(ks[0], (BATCH, SEQ, D_MODEL), f32)
    positions = jnp.broadcast_to(jnp.arange(SEQ, dtype=jnp.int32), (BATCH, SEQ))
    pre_norm = 1.0 + 0.1 * jax.random.normal(ks[1], (DEPTH, D_MODEL), f32)
    post_norm = 1.0 + 0.1 * jax.random.normal(ks[2], (DEPTH, D_MODEL), f32)
    ssm_w_in = jax.random.normal(ks[3], (nS, D_MODEL, SSM_IN_DIM), f32) * D_MODEL ** -0.5
    ssm_conv_w = jax.random.normal(ks[4], (nS, SSM_CONV, SSM_CONV_DIM), f32) * SSM_CONV ** -0.5
    ssm_conv_b = 0.02 * jax.random.normal(ks[5], (nS, SSM_CONV_DIM), f32)
    dt0 = jnp.exp(jax.random.uniform(ks[6], (nS, SSM_HEADS), f32)
                  * (np.log(0.1) - np.log(0.001)) + np.log(0.001)).astype(f32)
    ssm_dt_bias = dt0 + jnp.log(-jnp.expm1(-dt0))
    ssm_a_log = jnp.log(jax.random.uniform(ks[7], (nS, SSM_HEADS), f32, 1.0, 16.0))
    ssm_d = 1.0 + 0.1 * jax.random.normal(ks[8], (nS, SSM_HEADS), f32)
    ssm_gate_norm = 1.0 + 0.1 * jax.random.normal(ks[9], (nS, SSM_D_INNER), f32)
    ssm_w_out = jax.random.normal(ks[10], (nS, SSM_D_INNER, D_MODEL), f32) * SSM_D_INNER ** -0.5
    att_w_in = jax.random.normal(ks[11], (nA, D_MODEL, ATT_IN_DIM), f32) * D_MODEL ** -0.5
    att_sinks = 0.5 * jax.random.normal(ks[12], (nA, ATT_Q_HEADS), f32)
    att_w_out = jax.random.normal(ks[13], (nA, ATT_WIDTH, D_MODEL), f32) * ATT_WIDTH ** -0.5
    return {"x": x, "positions": positions, "pre_norm": pre_norm, "post_norm": post_norm,
            "ssm_w_in": ssm_w_in, "ssm_conv_w": ssm_conv_w, "ssm_conv_b": ssm_conv_b,
            "ssm_dt_bias": ssm_dt_bias, "ssm_a_log": ssm_a_log, "ssm_d": ssm_d,
            "ssm_gate_norm": ssm_gate_norm, "ssm_w_out": ssm_w_out,
            "att_w_in": att_w_in, "att_sinks": att_sinks, "att_w_out": att_w_out}

def first_block(x, positions, pre_norm, post_norm, ssm_w_in, ssm_conv_w, ssm_conv_b,
              ssm_dt_bias, ssm_a_log, ssm_d, ssm_gate_norm, ssm_w_out,
              att_w_in, att_sinks, att_w_out):
    cos, sin = rope_tables(positions)
    for i in range(DEPTH):
        h = rmsnorm(x, pre_norm[i])
        j = i // N_MIXERS
        if i % N_MIXERS == 0:
            y = mamba2_mixer(h, ssm_w_in[j], ssm_conv_w[j], ssm_conv_b[j], ssm_dt_bias[j],
                             ssm_a_log[j], ssm_d[j], ssm_gate_norm[j], ssm_w_out[j])
        else:
            y = swa_sink_mixer(h, cos, sin, att_w_in[j], att_sinks[j], att_w_out[j])
        x = x + rmsnorm(y, post_norm[i])
    return x


DEPTH_2 = 1

GDN_HEADS = 4
GDN_HEAD_DIM = 128
MLSTM_HEADS = 4
MLSTM_HEAD_DIM = 128
GDN_W = GDN_HEADS * GDN_HEAD_DIM
MLSTM_W = MLSTM_HEADS * MLSTM_HEAD_DIM
CONV_WIDTH = 4
GDN_CHUNK = 64
MLSTM_CHUNK = 64
PROJ_SIZES = (3 * GDN_W, GDN_W, GDN_HEADS, GDN_HEADS,
              2 * MLSTM_W, MLSTM_W, MLSTM_W, MLSTM_HEADS, MLSTM_HEADS)
PROJ_DIM = sum(PROJ_SIZES)
MEM_TOKENS = 256
XA_HEADS = 4
XA_HEAD_DIM = D_MODEL // XA_HEADS
PEER_HEADS = 8
PEER_N_KEYS = 128
PEER_N_EXPERTS = PEER_N_KEYS * PEER_N_KEYS
PEER_TOPK = 16
PEER_HALF = 128
PEER_QUERY_DIM = 2 * PEER_HALF
PEER_BLOCK = 128
NORM_EPS = 1e-6


def rmsnorm_2(x, w):
    xf = x.astype(jnp.float32)
    y = xf * lax.rsqrt(jnp.mean(xf * xf, axis=-1, keepdims=True) + NORM_EPS)
    return (y * w.astype(jnp.float32)).astype(x.dtype)

def l2norm(x):
    return x * lax.rsqrt(jnp.sum(x * x, axis=-1, keepdims=True) + NORM_EPS)

def causal_dwconv(x, w):
    kw = w.shape[0]
    return lax.conv_general_dilated(x, w[:, None, :].astype(x.dtype), window_strides=(1,),
                                    padding=[(kw - 1, 0)],
                                    dimension_numbers=('NWC', 'WIO', 'NWC'),
                                    feature_group_count=x.shape[-1])

def to_chunks(t, nc, lc):
    b, h = t.shape[0], t.shape[1]
    return jnp.moveaxis(t.reshape(b, h, nc, lc, *t.shape[3:]), 2, 0)

def gated_delta_rule(q, k, v, log_alpha, beta):
    b, nh, s, dk = q.shape
    dv = v.shape[-1]
    lc = GDN_CHUNK
    nc = s // lc
    q = q * dk ** -0.5
    q, k, v, log_alpha, beta = (to_chunks(t, nc, lc) for t in (q, k, v, log_alpha, beta))
    gc = jnp.cumsum(log_alpha, axis=-1)
    idx = jnp.arange(lc)
    causal = idx[:, None] >= idx[None, :]
    strict = idx[:, None] > idx[None, :]
    decay = jnp.exp(jnp.where(causal, gc[..., :, None] - gc[..., None, :], -jnp.inf))
    kb = k * beta[..., None]
    a = jnp.where(strict, jnp.einsum('nbhid,nbhjd->nbhij', kb, k) * decay, 0.0)
    eye = jnp.eye(lc, dtype=q.dtype)
    t_inv = lax.linalg.triangular_solve(a + eye, jnp.broadcast_to(eye, a.shape), left_side=True,
                                        lower=True, unit_diagonal=True)
    u = t_inv @ (v * beta[..., None])
    w = t_inv @ (kb * jnp.exp(gc)[..., None])
    qk = jnp.einsum('nbhid,nbhjd->nbhij', q, k) * decay
    q_dec = q * jnp.exp(gc)[..., None]
    k_dec = k * jnp.exp(gc[..., -1:] - gc)[..., None]
    g_last = jnp.exp(gc[..., -1])

    def step(state, xs):
        u_c, w_c, qk_c, qd_c, kd_c, gl_c = xs
        v_new = u_c - w_c @ state
        o = qd_c @ state + qk_c @ v_new
        state = state * gl_c[..., None, None] + jnp.einsum('bhld,bhle->bhde', kd_c, v_new)
        return state, o

    s0 = jnp.zeros((b, nh, dk, dv), q.dtype)
    _, o = lax.scan(step, s0, (u, w, qk, q_dec, k_dec, g_last))
    return jnp.moveaxis(o, 0, 2).reshape(b, nh, s, dv)

def mlstm_chunkwise(q, k, v, log_i, log_f):
    b, nh, s, dk = q.shape
    dv = v.shape[-1]
    lc = MLSTM_CHUNK
    nc = s // lc
    k = k * dk ** -0.5
    q, k, v, log_i, log_f = (to_chunks(t, nc, lc) for t in (q, k, v, log_i, log_f))
    bcum = jnp.cumsum(log_f, axis=-1)
    idx = jnp.arange(lc)
    causal = idx[:, None] >= idx[None, :]
    d_intra = jnp.where(causal, bcum[..., :, None] - bcum[..., None, :] + log_i[..., None, :], -jnp.inf)
    d_last = bcum[..., -1:] - bcum + log_i
    qk = jnp.einsum('nbhid,nbhjd->nbhij', q, k)

    def step(carry, xs):
        c, n, m = carry
        q_c, k_c, v_c, b_c, d_c, qk_c, dl_c = xs
        inter = b_c + m[..., None]
        m_t = jnp.maximum(inter, jnp.max(d_c, axis=-1))
        p = qk_c * jnp.exp(d_c - m_t[..., None])
        sc = jnp.exp(inter - m_t)
        num = sc[..., None] * (q_c @ c) + p @ v_c
        den = sc * jnp.einsum('bhld,bhd->bhl', q_c, n) + jnp.sum(p, axis=-1)
        h = num / jnp.maximum(jnp.abs(den), jnp.exp(-m_t))[..., None]
        b_last = b_c[..., -1]
        m_new = jnp.maximum(b_last + m, jnp.max(dl_c, axis=-1))
        wgt = jnp.exp(dl_c - m_new[..., None])
        dec = jnp.exp(b_last + m - m_new)
        c = dec[..., None, None] * c + jnp.einsum('bhld,bhle->bhde', k_c * wgt[..., None], v_c)
        n = dec[..., None] * n + jnp.einsum('bhld,bhl->bhd', k_c, wgt)
        return (c, n, m_new), h

    init = (jnp.zeros((b, nh, dk, dv), q.dtype), jnp.zeros((b, nh, dk), q.dtype),
            jnp.zeros((b, nh), q.dtype))
    _, hs = lax.scan(step, init, (q, k, v, bcum, d_intra, qk, d_last))
    return jnp.moveaxis(hs, 0, 2).reshape(b, nh, s, dv)

def hybrid_mixer(h, w_in, gdn_conv_w, gdn_a_log, gdn_dt_bias, gdn_norm_w,
                 mlstm_conv_w, mlstm_i_bias, mlstm_f_bias, mlstm_norm_w, w_out):
    b, s, _ = h.shape
    f32 = jnp.float32
    proj = (h @ w_in).astype(f32)
    cuts = np.cumsum(PROJ_SIZES)[:-1].tolist()
    g_qkv, g_z, g_a, g_b, m_qk, m_v, m_o, m_i, m_f = jnp.split(proj, cuts, axis=-1)

    def heads(t, nh):
        return t.reshape(b, s, nh, -1).transpose(0, 2, 1, 3)

    g_qkv = jax.nn.silu(causal_dwconv(g_qkv, gdn_conv_w.astype(f32)))
    gq, gk, gv = (heads(t, GDN_HEADS) for t in jnp.split(g_qkv, 3, axis=-1))
    gq, gk = l2norm(gq), l2norm(gk)
    log_alpha = -jnp.exp(gdn_a_log.astype(f32)) * jax.nn.softplus(g_a + gdn_dt_bias.astype(f32))
    beta = jax.nn.sigmoid(g_b)
    go = gated_delta_rule(gq, gk, gv, log_alpha.transpose(0, 2, 1), beta.transpose(0, 2, 1))
    go = rmsnorm_2(go.transpose(0, 2, 1, 3), gdn_norm_w) * jax.nn.silu(
        g_z.reshape(b, s, GDN_HEADS, GDN_HEAD_DIM))

    m_qk = jax.nn.silu(causal_dwconv(m_qk, mlstm_conv_w.astype(f32)))
    mq, mk = (heads(t, MLSTM_HEADS) for t in jnp.split(m_qk, 2, axis=-1))
    mv = heads(m_v, MLSTM_HEADS)
    log_i = (m_i + mlstm_i_bias.astype(f32)).transpose(0, 2, 1)
    log_f = jax.nn.log_sigmoid(m_f + mlstm_f_bias.astype(f32)).transpose(0, 2, 1)
    mh = mlstm_chunkwise(mq, mk, mv, log_i, log_f)
    mh = rmsnorm_2(mh.transpose(0, 2, 1, 3), mlstm_norm_w.reshape(MLSTM_HEADS, MLSTM_HEAD_DIM)) * \
        jax.nn.sigmoid(m_o.reshape(b, s, MLSTM_HEADS, MLSTM_HEAD_DIM))

    mixed = jnp.concatenate([go.reshape(b, s, GDN_W), mh.reshape(b, s, MLSTM_W)], axis=-1)
    return mixed.astype(h.dtype) @ w_out

def memory_cross_attention(h, m, wq, wkv, wo):
    b, s, _ = h.shape
    q = (h @ wq).reshape(b, s, XA_HEADS, XA_HEAD_DIM)
    k, v = jnp.split(m @ wkv, 2, axis=-1)
    k = k.reshape(b, -1, XA_HEADS, XA_HEAD_DIM)
    v = v.reshape(b, -1, XA_HEADS, XA_HEAD_DIM)
    scores = jnp.einsum('bshd,bmhd->bhsm', q, k).astype(jnp.float32) * XA_HEAD_DIM ** -0.5
    p = jax.nn.softmax(scores, axis=-1).astype(v.dtype)
    o = jnp.einsum('bhsm,bmhd->bshd', p, v).reshape(b, s, D_MODEL)
    return o @ wo

def peer_ffn(h, wq, sub_keys, u_table, v_table):
    b, s, d = h.shape
    t = b * s
    hf = h.reshape(t, d)
    q = (hf @ wq).reshape(t, PEER_HEADS, 2, PEER_HALF)
    sc = jnp.einsum('thpd,hpnd->thpn', q, sub_keys).astype(jnp.float32)
    top_v, top_i = lax.top_k(sc, PEER_TOPK)
    kk = PEER_TOPK * PEER_TOPK
    cand = (top_v[:, :, 0, :, None] + top_v[:, :, 1, None, :]).reshape(t, PEER_HEADS, kk)
    cand_id = (top_i[:, :, 0, :, None] * PEER_N_KEYS + top_i[:, :, 1, None, :]).reshape(t, PEER_HEADS, kk)
    best_v, best_pos = lax.top_k(cand, PEER_TOPK)
    expert_id = jnp.take_along_axis(cand_id, best_pos, axis=-1)
    gate = jax.nn.softmax(best_v, axis=-1)
    nb = t // PEER_BLOCK

    def block(args):
        xb, eb, gb = args
        u = jnp.take(u_table, eb, axis=0)
        act = jax.nn.gelu(jnp.einsum('phkd,pd->phk', u, xb).astype(jnp.float32), approximate=False)
        wgt = (gb * act).astype(v_table.dtype)
        return jnp.einsum('phk,phkd->pd', wgt, jnp.take(v_table, eb, axis=0))

    out = lax.map(block, (hf.reshape(nb, PEER_BLOCK, d),
                          expert_id.reshape(nb, PEER_BLOCK, PEER_HEADS, PEER_TOPK),
                          gate.reshape(nb, PEER_BLOCK, PEER_HEADS, PEER_TOPK)))
    return out.reshape(b, s, d).astype(h.dtype)

def second_inputs(seed: int = 0) -> dict:
    key = jax.random.key(seed)
    ks = jax.random.split(key, 24)
    f32 = jnp.float32
    L, D = DEPTH_2, D_MODEL

    def nrm(k, shape, scale):
        return jax.random.normal(k, shape, f32) * scale

    def gain(k, shape):
        return 1.0 + 0.01 * jax.random.normal(k, shape, f32)

    dt = jnp.exp(jax.random.uniform(ks[6], (L, GDN_HEADS), f32, math.log(1e-3), math.log(1e-1)))
    return {
        'x': nrm(ks[0], (BATCH, SEQ, D), 1.0),
        'mem': nrm(ks[1], (BATCH, MEM_TOKENS, D), 1.0),
        'norm_mix_w': gain(ks[2], (L, D)),
        'w_in': nrm(ks[3], (L, D, PROJ_DIM), D ** -0.5),
        'gdn_conv_w': nrm(ks[4], (L, CONV_WIDTH, 3 * GDN_W), CONV_WIDTH ** -0.5),
        'gdn_a_log': jnp.log(jax.random.uniform(ks[5], (L, GDN_HEADS), f32, 1.0, 16.0)),
        'gdn_dt_bias': dt + jnp.log(-jnp.expm1(-dt)),
        'gdn_norm_w': gain(ks[7], (L, GDN_HEAD_DIM)),
        'mlstm_conv_w': nrm(ks[8], (L, CONV_WIDTH, 2 * MLSTM_W), CONV_WIDTH ** -0.5),
        'mlstm_i_bias': nrm(ks[9], (L, MLSTM_HEADS), 0.5),
        'mlstm_f_bias': jax.random.uniform(ks[10], (L, MLSTM_HEADS), f32, 3.0, 6.0),
        'mlstm_norm_w': gain(ks[11], (L, MLSTM_W)),
        'w_out': nrm(ks[12], (L, GDN_W + MLSTM_W, D), (GDN_W + MLSTM_W) ** -0.5),
        'norm_xa_w': gain(ks[13], (L, D)),
        'norm_mem_w': gain(ks[14], (L, D)),
        'xa_wq': nrm(ks[15], (L, D, D), D ** -0.5),
        'xa_wkv': nrm(ks[16], (L, D, 2 * D), D ** -0.5),
        'xa_wo': nrm(ks[17], (L, D, D), D ** -0.5),
        'norm_ffn_w': gain(ks[18], (L, D)),
        'peer_wq': nrm(ks[19], (L, D, PEER_HEADS * PEER_QUERY_DIM), D ** -0.5),
        'peer_sub_keys': nrm(ks[20], (L, PEER_HEADS, 2, PEER_N_KEYS, PEER_HALF), PEER_HALF ** -0.5),
        'peer_u': nrm(ks[21], (L, PEER_N_EXPERTS, D), D ** -0.5),
        'peer_v': nrm(ks[22], (L, PEER_N_EXPERTS, D), (PEER_HEADS * PEER_TOPK) ** -0.5),
        'norm_final_w': gain(ks[23], (D,)),
    }

def second_block(x, mem, norm_mix_w, w_in, gdn_conv_w, gdn_a_log, gdn_dt_bias, gdn_norm_w,
              mlstm_conv_w, mlstm_i_bias, mlstm_f_bias, mlstm_norm_w, w_out,
              norm_xa_w, norm_mem_w, xa_wq, xa_wkv, xa_wo,
              norm_ffn_w, peer_wq, peer_sub_keys, peer_u, peer_v, norm_final_w):
    for l in range(DEPTH_2):
        x = x + hybrid_mixer(rmsnorm_2(x, norm_mix_w[l]), w_in[l], gdn_conv_w[l], gdn_a_log[l],
                             gdn_dt_bias[l], gdn_norm_w[l], mlstm_conv_w[l], mlstm_i_bias[l],
                             mlstm_f_bias[l], mlstm_norm_w[l], w_out[l])
        x = x + memory_cross_attention(rmsnorm_2(x, norm_xa_w[l]), rmsnorm_2(mem, norm_mem_w[l]),
                                       xa_wq[l], xa_wkv[l], xa_wo[l])
        x = x + peer_ffn(rmsnorm_2(x, norm_ffn_w[l]), peer_wq[l], peer_sub_keys[l], peer_u[l], peer_v[l])
    return rmsnorm_2(x, norm_final_w)


def setup_inputs(seed=0):
    out = dict(first_inputs(seed))
    for name, value in second_inputs(seed + 1).items():
        if name != "x":
            out[name + "_2"] = value
    return out


def reference(
    x, positions, pre_norm, post_norm, ssm_w_in, ssm_conv_w, ssm_conv_b, ssm_dt_bias, ssm_a_log,
    ssm_d, ssm_gate_norm, ssm_w_out, att_w_in, att_sinks, att_w_out, mem_2, norm_mix_w_2,
    w_in_2, gdn_conv_w_2, gdn_a_log_2, gdn_dt_bias_2, gdn_norm_w_2, mlstm_conv_w_2,
    mlstm_i_bias_2, mlstm_f_bias_2, mlstm_norm_w_2, w_out_2, norm_xa_w_2, norm_mem_w_2, xa_wq_2,
    xa_wkv_2, xa_wo_2, norm_ffn_w_2, peer_wq_2, peer_sub_keys_2, peer_u_2, peer_v_2,
    norm_final_w_2,
):
    x = first_block(
        x, positions, pre_norm, post_norm, ssm_w_in, ssm_conv_w, ssm_conv_b, ssm_dt_bias,
        ssm_a_log, ssm_d, ssm_gate_norm, ssm_w_out, att_w_in, att_sinks, att_w_out,
    )
    return second_block(
        x, mem_2, norm_mix_w_2, w_in_2, gdn_conv_w_2, gdn_a_log_2, gdn_dt_bias_2, gdn_norm_w_2,
        mlstm_conv_w_2, mlstm_i_bias_2, mlstm_f_bias_2, mlstm_norm_w_2, w_out_2, norm_xa_w_2,
        norm_mem_w_2, xa_wq_2, xa_wkv_2, xa_wo_2, norm_ffn_w_2, peer_wq_2, peer_sub_keys_2,
        peer_u_2, peer_v_2, norm_final_w_2,
    )


_drawn_inputs = setup_inputs


def setup_inputs(seed=0):
    import zlib

    import numpy as np

    out = dict(_drawn_inputs(seed))
    spreads = {}
    factors = {'att_sinks': 7.412,
     'norm_mix_w_2': 8.0,
     'gdn_norm_w_2': 22.122,
     'mlstm_i_bias_2': 41.374,
     'mlstm_norm_w_2': 64.0,
     'norm_xa_w_2': 22.646,
     'norm_mem_w_2': 22.414,
     'norm_ffn_w_2': 64.0,
     'peer_u_2': 2.676,
     'norm_final_w_2': 32.342}
    for name, (base, spread) in spreads.items():
        noise = np.random.default_rng([zlib.crc32(name.encode()), seed]).standard_normal(out[name].shape)
        drawn = base * np.exp(spread * noise) if base else spread * noise
        out[name] = __import__('jax').numpy.asarray(drawn.astype(out[name].dtype))
    for name, factor in factors.items():
        out[name] = (out[name] * factor).astype(out[name].dtype)
    return out
```

```python
from contextlib import ExitStack

import concourse.bass as bass
from concourse import mybir

F32 = mybir.dt.float32
U32 = mybir.dt.uint32
I32 = mybir.dt.int32
ALU = mybir.AluOpType
ACT = mybir.ActivationFunctionType
AX = mybir.AxisListType

P = 128
SEQ = 512
TT = SEQ // P
D = 1024
DT = D // P
EPS = 1e-6
RING = 4
UNIT = 1024

DI = 2048
HEADS, HD = 32, 64
GROUPS, STATE = 8, 128
HPG = HEADS // GROUPS
CONV = 4
XS_T, BC_T = DI // P, GROUPS * STATE // P
CM_T = XS_T + 2 * BC_T
QH, KVH, AD = 16, 4, 64
QW, KVW = QH * AD, KVH * AD
HEAD_ORDER = [8 * a + 4 * b + i for a in range(2) for i in range(4) for b in range(2)]
ROPE = AD // 4
HALF = ROPE // 2
THETA = 500000.0
GH, GD = 4, 128
MH, MD = 4, 128
MEM = 256
XH, XD = 4, 256
PH, KEYS, TOPK = 8, 128, 16
NEG = -3.0e38


class Steps:

    def __init__(self, eng, sem, start=0):
        self.eng, self.sem, self.n, self.turn = eng, sem, start, None

    def value(self):
        if self.turn is None:
            return self.n
        i, per, base = self.turn
        return i * per + (base + self.n)

    def __call__(self, ins):
        ins.then_inc(self.sem, 1)
        self.n += 1
        self.eng.wait_ge(self.sem, self.value())

    def loop(self, i, per):
        self.turn, self.n = (i, per, self.n), 0

    def end_loop(self, count):
        _, per, base = self.turn
        assert self.n == per
        self.turn, self.n = None, base + count * per


class Machine:

    def __init__(self, nc, ctx, ins):
        self.nc, self.ins = nc, ins
        self.spent = []
        self.steps_at = {}
        self.unit = ins.get("unit0", 0)
        self.streamed = ins.get("unit0", 0)
        self.banks = [ctx.enter_context(nc.psum_tensor(f"bank{i}", [P, 512], F32)) for i in range(8)]
        self.w_loaded = [ctx.enter_context(nc.semaphore(f"w_loaded{i}")) for i in range(RING)]
        self.w_used = ctx.enter_context(nc.semaphore("w_used"))
        self.dve_step = ctx.enter_context(nc.semaphore("dve_step"))
        self.act_step = ctx.enter_context(nc.semaphore("act_step"))
        self.pool_step = ctx.enter_context(nc.semaphore("pool_step"))
        sb = lambda n, s, d=F32: ctx.enter_context(nc.sbuf_tensor(n, s, d))
        self.ident = sb("ident", [P, P])
        self.ones = sb("ones", [P, P])
        self.upto = sb("upto", [P, P])
        self.after = sb("after", [P, P])
        self.ring = sb("ring", [P, RING, UNIT])
        self.resid = sb("resid", [P, TT, D])
        self.cols = sb("cols", [P, ins["cols"].shape[1]])

    def sem(self, scope, name):
        handle = self.nc.alloc_semaphore(name)
        scope.callback(self.spent.append, handle)
        return handle

    def clear_signals(self):
        self.nc.clear_and_free_semaphores(self.spent)
        self.nc.all_engine_barrier()
        self.spent = []

    def steps(self, eng, sem):
        key = id(sem)
        s = Steps(eng, sem, self.steps_at.get(key, 0))
        return s

    def keep(self, steps):
        self.steps_at[id(steps.sem)] = steps.n

    def row(self, name, width):
        return self.row_at(self.ins["row_at"][name], width)

    def row_at(self, at, width):
        r = self.ins["rows"]
        return bass.AP(tensor=r.tensor, offset=r.offset + at, ap=[[0, P], [1, width]])

    def col(self, name, i=0, n=1):
        at = self.ins["col_at"][name] + i
        return self.cols[:, at:at + n]



def stream_weights(m, sp, n):
    u0 = m.streamed
    assert u0 % RING == 0 and n % RING == 0
    w = m.ins["weights"]
    total = w.shape[0]
    n = min(n, total - u0)
    m.streamed += n
    if u0 == 0:
        for s in range(RING):
            sp.dma_start(m.ring[:, s, :], w[s]).then_inc(m.w_loaded[s], 16)
        u0, n = RING, n - RING
    if n <= 0:
        return
    with sp.Fori(0, n // RING) as i:
        for s in range(RING):
            sp.wait_ge(m.w_used, i * RING + (u0 - RING + s + 1))
            sp.dma_start(m.ring[:, s, :], w[i * RING + (u0 + s)]).then_inc(m.w_loaded[s], 16)


def columns_out(m, pe, n, rhs, width, free, free0, banks):
    u0 = m.unit
    m.unit += n
    with pe.Fori(0, n // RING) as i:
        for s in range(RING):
            pe.wait_ge(m.w_loaded[s], i * 16 + 16 * (u0 // RING + 1))
            pe.wait_ge(free, i * RING + (free0 + s))
            for k in range(DT):
                mm = pe.matmul(banks[s][:, 0:width], m.ring[:, s, k * P:(k + 1) * P], rhs[:, k, :],
                               start=(k == 0), stop=(k == DT - 1))
            mm.then_inc(m.w_used, 1)


def tokens_out(m, pe, chunks, kt, lhs, tiles, done, before_bank, bank_of):
    for c in range(chunks):
        for kk in range(kt // 2):
            u = m.unit
            m.unit += 1
            s = u % RING
            pe.wait_ge(m.w_loaded[s], 16 * (u // RING + 1))
            for t in range(tiles):
                if kk == 0:
                    before_bank(c, t)
                for k in (2 * kk, 2 * kk + 1):
                    mm = pe.matmul(bank_of(c, t)[:, :], lhs[:, k, t * P:(t + 1) * P],
                                   m.ring[:, s, (k % 2) * 512:(k % 2 + 1) * 512],
                                   start=(k == 0), stop=(k == kt - 1), skip_group_check=True)
                if kk == kt // 2 - 1:
                    if t < tiles - 1:
                        mm.then_inc(done, 1)
            mm.then_inc(m.w_used, 1)


def wait_tokens(m, eng, u0, kt, tiles, done, c, t):
    if t < tiles - 1:
        eng.wait_ge(done, (tiles - 1) * c + t + 1)
    else:
        eng.wait_ge(m.w_used, u0 + (c + 1) * kt // 2)



class NormTurn:

    def __init__(self, m, c, name, src, scaled, turned, gain, tiles, width, banks):
        self.m, self.src, self.scaled, self.turned = m, src, scaled, turned
        self.gain, self.tiles, self.width, self.banks = gain, tiles, width, banks
        nc = m.nc
        self.stat = c.enter_context(nc.sbuf_tensor(name + "_stat", [P, 3, tiles], F32))
        sem = lambda n: m.sem(c, f"{name}_{n}")
        self.mean_ready, self.rstd_ready = sem("mean"), sem("rstd")
        self.scaled_ready, self.turned_in_bank, self.turned_ready = sem("scaled"), sem("bank"), sem("turned")

    def vector(self, dve, step):
        st = self.stat
        for t in range(self.tiles):
            step(dve.tensor_tensor_reduce(self.scaled[:, t, :], self.src[:, t, :], self.src[:, t, :], 1.0, 0.0,
                                          ALU.mult, ALU.add, st[:, 0, t:t + 1]))
        step(dve.tensor_scalar(st[:, 1, :], st[:, 0, :], 1.0 / self.width, EPS, ALU.mult, ALU.add))
        dve.reciprocal(st[:, 2, :], st[:, 1, :]).then_inc(self.mean_ready, 1)
        dve.wait_ge(self.rstd_ready, 1)
        for t in range(self.tiles):
            dve.tensor_scalar(self.scaled[:, t, :], self.src[:, t, :], st[:, 0, t:t + 1], None, ALU.mult)\
               .then_inc(self.scaled_ready, 1)

    def scalar_rstd(self, act):
        act.wait_ge(self.mean_ready, 1)
        act.activation(self.stat[:, 0, :], self.stat[:, 2, :], ACT.Sqrt).then_inc(self.rstd_ready, 1)

    def tensor(self, pe):
        pe.wait_ge(self.scaled_ready, self.tiles)
        for k in range(self.width // P):
            if k >= 2:
                pe.wait_ge(self.turned_ready, k - 1)
            for t in range(self.tiles):
                mm = pe.transpose(self.banks[k % 2][:, t * P:(t + 1) * P], self.scaled[:, t, k * P:(k + 1) * P],
                                  self.m.ident[:, :])
            mm.then_inc(self.turned_in_bank, 1)

    def scalar_turned(self, act):
        for k in range(self.width // P):
            act.wait_ge(self.turned_in_bank, k + 1)
            act.activation(self.turned[:, k, :], self.banks[k % 2][:, 0:self.tiles * P], ACT.Copy,
                           scale=self.gain(k)).then_inc(self.turned_ready, 1)


class PostNorm:

    def __init__(self, m, c, name, y, gain_row, gain_loaded):
        self.m, self.y, self.gain_row, self.gain_loaded = m, y, gain_row, gain_loaded
        self.stat = c.enter_context(m.nc.sbuf_tensor(name + "_stat", [P, 3, TT], F32))
        self.junk = c.enter_context(m.nc.sbuf_tensor(name + "_junk", [P, D], F32))
        self.mean_ready = m.sem(c, name + "_mean")
        self.rstd_ready = m.sem(c, name + "_rstd")

    def vector(self, dve, step):
        st, y = self.stat, self.y
        for t in range(TT):
            step(dve.tensor_tensor_reduce(self.junk[:, :], y[:, t, :], y[:, t, :], 1.0, 0.0, ALU.mult, ALU.add,
                                          st[:, 0, t:t + 1]))
        step(dve.tensor_scalar(st[:, 1, :], st[:, 0, :], 1.0 / D, EPS, ALU.mult, ALU.add))
        dve.reciprocal(st[:, 2, :], st[:, 1, :]).then_inc(self.mean_ready, 1)
        dve.wait_ge(self.rstd_ready, 1)
        dve.wait_ge(self.gain_loaded, 16)
        for t in range(TT):
            step(dve.scalar_tensor_tensor(y[:, t, :], y[:, t, :], st[:, 0, t:t + 1], self.gain_row[:, :],
                                          ALU.mult, ALU.mult))
            step(dve.tensor_tensor(self.m.resid[:, t, :], self.m.resid[:, t, :], y[:, t, :], ALU.add))

    def scalar(self, act):
        act.wait_ge(self.mean_ready, 1)
        act.activation(self.stat[:, 0, :], self.stat[:, 2, :], ACT.Sqrt).then_inc(self.rstd_ready, 1)



def set_up(m):
    nc = m.nc
    with ExitStack() as c:
        const = m.sem(c, "const")
        loaded = m.sem(c, "loaded")
        block = c.enter_context(nc.Block())

        @block.sync
        def _(sp):
            sp.dma_start(m.resid[:, :, :], m.ins["x"].rearrange("(t p) d -> p t d", p=P)).then_inc(loaded, 16)
            sp.dma_start(m.cols[:, :], m.ins["cols"]).then_inc(loaded, 16)
            stream_weights(m, sp, RING)
            sp.wait_ge(loaded, 32)

        @block.gpsimd
        def _(pool):
            pool.memset(m.ident[:, :], 0.0).then_inc(const, 1)
            pool.memset(m.ones[:, :], 1.0).then_inc(const, 1)
            pool.wait_ge(const, 2)
            pool.affine_select(out=m.ident[:, :], in_=m.ident[:, :], compare_op=ALU.not_equal, fill=1.0, base=0,
                               pattern=[[-1, P]], channel_multiplier=1)
            pool.affine_select(out=m.upto[:, :], in_=m.ones[:, :], compare_op=ALU.is_ge, fill=0.0, base=0,
                               pattern=[[1, P]], channel_multiplier=-1)
            pool.affine_select(out=m.after[:, :], in_=m.ones[:, :], compare_op=ALU.is_gt, fill=0.0, base=0,
                               pattern=[[-1, P]], channel_multiplier=1)



def mamba(m):
    nc, ins, resid = m.nc, m.ins, m.resid
    with ExitStack() as c:
        sb = lambda n, s, d=F32: c.enter_context(nc.sbuf_tensor(n, s, d))
        dt_raw = sb("ssm_dt_raw", [P, TT, HEADS])
        z_gate = sb("ssm_z_gate", [P, TT, DI])
        conved = sb("ssm_conved", [P, CM_T, SEQ])
        mamba_in(m, z_gate, conved, dt_raw)
        with ExitStack() as c2:
            xs = c2.enter_context(nc.sbuf_tensor("ssm_xs", [P, TT, DI], F32))
            mamba_scan(m, z_gate, conved, dt_raw, xs)
        y_turned = conved[:, 0:XS_T, :]
        mamba_out(m, z_gate, conved[:, XS_T:XS_T + 16, :], y_turned)


def convolve(m, dve, step, tiles, u1, taps, bias, acc, silu_done, conv_done):
    tap_at = m.ins["col_at"][taps]
    dve.sem_inc(conv_done, 4)
    with dve.Fori(0, tiles // 4) as i:
        step.loop(i, 12)
        for b in range(4):
            tap = lambda n: m.cols[:, bass.ds(i * 16 + (tap_at + 4 * b + n), 1)]
            bank, half = m.banks[b], acc[:, b % 2, :]
            dve.wait_ge(m.w_used, i * 4 + (u1 + b + 1))
            dve.wait_ge(silu_done, i * 4 + (b + 1))
            if bias:
                shift = m.cols[:, bass.ds(i * 4 + (m.ins["col_at"][bias] + b), 1)]
                step(dve.tensor_scalar(half, bank[:, :], tap(3), shift, ALU.mult, ALU.add))
            else:
                step(dve.tensor_scalar(half, bank[:, :], tap(3), None, ALU.mult))
            for late in (1, 2):
                step(dve.scalar_tensor_tensor(half[:, late:], bank[:, 0:SEQ - late], tap(3 - late),
                                              half[:, late:], ALU.mult, ALU.add))
            dve.scalar_tensor_tensor(half[:, 3:], bank[:, 0:SEQ - 3], tap(0), half[:, 3:],
                                     ALU.mult, ALU.add).then_inc(conv_done, 1)
        step.end_loop(tiles // 4)


def silu_convolved(act, tiles, conved, acc, silu_done, conv_done):
    act.sem_inc(silu_done, 2)
    with act.Fori(0, tiles // 2) as i:
        for b in range(2):
            act.wait_ge(conv_done, i * 2 + (4 + b + 1))
            act.activation(conved[:, i * 2 + b, :], acc[:, b, :], ACT.Silu).then_inc(silu_done, 1)


def mamba_in(m, z_gate, conved, dt_raw):
    nc, ins = m.nc, m.ins
    ZC = DI // 512
    with ExitStack() as c:
        sb = lambda n, s, d=F32: c.enter_context(nc.sbuf_tensor(n, s, d))
        sem = lambda n: m.sem(c, n)
        h = sb("ssm_h", [P, DT, SEQ])
        acc = sb("ssm_acc", [P, 2, SEQ])
        w_dt = sb("ssm_w_dt", [P, DT, HEADS])
        scaled = conved[:, 0:TT * 2, :].rearrange("p (t a) n -> p t (a n)", t=TT)
        norm = NormTurn(m, c, "ssm_norm", m.resid, scaled, h, lambda k: m.col("pre_norm0", k), TT, D, m.banks[0:2])
        z_done, z_read = sem("ssm_z_done"), sem("ssm_z_read")
        conv_done, silu_done = sem("ssm_conv_done"), sem("ssm_silu_done")
        dt_done, dt_loaded = sem("ssm_dt_done"), sem("ssm_dt_loaded")
        u0 = m.unit
        u1 = u0 + 4 * ZC
        block = c.enter_context(nc.Block())

        @block.sync
        def _(sp):
            sp.dma_start(w_dt[:, :, :], ins["ssm_w_dt"]).then_inc(dt_loaded, 16)
            stream_weights(m, sp, 4 * ZC + CM_T)

        @block.tensor
        def _(pe):
            norm.tensor(pe)
            pe.wait_ge(norm.turned_ready, DT)

            def before_bank(ch, t):
                if ch >= 2:
                    pe.wait_ge(z_read, 4 * (ch - 2) + t + 1)

            tokens_out(m, pe, ZC, DT, h, TT, z_done, before_bank, lambda ch, t: m.banks[4 * (ch % 2) + t])
            pe.wait_ge(z_read, 4 * ZC)
            columns_out(m, pe, CM_T, h, SEQ, conv_done, 1, m.banks[0:4])
            pe.wait_ge(dt_loaded, 16)
            for t in range(TT):
                for k in range(DT):
                    mm = pe.matmul(m.banks[4][:, t * HEADS:(t + 1) * HEADS], h[:, k, t * P:(t + 1) * P],
                                   w_dt[:, k, :], start=(k == 0), stop=(k == DT - 1))
            mm.then_inc(dt_done, 1)

        @block.vector
        def _(dve):
            step = m.steps(dve, m.dve_step)
            norm.vector(dve, step)
            convolve(m, dve, step, CM_T, u1, "ssm_conv_w", "ssm_conv_b", acc, silu_done, conv_done)
            m.keep(step)

        @block.scalar
        def _(act):
            norm.scalar_rstd(act)
            norm.scalar_turned(act)
            for ch in range(ZC):
                for t in range(TT):
                    wait_tokens(m, act, u0, DT, TT, z_done, ch, t)
                    act.activation(z_gate[:, t, ch * 512:(ch + 1) * 512], m.banks[4 * (ch % 2) + t][:, :],
                                   ACT.Silu).then_inc(z_read, 1)
            silu_convolved(act, CM_T, conved, acc, silu_done, conv_done)
            act.wait_ge(dt_done, 1)
            act.activation(dt_raw[:, :, :], m.banks[4][:, 0:TT * HEADS], ACT.Copy)


def mamba_scan(m, z_gate, conved, dt_raw, xs):
    nc, ins = m.nc, m.ins
    GW = HPG * HD
    with ExitStack() as c:
        sb = lambda n, s, d=F32: c.enter_context(nc.sbuf_tensor(n, s, d))
        sem = lambda n: m.sem(c, n)
        b_tok = sb("ssm_b_tok", [P, TT, GROUPS * STATE])
        dt = sb("ssm_dt", [P, TT, HEADS])
        dt_end = sb("ssm_dt_end", [P, TT, HEADS])
        a = sb("ssm_a", [P, TT, HEADS])
        grow = sb("ssm_grow", [P, TT, HEADS])
        whole = sb("ssm_whole", [P, TT, HEADS])
        tmp = sb("ssm_tmp", [P, 3, TT * HEADS])
        rows = sb("ssm_rows", [P, 3, HEADS])
        b_tiles = conved[:, XS_T:XS_T + BC_T, :]
        c_tiles = conved[:, XS_T + BC_T:, :]
        every = lambda ap: ap.rearrange("p (o h) -> p o h", o=1).broadcast_to([P, TT, HEADS])

        with ExitStack() as cb:
            sem1 = lambda n: m.sem(cb, n)
            rows_loaded, turned, by_act, by_dve = sem1("ssm_rows_loaded"), sem1("ssm_turned"), sem1("ssm_by_act"), sem1("ssm_by_dve")
            dve_dt, act_dt, pe_dt = sem1("ssm_dve_dt"), sem1("ssm_act_dt"), sem1("ssm_pe_dt")
            block = cb.enter_context(nc.Block())
            N_TURN = XS_T + BC_T

            def place(j):
                dst = xs if j < XS_T else b_tok
                jj = j if j < XS_T else j - XS_T
                return dst[:, :, jj * P:(jj + 1) * P]

            @block.sync
            def _(sp):
                for n, name in enumerate(("ssm_dt_bias", "ssm_a_log", "ssm_d")):
                    sp.dma_start(rows[:, n, :], m.row(name, HEADS)).then_inc(rows_loaded, 16)

            @block.tensor
            def _(pe):
                for j in range(N_TURN):
                    if j >= 4:
                        pe.wait_ge(by_act if j % 2 else by_dve, (j - 4) // 2 + 1)
                    for t in range(TT):
                        mm = pe.transpose(m.banks[j % 4][:, t * P:(t + 1) * P], conved[:, j, t * P:(t + 1) * P],
                                          m.ident[:, :])
                    mm.then_inc(turned, 1)
                pe.wait_ge(dve_dt, 3)
                pe.matmul(m.banks[4][:, 0:P], m.upto[:, :], a[:, :, :].rearrange("p t h -> p (t h)"),
                          start=True, stop=True)
                pe.matmul(m.banks[4][:, P:2 * P], m.ones[:, :], a[:, :, :].rearrange("p t h -> p (t h)"),
                          start=True, stop=True).then_inc(pe_dt, 1)

            @block.vector
            def _(dve):
                step = m.steps(dve, m.dve_step)
                dve.wait_ge(rows_loaded, 48)
                dve.tensor_tensor(dt[:, :, :], dt_raw[:, :, :], every(rows[:, 0, :]), ALU.add).then_inc(dve_dt, 1)
                dve.wait_ge(act_dt, 1)
                step(dve.scalar_tensor_tensor(dt[:, :, :], dt[:, :, :], 0.0,
                                              tmp[:, 0, :].rearrange("p (t h) -> p t h", t=TT), ALU.max, ALU.add))
                dve.scalar_tensor_tensor(a[:, :, :], dt[:, :, :], -1.0, every(rows[:, 1, :]), ALU.mult, ALU.mult)\
                   .then_inc(dve_dt, 2)
                for j in range(0, N_TURN, 2):
                    dve.wait_ge(turned, j + 1)
                    dve.tensor_copy(place(j), m.banks[j % 4][:, :].rearrange("p (t n) -> p t n", t=TT))\
                       .then_inc(by_dve, 1)
                dve.wait_ge(act_dt, 2)
                dve.tensor_tensor(tmp[:, 2, :], m.banks[4][:, P:2 * P], tmp[:, 1, :], ALU.subtract).then_inc(dve_dt, 1)
                dve.wait_ge(act_dt, 3)
                step(dve.tensor_tensor(dt_end[:, :, :], dt[:, :, :], dt_end[:, :, :], ALU.mult))
                m.keep(step)

            @block.scalar
            def _(act):
                step = m.steps(act, m.act_step)
                act.wait_ge(dve_dt, 1)
                u = tmp[:, 0, :]
                step(act.activation(u, dt[:, :, :].rearrange("p t h -> p (t h)"), ACT.Abs))
                step(act.activation(u, u, ACT.Exp, scale=-1.0))
                act.activation(rows[:, 1, :], rows[:, 1, :], ACT.Exp)
                act.activation(u, u, ACT.Ln, bias=1.0).then_inc(act_dt, 1)
                for j in range(1, N_TURN, 2):
                    act.wait_ge(turned, j + 1)
                    act.activation(place(j), m.banks[j % 4][:, :].rearrange("p (t n) -> p t n", t=TT), ACT.Copy)\
                       .then_inc(by_act, 1)
                act.wait_ge(pe_dt, 1)
                act.activation(grow[:, :, :].rearrange("p t h -> p (t h)"), m.banks[4][:, 0:P], ACT.Exp)
                act.activation(whole[:, :, :].rearrange("p t h -> p (t h)"), m.banks[4][:, P:2 * P], ACT.Exp)
                act.activation(tmp[:, 1, :], m.banks[4][:, 0:P], ACT.Copy).then_inc(act_dt, 1)
                act.wait_ge(dve_dt, 4)
                act.activation(dt_end[:, :, :].rearrange("p t h -> p (t h)"), tmp[:, 2, :], ACT.Exp).then_inc(act_dt, 1)
                m.keep(step)

        x_dt = conved[:, 0:8, :].rearrange("p (b a) n -> p b (a n)", b=2)
        x_end = conved[:, 8:16, :].rearrange("p (b a) n -> p b (a n)", b=2)
        cut = sb("ssm_cut", [P, 2, HPG, P])
        decay = sb("ssm_decay", [P, 2, HPG, P])
        cb_low = sb("ssm_cb_low", [P, 2, P])
        mix = sb("ssm_mix", [P, 2, HPG, P])
        state = sb("ssm_state", [P, GROUPS, GW])
        part = sb("ssm_part", [P, 2, GW])
        units = [(ch, g) for ch in range(TT) for g in range(GROUPS)]
        N = len(units)
        with ExitStack() as cb:
            sem1 = lambda n: m.sem(cb, n)
            cut_ready, seg_done, decay_ready = sem1("ssm_cut_ready"), sem1("ssm_seg_done"), sem1("ssm_decay_ready")
            mix_ready, y_done, y_read, state_ready = sem1("ssm_mix_ready"), sem1("ssm_y_done"), sem1("ssm_y_read"), sem1("ssm_state_ready")
            cb_done, xdt_ready, xend_ready, skip_ready = sem1("ssm_cb_done"), sem1("ssm_xdt_ready"), sem1("ssm_xend_ready"), sem1("ssm_skip_ready")
            block = cb.enter_context(nc.Block())
            heads = lambda ap: ap.rearrange("p (h d) -> p h d", d=HD)
            per_head = lambda ap, n: ap.rearrange("p (h o) -> p h o", o=1).broadcast_to([P, n, HD])

            @block.gpsimd
            def _(pool):
                for i, (ch, g) in enumerate(units):
                    if g == 0:
                        if ch >= 2:
                            pool.wait_ge(y_done, GROUPS * (ch - 1))
                        pool.tensor_tensor(heads(x_end[:, ch % 2, :]), heads(xs[:, ch, :]),
                                           per_head(dt_end[:, ch, :], HEADS), ALU.mult).then_inc(xend_ready, 1)
                    if i >= 2:
                        pool.wait_ge(seg_done, i - 1)
                    pool.tensor_tensor(cut[:, i % 2, :, :],
                                       m.upto[:, :].rearrange("p (o l) -> p o l", o=1).broadcast_to([P, HPG, P]),
                                       a[:, ch, g * HPG:(g + 1) * HPG].rearrange("p (h o) -> p h o", o=1)
                                       .broadcast_to([P, HPG, P]), ALU.mult).then_inc(cut_ready, 1)
                    if g == 0:
                        pool.wait_ge(xdt_ready, ch + 1)
                        pool.wait_ge(xend_ready, ch + 1)
                        pool.tensor_tensor(heads(xs[:, ch, :]), heads(xs[:, ch, :]), per_head(rows[:, 2, :], HEADS),
                                           ALU.mult).then_inc(skip_ready, 1)

            @block.tensor
            def _(pe):
                for i in range(N + 1):
                    if i < N:
                        ch, g = units[i]
                        pe.wait_ge(cut_ready, i + 1)
                        if i >= 2:
                            pe.wait_ge(decay_ready, i - 1)
                            pe.wait_ge(mix_ready, i - 1)
                        pe.matmul(m.banks[i % 2][:, :], m.after[:, :],
                                  cut[:, i % 2, :, :].rearrange("p h l -> p (h l)"), start=True, stop=True)\
                          .then_inc(seg_done, 1)
                        at = slice(ch * P, (ch + 1) * P)
                        pe.matmul(m.banks[2 + i % 2][:, 0:P], b_tiles[:, g, at], c_tiles[:, g, at],
                                  start=True, stop=True).then_inc(cb_done, 1)
                    if i >= 1:
                        j = i - 1
                        ch, g = units[j]
                        at = slice(ch * P, (ch + 1) * P)
                        yb, sbk = m.banks[4 + j % 2], m.banks[6 + j % 2]
                        pe.wait_ge(mix_ready, j + 1)
                        pe.wait_ge(xdt_ready, ch + 1)
                        pe.wait_ge(xend_ready, ch + 1)
                        if j >= 2:
                            pe.wait_ge(y_read, j - 1)
                            pe.wait_ge(state_ready, j - 1)
                        for r in range(HPG):
                            h0 = (g * HPG + r) * HD
                            pe.matmul(yb[:, r * HD:(r + 1) * HD], mix[:, j % 2, r, :], x_dt[:, ch % 2, h0:h0 + HD],
                                      start=True, stop=True)
                        if ch > 0:
                            pe.matmul(yb[:, GW:2 * GW], c_tiles[:, g, at], state[:, g, :], start=True, stop=True)
                        pe.matmul(sbk[:, 0:GW], b_tok[:, ch, g * STATE:(g + 1) * STATE],
                                  x_end[:, ch % 2, g * GW:(g + 1) * GW], start=True, stop=True).then_inc(y_done, 1)

            @block.scalar
            def _(act):
                for i in range(N):
                    act.wait_ge(seg_done, i + 1)
                    if i >= 2:
                        act.wait_ge(mix_ready, i - 1)
                    act.activation(decay[:, i % 2, :, :].rearrange("p h l -> p (h l)"), m.banks[i % 2][:, :],
                                   ACT.Exp).then_inc(decay_ready, 1)

            @block.vector
            def _(dve):
                step = m.steps(dve, m.dve_step)
                for i in range(N + 1):
                    if i < N:
                        ch, g = units[i]
                        if g == 0:
                            if ch >= 2:
                                dve.wait_ge(y_done, GROUPS * (ch - 1))
                            dve.tensor_tensor(heads(x_dt[:, ch % 2, :]), heads(xs[:, ch, :]),
                                              per_head(dt[:, ch, :], HEADS), ALU.mult).then_inc(xdt_ready, 1)
                        dve.wait_ge(cb_done, i + 1)
                        step(dve.tensor_tensor(cb_low[:, i % 2, :], m.banks[2 + i % 2][:, 0:P], m.upto[:, :], ALU.mult))
                        dve.wait_ge(decay_ready, i + 1)
                        if i >= 2:
                            dve.wait_ge(y_done, i - 1)
                        dve.tensor_tensor(mix[:, i % 2, :, :], decay[:, i % 2, :, :],
                                          cb_low[:, i % 2, :].rearrange("p (o l) -> p o l", o=1)
                                          .broadcast_to([P, HPG, P]), ALU.mult).then_inc(mix_ready, 1)
                    if i >= 1:
                        j = i - 1
                        ch, g = units[j]
                        yb, sbk = m.banks[4 + j % 2], m.banks[6 + j % 2]
                        here = slice(g * GW, (g + 1) * GW)
                        y = part[:, j % 2, :]
                        dve.wait_ge(y_done, j + 1)
                        dve.wait_ge(skip_ready, ch + 1)
                        if ch > 0:
                            step(dve.tensor_tensor(heads(y), heads(yb[:, GW:2 * GW]),
                                                   per_head(grow[:, ch, g * HPG:(g + 1) * HPG], HPG), ALU.mult))
                            step(dve.tensor_tensor(y, y, xs[:, ch, here], ALU.add))
                            y2 = y
                        else:
                            y2 = xs[:, ch, here]
                        dve.tensor_tensor(y, yb[:, 0:GW], y2, ALU.add).then_inc(y_read, 1)
                        if ch == 0:
                            dve.tensor_copy(state[:, g, :], sbk[:, 0:GW]).then_inc(state_ready, 1)
                        else:
                            step(dve.tensor_tensor(heads(state[:, g, :]), heads(state[:, g, :]),
                                                   per_head(whole[:, ch, g * HPG:(g + 1) * HPG], HPG), ALU.mult))
                            dve.tensor_tensor(state[:, g, :], state[:, g, :], sbk[:, 0:GW], ALU.add)\
                               .then_inc(state_ready, 1)
                        dve.wait_ge(y_read, j + 1)
                        dve.tensor_tensor(z_gate[:, ch, here], z_gate[:, ch, here], y, ALU.mult)
                m.keep(step)


def mamba_out(m, y, scaled_tiles, turned):
    nc, ins = m.nc, m.ins
    with ExitStack() as c:
        scaled = scaled_tiles.rearrange("p (t a) n -> p t (a n)", t=TT)
        norm = NormTurn(m, c, "ssm_gnorm", y, scaled, turned, lambda k: m.col("ssm_gate_norm", k), TT, DI, m.banks[0:2])
        project_and_add(m, c, "ssm_o", norm, turned, DI // P, y[:, :, 0:D], "post_norm0")


def project_and_add(m, c, name, norm, turned, kt, y, gain, load=None):
    nc = m.nc
    sem = lambda n: m.sem(c, f"{name}_{n}")
    out_done, copied = sem("out_done"), sem("copied")
    if gain:
        gain_row = c.enter_context(nc.sbuf_tensor(name + "_gain", [P, D], F32))
        gain_loaded = sem("gain_loaded")
        post = PostNorm(m, c, name + "_post", y, gain_row, gain_loaded)
    u0 = m.unit
    block = c.enter_context(nc.Block())

    @block.sync
    def _(sp):
        if load:
            load(sp)
        if gain:
            sp.dma_start(gain_row[:, :], m.row(gain, D)).then_inc(gain_loaded, 16)
        stream_weights(m, sp, 2 * kt // 2)

    @block.tensor
    def _(pe):
        if norm:
            norm.tensor(pe)
            pe.wait_ge(norm.turned_ready, kt)
        tokens_out(m, pe, 2, kt, turned, TT, out_done, lambda ch, t: None, lambda ch, t: m.banks[(4 * ch + t + 2) % 8])

    @block.vector
    def _(dve):
        step = m.steps(dve, m.dve_step)
        if norm:
            norm.vector(dve, step)
        if gain:
            dve.wait_ge(copied, 2 * TT)
            post.vector(dve, step)
        else:
            for ch in range(2):
                for t in range(TT):
                    wait_tokens(m, dve, u0, kt, TT, out_done, ch, t)
                    here = m.resid[:, t, ch * 512:(ch + 1) * 512]
                    dve.tensor_tensor(here, here, m.banks[(4 * ch + t + 2) % 8][:, :], ALU.add)
        m.keep(step)

    @block.scalar
    def _(act):
        if norm:
            norm.scalar_rstd(act)
            norm.scalar_turned(act)
        if gain:
            for ch in range(2):
                for t in range(TT):
                    wait_tokens(m, act, u0, kt, TT, out_done, ch, t)
                    act.activation(y[:, t, ch * 512:(ch + 1) * 512], m.banks[(4 * ch + t + 2) % 8][:, :], ACT.Copy)\
                       .then_inc(copied, 1)
            post.scalar(act)



class PlainTurn:

    def __init__(self, m, c, name, src, turned, tiles, width, banks):
        self.m, self.src, self.turned, self.tiles, self.width, self.banks = m, src, turned, tiles, width, banks
        self.turned_in_bank = m.sem(c, name + "_bank")
        self.turned_ready = m.sem(c, name + "_turned")

    def vector(self, dve, step):
        pass

    def scalar_rstd(self, act):
        pass

    def tensor(self, pe):
        for k in range(self.width // P):
            if k >= 2:
                pe.wait_ge(self.turned_ready, k - 1)
            for t in range(self.tiles):
                mm = pe.transpose(self.banks[k % 2][:, t * P:(t + 1) * P], self.src[:, t, k * P:(k + 1) * P],
                                  self.m.ident[:, :])
            mm.then_inc(self.turned_in_bank, 1)

    def scalar_turned(self, act):
        for k in range(self.width // P):
            act.wait_ge(self.turned_in_bank, k + 1)
            act.activation(self.turned[:, k, :], self.banks[k % 2][:, 0:self.tiles * P], ACT.Copy)\
               .then_inc(self.turned_ready, 1)


def attention(m):
    nc, ins = m.nc, m.ins
    with ExitStack() as c:
        sb = lambda n, s, d=F32: c.enter_context(nc.sbuf_tensor(n, s, d))
        qk = sb("att_qk", [P, TT, QW + KVW])
        v = sb("att_v", [P, TT, KVW])
        gate = sb("att_gate", [P, TT, QW])
        attention_in(m, qk, v, gate)
        turned = sb("att_turned", [P, (QW + KVW) // P, SEQ])
        attention_core(m, qk, v, gate, turned)
        with ExitStack() as c2:
            turn = PlainTurn(m, c2, "att_oturn", gate, turned, TT, QW, m.banks[0:2])
            project_and_add(m, c2, "att_o", turn, turned, DT, qk[:, :, 0:D], "post_norm1")


def attention_in(m, qk, v, gate):
    nc, ins = m.nc, m.ins
    import math
    with ExitStack() as c:
        sb = lambda n, s, d=F32: c.enter_context(nc.sbuf_tensor(n, s, d))
        sem = lambda n: m.sem(c, n)
        h = sb("att_h", [P, DT, SEQ])
        scaled = sb("att_scaled", [P, TT, D])
        norm = NormTurn(m, c, "att_norm", m.resid, scaled, h, lambda k: m.col("pre_norm1", k), TT, D, m.banks[0:2])
        pos_i = sb("att_pos_i", [P, TT], I32)
        pos = sb("att_pos", [P, TT])
        freq = sb("att_freq", [P, HALF])
        ang = sb("att_ang", [P, 5, TT, HALF])
        rot = sb("att_rot", [P, 4, TT, QH + KVH, HALF])
        done, read, pos_loaded, sin_ready, ang_ready = (sem("att_in_done"), sem("att_in_read"), sem("att_pos_loaded"),
                                                        sem("att_sin_ready"), sem("att_ang_ready"))
        u0 = m.unit
        CH = 5
        block = c.enter_context(nc.Block())

        @block.sync
        def _(sp):
            sp.dma_start(pos_i[:, :], ins["positions"]).then_inc(pos_loaded, 16)
            stream_weights(m, sp, CH * DT // 2)

        @block.tensor
        def _(pe):
            norm.tensor(pe)
            pe.wait_ge(norm.turned_ready, DT)

            def before_bank(ch, t):
                if ch >= 2:
                    pe.wait_ge(read, TT * (ch - 2) + t + 1)

            tokens_out(m, pe, CH, DT, h, TT, done, before_bank, lambda ch, t: m.banks[4 * (ch % 2) + t])

        @block.scalar
        def _(act):
            norm.scalar_rstd(act)
            norm.scalar_turned(act)
            act.wait_ge(ang_ready, 1)
            act.activation(ang[:, 3:5, :, :], ang[:, 1:3, :, :], ACT.Sin).then_inc(sin_ready, 1)
            for ch in range(CH):
                for t in range(TT):
                    wait_tokens(m, act, u0, DT, TT, done, ch, t)
                    bank = m.banks[4 * (ch % 2) + t]
                    if ch < 2:
                        act.activation(qk[:, t, ch * 512:(ch + 1) * 512], bank[:, :], ACT.Copy).then_inc(read, 1)
                    elif ch == 2:
                        act.activation(qk[:, t, QW:QW + KVW], bank[:, 0:KVW], ACT.Copy)
                        act.activation(v[:, t, :], bank[:, KVW:2 * KVW], ACT.Copy).then_inc(read, 1)
                    else:
                        act.activation(gate[:, t, (ch - 3) * 512:(ch - 2) * 512], bank[:, :], ACT.Silu)\
                           .then_inc(read, 1)

        @block.vector
        def _(dve):
            step = m.steps(dve, m.dve_step)
            norm.vector(dve, step)
            for j in range(HALF):
                dve.memset(freq[:, j:j + 1], THETA ** (-2.0 * j / ROPE))
            dve.wait_ge(pos_loaded, 16)
            step(dve.tensor_copy(pos[:, :], pos_i[:, :]))
            x, turns = ang[:, 0, :, :], ang[:, 2, :, :]
            step(dve.tensor_tensor(x, pos[:, :].rearrange("p (t o) -> p t o", o=1).broadcast_to([P, TT, HALF]),
                                   freq[:, :].rearrange("p (o j) -> p o j", o=1).broadcast_to([P, TT, HALF]),
                                   ALU.mult))
            big = 1.5 * 2.0 ** 23
            step(dve.tensor_scalar(turns, x, 1.0 / (2 * math.pi), big, ALU.mult, ALU.add))
            step(dve.tensor_scalar(turns, turns, big, None, ALU.subtract))
            c1 = 6.28125
            c2 = round((2 * math.pi - c1) * 2.0 ** 19) / 2.0 ** 19
            c3 = 2 * math.pi - c1 - c2
            for part in (c1, c2, c3):
                step(dve.scalar_tensor_tensor(x, turns, -part, x, ALU.mult, ALU.add))
            step(dve.tensor_scalar(ang[:, 1, :, :], x, 3.1415925, -3.1415925, ALU.min, ALU.max))
            step(dve.tensor_scalar(ang[:, 2, :, :], ang[:, 1, :, :], -1.0, None, ALU.mult))
            step(dve.tensor_tensor(ang[:, 2, :, :], ang[:, 2, :, :], ang[:, 1, :, :], ALU.min))
            dve.tensor_scalar(ang[:, 2, :, :], ang[:, 2, :, :], math.pi / 2, None, ALU.add).then_inc(ang_ready, 1)
            dve.wait_ge(sin_ready, 1)
            dve.wait_ge(read, 3 * TT)
            n = QH + KVH
            for t in range(TT):
                heads = qk[:, t, :].rearrange("p (h d) -> p h d", d=AD)
                lo, hi = heads[:, :, 0:HALF], heads[:, :, HALF:ROPE]
                every = lambda ap: ap.rearrange("p (o j) -> p o j", o=1).broadcast_to([P, n, HALF])
                sin, cos = every(ang[:, 3, t, :]), every(ang[:, 4, t, :])
                dve.tensor_tensor(rot[:, 0, t, :, :], lo, cos, ALU.mult)
                dve.tensor_tensor(rot[:, 1, t, :, :], hi, sin, ALU.mult)
                dve.tensor_tensor(rot[:, 2, t, :, :], hi, cos, ALU.mult)
                step(dve.tensor_tensor(rot[:, 3, t, :, :], lo, sin, ALU.mult))
                dve.tensor_tensor(lo, rot[:, 0, t, :, :], rot[:, 1, t, :, :], ALU.subtract)
                dve.tensor_tensor(hi, rot[:, 2, t, :, :], rot[:, 3, t, :, :], ALU.add)
            m.keep(step)


def attention_core(m, qk, v, gate, turned):
    nc, ins = m.nc, m.ins
    NQ = QW // P
    with ExitStack() as c:
        sb = lambda n, s, d=F32: c.enter_context(nc.sbuf_tensor(n, s, d))
        sem = lambda n: m.sem(c, n)
        mask = sb("att_mask", [P, 2 * P])
        sinks = sb("att_sinks", [P, QH])
        s = sb("att_s", [P, 2, 4, 2 * P])
        p = sb("att_p", [P, 2, 4, 2 * P])
        pt = sb("att_pt", [P, 2, 4, 2 * P])
        stat = sb("att_stat", [P, 2, 8, 4])
        rden = sb("att_rden", [P, 4, 4])
        o = sb("att_ov", [P, 2, 4 * AD])
        sink_loaded, mask_made, turn_done, turn_read = (sem("att_sink_loaded"), sem("att_mask_made"),
                                                        sem("att_turn_done"), sem("att_turn_read"))
        scores_done, stat_ready, exp_done, pt_done, pt_ready, pv_done, out_ready = (
            sem("att_scores_done"), sem("att_stat_ready"), sem("att_exp_done"), sem("att_pt_done"),
            sem("att_pt_ready"), sem("att_pv_done"), sem("att_out_ready"))
        units = [(n, jj) for n in range(TT) for jj in range(4)]
        N = len(units)
        NT = (QW + KVW) // P
        lo_of = lambda n: P if n == 0 else 0
        block = c.enter_context(nc.Block())

        @block.sync
        def _(sp):
            sp.dma_start(sinks[:, :], m.row("att_sinks", QH)).then_inc(sink_loaded, 16)

        @block.gpsimd
        def _(pool):
            pool.memset(mask[:, :], 0.0).then_inc(mask_made, 1)
            pool.wait_ge(mask_made, 1)
            pool.affine_select(out=mask[:, 0:P], in_=mask[:, 0:P], compare_op=ALU.is_gt, fill=-1e30, base=0,
                               pattern=[[1, P]], channel_multiplier=-1)
            pool.affine_select(out=mask[:, P:], in_=mask[:, P:], compare_op=ALU.is_ge, fill=-1e30, base=0,
                               pattern=[[-1, P]], channel_multiplier=1).then_inc(mask_made, 1)

        @block.tensor
        def _(pe):
            for j in range(NT):
                if j >= 8:
                    pe.wait_ge(turn_read, j - 7)
                for t in range(TT):
                    mm = pe.transpose(m.banks[j % 8][:, t * P:(t + 1) * P], qk[:, t, j * P:(j + 1) * P], m.ident[:, :])
                mm.then_inc(turn_done, 1)
            pe.wait_ge(turn_read, NT)
            for i in range(N + 2):
                if i < N:
                    n, jj = units[i]
                    if i >= 2:
                        pe.wait_ge(stat_ready, 2 * (i - 1))
                    lo = lo_of(n)
                    for x in range(2):
                        j = 2 * jj + x
                        for b in range(2):
                            part = slice(64 * b, 64 * b + 64)
                            mm = pe.matmul(m.banks[2 * (i % 2) + b][:, x * 256 + lo:(x + 1) * 256],
                                           turned[part, j, n * P:(n + 1) * P],
                                           turned[part, NQ + j // 4, (n - 1) * P + lo:(n + 1) * P],
                                           start=True, stop=True)
                    mm.then_inc(scores_done, 1)
                if 1 <= i <= N:
                    u = i - 1
                    n, jj = units[u]
                    pe.wait_ge(exp_done, u + 1)
                    if u >= 1:
                        pe.wait_ge(pt_ready, u)
                    halves = (1,) if n == 0 else (0, 1)
                    for half in halves:
                        for q in range(4):
                            mm = pe.transpose(m.banks[4 + half][:, q * P:(q + 1) * P],
                                              p[:, u % 2, q, half * P:(half + 1) * P], m.ident[:, :])
                    mm.then_inc(pt_done, 1)
                if i >= 2:
                    u = i - 2
                    n, jj = units[u]
                    pe.wait_ge(pt_ready, u + 1)
                    if u >= 2:
                        pe.wait_ge(out_ready, u - 1)
                    halves = (1,) if n == 0 else (0, 1)
                    for q in range(4):
                        x, b = q // 2, q % 2
                        kv = 2 * ((2 * jj + x) // 4) + b
                        for half in halves:
                            mm = pe.matmul(m.banks[6 + u % 2][:, q * AD:(q + 1) * AD],
                                           pt[:, u % 2, q, half * P:(half + 1) * P],
                                           v[:, n - 1 + half, kv * AD:(kv + 1) * AD],
                                           start=(half == halves[0]), stop=(half == 1))
                    mm.then_inc(pv_done, 1)

        @block.vector
        def _(dve):
            step = m.steps(dve, m.dve_step)
            dve.wait_ge(sink_loaded, 16)
            dve.wait_ge(mask_made, 2)
            for i in range(N + 2):
                if i < N:
                    n, jj = units[i]
                    lo = lo_of(n)
                    w = 2 * P - lo
                    st = stat[:, i % 2, :, :]
                    dve.wait_ge(scores_done, i + 1)
                    if i >= 2:
                        dve.wait_ge(exp_done, i - 1)
                    for b in range(2):
                        bank = m.banks[2 * (i % 2) + b][:, :].rearrange("p (x k) -> p x k", x=2)[:, :, lo:]
                        step(dve.scalar_tensor_tensor(
                            s[:, i % 2, b:4:2, lo:], bank, AD ** -0.5,
                            mask[:, lo:].rearrange("p (o k) -> p o k", o=1).broadcast_to([P, 2, w]),
                            ALU.mult, ALU.add))
                    step(dve.tensor_reduce(st[:, 0, :], s[:, i % 2, :, lo:], AX.X, ALU.max))
                    step(dve.tensor_tensor(st[:, 0, :], st[:, 0, :], sinks[:, 4 * jj:4 * jj + 4], ALU.max))
                    dve.tensor_scalar(st[:, 1, :], st[:, 0, :], -1.0, None, ALU.mult).then_inc(stat_ready, 1)
                    dve.tensor_tensor(st[:, 2, :], sinks[:, 4 * jj:4 * jj + 4], st[:, 0, :], ALU.subtract)\
                       .then_inc(stat_ready, 1)
                if i >= 2:
                    u = i - 2
                    n, jj = units[u]
                    st = stat[:, u % 2, :, :]
                    out = o[:, u % 2, :]
                    per_head = lambda ap: ap.rearrange("p (h o) -> p h o", o=1).broadcast_to([P, 4, AD])
                    dve.wait_ge(pv_done, u + 1)
                    step(dve.tensor_tensor(out.rearrange("p (h d) -> p h d", d=AD),
                                           m.banks[6 + u % 2][:, 0:4 * AD].rearrange("p (h d) -> p h d", d=AD),
                                           per_head(rden[:, u % 4, :]), ALU.mult))
                    here = gate[:, n, 4 * jj * AD:4 * (jj + 1) * AD]
                    dve.tensor_tensor(here, here, out, ALU.mult).then_inc(out_ready, 1)
                if 1 <= i <= N:
                    u = i - 1
                    st = stat[:, u % 2, :, :]
                    dve.wait_ge(exp_done, u + 1)
                    step(dve.tensor_tensor(st[:, 5, :], st[:, 3, :], st[:, 4, :], ALU.add))
                    step(dve.reciprocal(rden[:, u % 4, :], st[:, 5, :]))
            m.keep(step)

        @block.scalar
        def _(act):
            for j in range(NT):
                act.wait_ge(turn_done, j + 1)
                act.activation(turned[:, j, :], m.banks[j % 8][:, :], ACT.Copy).then_inc(turn_read, 1)
            for i in range(N + 1):
                if i < N:
                    n, jj = units[i]
                    lo = lo_of(n)
                    st = stat[:, i % 2, :, :]
                    act.wait_ge(stat_ready, 2 * (i + 1))
                    if i >= 2:
                        act.wait_ge(pt_done, i - 1)
                    for q in range(4):
                        act.activation(p[:, i % 2, q, lo:], s[:, i % 2, q, lo:], ACT.Exp, bias=st[:, 1, q:q + 1],
                                       accum_out=st[:, 3, q:q + 1])
                    act.activation(st[:, 4, :], st[:, 2, :], ACT.Exp).then_inc(exp_done, 1)
                if i >= 1:
                    u = i - 1
                    n, jj = units[u]
                    act.wait_ge(pt_done, u + 1)
                    if u >= 2:
                        act.wait_ge(pv_done, u - 1)
                    halves = (1,) if n == 0 else (0, 1)
                    for half in halves:
                        cp = act.activation(pt[:, u % 2, :, half * P:(half + 1) * P],
                                            m.banks[4 + half][:, :].rearrange("p (q k) -> p q k", q=4), ACT.Copy)
                    cp.then_inc(pt_ready, 1)



HC_T = 3 * GH + 2 * MH


def hybrid(m):
    nc = m.nc
    with ExitStack() as c:
        sb = lambda n, s, d=F32: c.enter_context(nc.sbuf_tensor(n, s, d))
        conved = sb("hyb_conved", [P, HC_T, SEQ])
        gate = sb("hyb_gate", [P, TT, D])
        v_one = sb("hyb_v_one", [P, TT, MH, MD + 1])
        small = sb("hyb_small", [P, TT, 16])
        hybrid_in(m, conved, gate, v_one, small)
        mixed = sb("hyb_mixed", [P, TT, GH + MH, GD])
        with ExitStack() as c2:
            delta_net(m, c2, conved, mixed, small)
        with ExitStack() as c2:
            mlstm(m, c2, conved, mixed, v_one, small)
        hybrid_out(m, mixed, gate, conved)


def hybrid_in(m, conved, gate, v_one, small):
    nc, ins = m.nc, m.ins
    with ExitStack() as c:
        sb = lambda n, s, d=F32: c.enter_context(nc.sbuf_tensor(n, s, d))
        sem = lambda n: m.sem(c, n)
        h = sb("hyb_h", [P, DT, SEQ])
        scaled = sb("hyb_scaled", [P, TT, D])
        acc = sb("hyb_acc", [P, 2, SEQ])
        w_small = sb("hyb_w_small", [P, DT, 16])
        norm = NormTurn(m, c, "hyb_norm", m.resid, scaled, h, lambda k: m.col("norm_mix", k), TT, D, m.banks[0:2])
        done, read, small_loaded, small_done = (sem("hyb_in_done"), sem("hyb_in_read"), sem("hyb_small_loaded"),
                                                sem("hyb_small_done"))
        conv_done, silu_done = sem("hyb_conv_done"), sem("hyb_silu_done")
        CH = 3
        u0 = m.unit
        u1 = u0 + CH * DT // 2
        block = c.enter_context(nc.Block())

        @block.sync
        def _(sp):
            sp.dma_start(w_small[:, :, :], ins["hyb_w_small"]).then_inc(small_loaded, 16)
            stream_weights(m, sp, CH * DT // 2 + HC_T)

        @block.tensor
        def _(pe):
            norm.tensor(pe)
            pe.wait_ge(norm.turned_ready, DT)

            def before_bank(ch, t):
                if ch >= 2:
                    pe.wait_ge(read, TT * (ch - 2) + t + 1)

            tokens_out(m, pe, CH, DT, h, TT, done, before_bank, lambda ch, t: m.banks[4 * (ch % 2) + t])
            pe.wait_ge(read, TT * CH)
            columns_out(m, pe, HC_T, h, SEQ, conv_done, 1, m.banks[0:4])
            pe.wait_ge(small_loaded, 16)
            for t in range(TT):
                for k in range(DT):
                    mm = pe.matmul(m.banks[4][:, t * 16:(t + 1) * 16], h[:, k, t * P:(t + 1) * P],
                                   w_small[:, k, :], start=(k == 0), stop=(k == DT - 1))
            mm.then_inc(small_done, 1)

        @block.vector
        def _(dve):
            step = m.steps(dve, m.dve_step)
            norm.vector(dve, step)
            dve.memset(v_one[:, :, :, MD:MD + 1], 1.0)
            convolve(m, dve, step, HC_T, u1, "hyb_conv_w", None, acc, silu_done, conv_done)
            m.keep(step)

        @block.scalar
        def _(act):
            norm.scalar_rstd(act)
            norm.scalar_turned(act)
            for ch in range(CH):
                for t in range(TT):
                    wait_tokens(m, act, u0, DT, TT, done, ch, t)
                    bank = m.banks[4 * (ch % 2) + t][:, :]
                    if ch == 0:
                        act.activation(gate[:, t, 0:512], bank, ACT.Silu).then_inc(read, 1)
                    elif ch == 1:
                        act.activation(v_one[:, t, :, 0:MD], bank.rearrange("p (h d) -> p h d", h=MH), ACT.Copy)\
                           .then_inc(read, 1)
                    else:
                        act.activation(gate[:, t, 512:], bank, ACT.Sigmoid).then_inc(read, 1)
            silu_convolved(act, HC_T, conved, acc, silu_done, conv_done)
            act.wait_ge(small_done, 1)
            act.activation(small[:, :, :], m.banks[4][:, 0:TT * 16], ACT.Copy)


def spread(ap, n):
    return ap.rearrange("p (k o) -> p k o", o=1).broadcast_to([ap.shape[0], ap.shape[1], n])


def again(ap, n):
    return ap.rearrange("p (o k) -> p o k", o=1).broadcast_to([ap.shape[0], n, ap.shape[1]])


def delta_net(m, c, conved, mixed, small):
    nc, ins = m.nc, m.ins
    sb = lambda n, s, d=F32: c.enter_context(nc.sbuf_tensor(n, s, d))
    q_ch, k_ch = conved[:, 0:GH, :], conved[:, GH:2 * GH, :]
    k_tok = sb("gdn_k", [P, TT, GH, GD])
    v_tok = sb("gdn_v", [P, TT, GH, GD])
    k_in = sb("gdn_k_in", [P, TT, GH, GD])
    beta = sb("gdn_beta", [P, TT * GH])
    la = sb("gdn_la", [P, TT * GH])
    grow = sb("gdn_grow", [P, TT * GH])
    whole = sb("gdn_whole", [P, TT * GH])
    to_end = sb("gdn_to_end", [P, TT * GH])
    tmp = sb("gdn_tmp", [P, 4, TT * GH])
    rows = sb("gdn_rows", [P, 2, GH])
    flat = lambda ap: ap.rearrange("p a b -> p (a b)")

    with ExitStack() as cb:
        sem = lambda n: m.sem(cb, n)
        rows_loaded, dve_g, act_g, pe_g = sem("gdn_rows_loaded"), sem("gdn_dve_g"), sem("gdn_act_g"), sem("gdn_pe_g")
        sq_ready, sum_done, root_ready, unit_ready = sem("gdn_sq_ready"), sem("gdn_sum_done"), sem("gdn_root_ready"), sem("gdn_unit_ready")
        turned, turn_read = sem("gdn_turned"), sem("gdn_turn_read")
        square = cb.enter_context(nc.sbuf_tensor("gdn_square", [P, 2 * GH, SEQ], F32))
        eps = cb.enter_context(nc.sbuf_tensor("gdn_eps", [P, 1], F32))
        NL = 2 * GH
        block = cb.enter_context(nc.Block())

        @block.sync
        def _(sp):
            sp.dma_start(rows[:, 0, :], m.row("gdn_dt_bias", GH)).then_inc(rows_loaded, 16)
            sp.dma_start(rows[:, 1, :], m.row("gdn_a_log", GH)).then_inc(rows_loaded, 16)

        @block.tensor
        def _(pe):
            pe.wait_ge(dve_g, 3)
            pe.matmul(m.banks[6][:, 0:TT * GH], m.upto[:, :], la[:, :], start=True, stop=True)
            pe.matmul(m.banks[6][:, 16:16 + TT * GH], m.ones[:, :], la[:, :], start=True, stop=True).then_inc(pe_g, 1)
            for j in range(NL):
                pe.wait_ge(sq_ready, j + 1)
                if j >= 4:
                    pe.wait_ge(root_ready, j - 3)
                pe.matmul(m.banks[j % 4][:, :], m.ones[:, :], square[:, j, :], start=True, stop=True)\
                  .then_inc(sum_done, 1)
            for j in range(NL):
                src = 2 * GH + j if j < GH else j
                if j >= GH:
                    pe.wait_ge(unit_ready, src + 1)
                if j >= 2:
                    pe.wait_ge(turn_read, j - 1)
                for t in range(TT):
                    mm = pe.transpose(m.banks[4 + j % 2][:, t * P:(t + 1) * P], conved[:, src, t * P:(t + 1) * P],
                                      m.ident[:, :])
                mm.then_inc(turned, 1)

        @block.scalar
        def _(act):
            step = m.steps(act, m.act_step)
            for j in range(NL):
                act.activation(square[:, j, :], conved[:, j, :], ACT.Square).then_inc(sq_ready, 1)
            act.wait_ge(dve_g, 1)
            step(act.activation(tmp[:, 1, :], tmp[:, 0, :], ACT.Abs))
            act.activation(beta[:, :], small[:, :, GH:2 * GH], ACT.Sigmoid)
            step(act.activation(tmp[:, 1, :], tmp[:, 1, :], ACT.Exp, scale=-1.0))
            act.activation(rows[:, 1, :], rows[:, 1, :], ACT.Exp)
            act.activation(tmp[:, 1, :], tmp[:, 1, :], ACT.Ln, bias=1.0).then_inc(act_g, 1)
            act.wait_ge(pe_g, 1)
            act.activation(grow[:, :], m.banks[6][:, 0:TT * GH], ACT.Exp)
            act.activation(whole[:, :], m.banks[6][:, 16:16 + TT * GH], ACT.Exp)
            act.activation(tmp[:, 2, :], m.banks[6][:, 0:TT * GH], ACT.Copy).then_inc(act_g, 1)
            act.wait_ge(dve_g, 4)
            act.activation(to_end[:, :], tmp[:, 3, :], ACT.Exp).then_inc(act_g, 1)
            act.wait_ge(dve_g, 5)
            for j in range(NL):
                act.wait_ge(sum_done, j + 1)
                act.activation(square[:, j, :], m.banks[j % 4][:, :], ACT.Sqrt, bias=eps[:, 0:1]).then_inc(root_ready, 1)
            for j in range(NL):
                act.wait_ge(turned, j + 1)
                dst = v_tok if j < GH else k_tok
                act.activation(dst[:, :, j % GH, :], m.banks[4 + j % 2][:, :].rearrange("p (t n) -> p t n", t=TT),
                               ACT.Copy).then_inc(turn_read, 1)
            m.keep(step)

        @block.vector
        def _(dve):
            step = m.steps(dve, m.dve_step)
            dve.wait_ge(rows_loaded, 32)
            t3 = lambda ap: ap.rearrange("p (t h) -> p t h", t=TT)
            dve.tensor_tensor(t3(tmp[:, 0, :]), small[:, :, 0:GH], again(rows[:, 0, :], TT), ALU.add).then_inc(dve_g, 1)
            dve.wait_ge(act_g, 1)
            step(dve.scalar_tensor_tensor(tmp[:, 0, :], tmp[:, 0, :], 0.0, tmp[:, 1, :], ALU.max, ALU.add))
            dve.scalar_tensor_tensor(t3(la[:, :]), t3(tmp[:, 0, :]), -1.0, again(rows[:, 1, :], TT), ALU.mult, ALU.mult)\
               .then_inc(dve_g, 2)
            dve.wait_ge(act_g, 2)
            dve.tensor_tensor(tmp[:, 3, :], m.banks[6][:, 16:16 + TT * GH], tmp[:, 2, :], ALU.subtract).then_inc(dve_g, 1)
            dve.memset(eps[:, :], EPS).then_inc(dve_g, 1)
            for j in range(NL):
                dve.wait_ge(root_ready, j + 1)
                step(dve.reciprocal(square[:, j, :], square[:, j, :]))
                dve.tensor_tensor(conved[:, j, :], conved[:, j, :], square[:, j, :], ALU.mult).then_inc(unit_ready, 1)
            dve.wait_ge(turn_read, NL)
            dve.wait_ge(act_g, 3)
            step(dve.tensor_tensor(tmp[:, 0, :], beta[:, :], grow[:, :], ALU.mult))
            rows16 = lambda ap: ap.rearrange("p t h d -> p (t h) d")
            dve.tensor_tensor(rows16(v_tok[:, :, :, :]), rows16(v_tok[:, :, :, :]), spread(beta[:, :], GD), ALU.mult)
            step(dve.tensor_tensor(rows16(k_in[:, :, :, :]), rows16(k_tok[:, :, :, :]), spread(tmp[:, 0, :], GD), ALU.mult))
            dve.tensor_tensor(rows16(k_tok[:, :, :, :]), rows16(k_tok[:, :, :, :]), spread(to_end[:, :], GD), ALU.mult)
            m.keep(step)

    mats = lambda n: sb("gdn_" + n, [P, TT, GH * P])
    far_part, qk_t, W1, W2, X2, W3 = (mats(n) for n in ("far_part", "qk_t", "w1", "w2", "x2", "w3"))
    near_part = mixed[:, :, 0:GH, :].rearrange("p t h n -> p t (h n)")
    X1 = mixed[:, :, GH:, :].rearrange("p t h n -> p t (h n)")
    W4 = conved[:, 2 * GH:3 * GH, :]
    before = sb("gdn_before", [P, P])
    near = sb("gdn_near", [P, 4, P])
    first_level = [
        (X2, X1, [("copy", W1)]),
        (X1, X2, [("copy", W2), ("plus", W3)]),
        (W2, W1, [("plus", W4)]),
        (W3, W4, [("copy", W1)]),
        (X2, W1, [("copy", W2)]),
        (W1, X2, [("copy", W3)]),
    ]

    def next_level(L):
        return [
            (W3, L, [("copy", W1)]),
            (L, W3, [("copy", W4), ("minus", X1)]),
            (W1, W4, [("plus", X2)]),
            (X2, W2, [("copy", W1)]),
            (X1, W1, [("copy", W2)]),
            (W1, X1, [("copy", W3)]),
        ]

    inversion = first_level + next_level(near_part) + next_level(far_part)
    per4 = lambda ap: ap.rearrange("p (h n) -> p h n", h=GH)
    with ExitStack() as cb:
        sem = lambda n: m.sem(cb, n)
        made, cut_ready, exp_ready = sem("gdn_made"), sem("gdn_cut_ready"), sem("gdn_exp_ready")
        pe_done, bank_read = sem("gdn_pe_done"), sem("gdn_bank_read")
        block = cb.enter_context(nc.Block())
        blocks = lambda ap, n: ap.rearrange("p (b n) -> p b n", n=n)

        @block.gpsimd
        def _(pool):
            step = m.steps(pool, m.pool_step)
            pool.tensor_tensor(before[:, :], m.upto[:, :], m.ident[:, :], ALU.subtract)
            step(pool.memset(near[:, :, :], 1.0))
            for n, size in enumerate((8, 32)):
                step(pool.affine_select(out=blocks(near[:, n, :], size), in_=blocks(near[:, n, :], size),
                                        compare_op=ALU.is_ge, fill=0.0, base=0,
                                        pattern=[[-size, P // size], [0, size]], channel_multiplier=1))
                step(pool.affine_select(out=blocks(near[:, n, :], size), in_=blocks(near[:, n, :], size),
                                        compare_op=ALU.is_ge, fill=0.0, base=size - 1,
                                        pattern=[[size, P // size], [0, size]], channel_multiplier=-1))
            pool.tensor_tensor(near[:, 2, :], near[:, 1, :], near[:, 0, :], ALU.subtract)
            pool.tensor_tensor(near[:, 3, :], near[:, 3, :], near[:, 1, :], ALU.subtract).then_inc(made, 1)
            for ch in range(TT):
                pool.tensor_tensor(per4(qk_t[:, ch, :]), again(m.upto[:, :], GH), spread(la[:, ch * GH:(ch + 1) * GH], P),
                                   ALU.mult).then_inc(cut_ready, 1)
            m.keep(step)

        @block.tensor
        def _(pe):
            def result(stage, ch):
                if stage >= 1:
                    pe.wait_ge(bank_read, TT * (stage - 1) + ch + 1)
                return m.banks[(TT * stage + ch) % 8]

            def four(bank, lhs, rhs):
                for h in range(GH):
                    mm = pe.matmul(bank[:, h * P:(h + 1) * P], lhs(h), rhs(h), start=True, stop=True)
                mm.then_inc(pe_done, 1)

            mat = lambda X, ch: (lambda h: X[:, ch, h * P:(h + 1) * P])
            chunk = lambda X, ch: (lambda h: X[:, h, ch * P:(ch + 1) * P])
            for ch in range(TT):
                pe.wait_ge(cut_ready, ch + 1)
                pe.matmul(result(0, ch)[:, :], m.after[:, :], qk_t[:, ch, :], start=True, stop=True).then_inc(pe_done, 1)
            for ch in range(TT):
                four(result(1, ch), chunk(k_ch, ch), chunk(k_ch, ch))
            for ch in range(TT):
                four(result(2, ch), chunk(k_ch, ch), chunk(q_ch, ch))
            for stage, X in ((3, W2), (4, X1)):
                for ch in range(TT):
                    bank = result(stage, ch)
                    for h in range(GH):
                        mm = pe.transpose(bank[:, h * P:(h + 1) * P], mat(X, ch)(h), m.ident[:, :])
                    mm.then_inc(pe_done, 1)
            stage = 5
            for lhs, rhs, _outs in inversion:
                for ch in range(TT):
                    four(result(stage, ch), mat(lhs, ch), mat(rhs, ch))
                stage += 1
            for ch in range(TT):
                four(result(stage, ch), lambda h: k_in[:, ch, h, :], mat(W3, ch))
            for ch in range(TT):
                four(result(stage + 1, ch), mat(W3, ch), lambda h: v_tok[:, ch, h, :])

        @block.scalar
        def _(act):
            for ch in range(TT):
                act.wait_ge(pe_done, ch + 1)
                act.activation(W1[:, ch, :], m.banks[ch][:, :], ACT.Exp).then_inc(exp_ready, 1)

        @block.vector
        def _(dve):
            step = m.steps(dve, m.dve_step)

            def result(stage, ch):
                dve.wait_ge(pe_done, TT * stage + ch + 1)
                return m.banks[(TT * stage + ch) % 8][:, :]

            dve.wait_ge(made, 1)
            for ch in range(TT):
                dve.wait_ge(exp_ready, ch + 1)
                dve.tensor_tensor(per4(W1[:, ch, :]), per4(W1[:, ch, :]), again(m.upto[:, :], GH), ALU.mult)\
                   .then_inc(bank_read, 1)
            for ch in range(TT):
                dve.wait_ge(bank_read, ch + 1)
                step(dve.tensor_tensor(W2[:, ch, :], result(1, ch), W1[:, ch, :], ALU.mult))
                dve.tensor_tensor(per4(W2[:, ch, :]), per4(W2[:, ch, :]), again(before[:, :], GH), ALU.mult)\
                   .then_inc(bank_read, 1)
            for ch in range(TT):
                dve.scalar_tensor_tensor(qk_t[:, ch, :], result(2, ch), GD ** -0.5, W1[:, ch, :], ALU.mult, ALU.mult)\
                   .then_inc(bank_read, 1)
            for ch in range(TT):
                far = far_part[:, ch, :]
                step(dve.tensor_tensor(per4(far), per4(result(3, ch)), spread(beta[:, ch * GH:(ch + 1) * GH], P), ALU.mult))
                dve.tensor_tensor(per4(near_part[:, ch, :]), per4(far), again(near[:, 2, :], GH), ALU.mult)
                step(dve.tensor_tensor(per4(X1[:, ch, :]), per4(far), again(near[:, 0, :], GH), ALU.mult))
                dve.tensor_tensor(per4(far), per4(far), again(near[:, 3, :], GH), ALU.mult).then_inc(bank_read, 1)
            for ch in range(TT):
                dve.tensor_copy(X2[:, ch, :], result(4, ch)).then_inc(bank_read, 1)
            stage = 5
            for _lhs, _rhs, outs in inversion:
                for ch in range(TT):
                    bank = result(stage, ch)
                    for kind, X in outs:
                        if kind == "copy":
                            last = dve.tensor_copy(X[:, ch, :], bank)
                        else:
                            last = dve.scalar_tensor_tensor(per4(X[:, ch, :]), per4(bank), 1.0 if kind == "plus" else -1.0,
                                                            again(m.ident[:, :], GH), ALU.mult, ALU.add)
                    if stage == 6:
                        last = dve.scalar_tensor_tensor(per4(X2[:, ch, :]), per4(X2[:, ch, :]), -1.0,
                                                        again(m.ident[:, :], GH), ALU.mult, ALU.add)
                    last.then_inc(bank_read, 1)
                stage += 1
            for X in (W1, W2):
                for ch in range(TT):
                    dve.tensor_copy(X[:, ch, :], result(stage, ch)).then_inc(bank_read, 1)
                stage += 1
            m.keep(step)

    w_t, u = W1, W2
    state = sb("gdn_state", [P, GH * GD])
    carry = sb("gdn_carry", [P, 2, GH * GD])
    with ExitStack() as cb:
        sem = lambda n: m.sem(cb, n)
        old_done, new_ready, new_done, state_ready, out_read = (sem("gdn_old_done"), sem("gdn_new_ready"), sem("gdn_new_done"),
                                                                sem("gdn_state_ready"), sem("gdn_out_read"))
        block = cb.enter_context(nc.Block())
        mat = lambda X, ch, h: X[:, ch, h * P:(h + 1) * P]
        head = lambda X, h: X[:, h * P:(h + 1) * P]

        @block.tensor
        def _(pe):
            for ch in range(TT):
                bw, bq, bo, bs = m.banks[4 * (ch % 2):4 * (ch % 2) + 4]
                if ch > 0:
                    pe.wait_ge(state_ready, ch)
                    if ch >= 2:
                        pe.wait_ge(out_read, ch - 1)
                    for h in range(GH):
                        pe.matmul(head(bw, h), mat(w_t, ch, h), head(state, h), start=True, stop=True)
                    for h in range(GH):
                        mm = pe.matmul(head(bq, h), q_ch[:, h, ch * P:(ch + 1) * P], head(state, h), start=True, stop=True)
                    mm.then_inc(old_done, 1)
                    pe.wait_ge(new_ready, ch)
                for h in range(GH):
                    pe.matmul(head(bo, h), mat(qk_t, ch, h), mat(u, ch, h), start=True, stop=True)
                for h in range(GH):
                    mm = pe.matmul(head(bs, h), k_tok[:, ch, h, :], mat(u, ch, h), start=True, stop=True)
                mm.then_inc(new_done, 1)

        @block.vector
        def _(dve):
            step = m.steps(dve, m.dve_step)
            for ch in range(TT):
                bw, bq, bo, bs = m.banks[4 * (ch % 2):4 * (ch % 2) + 4]
                mine = slice(ch * GH, (ch + 1) * GH)
                if ch > 0:
                    dve.wait_ge(old_done, ch)
                    dve.tensor_tensor(u[:, ch, :], u[:, ch, :], bw[:, :], ALU.subtract).then_inc(new_ready, 1)
                    old = carry[:, ch % 2, :]
                    step(dve.tensor_tensor(per4(old), per4(bq[:, :]), spread(grow[:, mine], GD), ALU.mult))
                dve.wait_ge(new_done, ch + 1)
                if ch > 0:
                    step(dve.tensor_tensor(per4(state[:, :]), per4(state[:, :]), spread(whole[:, mine], GD), ALU.mult))
                    dve.tensor_tensor(state[:, :], state[:, :], bs[:, :], ALU.add).then_inc(state_ready, 1)
                    dve.scalar_tensor_tensor(mixed[:, ch, 0:GH, :], per4(old), GD ** -0.5, per4(bo[:, :]), ALU.mult, ALU.add)\
                       .then_inc(out_read, 1)
                else:
                    dve.tensor_copy(state[:, :], bs[:, :]).then_inc(state_ready, 1)
                    dve.tensor_copy(mixed[:, ch, 0:GH, :], per4(bo[:, :])).then_inc(out_read, 1)
            m.keep(step)


def mlstm(m, c, conved, mixed, v_one, small):
    nc, ins = m.nc, m.ins
    sb = lambda n, s, d=F32: c.enter_context(nc.sbuf_tensor(n, s, d))
    q_ch, k_ch = conved[:, 3 * GH:3 * GH + MH, :], conved[:, 3 * GH + MH:, :]
    W = TT * MH
    rows = sb("mls_rows", [P, 2, MH])
    tmp = sb("mls_tmp", [P, 4, W])
    g = sb("mls_g", [P, W])
    by_head = sb("mls_by_head", [MH, 6, SEQ])
    at_start = sb("mls_at_start", [MH, TT + 1])
    last = sb("mls_last", [MH, TT])
    diag = sb("mls_diag", [MH, TT, MH])
    M_diag = sb("mls_M_diag", [MH, TT, MH, P])
    weights = sb("mls_weights", [P, 4, W])
    k_end = sb("mls_k_end", [P, TT, MH, MD])
    w_end = sb("mls_w_end", [P, W])
    G, B, MX, A1, A2, A3 = (by_head[:, n, :] for n in range(6))
    part = lambda ap, ch: ap[:, ch * P:(ch + 1) * P]
    with ExitStack() as cb:
        sem = lambda n: m.sem(cb, n)
        loaded, dve_p, act_p, pe_p, turned, turn_read = (sem("mls_loaded"), sem("mls_dve_p"), sem("mls_act_p"), sem("mls_pe_p"),
                                                        sem("mls_turned"), sem("mls_turn_read"))
        block = cb.enter_context(nc.Block())

        @block.sync
        def _(sp):
            sp.dma_start(rows[:, 0, :], m.row("mls_i_bias", MH)).then_inc(loaded, 16)
            sp.dma_start(rows[:, 1, :], m.row("mls_f_bias", MH)).then_inc(loaded, 16)

        @block.vector
        def _(dve):
            step = m.steps(dve, m.dve_step)
            t3 = lambda ap: ap.rearrange("p (t h) -> p t h", t=TT)
            dve.wait_ge(loaded, 32)
            dve.tensor_tensor(t3(tmp[:, 0, :]), small[:, :, 3 * MH:], again(rows[:, 1, :], TT), ALU.add).then_inc(dve_p, 1)
            dve.tensor_tensor(t3(g[:, :]), small[:, :, 2 * MH:3 * MH], again(rows[:, 0, :], TT), ALU.add)
            dve.wait_ge(act_p, 1)
            dve.scalar_tensor_tensor(tmp[:, 2, :], tmp[:, 0, :], 0.0, tmp[:, 1, :], ALU.min, ALU.subtract).then_inc(dve_p, 1)
            dve.wait_ge(pe_p, 1)
            step(dve.tensor_copy(tmp[:, 3, :], m.banks[0][:, 0:W]))
            dve.tensor_tensor(g[:, :], g[:, :], tmp[:, 3, :], ALU.subtract).then_inc(dve_p, 1)
            dve.wait_ge(pe_p, 2)
            step(dve.tensor_copy(G, m.banks[1][0:MH, :]))
            step(dve.tensor_copy(B, m.banks[2][0:MH, :]))
            step(dve.memset(at_start[:, 0:1], 0.0))
            for ch in range(TT):
                end = (ch + 1) * P - 1
                step(dve.tensor_tensor_scan(part(MX, ch), part(G, ch), part(G, ch), at_start[:, ch:ch + 1], ALU.max, ALU.max))
                step(dve.tensor_tensor(at_start[:, ch + 1:ch + 2], B[:, end:end + 1], MX[:, end:end + 1], ALU.add))
                dve.tensor_scalar(part(A1, ch), part(MX, ch), -1.0, at_start[:, ch:ch + 1], ALU.mult, ALU.add)
                dve.tensor_scalar(part(A3, ch), part(G, ch), MX[:, end:end + 1], None, ALU.subtract)
                dve.tensor_tensor(last[:, ch:ch + 1], at_start[:, ch:ch + 1], MX[:, end:end + 1], ALU.subtract)
                dve.tensor_tensor(M_diag[:, ch, :, :], again(part(MX, ch), MH), spread(m.ident[0:MH, 0:MH], P), ALU.mult)
            step(dve.scalar_tensor_tensor(A2, B, -1.0, MX, ALU.mult, ALU.subtract))
            dve.tensor_tensor(diag[:, :, :], spread(last[:, :], MH), again(m.ident[0:MH, 0:MH], TT), ALU.mult).then_inc(dve_p, 1)
            dve.wait_ge(act_p, 2)
            step(dve.tensor_scalar(w_end[:, :], weights[:, 2, :], MD ** -0.5, None, ALU.mult))
            dve.wait_ge(turn_read, MH)
            k16 = k_end[:, :, :, :].rearrange("p t h d -> p (t h) d")
            dve.tensor_tensor(k16, k16, spread(w_end[:, :], MD), ALU.mult)
            m.keep(step)

        @block.scalar
        def _(act):
            step = m.steps(act, m.act_step)
            act.wait_ge(dve_p, 1)
            step(act.activation(tmp[:, 1, :], tmp[:, 0, :], ACT.Abs))
            step(act.activation(tmp[:, 1, :], tmp[:, 1, :], ACT.Exp, scale=-1.0))
            act.activation(tmp[:, 1, :], tmp[:, 1, :], ACT.Ln, bias=1.0).then_inc(act_p, 1)
            for h in range(MH):
                act.wait_ge(turned, h + 1)
                act.activation(k_end[:, :, h, :], m.banks[4 + h % 2][:, :].rearrange("p (t n) -> p t n", t=TT), ACT.Copy)\
                   .then_inc(turn_read, 1)
            act.wait_ge(pe_p, 3)
            act.activation(weights[:, :, :].rearrange("p k w -> p (k w)"), m.banks[3][:, 0:4 * W], ACT.Exp).then_inc(act_p, 1)
            m.keep(step)

        @block.tensor
        def _(pe):
            for h in range(MH):
                if h >= 2:
                    pe.wait_ge(turn_read, h - 1)
                for t in range(TT):
                    mm = pe.transpose(m.banks[4 + h % 2][:, t * P:(t + 1) * P], k_ch[:, h, t * P:(t + 1) * P], m.ident[:, :])
                mm.then_inc(turned, 1)
            pe.wait_ge(dve_p, 2)
            pe.matmul(m.banks[0][:, 0:W], m.upto[:, :], tmp[:, 2, :], start=True, stop=True).then_inc(pe_p, 1)
            pe.wait_ge(dve_p, 3)
            for t in range(TT):
                pe.transpose(m.banks[1][0:MH, t * P:(t + 1) * P], g[:, t * MH:(t + 1) * MH], m.ident[:, :])
                mm = pe.transpose(m.banks[2][0:MH, t * P:(t + 1) * P], tmp[:, 3, t * MH:(t + 1) * MH], m.ident[:, :])
            mm.then_inc(pe_p, 1)
            pe.wait_ge(dve_p, 4)
            for n, rowset in enumerate((A1, A2, A3)):
                for t in range(TT):
                    pe.transpose(m.banks[3][:, n * W + t * MH:n * W + (t + 1) * MH], part(rowset, t), m.ident[0:MH, 0:MH])
            pe.matmul(m.banks[3][:, 3 * W:4 * W], m.ones[0:MH, :], diag[:, :, :].rearrange("p t h -> p (t h)"),
                      start=True, stop=True).then_inc(pe_p, 1)

    fade = sb("mls_fade", [P, TT, MH, P])
    state = sb("mls_state", [P, MH, MD + 1])
    acc = sb("mls_acc", [P, 2, MH, MD + 1])
    den = sb("mls_den", [P, 2, 3, MH])
    with ExitStack() as cb:
        sem = lambda n: m.sem(cb, n)
        m_done, gap_ready, fade_ready, low_ready, qk_done, p_ready = (sem("mls_m_done"), sem("mls_gap_ready"), sem("mls_fade_ready"),
                                                                    sem("mls_low_ready"), sem("mls_qk_done"), sem("mls_p_ready"))
        out_done, out_read, state_ready = sem("mls_out_done"), sem("mls_out_read"), sem("mls_state_ready")
        two = lambda n: m.banks[n][:, 0:2 * (MD + 1)].rearrange("p (h d) -> p h d", h=2)
        block = cb.enter_context(nc.Block())

        @block.tensor
        def _(pe):
            for ch in range(TT):
                if ch >= 2:
                    pe.wait_ge(gap_ready, ch - 1)
                pe.matmul(m.banks[ch % 2][:, :], m.ones[0:MH, :], M_diag[:, ch, :, :].rearrange("p h n -> p (h n)"),
                          start=True, stop=True).then_inc(m_done, 1)
            for ch in range(TT):
                at = slice(ch * P, (ch + 1) * P)
                pe.wait_ge(gap_ready, TT)
                if ch >= 2:
                    pe.wait_ge(p_ready, ch - 1)
                for h in range(MH):
                    mm = pe.matmul(m.banks[ch % 2][:, h * P:(h + 1) * P], k_ch[:, h, at], q_ch[:, h, at], start=True, stop=True)
                mm.then_inc(qk_done, 1)
                if ch > 0:
                    pe.wait_ge(out_read, ch)
                    pe.wait_ge(state_ready, ch)
                    for h in range(MH):
                        pe.matmul(two(4 + h // 2)[:, h % 2, :], q_ch[:, h, at], state[:, h, :], start=True, stop=True)
                for h in range(MH):
                    pe.matmul(two(6 + h // 2)[:, h % 2, :], k_end[:, ch, h, :], v_one[:, ch, h, :], start=True, stop=True)
                pe.wait_ge(p_ready, ch + 1)
                for h in range(MH):
                    mm = pe.matmul(two(2 + h // 2)[:, h % 2, :], fade[:, ch, h, :], v_one[:, ch, h, :], start=True, stop=True)
                mm.then_inc(out_done, 1)

        @block.scalar
        def _(act):
            for ch in range(TT):
                act.wait_ge(gap_ready, ch + 1)
                act.activation(fade[:, ch, :, :], fade[:, ch, :, :], ACT.Exp, scale=-1.0).then_inc(fade_ready, 1)

        @block.gpsimd
        def _(pool):
            for ch in range(TT):
                pool.wait_ge(fade_ready, ch + 1)
                pool.tensor_tensor(fade[:, ch, :, :], fade[:, ch, :, :], again(m.upto[:, :], MH), ALU.mult).then_inc(low_ready, 1)

        @block.vector
        def _(dve):
            step = m.steps(dve, m.dve_step)
            for ch in range(TT):
                dve.wait_ge(m_done, ch + 1)
                for h in range(MH):
                    col = g[:, ch * MH + h:ch * MH + h + 1]
                    gap = dve.tensor_scalar(fade[:, ch, h, :], m.banks[ch % 2][:, h * P:(h + 1) * P], col, 0.0,
                                            ALU.subtract, ALU.max)
                gap.then_inc(gap_ready, 1)
            for ch in range(TT):
                mine = slice(ch * MH, (ch + 1) * MH)
                dve.wait_ge(qk_done, ch + 1)
                dve.wait_ge(low_ready, ch + 1)
                dve.scalar_tensor_tensor(fade[:, ch, :, :], m.banks[ch % 2][:, :].rearrange("p (h n) -> p h n", h=MH),
                                         MD ** -0.5, fade[:, ch, :, :], ALU.mult, ALU.mult).then_inc(p_ready, 1)
                dve.wait_ge(out_done, ch + 1)
                a = acc[:, ch % 2, :, :]
                for x in range(2):
                    pair = slice(2 * x, 2 * x + 2)
                    if ch > 0:
                        step(dve.tensor_tensor(a[:, pair, :], two(4 + x), spread(weights[:, 0, ch * MH + 2 * x:ch * MH + 2 * x + 2], MD + 1), ALU.mult))
                        step(dve.tensor_tensor(a[:, pair, :], a[:, pair, :], two(2 + x), ALU.add))
                        step(dve.tensor_tensor(state[:, pair, :], state[:, pair, :], spread(weights[:, 3, ch * MH + 2 * x:ch * MH + 2 * x + 2], MD + 1), ALU.mult))
                        step(dve.tensor_tensor(state[:, pair, :], state[:, pair, :], two(6 + x), ALU.add))
                    else:
                        step(dve.tensor_copy(a[:, pair, :], two(2 + x)))
                        step(dve.tensor_copy(state[:, pair, :], two(6 + x)))
                dve.sem_inc(state_ready, 1)
                dve.sem_inc(out_read, 1)
                d = den[:, ch % 2, :, :]
                step(dve.tensor_scalar(d[:, 0, :], a[:, :, MD], -1.0, None, ALU.mult))
                step(dve.tensor_tensor(d[:, 0, :], d[:, 0, :], a[:, :, MD], ALU.max))
                step(dve.tensor_tensor(d[:, 1, :], d[:, 0, :], weights[:, 1, mine], ALU.max))
                step(dve.reciprocal(d[:, 2, :], d[:, 1, :]))
                dve.tensor_tensor(mixed[:, ch, GH:, :], a[:, :, 0:MD], spread(d[:, 2, :], MD), ALU.mult)
            m.keep(step)


class HeadNormTurn(PlainTurn):

    def __init__(self, m, c, name, mixed, gate, gains, gains_loaded, square, turned, banks):
        super().__init__(m, c, name, mixed.rearrange("p t h d -> p t (h d)"), turned, TT, D, banks)
        self.mixed, self.gate, self.gains, self.gains_loaded, self.square = mixed, gate, gains, gains_loaded, square
        self.stat = c.enter_context(m.nc.sbuf_tensor(name + "_stat", [P, 3, TT * (GH + MH)], F32))
        self.mean_ready, self.rstd_ready, self.done = (m.sem(c, name + x) for x in ("_mean", "_rstd", "_done"))

    def vector(self, dve, step):
        st, n = self.stat, GH + MH
        flat = lambda ap: ap.rearrange("p t h d -> p (t h) d")
        step(dve.tensor_tensor(flat(self.square), flat(self.mixed), flat(self.mixed), ALU.mult))
        step(dve.tensor_reduce(st[:, 0, :], flat(self.square), AX.X, ALU.add))
        step(dve.tensor_scalar(st[:, 1, :], st[:, 0, :], 1.0 / GD, EPS, ALU.mult, ALU.add))
        dve.reciprocal(st[:, 2, :], st[:, 1, :]).then_inc(self.mean_ready, 1)
        dve.wait_ge(self.gains_loaded, 16)
        for t in range(TT):
            step(dve.tensor_tensor(self.gate[:, t, :], self.gate[:, t, :], self.gains, ALU.mult))
        dve.wait_ge(self.rstd_ready, 1)
        for t in range(TT):
            step(dve.tensor_tensor(self.mixed[:, t, :, :], self.mixed[:, t, :, :], spread(st[:, 0, t * n:(t + 1) * n], GD), ALU.mult))
            dve.tensor_tensor(self.src[:, t, :], self.src[:, t, :], self.gate[:, t, :], ALU.mult).then_inc(self.done, 1)

    def scalar_rstd(self, act):
        act.wait_ge(self.mean_ready, 1)
        act.activation(self.stat[:, 0, :], self.stat[:, 2, :], ACT.Sqrt).then_inc(self.rstd_ready, 1)

    def tensor(self, pe):
        pe.wait_ge(self.done, TT)
        super().tensor(pe)


def hybrid_out(m, mixed, gate, conved):
    nc = m.nc
    with ExitStack() as c:
        gains = c.enter_context(nc.sbuf_tensor("hyb_gains", [P, D], F32))
        gains_loaded = m.sem(c, "hyb_gains_loaded")
        square = conved[:, 0:8, :].rearrange("p (t a) (b d) -> p t (a b) d", t=TT, d=GD)
        turn = HeadNormTurn(m, c, "hyb_hnorm", mixed[:, :, :, :], gate, gains[:, :], gains_loaded, square,
                            conved[:, 8:16, :], m.banks[0:2])
        project_and_add(m, c, "hyb_o", turn, conved[:, 8:16, :], DT, None, None,
                        load=lambda sp: sp.dma_start(gains[:, :], m.row("hyb_gains", D)).then_inc(gains_loaded, 16))



MT = MEM // P


def copy_columns(m, act, n, u0, free, dst, banks, width):
    act.sem_inc(free, RING)
    with act.Fori(0, n // RING) as i:
        for b in range(RING):
            act.wait_ge(m.w_used, i * RING + (u0 + b + 1))
            act.activation(dst[:, i * RING + b, :], banks[b][:, 0:width], ACT.Copy).then_inc(free, 1)


def cross_attention(m):
    nc = m.nc
    with ExitStack() as c:
        sb = lambda n, s, d=F32: c.enter_context(nc.sbuf_tensor(n, s, d))
        q_ch = sb("xa_q", [P, DT, SEQ])
        k_ch = sb("xa_k", [P, DT, MEM])
        v_tok = sb("xa_v", [P, MT, D])
        cross_in(m, q_ch, k_ch, v_tok)
        o_ch = sb("xa_o", [P, DT, SEQ])
        cross_core(m, q_ch, k_ch, v_tok, o_ch)
        with ExitStack() as c2:
            project_and_add(m, c2, "xa_out", None, o_ch, DT, None, None)


def cross_in(m, q_ch, k_ch, v_tok):
    nc, ins = m.nc, m.ins
    with ExitStack() as c:
        sb = lambda n, s, d=F32: c.enter_context(nc.sbuf_tensor(n, s, d))
        sem = lambda n: m.sem(c, n)
        mem = sb("xa_mem", [P, MT, D])
        mem_scaled = sb("xa_mem_scaled", [P, MT, D])
        mem_h = sb("xa_mem_h", [P, DT, MEM])
        h = sb("xa_h", [P, DT, SEQ])
        scaled = sb("xa_scaled", [P, TT, D])
        norm_m = NormTurn(m, c, "xa_mnorm", mem, mem_scaled, mem_h, lambda k: m.col("norm_mem", k), MT, D, m.banks[2:4])
        norm = NormTurn(m, c, "xa_norm", m.resid, scaled, h, lambda k: m.col("norm_xa", k), TT, D, m.banks[0:2])
        mem_loaded, q_copied, k_copied, v_done, v_copied = (sem("xa_mem_loaded"), sem("xa_q_copied"), sem("xa_k_copied"),
                                                           sem("xa_v_done"), sem("xa_v_copied"))
        u_q = m.unit
        u_k = u_q + DT
        u_v = u_k + DT
        block = c.enter_context(nc.Block())

        @block.sync
        def _(sp):
            sp.dma_start(mem[:, :, :], ins["mem"].rearrange("(t p) d -> p t d", p=P)).then_inc(mem_loaded, 16)
            stream_weights(m, sp, 2 * DT + 2 * DT // 2)

        @block.tensor
        def _(pe):
            norm.tensor(pe)
            norm_m.tensor(pe)
            pe.wait_ge(norm.turned_ready, DT)
            columns_out(m, pe, DT, h, SEQ, q_copied, 1, m.banks[4:8])
            pe.wait_ge(norm_m.turned_ready, DT)
            pe.wait_ge(q_copied, RING + DT)
            columns_out(m, pe, DT, mem_h, MEM, k_copied, 1, m.banks[4:8])
            tokens_out(m, pe, 2, DT, mem_h, MT, v_done, lambda ch, t: None, lambda ch, t: m.banks[MT * ch + t])

        @block.vector
        def _(dve):
            step = m.steps(dve, m.dve_step)
            norm.vector(dve, step)
            dve.wait_ge(mem_loaded, 16)
            norm_m.vector(dve, step)
            m.keep(step)

        @block.scalar
        def _(act):
            norm.scalar_rstd(act)
            norm_m.scalar_rstd(act)
            norm.scalar_turned(act)
            norm_m.scalar_turned(act)
            copy_columns(m, act, DT, u_q, q_copied, q_ch, m.banks[4:8], SEQ)
            copy_columns(m, act, DT, u_k, k_copied, k_ch, m.banks[4:8], MEM)
            for ch in range(2):
                for t in range(MT):
                    wait_tokens(m, act, u_v, DT, MT, v_done, ch, t)
                    act.activation(v_tok[:, t, ch * 512:(ch + 1) * 512], m.banks[MT * ch + t][:, :], ACT.Copy)\
                       .then_inc(v_copied, 1)


def cross_core(m, q_ch, k_ch, v_tok, o_ch):
    nc = m.nc
    HT = XD // P
    SCALE = XD ** -0.5
    units = [(t, pair) for t in range(TT) for pair in range(XH // 2)]
    N = len(units)
    with ExitStack() as c:
        sb = lambda n, s, d=F32: c.enter_context(nc.sbuf_tensor(n, s, d))
        sem = lambda n: m.sem(c, n)
        p = sb("xa_p", [P, 2, 2, MEM])
        pt = sb("xa_pt", [P, XH, MT, SEQ])
        stat = sb("xa_stat", [P, 2, 4, 2])
        scores_done, max_ready, exp_done, p_ready, turned, turn_read, out_done = (
            sem("xa_scores_done"), sem("xa_max_ready"), sem("xa_exp_done"), sem("xa_p_ready"), sem("xa_turned"),
            sem("xa_turn_read"), sem("xa_out_done"))
        block = c.enter_context(nc.Block())

        @block.tensor
        def _(pe):
            for i in range(N + 1):
                if i < N:
                    t, pair = units[i]
                    if i >= 2:
                        pe.wait_ge(exp_done, i - 1)
                    for x in range(2):
                        for k in range(HT):
                            j = (2 * pair + x) * HT + k
                            mm = pe.matmul(m.banks[i % 2][:, x * MEM:(x + 1) * MEM], q_ch[:, j, t * P:(t + 1) * P],
                                           k_ch[:, j, :], start=(k == 0), stop=(k == HT - 1))
                    mm.then_inc(scores_done, 1)
                if i >= 1:
                    u = i - 1
                    pe.wait_ge(p_ready, u + 1)
                    if u >= 2:
                        pe.wait_ge(turn_read, u - 1)
                    for x in range(2):
                        for half in range(MT):
                            n = MT * x + half
                            mm = pe.transpose(m.banks[2 + u % 2][:, n * P:(n + 1) * P],
                                              p[:, u % 2, x, half * P:(half + 1) * P], m.ident[:, :])
                    mm.then_inc(turned, 1)
            pe.wait_ge(turn_read, N)
            for j in range(DT):
                if j >= 4:
                    pass
                for half in range(MT):
                    mm = pe.matmul(m.banks[(4 + j) % 8][:, :], v_tok[:, half, j * P:(j + 1) * P],
                                   pt[:, j // HT, half, :], start=(half == 0), stop=(half == MT - 1))
                mm.then_inc(out_done, 1)

        @block.vector
        def _(dve):
            step = m.steps(dve, m.dve_step)
            for i in range(N):
                st = stat[:, i % 2, :, :]
                dve.wait_ge(scores_done, i + 1)
                step(dve.tensor_reduce(st[:, 0, :], m.banks[i % 2][:, :].rearrange("p (x k) -> p x k", x=2), AX.X, ALU.max))
                dve.tensor_scalar(st[:, 1, :], st[:, 0, :], -SCALE, None, ALU.mult).then_inc(max_ready, 1)
                dve.wait_ge(exp_done, i + 1)
                step(dve.reciprocal(st[:, 3, :], st[:, 2, :]))
                for x in range(2):
                    mul = dve.tensor_scalar(p[:, i % 2, x, :], p[:, i % 2, x, :], st[:, 3, x:x + 1], None, ALU.mult)
                mul.then_inc(p_ready, 1)
            m.keep(step)

        @block.scalar
        def _(act):
            for i in range(N + 1):
                if i < N:
                    st = stat[:, i % 2, :, :]
                    act.wait_ge(max_ready, i + 1)
                    if i >= 2:
                        act.wait_ge(turned, i - 1)
                    for x in range(2):
                        e = act.activation(p[:, i % 2, x, :], m.banks[i % 2][:, x * MEM:(x + 1) * MEM], ACT.Exp,
                                           bias=st[:, 1, x:x + 1], scale=SCALE, accum_out=st[:, 2, x:x + 1])
                    e.then_inc(exp_done, 1)
                if i >= 1:
                    u = i - 1
                    t, pair = units[u]
                    act.wait_ge(turned, u + 1)
                    act.activation(pt[:, 2 * pair:2 * pair + 2, :, t * P:(t + 1) * P],
                                   m.banks[2 + u % 2][:, :].rearrange("p (x a n) -> p x a n", x=2, a=MT), ACT.Copy)\
                       .then_inc(turn_read, 1)
            for j in range(DT):
                act.wait_ge(out_done, j + 1)
                act.activation(o_ch[:, j, :], m.banks[(4 + j) % 8][:, :], ACT.Copy)



HP = 2 * PH
SLOTS = PH * TOPK
ROWS = 16
GROUP = 4


def peer(m):
    nc = m.nc
    with ExitStack() as c:
        sb = lambda n, s, d=F32: c.enter_context(nc.sbuf_tensor(n, s, d))
        h_tok = sb("peer_h_tok", [P, TT, D])
        gates = sb("peer_gates", [P, TT, SLOTS])
        ids = sb("peer_ids", [P, TT, SLOTS], U32)
        with ExitStack() as c2:
            q_ch = c2.enter_context(nc.sbuf_tensor("peer_q", [P, HP, SEQ], F32))
            peer_in(m, h_tok, q_ch)
            peer_choose(m, q_ch, gates, ids)
        peer_experts(m, h_tok, gates, ids)


def peer_in(m, h_tok, q_ch):
    nc, ins = m.nc, m.ins
    with ExitStack() as c:
        sb = lambda n, s, d=F32: c.enter_context(nc.sbuf_tensor(n, s, d))
        sem = lambda n: m.sem(c, n)
        h = sb("peer_h", [P, DT, SEQ])
        gain = sb("peer_gain", [P, D])
        norm = NormTurn(m, c, "peer_norm", m.resid, h_tok, h, lambda k: m.col("norm_ffn", k), TT, D, m.banks[0:2])
        gain_loaded, copied = sem("peer_gain_loaded"), sem("peer_copied")
        u0 = m.unit
        block = c.enter_context(nc.Block())

        @block.sync
        def _(sp):
            sp.dma_start(gain[:, :], m.row("norm_ffn", D)).then_inc(gain_loaded, 16)
            stream_weights(m, sp, HP)

        @block.tensor
        def _(pe):
            norm.tensor(pe)
            pe.wait_ge(norm.turned_ready, DT)
            columns_out(m, pe, HP, h, SEQ, copied, 1, m.banks[4:8])

        @block.vector
        def _(dve):
            step = m.steps(dve, m.dve_step)
            norm.vector(dve, step)
            dve.wait_ge(gain_loaded, 16)
            dve.wait_ge(norm.turned_in_bank, DT)
            for t in range(TT):
                dve.tensor_tensor(h_tok[:, t, :], h_tok[:, t, :], gain[:, :], ALU.mult)
            m.keep(step)

        @block.scalar
        def _(act):
            norm.scalar_rstd(act)
            norm.scalar_turned(act)
            copy_columns(m, act, HP, u0, copied, q_ch, m.banks[4:8], SEQ)


def peer_choose(m, q_ch, gates, ids):
    nc, ins = m.nc, m.ins
    with ExitStack() as c:
        sb = lambda n, s, d=F32: c.enter_context(nc.sbuf_tensor(n, s, d))
        sem = lambda n: m.sem(c, n)
        keys = sb("peer_keys", [P, HP, KEYS])
        sc = sb("peer_sc", [P, 2, HP, KEYS])
        sc2 = sb("peer_sc2", [P, HP, KEYS])
        top_v = sb("peer_top_v", [P, HP, TOPK])
        top_i = sb("peer_top_i", [P, HP, TOPK], U32)
        top_f = sb("peer_top_f", [P, HP, TOPK])
        cand = sb("peer_cand", [P, PH, TOPK * TOPK])
        cand2 = sb("peer_cand2", [P, PH, TOPK * TOPK])
        best_v = sb("peer_best_v", [P, PH, TOPK])
        place = sb("peer_place", [P, PH, TOPK], U32)
        digit = sb("peer_digit", [P, 2, PH, TOPK], U32)
        digit_f = sb("peer_digit_f", [P, 2, PH, TOPK])
        chosen = sb("peer_chosen", [P, 2, PH, TOPK])
        picked = sb("peer_picked", [P, PH * TOPK, TOPK])
        count = sb("peer_count", [P, TOPK])
        soft = sb("peer_soft", [P, PH, TOPK])
        total = sb("peer_total", [P, 2, PH])
        keys_loaded, scores_done, scores_read, soft_in, soft_out, count_made = (
            sem("peer_keys_loaded"), sem("peer_scores_done"), sem("peer_scores_read"), sem("peer_soft_in"),
            sem("peer_soft_out"), sem("peer_count_made"))
        sc_free = sem("peer_sc_free")
        block = c.enter_context(nc.Block())
        G = HP // 4

        @block.sync
        def _(sp):
            sp.dma_start(keys[:, :, :], ins["peer_keys"]).then_inc(keys_loaded, 16)

        @block.gpsimd
        def _(pool):
            pool.iota(count[:, :], [[1, TOPK]], base=0, channel_multiplier=0, allow_small_or_imprecise_dtypes=True)\
                .then_inc(count_made, 1)

        @block.tensor
        def _(pe):
            pe.wait_ge(keys_loaded, 16)
            for t in range(TT):
                for g in range(G):
                    r = G * t + g
                    if r >= 8:
                        pe.wait_ge(scores_read, r - 7)
                    for x in range(4):
                        mm = pe.matmul(m.banks[r % 8][:, x * KEYS:(x + 1) * KEYS], q_ch[:, 4 * g + x, t * P:(t + 1) * P],
                                       keys[:, 4 * g + x, :], start=True, stop=True)
                    mm.then_inc(scores_done, 1)

        @block.scalar
        def _(act):
            def softmax_part(t):
                act.wait_ge(soft_in, t + 1)
                act.activation(gates[:, t, :], soft[:, :, :], ACT.Exp).then_inc(soft_out, 1)

            for t in range(TT):
                if t >= 2:
                    act.wait_ge(sc_free, t - 1)
                for g in range(G):
                    r = G * t + g
                    act.wait_ge(scores_done, r + 1)
                    act.activation(sc[:, t % 2, 4 * g:4 * g + 4, :], m.banks[r % 8][:, :], ACT.Copy).then_inc(scores_read, 1)
                if t >= 1:
                    softmax_part(t - 1)
            softmax_part(TT - 1)

        @block.vector
        def _(dve):
            step = m.steps(dve, m.dve_step)

            def best_16(n, values, left, out_v, out_i):
                for pick in range(2):
                    of = values if pick == 0 else left
                    eight = slice(8 * pick, 8 * pick + 8)
                    for r in range(n):
                        last = dve.max(out_v[:, r, eight], of[:, r, :])
                    step(last)
                    for r in range(n):
                        last = dve.max_index(out_i[:, r, eight], out_v[:, r, eight], of[:, r, :])
                    if pick == 0:
                        for r in range(n):
                            last = dve.match_replace(left[:, r, :], out_v[:, r, eight], values[:, r, :], NEG)
                    step(last)

            dve.wait_ge(count_made, 1)
            for t in range(TT):
                dve.wait_ge(scores_read, G * (t + 1))
                best_16(HP, sc[:, t % 2, :, :], sc2, top_v, top_i)
                dve.sem_inc(sc_free, 1)
                v4 = top_v[:, :, :].rearrange("p (h two) k -> p h two k", two=2)
                a = v4[:, :, 0, :].rearrange("p h (k o) -> p h k o", o=1).broadcast_to([P, PH, TOPK, TOPK])
                b = v4[:, :, 1, :].rearrange("p h (o k) -> p h o k", o=1).broadcast_to([P, PH, TOPK, TOPK])
                dve.tensor_copy(top_f[:, :, :], top_i[:, :, :])
                step(dve.tensor_tensor(cand[:, :, :].rearrange("p h (a b) -> p h a b", a=TOPK), a, b, ALU.add))
                best_16(PH, cand, cand2, best_v, place)
                dve.tensor_tensor(soft[:, :, :], best_v[:, :, :], best_v[:, :, 0:1].broadcast_to([P, PH, TOPK]),
                                  ALU.subtract).then_inc(soft_in, 1)
                dve.tensor_scalar(digit[:, 0, :, :], place[:, :, :], 4, None, ALU.logical_shift_right)
                step(dve.tensor_scalar(digit[:, 1, :, :], place[:, :, :], 15, None, ALU.bitwise_and))
                step(dve.tensor_copy(digit_f[:, :, :, :], digit[:, :, :, :]))
                f4 = top_f[:, :, :].rearrange("p (h two) k -> p h two k", two=2)
                p4 = picked[:, :, :].rearrange("p (h k) n -> p h k n", h=PH)
                for half in range(2):
                    which = digit_f[:, half, :, :].rearrange("p h k -> p (h k)")
                    step(dve.tensor_tensor(picked[:, :, :], spread(which, TOPK), again(count[:, :], PH * TOPK), ALU.is_equal))
                    step(dve.tensor_tensor(p4, p4, f4[:, :, half, :].rearrange("p h (o k) -> p h o k", o=1)
                                           .broadcast_to([P, PH, TOPK, TOPK]), ALU.mult))
                    step(dve.tensor_reduce(chosen[:, half, :, :].rearrange("p h k -> p (h k)"), picked[:, :, :], AX.X, ALU.add))
                step(dve.scalar_tensor_tensor(chosen[:, 0, :, :], chosen[:, 0, :, :], float(KEYS), chosen[:, 1, :, :],
                                              ALU.mult, ALU.add))
                dve.tensor_copy(ids[:, t, :], chosen[:, 0, :, :].rearrange("p h k -> p (h k)"))
                dve.wait_ge(soft_out, t + 1)
                g3 = gates[:, t, :].rearrange("p (h k) -> p h k", h=PH)
                step(dve.tensor_reduce(total[:, 0, :], g3, AX.X, ALU.add))
                step(dve.reciprocal(total[:, 1, :], total[:, 0, :]))
                step(dve.tensor_tensor(g3, g3, spread(total[:, 1, :], TOPK), ALU.mult))
            m.keep(step)


def peer_experts(m, h_tok, gates, ids):
    nc, ins = m.nc, m.ins
    TURNS = SLOTS // ROWS
    NG = ROWS // GROUP
    with ExitStack() as c:
        sb = lambda n, s, d=F32: c.enter_context(nc.sbuf_tensor(n, s, d))
        sem = lambda n: m.sem(c, n)
        rows = sb("peer_rows", [P, ROWS, 2 * D])
        at = sb("peer_at", [P, NG, GROUP], U32)
        dots = sb("peer_dots", [P, NG, GROUP])
        acts = sb("peer_acts", [P, NG, GROUP])
        weight = sb("peer_weight", [P, NG, GROUP])
        diag = sb("peer_diag", [P, 2 * GROUP, P])
        zero = sb("peer_zero", [P, P])
        loaded = [sem(f"peer_loaded{s}") for s in range(ROWS)]
        at_ready, held, dots_ready, acts_ready, weight_ready, diag_ready, row_used, zero_made = (
            sem("peer_at_ready"), sem("peer_held"), sem("peer_dots_ready"), sem("peer_acts_ready"), sem("peer_weight_ready"),
            sem("peer_diag_ready"), sem("peer_row_used"), sem("peer_zero_made"))
        block = c.enter_context(nc.Block())

        @block.gpsimd
        def _(pool):
            pool.memset(zero[:, :], 0.0).then_inc(zero_made, 1)
            pool.sem_inc(row_used, ROWS)
            for t in range(TT):
                with pool.Fori(0, TURNS) as i:
                    for g in range(NG):
                        pool.wait_ge(row_used, i * ROWS + (t * SLOTS + GROUP * g + 1))
                        pool.sem_inc(held, 1)
                        pool.tensor_copy(at[:, g, :], ids[:, t, bass.ds(i * ROWS + GROUP * g, GROUP)]).then_inc(at_ready, 1)
                        pool.wait_ge(at_ready, i * NG + (t * TURNS * NG + g + 1))
                        pool.sem_inc(held, 1)
                        for r in range(GROUP):
                            s = GROUP * g + r
                            if r > 0:
                                pool.wait_ge(row_used, i * ROWS + (t * SLOTS + s + 1))
                                pool.sem_inc(held, 1)
                            pool.indirect_dma_start(rows[:, s, :], None, ins["peer_uv"],
                                                    bass.IndirectOffsetOnAxis(ap=at[:, g, r:r + 1], axis=0))\
                                .then_inc(loaded[s], 16)

        @block.vector
        def _(dve):
            step = m.steps(dve, m.dve_step)
            for t in range(TT):
                def weigh(i, g, turn):
                    n = i * NG + (t * TURNS * NG + g + 1)
                    dve.wait_ge(acts_ready, n)
                    dve.tensor_tensor(weight[:, g, :], acts[:, g, :], gates[:, t, bass.ds(i * ROWS + GROUP * g, GROUP)],
                                      ALU.mult).then_inc(weight_ready, 1)

                with dve.Fori(0, TURNS) as i:
                    for g in range(NG):
                        for r in range(GROUP):
                            s = GROUP * g + r
                            dve.wait_ge(loaded[s], i * 16 + 16 * (t * TURNS + 1))
                            dot = dve.tensor_tensor_reduce(rows[:, s, 0:D], rows[:, s, 0:D], h_tok[:, t, :], 1.0, 0.0,
                                                           ALU.mult, ALU.add, dots[:, g, r:r + 1])
                        dot.then_inc(dots_ready, 1)
                        weigh(i, g, 0)
            for t in range(TT):
                dve.wait_ge(row_used, ROWS + SLOTS * TT)
                for half in range(2):
                    here = m.resid[:, t, half * 512:(half + 1) * 512]
                    dve.tensor_tensor(here, here, m.banks[2 * t + half][:, :], ALU.add)
            m.keep(step)

        @block.scalar
        def _(act):
            for t in range(TT):
                with act.Fori(0, TURNS) as i:
                    for g in range(NG):
                        n = i * NG + (t * TURNS * NG + g + 1)
                        act.wait_ge(dots_ready, n)
                        act.activation(acts[:, g, :], dots[:, g, :], ACT.Gelu).then_inc(acts_ready, 1)
                        act.wait_ge(weight_ready, n)
                        for r in range(GROUP):
                            d = GROUP * (g % 2) + r
                            act.wait_ge(row_used, i * ROWS + (t * SLOTS + GROUP * g + r + 1 + ROWS - 2 * GROUP))
                            act.activation(diag[:, d, :], m.ident[:, :], ACT.Copy, scale=weight[:, g, r:r + 1])\
                               .then_inc(diag_ready, 1)

        @block.tensor
        def _(pe):
            pe.wait_ge(zero_made, 1)
            for t in range(TT):
                for half in range(2):
                    pe.matmul(m.banks[2 * t + half][:, :], zero[:, :], h_tok[:, t, 0:512], start=True, stop=False,
                              skip_group_check=True)
                with pe.Fori(0, TURNS) as i:
                    for s in range(ROWS):
                        pe.wait_ge(diag_ready, i * ROWS + (t * SLOTS + s + 1))
                        for half in range(2):
                            mm = pe.matmul(m.banks[2 * t + half][:, :], diag[:, s % (2 * GROUP), :],
                                           rows[:, s, D + half * 512:D + (half + 1) * 512], start=False, stop=False,
                                           skip_group_check=True)
                        mm.then_inc(row_used, 1)


def final_norm(m, out):
    nc = m.nc
    with ExitStack() as c:
        sb = lambda n, s, d=F32: c.enter_context(nc.sbuf_tensor(n, s, d))
        sem = lambda n: m.sem(c, n)
        stat = sb("fin_stat", [P, 3, TT])
        gain = sb("fin_gain", [P, D])
        y = sb("fin_y", [P, TT, D])
        gain_loaded, mean_ready, rstd_ready, y_ready, stored = (sem("fin_gain_loaded"), sem("fin_mean"), sem("fin_rstd"),
                                                                sem("fin_y_ready"), sem("fin_stored"))
        block = c.enter_context(nc.Block())

        @block.sync
        def _(sp):
            sp.dma_start(gain[:, :], m.row("norm_final", D)).then_inc(gain_loaded, 16)
            for t in range(TT):
                sp.wait_ge(y_ready, t + 1)
                sp.dma_start(out[t * P:(t + 1) * P, :], y[:, t, :]).then_inc(stored, 16)
            sp.wait_ge(stored, 16 * TT)

        @block.vector
        def _(dve):
            step = m.steps(dve, m.dve_step)
            for t in range(TT):
                last = dve.tensor_tensor_reduce(y[:, t, :], m.resid[:, t, :], m.resid[:, t, :], 1.0, 0.0, ALU.mult,
                                                ALU.add, stat[:, 0, t:t + 1])
            step(last)
            step(dve.tensor_scalar(stat[:, 1, :], stat[:, 0, :], 1.0 / D, EPS, ALU.mult, ALU.add))
            dve.reciprocal(stat[:, 2, :], stat[:, 1, :]).then_inc(mean_ready, 1)
            dve.wait_ge(rstd_ready, 1)
            dve.wait_ge(gain_loaded, 16)
            for t in range(TT):
                dve.scalar_tensor_tensor(y[:, t, :], m.resid[:, t, :], stat[:, 0, t:t + 1], gain[:, :], ALU.mult,
                                         ALU.mult).then_inc(y_ready, 1)
            m.keep(step)

        @block.scalar
        def _(act):
            act.wait_ge(mean_ready, 1)
            act.activation(stat[:, 0, :], stat[:, 2, :], ACT.Sqrt).then_inc(rstd_ready, 1)



def column_units(w):
    import numpy as np
    kt, n = w.shape[0] // P, w.shape[1] // P
    return np.ascontiguousarray(w.reshape(kt, P, n, P).transpose(2, 1, 0, 3)).reshape(n, P, kt * P)


def token_units(w):
    import numpy as np
    kt, n = w.shape[0] // P, w.shape[1] // 512
    return np.ascontiguousarray(w.reshape(kt // 2, 2, P, n, 512).transpose(3, 0, 2, 1, 4)).reshape(n * kt // 2, P, UNIT)


def lay_out(a):
    import numpy as np
    units, col, row = [], [], []
    col_at, row_at = {}, {}

    def add_cols(name, v):
        col_at[name] = sum(x.shape[1] for x in col)
        col.append(v)

    def add_row(name, v):
        row_at[name] = sum(x.shape[0] for x in row)
        row.append(v.reshape(-1))

    def by_tile(v):
        return v.reshape(-1, P).T

    def taps(w):
        return w.reshape(CONV, -1, P).transpose(2, 1, 0).reshape(P, -1)

    w = a["ssm_w_in"][0]
    units += [token_units(w[:, 0:DI]), column_units(w[:, DI:DI + CM_T * P])]
    arrays = {"ssm_w_dt": w[:, DI + CM_T * P:].reshape(DT, P, HEADS).transpose(1, 0, 2)}
    units += [token_units(a["ssm_w_out"][0])]
    add_cols("pre_norm0", by_tile(a["pre_norm"][0]))
    add_cols("ssm_conv_w", taps(a["ssm_conv_w"][0]))
    add_cols("ssm_conv_b", by_tile(a["ssm_conv_b"][0]))
    add_cols("ssm_gate_norm", by_tile(a["ssm_gate_norm"][0]))
    add_row("ssm_dt_bias", a["ssm_dt_bias"][0])
    add_row("ssm_a_log", a["ssm_a_log"][0])
    add_row("ssm_d", a["ssm_d"][0])
    add_row("post_norm0", a["post_norm"][0])

    heads = lambda w: w.reshape(w.shape[0], QH, AD)[:, HEAD_ORDER].reshape(w.shape[0], QW)
    w = a["att_w_in"][0]
    units += [token_units(np.concatenate([heads(w[:, 0:QW]), w[:, QW:QW + 2 * KVW], heads(w[:, QW + 2 * KVW:])], axis=1))]
    units += [token_units(a["att_w_out"][0].reshape(QH, AD, D)[HEAD_ORDER].reshape(QW, D))]
    add_cols("pre_norm1", by_tile(a["pre_norm"][1]))
    add_row("att_sinks", a["att_sinks"][0][HEAD_ORDER])
    add_row("post_norm1", a["post_norm"][1])
    arrays["positions"] = a["positions"].reshape(TT, P).T

    w = a["w_in_2"][0]
    GW, MW = GH * GD, MH * MD
    cuts = np.cumsum([3 * GW, GW, GH, GH, 2 * MW, MW, MW, MH, MH])
    g_qkv, g_z, g_a, g_b, m_qk, m_v, m_o, m_i, m_f = np.split(w, cuts[:-1], axis=1)
    units += [token_units(np.concatenate([g_z, m_v, m_o], axis=1)), column_units(np.concatenate([g_qkv, m_qk], axis=1))]
    arrays["hyb_w_small"] = np.concatenate([g_a, g_b, m_i, m_f], axis=1).reshape(DT, P, 16).transpose(1, 0, 2)
    units += [token_units(a["w_out_2"][0])]
    add_cols("norm_mix", by_tile(a["norm_mix_w_2"][0]))
    add_cols("hyb_conv_w", taps(np.concatenate([a["gdn_conv_w_2"][0], a["mlstm_conv_w_2"][0]], axis=1)))
    add_row("gdn_dt_bias", a["gdn_dt_bias_2"][0])
    add_row("gdn_a_log", a["gdn_a_log_2"][0])
    add_row("mls_i_bias", a["mlstm_i_bias_2"][0])
    add_row("mls_f_bias", a["mlstm_f_bias_2"][0])
    add_row("hyb_gains", np.concatenate([a["gdn_norm_w_2"][0]] * GH + [a["mlstm_norm_w_2"][0]]))

    units += [column_units(a["xa_wq_2"][0]), column_units(a["xa_wkv_2"][0][:, 0:D]), token_units(a["xa_wkv_2"][0][:, D:])]
    units += [token_units(a["xa_wo_2"][0]), column_units(a["peer_wq_2"][0])]
    arrays["mem"] = a["mem_2"].reshape(MEM, D)
    add_cols("norm_xa", by_tile(a["norm_xa_w_2"][0]))
    add_cols("norm_mem", by_tile(a["norm_mem_w_2"][0]))
    add_cols("norm_ffn", by_tile(a["norm_ffn_w_2"][0]))
    add_row("norm_ffn", a["norm_ffn_w_2"][0])
    add_row("norm_final", a["norm_final_w_2"])
    arrays["peer_keys"] = a["peer_sub_keys_2"][0].reshape(HP, KEYS, P).transpose(2, 0, 1)
    arrays["peer_uv"] = np.concatenate([a["peer_u_2"][0], a["peer_v_2"][0]], axis=1)
    arrays["x"] = a["x"].reshape(SEQ, D)
    arrays["weights"] = np.concatenate(units)
    arrays["cols"] = np.concatenate(col, axis=1)
    arrays["rows"] = np.concatenate(row)[None, :]
    return arrays, col_at, row_at



STAGES = [mamba, attention, hybrid, cross_attention, peer]


def program(nc, ins, out):
    with ExitStack() as ctx:
        m = Machine(nc, ctx, ins)
        set_up(m)
        for stage in STAGES:
            stage(m)
            m.clear_signals()
        final_norm(m, out)



def kernel(**inputs):
    import numpy as np
    from concourse import bacc
    from concourse.bass_utils import run_bass_kernel_spmd

    laid, col_at, row_at = lay_out({k: np.asarray(v) for k, v in inputs.items()})
    nc = bacc.Bacc("TRN2", target_bir_lowering=False, num_devices=1)
    arrays, ins = {}, {"col_at": col_at, "row_at": row_at}
    for name, a in laid.items():
        a = np.ascontiguousarray(a)
        arrays[f"in_{name}"] = a
        ins[name] = nc.dram_tensor(f"in_{name}", a.shape, mybir.dt.from_np(a.dtype), kind="ExternalInput").ap()
    out = nc.dram_tensor("out_0", (SEQ, D), F32, kind="ExternalOutput").ap()
    program(nc, ins, out)
    r = run_bass_kernel_spmd(nc, [arrays], core_ids=[0])
    return r.results[0]["out_0"].reshape(1, SEQ, D)
```

```python
from contextlib import ExitStack

import concourse.bass as bass
from concourse import mybir

F32 = mybir.dt.float32
F32R = mybir.dt.float32r
U32 = mybir.dt.uint32
I32 = mybir.dt.int32
ALU = mybir.AluOpType
ACT = mybir.ActivationFunctionType
AX = mybir.AxisListType

P = 128
SEQ = 512
TT = SEQ // P
D = 1024
DT = D // P
EPS = 1e-6
RING = 4
UNIT = 1024

DI = 2048
HEADS, HD = 32, 64
GROUPS, STATE = 8, 128
HPG = HEADS // GROUPS
CONV = 4
XS_T, BC_T = DI // P, GROUPS * STATE // P
CM_T = XS_T + 2 * BC_T
QH, KVH, AD = 16, 4, 64
QW, KVW = QH * AD, KVH * AD
HEAD_ORDER = [8 * a + 4 * b + i for a in range(2) for i in range(4) for b in range(2)]
ROPE = AD // 4
HALF = ROPE // 2
THETA = 500000.0
GH, GD = 4, 128
MH, MD = 4, 128
MEM = 256
XH, XD = 4, 256
PH, KEYS, TOPK = 8, 128, 16
NEG = -3.0e38


class Steps:

    def __init__(self, eng, sem, start=0):
        self.eng, self.sem, self.n, self.turn = eng, sem, start, None

    def value(self):
        if self.turn is None:
            return self.n
        i, per, base = self.turn
        return i * per + (base + self.n)

    def __call__(self, ins):
        ins.then_inc(self.sem, 1)
        self.n += 1
        self.eng.wait_ge(self.sem, self.value())

    def loop(self, i, per):
        self.turn, self.n = (i, per, self.n), 0

    def end_loop(self, count):
        _, per, base = self.turn
        assert self.n == per
        self.turn, self.n = None, base + count * per


class Machine:

    def __init__(self, nc, ctx, ins):
        self.nc, self.ins = nc, ins
        self.spent = []
        self.steps_at = {}
        self.unit = ins.get("unit0", 0)
        self.streamed = ins.get("unit0", 0)
        self.banks = [ctx.enter_context(nc.psum_tensor(f"bank{i}", [P, 512], F32)) for i in range(8)]
        self.w_loaded = [ctx.enter_context(nc.semaphore(f"w_loaded{i}")) for i in range(RING)]
        self.w_high = ctx.enter_context(nc.semaphore("w_high"))
        self.w_split = ctx.enter_context(nc.semaphore("w_split"))
        self.w_held = ctx.enter_context(nc.semaphore("w_held"))
        self.w_used = ctx.enter_context(nc.semaphore("w_used"))
        self.split = ins.get("unit0", 0)
        self.parts = None
        self.dve_step = ctx.enter_context(nc.semaphore("dve_step"))
        self.act_step = ctx.enter_context(nc.semaphore("act_step"))
        self.pool_step = ctx.enter_context(nc.semaphore("pool_step"))
        sb = lambda n, s, d=F32: ctx.enter_context(nc.sbuf_tensor(n, s, d))
        self.ident = sb("ident", [P, P])
        self.ones = sb("ones", [P, P])
        self.zero = sb("zero", [P, 1])
        self.upto = sb("upto", [P, P])
        self.after = sb("after", [P, P])
        self.ring = sb("ring", [P, RING, UNIT])
        self.resid = sb("resid", [P, TT, D])
        self.cols = sb("cols", [P, ins["cols"].shape[1]])

    def sem(self, scope, name):
        handle = self.nc.alloc_semaphore(name)
        scope.callback(self.spent.append, handle)
        return handle

    def clear_signals(self):
        self.nc.clear_and_free_semaphores(self.spent)
        self.nc.all_engine_barrier()
        self.spent = []

    def open_parts(self, scope):
        self.parts = scope.enter_context(self.nc.sbuf_tensor(f"w_parts_{self.unit}", [P, 2, 2, UNIT], F32R))

    def steps(self, eng, sem):
        key = id(sem)
        s = Steps(eng, sem, self.steps_at.get(key, 0))
        return s

    def keep(self, steps):
        self.steps_at[id(steps.sem)] = steps.n

    def row(self, name, width):
        return self.row_at(self.ins["row_at"][name], width)

    def row_at(self, at, width):
        r = self.ins["rows"]
        return bass.AP(tensor=r.tensor, offset=r.offset + at, ap=[[0, P], [1, width]])

    def col(self, name, i=0, n=1):
        at = self.ins["col_at"][name] + i
        return self.cols[:, at:at + n]



def stream_weights(m, sp, n):
    u0 = m.streamed
    assert u0 % RING == 0 and n % RING == 0
    w = m.ins["weights"]
    total = w.shape[0]
    n = min(n, total - u0)
    m.streamed += n
    if u0 == 0:
        for s in range(RING):
            sp.dma_start(m.ring[:, s, :], w[s]).then_inc(m.w_loaded[s], 16)
        u0, n = RING, n - RING
    if n <= 0:
        return
    with sp.Fori(0, n // RING) as i:
        for s in range(RING):
            sp.wait_ge(m.w_split, i * RING + (u0 - RING + s + 1))
            sp.dma_start(m.ring[:, s, :], w[i * RING + (u0 + s)]).then_inc(m.w_loaded[s], 16)


def split_weights(m, pool, n):
    u0 = m.split
    m.split += n

    zeros = m.zero[:, :].broadcast_to([P, UNIT])

    def four(i, first, fresh):
        for s in range(RING):
            pool.wait_ge(m.w_loaded[s], i * 16 + 16 * (first // RING + 1))
            pool.sem_inc(m.w_held, 1)
            if s >= 2 or not fresh:
                pool.wait_ge(m.w_used, i * RING + (first + s - 1))
                pool.sem_inc(m.w_held, 1)
            high, low = (m.parts[:, s % 2, x, :] for x in range(2))
            pool.tensor_tensor(high, m.ring[:, s, :], zeros, ALU.add).then_inc(m.w_high, 1)
            pool.wait_ge(m.w_high, i * RING + (first + s + 1))
            pool.sem_inc(m.w_held, 1)
            pool.tensor_tensor(low, m.ring[:, s, :], high, ALU.subtract).then_inc(m.w_split, 1)

    if u0 == 0:
        four(0, 0, True)
        u0, n = RING, n - RING
    with pool.Fori(0, n // RING) as i:
        four(i, u0, False)


PASSES = ((0, 0), (0, 1), (1, 0))


def columns_out(m, pe, n, rhs, width, free, free0, banks):
    u0 = m.unit
    m.unit += n
    with pe.Fori(0, n // RING) as i:
        for s in range(RING):
            pe.wait_ge(m.w_split, i * RING + (u0 + s + 1))
            pe.wait_ge(free, i * RING + (free0 + s))
            mm = column(m, pe, s, rhs, banks[s][:, 0:width])
            mm.then_inc(m.w_used, 1)


def column(m, pe, s, rhs, out):
    for k in range(DT):
        for a, b in PASSES:
            mm = pe.matmul(out, m.parts[:, s % 2, a, k * P:(k + 1) * P], rhs[b][:, k, :],
                           start=(k == 0 and (a, b) == PASSES[0]), stop=(k == DT - 1 and (a, b) == PASSES[-1]))
    return mm


def tokens_out(m, pe, chunks, kt, lhs, tiles, done, before_bank, bank_of):
    for c in range(chunks):
        for kk in range(kt // 2):
            u = m.unit
            m.unit += 1
            pe.wait_ge(m.w_split, u + 1)
            for t in range(tiles):
                if kk == 0:
                    before_bank(c, t)
                for k in (2 * kk, 2 * kk + 1):
                    for a, b in PASSES:
                        mm = pe.matmul(bank_of(c, t)[:, :], lhs[a][:, k, t * P:(t + 1) * P],
                                       m.parts[:, u % 2, b, (k % 2) * 512:(k % 2 + 1) * 512],
                                       start=(k == 0 and (a, b) == PASSES[0]),
                                       stop=(k == kt - 1 and (a, b) == PASSES[-1]), skip_group_check=True)
                if kk == kt // 2 - 1:
                    if t < tiles - 1:
                        mm.then_inc(done, 1)
            mm.then_inc(m.w_used, 1)


def wait_tokens(m, eng, u0, kt, tiles, done, c, t):
    if t < tiles - 1:
        eng.wait_ge(done, (tiles - 1) * c + t + 1)
    else:
        eng.wait_ge(m.w_used, u0 + (c + 1) * kt // 2)



class NormTurn:

    def __init__(self, m, c, name, src, scaled, turned, gain, tiles, width, banks):
        self.m, self.src, self.scaled, self.turned = m, src, scaled, turned
        self.gain, self.tiles, self.width, self.banks = gain, tiles, width, banks
        nc = m.nc
        self.stat = c.enter_context(nc.sbuf_tensor(name + "_stat", [P, 3, tiles], F32))
        sem = lambda n: m.sem(c, f"{name}_{n}")
        self.mean_ready, self.rstd_ready = sem("mean"), sem("rstd")
        self.scaled_ready, self.turned_in_bank = sem("scaled"), sem("bank")
        self.high_ready, self.turned_ready = sem("high"), sem("turned")

    def vector(self, dve, step):
        st = self.stat
        for t in range(self.tiles):
            step(dve.tensor_tensor_reduce(self.scaled[:, t, :], self.src[:, t, :], self.src[:, t, :], 1.0, 0.0,
                                          ALU.mult, ALU.add, st[:, 0, t:t + 1]))
        step(dve.tensor_scalar(st[:, 1, :], st[:, 0, :], 1.0 / self.width, EPS, ALU.mult, ALU.add))
        dve.reciprocal(st[:, 2, :], st[:, 1, :]).then_inc(self.mean_ready, 1)
        dve.wait_ge(self.rstd_ready, 1)
        for t in range(self.tiles):
            dve.tensor_scalar(self.scaled[:, t, :], self.src[:, t, :], st[:, 0, t:t + 1], None, ALU.mult)\
               .then_inc(self.scaled_ready, 1)

    def scalar_rstd(self, act):
        act.wait_ge(self.mean_ready, 1)
        act.activation(self.stat[:, 0, :], self.stat[:, 2, :], ACT.Sqrt).then_inc(self.rstd_ready, 1)

    def tensor(self, pe):
        pe.wait_ge(self.scaled_ready, self.tiles)
        for k in range(self.width // P):
            if k >= 2:
                pe.wait_ge(self.turned_ready, k - 1)
            for t in range(self.tiles):
                mm = pe.transpose(self.banks[k % 2][:, t * P:(t + 1) * P], self.scaled[:, t, k * P:(k + 1) * P],
                                  self.m.ident[:, :])
            mm.then_inc(self.turned_in_bank, 1)

    def scalar_turned(self, act):
        for k in range(self.width // P):
            act.wait_ge(self.turned_in_bank, k + 1)
            act.activation(self.turned[0][:, k, :], self.banks[k % 2][:, 0:self.tiles * P], ACT.Copy,
                           scale=self.gain(k)).then_inc(self.high_ready, 1)

    def vector_turned(self, dve):
        for k in range(self.width // P):
            dve.wait_ge(self.high_ready, k + 1)
            dve.scalar_tensor_tensor(self.turned[1][:, k, :], self.banks[k % 2][:, 0:self.tiles * P], self.gain(k),
                                     self.turned[0][:, k, :], ALU.mult, ALU.subtract).then_inc(self.turned_ready, 1)


class PostNorm:

    def __init__(self, m, c, name, y, gain_row, gain_loaded):
        self.m, self.y, self.gain_row, self.gain_loaded = m, y, gain_row, gain_loaded
        self.stat = c.enter_context(m.nc.sbuf_tensor(name + "_stat", [P, 3, TT], F32))
        self.junk = c.enter_context(m.nc.sbuf_tensor(name + "_junk", [P, D], F32))
        self.mean_ready = m.sem(c, name + "_mean")
        self.rstd_ready = m.sem(c, name + "_rstd")

    def vector(self, dve, step):
        st, y = self.stat, self.y
        for t in range(TT):
            step(dve.tensor_tensor_reduce(self.junk[:, :], y[:, t, :], y[:, t, :], 1.0, 0.0, ALU.mult, ALU.add,
                                          st[:, 0, t:t + 1]))
        step(dve.tensor_scalar(st[:, 1, :], st[:, 0, :], 1.0 / D, EPS, ALU.mult, ALU.add))
        dve.reciprocal(st[:, 2, :], st[:, 1, :]).then_inc(self.mean_ready, 1)
        dve.wait_ge(self.rstd_ready, 1)
        dve.wait_ge(self.gain_loaded, 16)
        for t in range(TT):
            step(dve.scalar_tensor_tensor(y[:, t, :], y[:, t, :], st[:, 0, t:t + 1], self.gain_row[:, :],
                                          ALU.mult, ALU.mult))
            step(dve.tensor_tensor(self.m.resid[:, t, :], self.m.resid[:, t, :], y[:, t, :], ALU.add))

    def scalar(self, act):
        act.wait_ge(self.mean_ready, 1)
        act.activation(self.stat[:, 0, :], self.stat[:, 2, :], ACT.Sqrt).then_inc(self.rstd_ready, 1)



def set_up(m):
    nc = m.nc
    with ExitStack() as c:
        const = m.sem(c, "const")
        loaded = m.sem(c, "loaded")
        block = c.enter_context(nc.Block())

        @block.sync
        def _(sp):
            sp.dma_start(m.resid[:, :, :], m.ins["x"].rearrange("(t p) d -> p t d", p=P)).then_inc(loaded, 16)
            sp.dma_start(m.cols[:, :], m.ins["cols"]).then_inc(loaded, 16)
            stream_weights(m, sp, RING)
            sp.wait_ge(loaded, 32)

        @block.gpsimd
        def _(pool):
            pool.memset(m.zero[:, :], 0.0)
            pool.memset(m.ident[:, :], 0.0).then_inc(const, 1)
            pool.memset(m.ones[:, :], 1.0).then_inc(const, 1)
            pool.wait_ge(const, 2)
            pool.affine_select(out=m.ident[:, :], in_=m.ident[:, :], compare_op=ALU.not_equal, fill=1.0, base=0,
                               pattern=[[-1, P]], channel_multiplier=1)
            pool.affine_select(out=m.upto[:, :], in_=m.ones[:, :], compare_op=ALU.is_ge, fill=0.0, base=0,
                               pattern=[[1, P]], channel_multiplier=-1)
            pool.affine_select(out=m.after[:, :], in_=m.ones[:, :], compare_op=ALU.is_gt, fill=0.0, base=0,
                               pattern=[[-1, P]], channel_multiplier=1)



def mamba(m):
    nc, ins, resid = m.nc, m.ins, m.resid
    with ExitStack() as c:
        sb = lambda n, s, d=F32: c.enter_context(nc.sbuf_tensor(n, s, d))
        dt_raw = sb("ssm_dt_raw", [P, TT, HEADS])
        z_gate = sb("ssm_z_gate", [P, TT, DI])
        with ExitStack() as c2:
            conved = c2.enter_context(nc.sbuf_tensor("ssm_conved", [P, CM_T, SEQ], F32))
            mamba_in(m, z_gate, conved, dt_raw)
            xs = c2.enter_context(nc.sbuf_tensor("ssm_xs", [P, TT, DI], F32))
            mamba_scan(m, z_gate, conved, dt_raw, xs)
        mamba_out(m, z_gate)


def convolve(m, dve, step, tiles, u1, taps, bias, acc, silu_done, conv_done):
    tap_at = m.ins["col_at"][taps]
    dve.sem_inc(conv_done, 4)
    with dve.Fori(0, tiles // 4) as i:
        step.loop(i, 12)
        for b in range(4):
            tap = lambda n: m.cols[:, bass.ds(i * 16 + (tap_at + 4 * b + n), 1)]
            bank, half = m.banks[b], acc[:, b % 2, :]
            dve.wait_ge(m.w_used, i * 4 + (u1 + b + 1))
            dve.wait_ge(silu_done, i * 4 + (b + 1))
            if bias:
                shift = m.cols[:, bass.ds(i * 4 + (m.ins["col_at"][bias] + b), 1)]
                step(dve.tensor_scalar(half, bank[:, :], tap(3), shift, ALU.mult, ALU.add))
            else:
                step(dve.tensor_scalar(half, bank[:, :], tap(3), None, ALU.mult))
            for late in (1, 2):
                step(dve.scalar_tensor_tensor(half[:, late:], bank[:, 0:SEQ - late], tap(3 - late),
                                              half[:, late:], ALU.mult, ALU.add))
            dve.scalar_tensor_tensor(half[:, 3:], bank[:, 0:SEQ - 3], tap(0), half[:, 3:],
                                     ALU.mult, ALU.add).then_inc(conv_done, 1)
        step.end_loop(tiles // 4)


def silu_convolved(act, tiles, conved, acc, silu_done, conv_done):
    act.sem_inc(silu_done, 2)
    with act.Fori(0, tiles // 2) as i:
        for b in range(2):
            act.wait_ge(conv_done, i * 2 + (4 + b + 1))
            act.activation(conved[:, i * 2 + b, :], acc[:, b, :], ACT.Silu).then_inc(silu_done, 1)


def split_small(pool, w, parts, loaded, split):
    pool.wait_ge(loaded, 16)
    pool.tensor_copy(parts[:, 0, :, :], w[:, :, :]).then_inc(split, 1)
    pool.wait_ge(split, 1)
    pool.tensor_tensor(parts[:, 1, :, :], w[:, :, :], parts[:, 0, :, :], ALU.subtract).then_inc(split, 1)


def small_out(pe, h, parts, width, bank, split, done):
    pe.wait_ge(split, 2)
    for t in range(TT):
        for k in range(DT):
            for a, b in PASSES:
                mm = pe.matmul(bank[:, t * width:(t + 1) * width], h[a][:, k, t * P:(t + 1) * P], parts[:, b, k, :],
                               start=(k == 0 and (a, b) == PASSES[0]), stop=(k == DT - 1 and (a, b) == PASSES[-1]))
    mm.then_inc(done, 1)


def mamba_in(m, z_gate, conved, dt_raw):
    nc, ins = m.nc, m.ins
    ZC = DI // 512
    with ExitStack() as c:
        sb = lambda n, s, d=F32: c.enter_context(nc.sbuf_tensor(n, s, d))
        sem = lambda n: m.sem(c, n)
        h = [sb(f"ssm_h_{x}", [P, DT, SEQ], F32R) for x in ("high", "low")]
        m.open_parts(c)
        w_dt_parts = sb("ssm_w_dt_parts", [P, 2, DT, HEADS], F32R)
        acc = sb("ssm_acc", [P, 2, SEQ])
        w_dt = sb("ssm_w_dt", [P, DT, HEADS])
        scaled = conved[:, 0:TT * 2, :].rearrange("p (t a) n -> p t (a n)", t=TT)
        norm = NormTurn(m, c, "ssm_norm", m.resid, scaled, h, lambda k: m.col("pre_norm0", k), TT, D, m.banks[0:2])
        z_done, z_read = sem("ssm_z_done"), sem("ssm_z_read")
        conv_done, silu_done = sem("ssm_conv_done"), sem("ssm_silu_done")
        dt_done, dt_loaded, dt_split = sem("ssm_dt_done"), sem("ssm_dt_loaded"), sem("ssm_dt_split")
        u0 = m.unit
        u1 = u0 + 4 * ZC
        block = c.enter_context(nc.Block())

        @block.sync
        def _(sp):
            sp.dma_start(w_dt[:, :, :], ins["ssm_w_dt"]).then_inc(dt_loaded, 16)
            stream_weights(m, sp, 4 * ZC + CM_T)

        @block.gpsimd
        def _(pool):
            split_weights(m, pool, 4 * ZC + CM_T)
            split_small(pool, w_dt, w_dt_parts, dt_loaded, dt_split)

        @block.tensor
        def _(pe):
            norm.tensor(pe)
            pe.wait_ge(norm.turned_ready, DT)

            def before_bank(ch, t):
                if ch >= 2:
                    pe.wait_ge(z_read, 4 * (ch - 2) + t + 1)

            tokens_out(m, pe, ZC, DT, h, TT, z_done, before_bank, lambda ch, t: m.banks[4 * (ch % 2) + t])
            pe.wait_ge(z_read, 4 * ZC)
            columns_out(m, pe, CM_T, h, SEQ, conv_done, 1, m.banks[0:4])
            small_out(pe, h, w_dt_parts, HEADS, m.banks[4], dt_split, dt_done)

        @block.vector
        def _(dve):
            step = m.steps(dve, m.dve_step)
            norm.vector(dve, step)
            norm.vector_turned(dve)
            convolve(m, dve, step, CM_T, u1, "ssm_conv_w", "ssm_conv_b", acc, silu_done, conv_done)
            m.keep(step)

        @block.scalar
        def _(act):
            norm.scalar_rstd(act)
            norm.scalar_turned(act)
            for ch in range(ZC):
                for t in range(TT):
                    wait_tokens(m, act, u0, DT, TT, z_done, ch, t)
                    act.activation(z_gate[:, t, ch * 512:(ch + 1) * 512], m.banks[4 * (ch % 2) + t][:, :],
                                   ACT.Silu).then_inc(z_read, 1)
            silu_convolved(act, CM_T, conved, acc, silu_done, conv_done)
            act.wait_ge(dt_done, 1)
            act.activation(dt_raw[:, :, :], m.banks[4][:, 0:TT * HEADS], ACT.Copy)


def mamba_scan(m, z_gate, conved, dt_raw, xs):
    nc, ins = m.nc, m.ins
    GW = HPG * HD
    with ExitStack() as c:
        sb = lambda n, s, d=F32: c.enter_context(nc.sbuf_tensor(n, s, d))
        sem = lambda n: m.sem(c, n)
        b_tok = sb("ssm_b_tok", [P, TT, GROUPS * STATE])
        dt = sb("ssm_dt", [P, TT, HEADS])
        dt_end = sb("ssm_dt_end", [P, TT, HEADS])
        a = sb("ssm_a", [P, TT, HEADS])
        grow = sb("ssm_grow", [P, TT, HEADS])
        whole = sb("ssm_whole", [P, TT, HEADS])
        tmp = sb("ssm_tmp", [P, 3, TT * HEADS])
        rows = sb("ssm_rows", [P, 3, HEADS])
        b_tiles = conved[:, XS_T:XS_T + BC_T, :]
        c_tiles = conved[:, XS_T + BC_T:, :]
        every = lambda ap: ap.rearrange("p (o h) -> p o h", o=1).broadcast_to([P, TT, HEADS])

        with ExitStack() as cb:
            sem1 = lambda n: m.sem(cb, n)
            rows_loaded, turned, by_act, by_dve = sem1("ssm_rows_loaded"), sem1("ssm_turned"), sem1("ssm_by_act"), sem1("ssm_by_dve")
            dve_dt, act_dt, pe_dt = sem1("ssm_dve_dt"), sem1("ssm_act_dt"), sem1("ssm_pe_dt")
            block = cb.enter_context(nc.Block())
            N_TURN = XS_T + BC_T

            def place(j):
                dst = xs if j < XS_T else b_tok
                jj = j if j < XS_T else j - XS_T
                return dst[:, :, jj * P:(jj + 1) * P]

            @block.sync
            def _(sp):
                for n, name in enumerate(("ssm_dt_bias", "ssm_a_log", "ssm_d")):
                    sp.dma_start(rows[:, n, :], m.row(name, HEADS)).then_inc(rows_loaded, 16)

            @block.tensor
            def _(pe):
                for j in range(N_TURN):
                    if j >= 4:
                        pe.wait_ge(by_act if j % 2 else by_dve, (j - 4) // 2 + 1)
                    for t in range(TT):
                        mm = pe.transpose(m.banks[j % 4][:, t * P:(t + 1) * P], conved[:, j, t * P:(t + 1) * P],
                                          m.ident[:, :])
                    mm.then_inc(turned, 1)
                pe.wait_ge(dve_dt, 3)
                pe.matmul(m.banks[4][:, 0:P], m.upto[:, :], a[:, :, :].rearrange("p t h -> p (t h)"),
                          start=True, stop=True)
                pe.matmul(m.banks[4][:, P:2 * P], m.ones[:, :], a[:, :, :].rearrange("p t h -> p (t h)"),
                          start=True, stop=True).then_inc(pe_dt, 1)

            @block.vector
            def _(dve):
                step = m.steps(dve, m.dve_step)
                dve.wait_ge(rows_loaded, 48)
                dve.tensor_tensor(dt[:, :, :], dt_raw[:, :, :], every(rows[:, 0, :]), ALU.add).then_inc(dve_dt, 1)
                dve.wait_ge(act_dt, 1)
                step(dve.scalar_tensor_tensor(dt[:, :, :], dt[:, :, :], 0.0,
                                              tmp[:, 0, :].rearrange("p (t h) -> p t h", t=TT), ALU.max, ALU.add))
                dve.scalar_tensor_tensor(a[:, :, :], dt[:, :, :], -1.0, every(rows[:, 1, :]), ALU.mult, ALU.mult)\
                   .then_inc(dve_dt, 2)
                for j in range(0, N_TURN, 2):
                    dve.wait_ge(turned, j + 1)
                    dve.tensor_copy(place(j), m.banks[j % 4][:, :].rearrange("p (t n) -> p t n", t=TT))\
                       .then_inc(by_dve, 1)
                dve.wait_ge(act_dt, 2)
                dve.tensor_tensor(tmp[:, 2, :], m.banks[4][:, P:2 * P], tmp[:, 1, :], ALU.subtract).then_inc(dve_dt, 1)
                dve.wait_ge(act_dt, 3)
                step(dve.tensor_tensor(dt_end[:, :, :], dt[:, :, :], dt_end[:, :, :], ALU.mult))
                m.keep(step)

            @block.scalar
            def _(act):
                step = m.steps(act, m.act_step)
                act.wait_ge(dve_dt, 1)
                u = tmp[:, 0, :]
                step(act.activation(u, dt[:, :, :].rearrange("p t h -> p (t h)"), ACT.Abs))
                step(act.activation(u, u, ACT.Exp, scale=-1.0))
                act.activation(rows[:, 1, :], rows[:, 1, :], ACT.Exp)
                act.activation(u, u, ACT.Ln, bias=1.0).then_inc(act_dt, 1)
                for j in range(1, N_TURN, 2):
                    act.wait_ge(turned, j + 1)
                    act.activation(place(j), m.banks[j % 4][:, :].rearrange("p (t n) -> p t n", t=TT), ACT.Copy)\
                       .then_inc(by_act, 1)
                act.wait_ge(pe_dt, 1)
                act.activation(grow[:, :, :].rearrange("p t h -> p (t h)"), m.banks[4][:, 0:P], ACT.Exp)
                act.activation(whole[:, :, :].rearrange("p t h -> p (t h)"), m.banks[4][:, P:2 * P], ACT.Exp)
                act.activation(tmp[:, 1, :], m.banks[4][:, 0:P], ACT.Copy).then_inc(act_dt, 1)
                act.wait_ge(dve_dt, 4)
                act.activation(dt_end[:, :, :].rearrange("p t h -> p (t h)"), tmp[:, 2, :], ACT.Exp).then_inc(act_dt, 1)
                m.keep(step)

        x_dt = conved[:, 0:8, :].rearrange("p (b a) n -> p b (a n)", b=2)
        x_end = conved[:, 8:16, :].rearrange("p (b a) n -> p b (a n)", b=2)
        cut = sb("ssm_cut", [P, 2, HPG, P])
        decay = sb("ssm_decay", [P, 2, HPG, P])
        cb_low = sb("ssm_cb_low", [P, 2, P])
        mix = sb("ssm_mix", [P, 2, HPG, P])
        state = sb("ssm_state", [P, GROUPS, GW])
        part = sb("ssm_part", [P, 2, GW])
        units = [(ch, g) for ch in range(TT) for g in range(GROUPS)]
        N = len(units)
        with ExitStack() as cb:
            sem1 = lambda n: m.sem(cb, n)
            cut_ready, seg_done, decay_ready = sem1("ssm_cut_ready"), sem1("ssm_seg_done"), sem1("ssm_decay_ready")
            mix_ready, y_done, y_read, state_ready = sem1("ssm_mix_ready"), sem1("ssm_y_done"), sem1("ssm_y_read"), sem1("ssm_state_ready")
            cb_done, xdt_ready, xend_ready, skip_ready = sem1("ssm_cb_done"), sem1("ssm_xdt_ready"), sem1("ssm_xend_ready"), sem1("ssm_skip_ready")
            block = cb.enter_context(nc.Block())
            heads = lambda ap: ap.rearrange("p (h d) -> p h d", d=HD)
            per_head = lambda ap, n: ap.rearrange("p (h o) -> p h o", o=1).broadcast_to([P, n, HD])

            @block.gpsimd
            def _(pool):
                for i, (ch, g) in enumerate(units):
                    if g == 0:
                        if ch >= 2:
                            pool.wait_ge(y_done, GROUPS * (ch - 1))
                        pool.tensor_tensor(heads(x_end[:, ch % 2, :]), heads(xs[:, ch, :]),
                                           per_head(dt_end[:, ch, :], HEADS), ALU.mult).then_inc(xend_ready, 1)
                    if i >= 2:
                        pool.wait_ge(seg_done, i - 1)
                    pool.tensor_tensor(cut[:, i % 2, :, :],
                                       m.upto[:, :].rearrange("p (o l) -> p o l", o=1).broadcast_to([P, HPG, P]),
                                       a[:, ch, g * HPG:(g + 1) * HPG].rearrange("p (h o) -> p h o", o=1)
                                       .broadcast_to([P, HPG, P]), ALU.mult).then_inc(cut_ready, 1)
                    if g == 0:
                        pool.wait_ge(xdt_ready, ch + 1)
                        pool.wait_ge(xend_ready, ch + 1)
                        pool.tensor_tensor(heads(xs[:, ch, :]), heads(xs[:, ch, :]), per_head(rows[:, 2, :], HEADS),
                                           ALU.mult).then_inc(skip_ready, 1)

            @block.tensor
            def _(pe):
                for i in range(N + 1):
                    if i < N:
                        ch, g = units[i]
                        pe.wait_ge(cut_ready, i + 1)
                        if i >= 2:
                            pe.wait_ge(decay_ready, i - 1)
                            pe.wait_ge(mix_ready, i - 1)
                        pe.matmul(m.banks[i % 2][:, :], m.after[:, :],
                                  cut[:, i % 2, :, :].rearrange("p h l -> p (h l)"), start=True, stop=True)\
                          .then_inc(seg_done, 1)
                        at = slice(ch * P, (ch + 1) * P)
                        pe.matmul(m.banks[2 + i % 2][:, 0:P], b_tiles[:, g, at], c_tiles[:, g, at],
                                  start=True, stop=True).then_inc(cb_done, 1)
                    if i >= 1:
                        j = i - 1
                        ch, g = units[j]
                        at = slice(ch * P, (ch + 1) * P)
                        yb, sbk = m.banks[4 + j % 2], m.banks[6 + j % 2]
                        pe.wait_ge(mix_ready, j + 1)
                        pe.wait_ge(xdt_ready, ch + 1)
                        pe.wait_ge(xend_ready, ch + 1)
                        if j >= 2:
                            pe.wait_ge(y_read, j - 1)
                            pe.wait_ge(state_ready, j - 1)
                        for r in range(HPG):
                            h0 = (g * HPG + r) * HD
                            pe.matmul(yb[:, r * HD:(r + 1) * HD], mix[:, j % 2, r, :], x_dt[:, ch % 2, h0:h0 + HD],
                                      start=True, stop=True)
                        if ch > 0:
                            pe.matmul(yb[:, GW:2 * GW], c_tiles[:, g, at], state[:, g, :], start=True, stop=True)
                        pe.matmul(sbk[:, 0:GW], b_tok[:, ch, g * STATE:(g + 1) * STATE],
                                  x_end[:, ch % 2, g * GW:(g + 1) * GW], start=True, stop=True).then_inc(y_done, 1)

            @block.scalar
            def _(act):
                for i in range(N):
                    act.wait_ge(seg_done, i + 1)
                    if i >= 2:
                        act.wait_ge(mix_ready, i - 1)
                    act.activation(decay[:, i % 2, :, :].rearrange("p h l -> p (h l)"), m.banks[i % 2][:, :],
                                   ACT.Exp).then_inc(decay_ready, 1)

            @block.vector
            def _(dve):
                step = m.steps(dve, m.dve_step)
                for i in range(N + 1):
                    if i < N:
                        ch, g = units[i]
                        if g == 0:
                            if ch >= 2:
                                dve.wait_ge(y_done, GROUPS * (ch - 1))
                            dve.tensor_tensor(heads(x_dt[:, ch % 2, :]), heads(xs[:, ch, :]),
                                              per_head(dt[:, ch, :], HEADS), ALU.mult).then_inc(xdt_ready, 1)
                        dve.wait_ge(cb_done, i + 1)
                        step(dve.tensor_tensor(cb_low[:, i % 2, :], m.banks[2 + i % 2][:, 0:P], m.upto[:, :], ALU.mult))
                        dve.wait_ge(decay_ready, i + 1)
                        if i >= 2:
                            dve.wait_ge(y_done, i - 1)
                        dve.tensor_tensor(mix[:, i % 2, :, :], decay[:, i % 2, :, :],
                                          cb_low[:, i % 2, :].rearrange("p (o l) -> p o l", o=1)
                                          .broadcast_to([P, HPG, P]), ALU.mult).then_inc(mix_ready, 1)
                    if i >= 1:
                        j = i - 1
                        ch, g = units[j]
                        yb, sbk = m.banks[4 + j % 2], m.banks[6 + j % 2]
                        here = slice(g * GW, (g + 1) * GW)
                        y = part[:, j % 2, :]
                        dve.wait_ge(y_done, j + 1)
                        dve.wait_ge(skip_ready, ch + 1)
                        if ch > 0:
                            step(dve.tensor_tensor(heads(y), heads(yb[:, GW:2 * GW]),
                                                   per_head(grow[:, ch, g * HPG:(g + 1) * HPG], HPG), ALU.mult))
                            step(dve.tensor_tensor(y, y, xs[:, ch, here], ALU.add))
                            y2 = y
                        else:
                            y2 = xs[:, ch, here]
                        dve.tensor_tensor(y, yb[:, 0:GW], y2, ALU.add).then_inc(y_read, 1)
                        if ch == 0:
                            dve.tensor_copy(state[:, g, :], sbk[:, 0:GW]).then_inc(state_ready, 1)
                        else:
                            step(dve.tensor_tensor(heads(state[:, g, :]), heads(state[:, g, :]),
                                                   per_head(whole[:, ch, g * HPG:(g + 1) * HPG], HPG), ALU.mult))
                            dve.tensor_tensor(state[:, g, :], state[:, g, :], sbk[:, 0:GW], ALU.add)\
                               .then_inc(state_ready, 1)
                        dve.wait_ge(y_read, j + 1)
                        dve.tensor_tensor(z_gate[:, ch, here], z_gate[:, ch, here], y, ALU.mult)
                m.keep(step)


def mamba_out(m, y):
    nc, ins = m.nc, m.ins
    with ExitStack() as c:
        scaled = c.enter_context(nc.sbuf_tensor("ssm_y_scaled", [P, TT, DI], F32))
        turned = [c.enter_context(nc.sbuf_tensor(f"ssm_y_{x}", [P, XS_T, SEQ], F32R)) for x in ("high", "low")]
        norm = NormTurn(m, c, "ssm_gnorm", y, scaled, turned, lambda k: m.col("ssm_gate_norm", k), TT, DI, m.banks[0:2])
        project_and_add(m, c, "ssm_o", norm, turned, DI // P, y[:, :, 0:D], "post_norm0")


def project_and_add(m, c, name, norm, turned, kt, y, gain, load=None):
    nc = m.nc
    sem = lambda n: m.sem(c, f"{name}_{n}")
    out_done, copied = sem("out_done"), sem("copied")
    if gain:
        gain_row = c.enter_context(nc.sbuf_tensor(name + "_gain", [P, D], F32))
        gain_loaded = sem("gain_loaded")
        post = PostNorm(m, c, name + "_post", y, gain_row, gain_loaded)
    m.open_parts(c)
    u0 = m.unit
    block = c.enter_context(nc.Block())

    @block.sync
    def _(sp):
        if load:
            load(sp)
        if gain:
            sp.dma_start(gain_row[:, :], m.row(gain, D)).then_inc(gain_loaded, 16)
        stream_weights(m, sp, 2 * kt // 2)

    @block.gpsimd
    def _(pool):
        split_weights(m, pool, 2 * kt // 2)

    @block.tensor
    def _(pe):
        if norm:
            norm.tensor(pe)
            pe.wait_ge(norm.turned_ready, kt)
        tokens_out(m, pe, 2, kt, turned, TT, out_done, lambda ch, t: None, lambda ch, t: m.banks[(4 * ch + t + 2) % 8])

    @block.vector
    def _(dve):
        step = m.steps(dve, m.dve_step)
        if norm:
            norm.vector(dve, step)
            norm.vector_turned(dve)
        if gain:
            dve.wait_ge(copied, 2 * TT)
            post.vector(dve, step)
        else:
            for ch in range(2):
                for t in range(TT):
                    wait_tokens(m, dve, u0, kt, TT, out_done, ch, t)
                    here = m.resid[:, t, ch * 512:(ch + 1) * 512]
                    dve.tensor_tensor(here, here, m.banks[(4 * ch + t + 2) % 8][:, :], ALU.add)
        m.keep(step)

    @block.scalar
    def _(act):
        if norm:
            norm.scalar_rstd(act)
            norm.scalar_turned(act)
        if gain:
            for ch in range(2):
                for t in range(TT):
                    wait_tokens(m, act, u0, kt, TT, out_done, ch, t)
                    act.activation(y[:, t, ch * 512:(ch + 1) * 512], m.banks[(4 * ch + t + 2) % 8][:, :], ACT.Copy)\
                       .then_inc(copied, 1)
            post.scalar(act)



class PlainTurn:

    def __init__(self, m, c, name, src, turned, tiles, width, banks):
        self.m, self.src, self.turned, self.tiles, self.width, self.banks = m, src, turned, tiles, width, banks
        self.turned_in_bank = m.sem(c, name + "_bank")
        self.high_ready = m.sem(c, name + "_high")
        self.turned_ready = m.sem(c, name + "_turned")

    def vector(self, dve, step):
        pass

    def scalar_rstd(self, act):
        pass

    def tensor(self, pe):
        for k in range(self.width // P):
            if k >= 2:
                pe.wait_ge(self.turned_ready, k - 1)
            for t in range(self.tiles):
                mm = pe.transpose(self.banks[k % 2][:, t * P:(t + 1) * P], self.src[:, t, k * P:(k + 1) * P],
                                  self.m.ident[:, :])
            mm.then_inc(self.turned_in_bank, 1)

    def scalar_turned(self, act):
        for k in range(self.width // P):
            act.wait_ge(self.turned_in_bank, k + 1)
            act.activation(self.turned[0][:, k, :], self.banks[k % 2][:, 0:self.tiles * P], ACT.Copy)\
               .then_inc(self.high_ready, 1)

    def vector_turned(self, dve):
        for k in range(self.width // P):
            dve.wait_ge(self.high_ready, k + 1)
            dve.tensor_tensor(self.turned[1][:, k, :], self.banks[k % 2][:, 0:self.tiles * P], self.turned[0][:, k, :],
                              ALU.subtract).then_inc(self.turned_ready, 1)


def attention(m):
    nc, ins = m.nc, m.ins
    with ExitStack() as c:
        sb = lambda n, s, d=F32: c.enter_context(nc.sbuf_tensor(n, s, d))
        qk = sb("att_qk", [P, TT, QW + KVW])
        v = sb("att_v", [P, TT, KVW])
        gate = sb("att_gate", [P, TT, QW])
        attention_in(m, qk, v, gate)
        turned = sb("att_turned", [P, (QW + KVW) // P, SEQ])
        attention_core(m, qk, v, gate, turned)
        with ExitStack() as c2:
            parts = [c2.enter_context(nc.sbuf_tensor(f"att_turned_{x}", [P, DT, SEQ], F32R)) for x in ("high", "low")]
            turn = PlainTurn(m, c2, "att_oturn", gate, parts, TT, QW, m.banks[0:2])
            project_and_add(m, c2, "att_o", turn, parts, DT, qk[:, :, 0:D], "post_norm1")


def attention_in(m, qk, v, gate):
    nc, ins = m.nc, m.ins
    import math
    with ExitStack() as c:
        sb = lambda n, s, d=F32: c.enter_context(nc.sbuf_tensor(n, s, d))
        sem = lambda n: m.sem(c, n)
        h = [sb(f"att_h_{x}", [P, DT, SEQ], F32R) for x in ("high", "low")]
        m.open_parts(c)
        scaled = sb("att_scaled", [P, TT, D])
        norm = NormTurn(m, c, "att_norm", m.resid, scaled, h, lambda k: m.col("pre_norm1", k), TT, D, m.banks[0:2])
        pos_i = sb("att_pos_i", [P, TT], I32)
        pos = sb("att_pos", [P, TT])
        freq = sb("att_freq", [P, HALF])
        ang = sb("att_ang", [P, 5, TT, HALF])
        rot = sb("att_rot", [P, 4, TT, QH + KVH, HALF])
        done, read, pos_loaded, sin_ready, ang_ready = (sem("att_in_done"), sem("att_in_read"), sem("att_pos_loaded"),
                                                        sem("att_sin_ready"), sem("att_ang_ready"))
        u0 = m.unit
        CH = 5
        block = c.enter_context(nc.Block())

        @block.sync
        def _(sp):
            sp.dma_start(pos_i[:, :], ins["positions"]).then_inc(pos_loaded, 16)
            stream_weights(m, sp, CH * DT // 2)

        @block.gpsimd
        def _(pool):
            split_weights(m, pool, CH * DT // 2)

        @block.tensor
        def _(pe):
            norm.tensor(pe)
            pe.wait_ge(norm.turned_ready, DT)

            def before_bank(ch, t):
                if ch >= 2:
                    pe.wait_ge(read, TT * (ch - 2) + t + 1)

            tokens_out(m, pe, CH, DT, h, TT, done, before_bank, lambda ch, t: m.banks[4 * (ch % 2) + t])

        @block.scalar
        def _(act):
            norm.scalar_rstd(act)
            norm.scalar_turned(act)
            act.wait_ge(ang_ready, 1)
            act.activation(ang[:, 3:5, :, :], ang[:, 1:3, :, :], ACT.Sin).then_inc(sin_ready, 1)
            for ch in range(CH):
                for t in range(TT):
                    wait_tokens(m, act, u0, DT, TT, done, ch, t)
                    bank = m.banks[4 * (ch % 2) + t]
                    if ch < 2:
                        act.activation(qk[:, t, ch * 512:(ch + 1) * 512], bank[:, :], ACT.Copy).then_inc(read, 1)
                    elif ch == 2:
                        act.activation(qk[:, t, QW:QW + KVW], bank[:, 0:KVW], ACT.Copy)
                        act.activation(v[:, t, :], bank[:, KVW:2 * KVW], ACT.Copy).then_inc(read, 1)
                    else:
                        act.activation(gate[:, t, (ch - 3) * 512:(ch - 2) * 512], bank[:, :], ACT.Silu)\
                           .then_inc(read, 1)

        @block.vector
        def _(dve):
            step = m.steps(dve, m.dve_step)
            norm.vector(dve, step)
            norm.vector_turned(dve)
            for j in range(HALF):
                dve.memset(freq[:, j:j + 1], THETA ** (-2.0 * j / ROPE))
            dve.wait_ge(pos_loaded, 16)
            step(dve.tensor_copy(pos[:, :], pos_i[:, :]))
            x, turns = ang[:, 0, :, :], ang[:, 2, :, :]
            step(dve.tensor_tensor(x, pos[:, :].rearrange("p (t o) -> p t o", o=1).broadcast_to([P, TT, HALF]),
                                   freq[:, :].rearrange("p (o j) -> p o j", o=1).broadcast_to([P, TT, HALF]),
                                   ALU.mult))
            big = 1.5 * 2.0 ** 23
            step(dve.tensor_scalar(turns, x, 1.0 / (2 * math.pi), big, ALU.mult, ALU.add))
            step(dve.tensor_scalar(turns, turns, big, None, ALU.subtract))
            c1 = 6.28125
            c2 = round((2 * math.pi - c1) * 2.0 ** 19) / 2.0 ** 19
            c3 = 2 * math.pi - c1 - c2
            for part in (c1, c2, c3):
                step(dve.scalar_tensor_tensor(x, turns, -part, x, ALU.mult, ALU.add))
            step(dve.tensor_scalar(ang[:, 1, :, :], x, 3.1415925, -3.1415925, ALU.min, ALU.max))
            step(dve.tensor_scalar(ang[:, 2, :, :], ang[:, 1, :, :], -1.0, None, ALU.mult))
            step(dve.tensor_tensor(ang[:, 2, :, :], ang[:, 2, :, :], ang[:, 1, :, :], ALU.min))
            dve.tensor_scalar(ang[:, 2, :, :], ang[:, 2, :, :], math.pi / 2, None, ALU.add).then_inc(ang_ready, 1)
            dve.wait_ge(sin_ready, 1)
            dve.wait_ge(read, 3 * TT)
            n = QH + KVH
            for t in range(TT):
                heads = qk[:, t, :].rearrange("p (h d) -> p h d", d=AD)
                lo, hi = heads[:, :, 0:HALF], heads[:, :, HALF:ROPE]
                every = lambda ap: ap.rearrange("p (o j) -> p o j", o=1).broadcast_to([P, n, HALF])
                sin, cos = every(ang[:, 3, t, :]), every(ang[:, 4, t, :])
                dve.tensor_tensor(rot[:, 0, t, :, :], lo, cos, ALU.mult)
                dve.tensor_tensor(rot[:, 1, t, :, :], hi, sin, ALU.mult)
                dve.tensor_tensor(rot[:, 2, t, :, :], hi, cos, ALU.mult)
                step(dve.tensor_tensor(rot[:, 3, t, :, :], lo, sin, ALU.mult))
                dve.tensor_tensor(lo, rot[:, 0, t, :, :], rot[:, 1, t, :, :], ALU.subtract)
                dve.tensor_tensor(hi, rot[:, 2, t, :, :], rot[:, 3, t, :, :], ALU.add)
            m.keep(step)


def attention_core(m, qk, v, gate, turned):
    nc, ins = m.nc, m.ins
    NQ = QW // P
    with ExitStack() as c:
        sb = lambda n, s, d=F32: c.enter_context(nc.sbuf_tensor(n, s, d))
        sem = lambda n: m.sem(c, n)
        mask = sb("att_mask", [P, 2 * P])
        sinks = sb("att_sinks", [P, QH])
        s = sb("att_s", [P, 2, 4, 2 * P])
        p = sb("att_p", [P, 2, 4, 2 * P])
        pt = sb("att_pt", [P, 2, 4, 2 * P])
        stat = sb("att_stat", [P, 2, 8, 4])
        rden = sb("att_rden", [P, 4, 4])
        o = sb("att_ov", [P, 2, 4 * AD])
        sink_loaded, mask_made, turn_done, turn_read = (sem("att_sink_loaded"), sem("att_mask_made"),
                                                        sem("att_turn_done"), sem("att_turn_read"))
        scores_done, stat_ready, exp_done, pt_done, pt_ready, pv_done, out_ready = (
            sem("att_scores_done"), sem("att_stat_ready"), sem("att_exp_done"), sem("att_pt_done"),
            sem("att_pt_ready"), sem("att_pv_done"), sem("att_out_ready"))
        units = [(n, jj) for n in range(TT) for jj in range(4)]
        N = len(units)
        NT = (QW + KVW) // P
        lo_of = lambda n: P if n == 0 else 0
        block = c.enter_context(nc.Block())

        @block.sync
        def _(sp):
            sp.dma_start(sinks[:, :], m.row("att_sinks", QH)).then_inc(sink_loaded, 16)

        @block.gpsimd
        def _(pool):
            pool.memset(mask[:, :], 0.0).then_inc(mask_made, 1)
            pool.wait_ge(mask_made, 1)
            pool.affine_select(out=mask[:, 0:P], in_=mask[:, 0:P], compare_op=ALU.is_gt, fill=-1e30, base=0,
                               pattern=[[1, P]], channel_multiplier=-1)
            pool.affine_select(out=mask[:, P:], in_=mask[:, P:], compare_op=ALU.is_ge, fill=-1e30, base=0,
                               pattern=[[-1, P]], channel_multiplier=1).then_inc(mask_made, 1)

        @block.tensor
        def _(pe):
            for j in range(NT):
                if j >= 8:
                    pe.wait_ge(turn_read, j - 7)
                for t in range(TT):
                    mm = pe.transpose(m.banks[j % 8][:, t * P:(t + 1) * P], qk[:, t, j * P:(j + 1) * P], m.ident[:, :])
                mm.then_inc(turn_done, 1)
            pe.wait_ge(turn_read, NT)
            for i in range(N + 2):
                if i < N:
                    n, jj = units[i]
                    if i >= 2:
                        pe.wait_ge(stat_ready, 2 * (i - 1))
                    lo = lo_of(n)
                    for x in range(2):
                        j = 2 * jj + x
                        for b in range(2):
                            part = slice(64 * b, 64 * b + 64)
                            mm = pe.matmul(m.banks[2 * (i % 2) + b][:, x * 256 + lo:(x + 1) * 256],
                                           turned[part, j, n * P:(n + 1) * P],
                                           turned[part, NQ + j // 4, (n - 1) * P + lo:(n + 1) * P],
                                           start=True, stop=True)
                    mm.then_inc(scores_done, 1)
                if 1 <= i <= N:
                    u = i - 1
                    n, jj = units[u]
                    pe.wait_ge(exp_done, u + 1)
                    if u >= 1:
                        pe.wait_ge(pt_ready, u)
                    halves = (1,) if n == 0 else (0, 1)
                    for half in halves:
                        for q in range(4):
                            mm = pe.transpose(m.banks[4 + half][:, q * P:(q + 1) * P],
                                              p[:, u % 2, q, half * P:(half + 1) * P], m.ident[:, :])
                    mm.then_inc(pt_done, 1)
                if i >= 2:
                    u = i - 2
                    n, jj = units[u]
                    pe.wait_ge(pt_ready, u + 1)
                    if u >= 2:
                        pe.wait_ge(out_ready, u - 1)
                    halves = (1,) if n == 0 else (0, 1)
                    for q in range(4):
                        x, b = q // 2, q % 2
                        kv = 2 * ((2 * jj + x) // 4) + b
                        for half in halves:
                            mm = pe.matmul(m.banks[6 + u % 2][:, q * AD:(q + 1) * AD],
                                           pt[:, u % 2, q, half * P:(half + 1) * P],
                                           v[:, n - 1 + half, kv * AD:(kv + 1) * AD],
                                           start=(half == halves[0]), stop=(half == 1))
                    mm.then_inc(pv_done, 1)

        @block.vector
        def _(dve):
            step = m.steps(dve, m.dve_step)
            dve.wait_ge(sink_loaded, 16)
            dve.wait_ge(mask_made, 2)
            for i in range(N + 2):
                if i < N:
                    n, jj = units[i]
                    lo = lo_of(n)
                    w = 2 * P - lo
                    st = stat[:, i % 2, :, :]
                    dve.wait_ge(scores_done, i + 1)
                    if i >= 2:
                        dve.wait_ge(exp_done, i - 1)
                    for b in range(2):
                        bank = m.banks[2 * (i % 2) + b][:, :].rearrange("p (x k) -> p x k", x=2)[:, :, lo:]
                        step(dve.scalar_tensor_tensor(
                            s[:, i % 2, b:4:2, lo:], bank, AD ** -0.5,
                            mask[:, lo:].rearrange("p (o k) -> p o k", o=1).broadcast_to([P, 2, w]),
                            ALU.mult, ALU.add))
                    step(dve.tensor_reduce(st[:, 0, :], s[:, i % 2, :, lo:], AX.X, ALU.max))
                    step(dve.tensor_tensor(st[:, 0, :], st[:, 0, :], sinks[:, 4 * jj:4 * jj + 4], ALU.max))
                    dve.tensor_scalar(st[:, 1, :], st[:, 0, :], -1.0, None, ALU.mult).then_inc(stat_ready, 1)
                    dve.tensor_tensor(st[:, 2, :], sinks[:, 4 * jj:4 * jj + 4], st[:, 0, :], ALU.subtract)\
                       .then_inc(stat_ready, 1)
                if i >= 2:
                    u = i - 2
                    n, jj = units[u]
                    st = stat[:, u % 2, :, :]
                    out = o[:, u % 2, :]
                    per_head = lambda ap: ap.rearrange("p (h o) -> p h o", o=1).broadcast_to([P, 4, AD])
                    dve.wait_ge(pv_done, u + 1)
                    step(dve.tensor_tensor(out.rearrange("p (h d) -> p h d", d=AD),
                                           m.banks[6 + u % 2][:, 0:4 * AD].rearrange("p (h d) -> p h d", d=AD),
                                           per_head(rden[:, u % 4, :]), ALU.mult))
                    here = gate[:, n, 4 * jj * AD:4 * (jj + 1) * AD]
                    dve.tensor_tensor(here, here, out, ALU.mult).then_inc(out_ready, 1)
                if 1 <= i <= N:
                    u = i - 1
                    st = stat[:, u % 2, :, :]
                    dve.wait_ge(exp_done, u + 1)
                    step(dve.tensor_tensor(st[:, 5, :], st[:, 3, :], st[:, 4, :], ALU.add))
                    step(dve.reciprocal(rden[:, u % 4, :], st[:, 5, :]))
            m.keep(step)

        @block.scalar
        def _(act):
            for j in range(NT):
                act.wait_ge(turn_done, j + 1)
                act.activation(turned[:, j, :], m.banks[j % 8][:, :], ACT.Copy).then_inc(turn_read, 1)
            for i in range(N + 1):
                if i < N:
                    n, jj = units[i]
                    lo = lo_of(n)
                    st = stat[:, i % 2, :, :]
                    act.wait_ge(stat_ready, 2 * (i + 1))
                    if i >= 2:
                        act.wait_ge(pt_done, i - 1)
                    for q in range(4):
                        act.activation(p[:, i % 2, q, lo:], s[:, i % 2, q, lo:], ACT.Exp, bias=st[:, 1, q:q + 1],
                                       accum_out=st[:, 3, q:q + 1])
                    act.activation(st[:, 4, :], st[:, 2, :], ACT.Exp).then_inc(exp_done, 1)
                if i >= 1:
                    u = i - 1
                    n, jj = units[u]
                    act.wait_ge(pt_done, u + 1)
                    if u >= 2:
                        act.wait_ge(pv_done, u - 1)
                    halves = (1,) if n == 0 else (0, 1)
                    for half in halves:
                        cp = act.activation(pt[:, u % 2, :, half * P:(half + 1) * P],
                                            m.banks[4 + half][:, :].rearrange("p (q k) -> p q k", q=4), ACT.Copy)
                    cp.then_inc(pt_ready, 1)



HC_T = 3 * GH + 2 * MH


def hybrid(m):
    nc = m.nc
    with ExitStack() as c:
        sb = lambda n, s, d=F32: c.enter_context(nc.sbuf_tensor(n, s, d))
        conved = sb("hyb_conved", [P, HC_T, SEQ])
        gate = sb("hyb_gate", [P, TT, D])
        v_one = sb("hyb_v_one", [P, TT, MH, MD + 1])
        small = sb("hyb_small", [P, TT, 16])
        hybrid_in(m, conved, gate, v_one, small)
        mixed = sb("hyb_mixed", [P, TT, GH + MH, GD])
        with ExitStack() as c2:
            delta_net(m, c2, conved, mixed, small)
        with ExitStack() as c2:
            mlstm(m, c2, conved, mixed, v_one, small)
        hybrid_out(m, mixed, gate, conved)


def hybrid_in(m, conved, gate, v_one, small):
    nc, ins = m.nc, m.ins
    with ExitStack() as c:
        sb = lambda n, s, d=F32: c.enter_context(nc.sbuf_tensor(n, s, d))
        sem = lambda n: m.sem(c, n)
        h = [sb(f"hyb_h_{x}", [P, DT, SEQ], F32R) for x in ("high", "low")]
        m.open_parts(c)
        w_small_parts = sb("hyb_w_small_parts", [P, 2, DT, 16], F32R)
        scaled = sb("hyb_scaled", [P, TT, D])
        acc = sb("hyb_acc", [P, 2, SEQ])
        w_small = sb("hyb_w_small", [P, DT, 16])
        norm = NormTurn(m, c, "hyb_norm", m.resid, scaled, h, lambda k: m.col("norm_mix", k), TT, D, m.banks[0:2])
        done, read, small_loaded, small_done = (sem("hyb_in_done"), sem("hyb_in_read"), sem("hyb_small_loaded"),
                                                sem("hyb_small_done"))
        conv_done, silu_done, small_split = sem("hyb_conv_done"), sem("hyb_silu_done"), sem("hyb_small_split")
        CH = 3
        u0 = m.unit
        u1 = u0 + CH * DT // 2
        block = c.enter_context(nc.Block())

        @block.sync
        def _(sp):
            sp.dma_start(w_small[:, :, :], ins["hyb_w_small"]).then_inc(small_loaded, 16)
            stream_weights(m, sp, CH * DT // 2 + HC_T)

        @block.gpsimd
        def _(pool):
            split_weights(m, pool, CH * DT // 2 + HC_T)
            split_small(pool, w_small, w_small_parts, small_loaded, small_split)

        @block.tensor
        def _(pe):
            norm.tensor(pe)
            pe.wait_ge(norm.turned_ready, DT)

            def before_bank(ch, t):
                if ch >= 2:
                    pe.wait_ge(read, TT * (ch - 2) + t + 1)

            tokens_out(m, pe, CH, DT, h, TT, done, before_bank, lambda ch, t: m.banks[4 * (ch % 2) + t])
            pe.wait_ge(read, TT * CH)
            columns_out(m, pe, HC_T, h, SEQ, conv_done, 1, m.banks[0:4])
            small_out(pe, h, w_small_parts, 16, m.banks[4], small_split, small_done)

        @block.vector
        def _(dve):
            step = m.steps(dve, m.dve_step)
            norm.vector(dve, step)
            norm.vector_turned(dve)
            dve.memset(v_one[:, :, :, MD:MD + 1], 1.0)
            convolve(m, dve, step, HC_T, u1, "hyb_conv_w", None, acc, silu_done, conv_done)
            m.keep(step)

        @block.scalar
        def _(act):
            norm.scalar_rstd(act)
            norm.scalar_turned(act)
            for ch in range(CH):
                for t in range(TT):
                    wait_tokens(m, act, u0, DT, TT, done, ch, t)
                    bank = m.banks[4 * (ch % 2) + t][:, :]
                    if ch == 0:
                        act.activation(gate[:, t, 0:512], bank, ACT.Silu).then_inc(read, 1)
                    elif ch == 1:
                        act.activation(v_one[:, t, :, 0:MD], bank.rearrange("p (h d) -> p h d", h=MH), ACT.Copy)\
                           .then_inc(read, 1)
                    else:
                        act.activation(gate[:, t, 512:], bank, ACT.Sigmoid).then_inc(read, 1)
            silu_convolved(act, HC_T, conved, acc, silu_done, conv_done)
            act.wait_ge(small_done, 1)
            act.activation(small[:, :, :], m.banks[4][:, 0:TT * 16], ACT.Copy)


def spread(ap, n):
    return ap.rearrange("p (k o) -> p k o", o=1).broadcast_to([ap.shape[0], ap.shape[1], n])


def again(ap, n):
    return ap.rearrange("p (o k) -> p o k", o=1).broadcast_to([ap.shape[0], n, ap.shape[1]])


def delta_net(m, c, conved, mixed, small):
    nc, ins = m.nc, m.ins
    sb = lambda n, s, d=F32: c.enter_context(nc.sbuf_tensor(n, s, d))
    q_ch, k_ch = conved[:, 0:GH, :], conved[:, GH:2 * GH, :]
    k_tok = sb("gdn_k", [P, TT, GH, GD])
    v_tok = sb("gdn_v", [P, TT, GH, GD])
    k_in = sb("gdn_k_in", [P, TT, GH, GD])
    beta = sb("gdn_beta", [P, TT * GH])
    la = sb("gdn_la", [P, TT * GH])
    grow = sb("gdn_grow", [P, TT * GH])
    whole = sb("gdn_whole", [P, TT * GH])
    to_end = sb("gdn_to_end", [P, TT * GH])
    tmp = sb("gdn_tmp", [P, 4, TT * GH])
    rows = sb("gdn_rows", [P, 2, GH])
    flat = lambda ap: ap.rearrange("p a b -> p (a b)")

    with ExitStack() as cb:
        sem = lambda n: m.sem(cb, n)
        rows_loaded, dve_g, act_g, pe_g = sem("gdn_rows_loaded"), sem("gdn_dve_g"), sem("gdn_act_g"), sem("gdn_pe_g")
        sq_ready, sum_done, root_ready, unit_ready = sem("gdn_sq_ready"), sem("gdn_sum_done"), sem("gdn_root_ready"), sem("gdn_unit_ready")
        turned, turn_read = sem("gdn_turned"), sem("gdn_turn_read")
        square = cb.enter_context(nc.sbuf_tensor("gdn_square", [P, 2 * GH, SEQ], F32))
        eps = cb.enter_context(nc.sbuf_tensor("gdn_eps", [P, 1], F32))
        NL = 2 * GH
        block = cb.enter_context(nc.Block())

        @block.sync
        def _(sp):
            sp.dma_start(rows[:, 0, :], m.row("gdn_dt_bias", GH)).then_inc(rows_loaded, 16)
            sp.dma_start(rows[:, 1, :], m.row("gdn_a_log", GH)).then_inc(rows_loaded, 16)

        @block.tensor
        def _(pe):
            pe.wait_ge(dve_g, 3)
            pe.matmul(m.banks[6][:, 0:TT * GH], m.upto[:, :], la[:, :], start=True, stop=True)
            pe.matmul(m.banks[6][:, 16:16 + TT * GH], m.ones[:, :], la[:, :], start=True, stop=True).then_inc(pe_g, 1)
            for j in range(NL):
                pe.wait_ge(sq_ready, j + 1)
                if j >= 4:
                    pe.wait_ge(root_ready, j - 3)
                pe.matmul(m.banks[j % 4][:, :], m.ones[:, :], square[:, j, :], start=True, stop=True)\
                  .then_inc(sum_done, 1)
            for j in range(NL):
                src = 2 * GH + j if j < GH else j
                if j >= GH:
                    pe.wait_ge(unit_ready, src + 1)
                if j >= 2:
                    pe.wait_ge(turn_read, j - 1)
                for t in range(TT):
                    mm = pe.transpose(m.banks[4 + j % 2][:, t * P:(t + 1) * P], conved[:, src, t * P:(t + 1) * P],
                                      m.ident[:, :])
                mm.then_inc(turned, 1)

        @block.scalar
        def _(act):
            step = m.steps(act, m.act_step)
            for j in range(NL):
                act.activation(square[:, j, :], conved[:, j, :], ACT.Square).then_inc(sq_ready, 1)
            act.wait_ge(dve_g, 1)
            step(act.activation(tmp[:, 1, :], tmp[:, 0, :], ACT.Abs))
            act.activation(beta[:, :], small[:, :, GH:2 * GH], ACT.Sigmoid)
            step(act.activation(tmp[:, 1, :], tmp[:, 1, :], ACT.Exp, scale=-1.0))
            act.activation(rows[:, 1, :], rows[:, 1, :], ACT.Exp)
            act.activation(tmp[:, 1, :], tmp[:, 1, :], ACT.Ln, bias=1.0).then_inc(act_g, 1)
            act.wait_ge(pe_g, 1)
            act.activation(grow[:, :], m.banks[6][:, 0:TT * GH], ACT.Exp)
            act.activation(whole[:, :], m.banks[6][:, 16:16 + TT * GH], ACT.Exp)
            act.activation(tmp[:, 2, :], m.banks[6][:, 0:TT * GH], ACT.Copy).then_inc(act_g, 1)
            act.wait_ge(dve_g, 4)
            act.activation(to_end[:, :], tmp[:, 3, :], ACT.Exp).then_inc(act_g, 1)
            act.wait_ge(dve_g, 5)
            for j in range(NL):
                act.wait_ge(sum_done, j + 1)
                act.activation(square[:, j, :], m.banks[j % 4][:, :], ACT.Sqrt, bias=eps[:, 0:1]).then_inc(root_ready, 1)
            for j in range(NL):
                act.wait_ge(turned, j + 1)
                dst = v_tok if j < GH else k_tok
                act.activation(dst[:, :, j % GH, :], m.banks[4 + j % 2][:, :].rearrange("p (t n) -> p t n", t=TT),
                               ACT.Copy).then_inc(turn_read, 1)
            m.keep(step)

        @block.vector
        def _(dve):
            step = m.steps(dve, m.dve_step)
            dve.wait_ge(rows_loaded, 32)
            t3 = lambda ap: ap.rearrange("p (t h) -> p t h", t=TT)
            dve.tensor_tensor(t3(tmp[:, 0, :]), small[:, :, 0:GH], again(rows[:, 0, :], TT), ALU.add).then_inc(dve_g, 1)
            dve.wait_ge(act_g, 1)
            step(dve.scalar_tensor_tensor(tmp[:, 0, :], tmp[:, 0, :], 0.0, tmp[:, 1, :], ALU.max, ALU.add))
            dve.scalar_tensor_tensor(t3(la[:, :]), t3(tmp[:, 0, :]), -1.0, again(rows[:, 1, :], TT), ALU.mult, ALU.mult)\
               .then_inc(dve_g, 2)
            dve.wait_ge(act_g, 2)
            dve.tensor_tensor(tmp[:, 3, :], m.banks[6][:, 16:16 + TT * GH], tmp[:, 2, :], ALU.subtract).then_inc(dve_g, 1)
            dve.memset(eps[:, :], EPS).then_inc(dve_g, 1)
            for j in range(NL):
                dve.wait_ge(root_ready, j + 1)
                step(dve.reciprocal(square[:, j, :], square[:, j, :]))
                dve.tensor_tensor(conved[:, j, :], conved[:, j, :], square[:, j, :], ALU.mult).then_inc(unit_ready, 1)
            dve.wait_ge(turn_read, NL)
            dve.wait_ge(act_g, 3)
            step(dve.tensor_tensor(tmp[:, 0, :], beta[:, :], grow[:, :], ALU.mult))
            rows16 = lambda ap: ap.rearrange("p t h d -> p (t h) d")
            dve.tensor_tensor(rows16(v_tok[:, :, :, :]), rows16(v_tok[:, :, :, :]), spread(beta[:, :], GD), ALU.mult)
            step(dve.tensor_tensor(rows16(k_in[:, :, :, :]), rows16(k_tok[:, :, :, :]), spread(tmp[:, 0, :], GD), ALU.mult))
            dve.tensor_tensor(rows16(k_tok[:, :, :, :]), rows16(k_tok[:, :, :, :]), spread(to_end[:, :], GD), ALU.mult)
            m.keep(step)

    mats = lambda n: sb("gdn_" + n, [P, TT, GH * P])
    far_part, qk_t, W1, W2, X2, W3 = (mats(n) for n in ("far_part", "qk_t", "w1", "w2", "x2", "w3"))
    near_part = mixed[:, :, 0:GH, :].rearrange("p t h n -> p t (h n)")
    X1 = mixed[:, :, GH:, :].rearrange("p t h n -> p t (h n)")
    W4 = conved[:, 2 * GH:3 * GH, :]
    before = sb("gdn_before", [P, P])
    near = sb("gdn_near", [P, 4, P])
    first_level = [
        (X2, X1, [("copy", W1)]),
        (X1, X2, [("copy", W2), ("plus", W3)]),
        (W2, W1, [("plus", W4)]),
        (W3, W4, [("copy", W1)]),
        (X2, W1, [("copy", W2)]),
        (W1, X2, [("copy", W3)]),
    ]

    def next_level(L):
        return [
            (W3, L, [("copy", W1)]),
            (L, W3, [("copy", W4), ("minus", X1)]),
            (W1, W4, [("plus", X2)]),
            (X2, W2, [("copy", W1)]),
            (X1, W1, [("copy", W2)]),
            (W1, X1, [("copy", W3)]),
        ]

    inversion = first_level + next_level(near_part) + next_level(far_part)
    per4 = lambda ap: ap.rearrange("p (h n) -> p h n", h=GH)
    with ExitStack() as cb:
        sem = lambda n: m.sem(cb, n)
        made, cut_ready, exp_ready = sem("gdn_made"), sem("gdn_cut_ready"), sem("gdn_exp_ready")
        pe_done, bank_read = sem("gdn_pe_done"), sem("gdn_bank_read")
        block = cb.enter_context(nc.Block())
        blocks = lambda ap, n: ap.rearrange("p (b n) -> p b n", n=n)

        @block.gpsimd
        def _(pool):
            step = m.steps(pool, m.pool_step)
            pool.tensor_tensor(before[:, :], m.upto[:, :], m.ident[:, :], ALU.subtract)
            step(pool.memset(near[:, :, :], 1.0))
            for n, size in enumerate((8, 32)):
                step(pool.affine_select(out=blocks(near[:, n, :], size), in_=blocks(near[:, n, :], size),
                                        compare_op=ALU.is_ge, fill=0.0, base=0,
                                        pattern=[[-size, P // size], [0, size]], channel_multiplier=1))
                step(pool.affine_select(out=blocks(near[:, n, :], size), in_=blocks(near[:, n, :], size),
                                        compare_op=ALU.is_ge, fill=0.0, base=size - 1,
                                        pattern=[[size, P // size], [0, size]], channel_multiplier=-1))
            pool.tensor_tensor(near[:, 2, :], near[:, 1, :], near[:, 0, :], ALU.subtract)
            pool.tensor_tensor(near[:, 3, :], near[:, 3, :], near[:, 1, :], ALU.subtract).then_inc(made, 1)
            for ch in range(TT):
                pool.tensor_tensor(per4(qk_t[:, ch, :]), again(m.upto[:, :], GH), spread(la[:, ch * GH:(ch + 1) * GH], P),
                                   ALU.mult).then_inc(cut_ready, 1)
            m.keep(step)

        @block.tensor
        def _(pe):
            def result(stage, ch):
                if stage >= 1:
                    pe.wait_ge(bank_read, TT * (stage - 1) + ch + 1)
                return m.banks[(TT * stage + ch) % 8]

            def four(bank, lhs, rhs):
                for h in range(GH):
                    mm = pe.matmul(bank[:, h * P:(h + 1) * P], lhs(h), rhs(h), start=True, stop=True)
                mm.then_inc(pe_done, 1)

            mat = lambda X, ch: (lambda h: X[:, ch, h * P:(h + 1) * P])
            chunk = lambda X, ch: (lambda h: X[:, h, ch * P:(ch + 1) * P])
            for ch in range(TT):
                pe.wait_ge(cut_ready, ch + 1)
                pe.matmul(result(0, ch)[:, :], m.after[:, :], qk_t[:, ch, :], start=True, stop=True).then_inc(pe_done, 1)
            for ch in range(TT):
                four(result(1, ch), chunk(k_ch, ch), chunk(k_ch, ch))
            for ch in range(TT):
                four(result(2, ch), chunk(k_ch, ch), chunk(q_ch, ch))
            for stage, X in ((3, W2), (4, X1)):
                for ch in range(TT):
                    bank = result(stage, ch)
                    for h in range(GH):
                        mm = pe.transpose(bank[:, h * P:(h + 1) * P], mat(X, ch)(h), m.ident[:, :])
                    mm.then_inc(pe_done, 1)
            stage = 5
            for lhs, rhs, _outs in inversion:
                for ch in range(TT):
                    four(result(stage, ch), mat(lhs, ch), mat(rhs, ch))
                stage += 1
            for ch in range(TT):
                four(result(stage, ch), lambda h: k_in[:, ch, h, :], mat(W3, ch))
            for ch in range(TT):
                four(result(stage + 1, ch), mat(W3, ch), lambda h: v_tok[:, ch, h, :])

        @block.scalar
        def _(act):
            for ch in range(TT):
                act.wait_ge(pe_done, ch + 1)
                act.activation(W1[:, ch, :], m.banks[ch][:, :], ACT.Exp).then_inc(exp_ready, 1)

        @block.vector
        def _(dve):
            step = m.steps(dve, m.dve_step)

            def result(stage, ch):
                dve.wait_ge(pe_done, TT * stage + ch + 1)
                return m.banks[(TT * stage + ch) % 8][:, :]

            dve.wait_ge(made, 1)
            for ch in range(TT):
                dve.wait_ge(exp_ready, ch + 1)
                dve.tensor_tensor(per4(W1[:, ch, :]), per4(W1[:, ch, :]), again(m.upto[:, :], GH), ALU.mult)\
                   .then_inc(bank_read, 1)
            for ch in range(TT):
                dve.wait_ge(bank_read, ch + 1)
                step(dve.tensor_tensor(W2[:, ch, :], result(1, ch), W1[:, ch, :], ALU.mult))
                dve.tensor_tensor(per4(W2[:, ch, :]), per4(W2[:, ch, :]), again(before[:, :], GH), ALU.mult)\
                   .then_inc(bank_read, 1)
            for ch in range(TT):
                dve.scalar_tensor_tensor(qk_t[:, ch, :], result(2, ch), GD ** -0.5, W1[:, ch, :], ALU.mult, ALU.mult)\
                   .then_inc(bank_read, 1)
            for ch in range(TT):
                far = far_part[:, ch, :]
                step(dve.tensor_tensor(per4(far), per4(result(3, ch)), spread(beta[:, ch * GH:(ch + 1) * GH], P), ALU.mult))
                dve.tensor_tensor(per4(near_part[:, ch, :]), per4(far), again(near[:, 2, :], GH), ALU.mult)
                step(dve.tensor_tensor(per4(X1[:, ch, :]), per4(far), again(near[:, 0, :], GH), ALU.mult))
                dve.tensor_tensor(per4(far), per4(far), again(near[:, 3, :], GH), ALU.mult).then_inc(bank_read, 1)
            for ch in range(TT):
                dve.tensor_copy(X2[:, ch, :], result(4, ch)).then_inc(bank_read, 1)
            stage = 5
            for _lhs, _rhs, outs in inversion:
                for ch in range(TT):
                    bank = result(stage, ch)
                    for kind, X in outs:
                        if kind == "copy":
                            last = dve.tensor_copy(X[:, ch, :], bank)
                        else:
                            last = dve.scalar_tensor_tensor(per4(X[:, ch, :]), per4(bank), 1.0 if kind == "plus" else -1.0,
                                                            again(m.ident[:, :], GH), ALU.mult, ALU.add)
                    if stage == 6:
                        last = dve.scalar_tensor_tensor(per4(X2[:, ch, :]), per4(X2[:, ch, :]), -1.0,
                                                        again(m.ident[:, :], GH), ALU.mult, ALU.add)
                    last.then_inc(bank_read, 1)
                stage += 1
            for X in (W1, W2):
                for ch in range(TT):
                    dve.tensor_copy(X[:, ch, :], result(stage, ch)).then_inc(bank_read, 1)
                stage += 1
            m.keep(step)

    w_t, u = W1, W2
    state = sb("gdn_state", [P, GH * GD])
    carry = sb("gdn_carry", [P, 2, GH * GD])
    with ExitStack() as cb:
        sem = lambda n: m.sem(cb, n)
        old_done, new_ready, new_done, state_ready, out_read = (sem("gdn_old_done"), sem("gdn_new_ready"), sem("gdn_new_done"),
                                                                sem("gdn_state_ready"), sem("gdn_out_read"))
        block = cb.enter_context(nc.Block())
        mat = lambda X, ch, h: X[:, ch, h * P:(h + 1) * P]
        head = lambda X, h: X[:, h * P:(h + 1) * P]

        @block.tensor
        def _(pe):
            for ch in range(TT):
                bw, bq, bo, bs = m.banks[4 * (ch % 2):4 * (ch % 2) + 4]
                if ch > 0:
                    pe.wait_ge(state_ready, ch)
                    if ch >= 2:
                        pe.wait_ge(out_read, ch - 1)
                    for h in range(GH):
                        pe.matmul(head(bw, h), mat(w_t, ch, h), head(state, h), start=True, stop=True)
                    for h in range(GH):
                        mm = pe.matmul(head(bq, h), q_ch[:, h, ch * P:(ch + 1) * P], head(state, h), start=True, stop=True)
                    mm.then_inc(old_done, 1)
                    pe.wait_ge(new_ready, ch)
                for h in range(GH):
                    pe.matmul(head(bo, h), mat(qk_t, ch, h), mat(u, ch, h), start=True, stop=True)
                for h in range(GH):
                    mm = pe.matmul(head(bs, h), k_tok[:, ch, h, :], mat(u, ch, h), start=True, stop=True)
                mm.then_inc(new_done, 1)

        @block.vector
        def _(dve):
            step = m.steps(dve, m.dve_step)
            for ch in range(TT):
                bw, bq, bo, bs = m.banks[4 * (ch % 2):4 * (ch % 2) + 4]
                mine = slice(ch * GH, (ch + 1) * GH)
                if ch > 0:
                    dve.wait_ge(old_done, ch)
                    dve.tensor_tensor(u[:, ch, :], u[:, ch, :], bw[:, :], ALU.subtract).then_inc(new_ready, 1)
                    old = carry[:, ch % 2, :]
                    step(dve.tensor_tensor(per4(old), per4(bq[:, :]), spread(grow[:, mine], GD), ALU.mult))
                dve.wait_ge(new_done, ch + 1)
                if ch > 0:
                    step(dve.tensor_tensor(per4(state[:, :]), per4(state[:, :]), spread(whole[:, mine], GD), ALU.mult))
                    dve.tensor_tensor(state[:, :], state[:, :], bs[:, :], ALU.add).then_inc(state_ready, 1)
                    dve.scalar_tensor_tensor(mixed[:, ch, 0:GH, :], per4(old), GD ** -0.5, per4(bo[:, :]), ALU.mult, ALU.add)\
                       .then_inc(out_read, 1)
                else:
                    dve.tensor_copy(state[:, :], bs[:, :]).then_inc(state_ready, 1)
                    dve.tensor_copy(mixed[:, ch, 0:GH, :], per4(bo[:, :])).then_inc(out_read, 1)
            m.keep(step)


def mlstm(m, c, conved, mixed, v_one, small):
    nc, ins = m.nc, m.ins
    sb = lambda n, s, d=F32: c.enter_context(nc.sbuf_tensor(n, s, d))
    q_ch, k_ch = conved[:, 3 * GH:3 * GH + MH, :], conved[:, 3 * GH + MH:, :]
    W = TT * MH
    rows = sb("mls_rows", [P, 2, MH])
    tmp = sb("mls_tmp", [P, 4, W])
    g = sb("mls_g", [P, W])
    by_head = sb("mls_by_head", [MH, 6, SEQ])
    at_start = sb("mls_at_start", [MH, TT + 1])
    last = sb("mls_last", [MH, TT])
    diag = sb("mls_diag", [MH, TT, MH])
    M_diag = sb("mls_M_diag", [MH, TT, MH, P])
    weights = sb("mls_weights", [P, 4, W])
    k_end = sb("mls_k_end", [P, TT, MH, MD])
    w_end = sb("mls_w_end", [P, W])
    G, B, MX, A1, A2, A3 = (by_head[:, n, :] for n in range(6))
    part = lambda ap, ch: ap[:, ch * P:(ch + 1) * P]
    with ExitStack() as cb:
        sem = lambda n: m.sem(cb, n)
        loaded, dve_p, act_p, pe_p, turned, turn_read = (sem("mls_loaded"), sem("mls_dve_p"), sem("mls_act_p"), sem("mls_pe_p"),
                                                        sem("mls_turned"), sem("mls_turn_read"))
        block = cb.enter_context(nc.Block())

        @block.sync
        def _(sp):
            sp.dma_start(rows[:, 0, :], m.row("mls_i_bias", MH)).then_inc(loaded, 16)
            sp.dma_start(rows[:, 1, :], m.row("mls_f_bias", MH)).then_inc(loaded, 16)

        @block.vector
        def _(dve):
            step = m.steps(dve, m.dve_step)
            t3 = lambda ap: ap.rearrange("p (t h) -> p t h", t=TT)
            dve.wait_ge(loaded, 32)
            dve.tensor_tensor(t3(tmp[:, 0, :]), small[:, :, 3 * MH:], again(rows[:, 1, :], TT), ALU.add).then_inc(dve_p, 1)
            dve.tensor_tensor(t3(g[:, :]), small[:, :, 2 * MH:3 * MH], again(rows[:, 0, :], TT), ALU.add)
            dve.wait_ge(act_p, 1)
            dve.scalar_tensor_tensor(tmp[:, 2, :], tmp[:, 0, :], 0.0, tmp[:, 1, :], ALU.min, ALU.subtract).then_inc(dve_p, 1)
            dve.wait_ge(pe_p, 1)
            step(dve.tensor_copy(tmp[:, 3, :], m.banks[0][:, 0:W]))
            dve.tensor_tensor(g[:, :], g[:, :], tmp[:, 3, :], ALU.subtract).then_inc(dve_p, 1)
            dve.wait_ge(pe_p, 2)
            step(dve.tensor_copy(G, m.banks[1][0:MH, :]))
            step(dve.tensor_copy(B, m.banks[2][0:MH, :]))
            step(dve.memset(at_start[:, 0:1], 0.0))
            for ch in range(TT):
                end = (ch + 1) * P - 1
                step(dve.tensor_tensor_scan(part(MX, ch), part(G, ch), part(G, ch), at_start[:, ch:ch + 1], ALU.max, ALU.max))
                step(dve.tensor_tensor(at_start[:, ch + 1:ch + 2], B[:, end:end + 1], MX[:, end:end + 1], ALU.add))
                dve.tensor_scalar(part(A1, ch), part(MX, ch), -1.0, at_start[:, ch:ch + 1], ALU.mult, ALU.add)
                dve.tensor_scalar(part(A3, ch), part(G, ch), MX[:, end:end + 1], None, ALU.subtract)
                dve.tensor_tensor(last[:, ch:ch + 1], at_start[:, ch:ch + 1], MX[:, end:end + 1], ALU.subtract)
                dve.tensor_tensor(M_diag[:, ch, :, :], again(part(MX, ch), MH), spread(m.ident[0:MH, 0:MH], P), ALU.mult)
            step(dve.scalar_tensor_tensor(A2, B, -1.0, MX, ALU.mult, ALU.subtract))
            dve.tensor_tensor(diag[:, :, :], spread(last[:, :], MH), again(m.ident[0:MH, 0:MH], TT), ALU.mult).then_inc(dve_p, 1)
            dve.wait_ge(act_p, 2)
            step(dve.tensor_scalar(w_end[:, :], weights[:, 2, :], MD ** -0.5, None, ALU.mult))
            dve.wait_ge(turn_read, MH)
            k16 = k_end[:, :, :, :].rearrange("p t h d -> p (t h) d")
            dve.tensor_tensor(k16, k16, spread(w_end[:, :], MD), ALU.mult)
            m.keep(step)

        @block.scalar
        def _(act):
            step = m.steps(act, m.act_step)
            act.wait_ge(dve_p, 1)
            step(act.activation(tmp[:, 1, :], tmp[:, 0, :], ACT.Abs))
            step(act.activation(tmp[:, 1, :], tmp[:, 1, :], ACT.Exp, scale=-1.0))
            act.activation(tmp[:, 1, :], tmp[:, 1, :], ACT.Ln, bias=1.0).then_inc(act_p, 1)
            for h in range(MH):
                act.wait_ge(turned, h + 1)
                act.activation(k_end[:, :, h, :], m.banks[4 + h % 2][:, :].rearrange("p (t n) -> p t n", t=TT), ACT.Copy)\
                   .then_inc(turn_read, 1)
            act.wait_ge(pe_p, 3)
            act.activation(weights[:, :, :].rearrange("p k w -> p (k w)"), m.banks[3][:, 0:4 * W], ACT.Exp).then_inc(act_p, 1)
            m.keep(step)

        @block.tensor
        def _(pe):
            for h in range(MH):
                if h >= 2:
                    pe.wait_ge(turn_read, h - 1)
                for t in range(TT):
                    mm = pe.transpose(m.banks[4 + h % 2][:, t * P:(t + 1) * P], k_ch[:, h, t * P:(t + 1) * P], m.ident[:, :])
                mm.then_inc(turned, 1)
            pe.wait_ge(dve_p, 2)
            pe.matmul(m.banks[0][:, 0:W], m.upto[:, :], tmp[:, 2, :], start=True, stop=True).then_inc(pe_p, 1)
            pe.wait_ge(dve_p, 3)
            for t in range(TT):
                pe.transpose(m.banks[1][0:MH, t * P:(t + 1) * P], g[:, t * MH:(t + 1) * MH], m.ident[:, :])
                mm = pe.transpose(m.banks[2][0:MH, t * P:(t + 1) * P], tmp[:, 3, t * MH:(t + 1) * MH], m.ident[:, :])
            mm.then_inc(pe_p, 1)
            pe.wait_ge(dve_p, 4)
            for n, rowset in enumerate((A1, A2, A3)):
                for t in range(TT):
                    pe.transpose(m.banks[3][:, n * W + t * MH:n * W + (t + 1) * MH], part(rowset, t), m.ident[0:MH, 0:MH])
            pe.matmul(m.banks[3][:, 3 * W:4 * W], m.ones[0:MH, :], diag[:, :, :].rearrange("p t h -> p (t h)"),
                      start=True, stop=True).then_inc(pe_p, 1)

    fade = sb("mls_fade", [P, TT, MH, P])
    state = sb("mls_state", [P, MH, MD + 1])
    acc = sb("mls_acc", [P, 2, MH, MD + 1])
    den = sb("mls_den", [P, 2, 3, MH])
    with ExitStack() as cb:
        sem = lambda n: m.sem(cb, n)
        m_done, gap_ready, fade_ready, low_ready, qk_done, p_ready = (sem("mls_m_done"), sem("mls_gap_ready"), sem("mls_fade_ready"),
                                                                    sem("mls_low_ready"), sem("mls_qk_done"), sem("mls_p_ready"))
        out_done, out_read, state_ready = sem("mls_out_done"), sem("mls_out_read"), sem("mls_state_ready")
        two = lambda n: m.banks[n][:, 0:2 * (MD + 1)].rearrange("p (h d) -> p h d", h=2)
        block = cb.enter_context(nc.Block())

        @block.tensor
        def _(pe):
            for ch in range(TT):
                if ch >= 2:
                    pe.wait_ge(gap_ready, ch - 1)
                pe.matmul(m.banks[ch % 2][:, :], m.ones[0:MH, :], M_diag[:, ch, :, :].rearrange("p h n -> p (h n)"),
                          start=True, stop=True).then_inc(m_done, 1)
            for ch in range(TT):
                at = slice(ch * P, (ch + 1) * P)
                pe.wait_ge(gap_ready, TT)
                if ch >= 2:
                    pe.wait_ge(p_ready, ch - 1)
                for h in range(MH):
                    mm = pe.matmul(m.banks[ch % 2][:, h * P:(h + 1) * P], k_ch[:, h, at], q_ch[:, h, at], start=True, stop=True)
                mm.then_inc(qk_done, 1)
                if ch > 0:
                    pe.wait_ge(out_read, ch)
                    pe.wait_ge(state_ready, ch)
                    for h in range(MH):
                        pe.matmul(two(4 + h // 2)[:, h % 2, :], q_ch[:, h, at], state[:, h, :], start=True, stop=True)
                for h in range(MH):
                    pe.matmul(two(6 + h // 2)[:, h % 2, :], k_end[:, ch, h, :], v_one[:, ch, h, :], start=True, stop=True)
                pe.wait_ge(p_ready, ch + 1)
                for h in range(MH):
                    mm = pe.matmul(two(2 + h // 2)[:, h % 2, :], fade[:, ch, h, :], v_one[:, ch, h, :], start=True, stop=True)
                mm.then_inc(out_done, 1)

        @block.scalar
        def _(act):
            for ch in range(TT):
                act.wait_ge(gap_ready, ch + 1)
                act.activation(fade[:, ch, :, :], fade[:, ch, :, :], ACT.Exp, scale=-1.0).then_inc(fade_ready, 1)

        @block.gpsimd
        def _(pool):
            for ch in range(TT):
                pool.wait_ge(fade_ready, ch + 1)
                pool.tensor_tensor(fade[:, ch, :, :], fade[:, ch, :, :], again(m.upto[:, :], MH), ALU.mult).then_inc(low_ready, 1)

        @block.vector
        def _(dve):
            step = m.steps(dve, m.dve_step)
            for ch in range(TT):
                dve.wait_ge(m_done, ch + 1)
                for h in range(MH):
                    col = g[:, ch * MH + h:ch * MH + h + 1]
                    gap = dve.tensor_scalar(fade[:, ch, h, :], m.banks[ch % 2][:, h * P:(h + 1) * P], col, 0.0,
                                            ALU.subtract, ALU.max)
                gap.then_inc(gap_ready, 1)
            for ch in range(TT):
                mine = slice(ch * MH, (ch + 1) * MH)
                dve.wait_ge(qk_done, ch + 1)
                dve.wait_ge(low_ready, ch + 1)
                dve.scalar_tensor_tensor(fade[:, ch, :, :], m.banks[ch % 2][:, :].rearrange("p (h n) -> p h n", h=MH),
                                         MD ** -0.5, fade[:, ch, :, :], ALU.mult, ALU.mult).then_inc(p_ready, 1)
                dve.wait_ge(out_done, ch + 1)
                a = acc[:, ch % 2, :, :]
                for x in range(2):
                    pair = slice(2 * x, 2 * x + 2)
                    if ch > 0:
                        step(dve.tensor_tensor(a[:, pair, :], two(4 + x), spread(weights[:, 0, ch * MH + 2 * x:ch * MH + 2 * x + 2], MD + 1), ALU.mult))
                        step(dve.tensor_tensor(a[:, pair, :], a[:, pair, :], two(2 + x), ALU.add))
                        step(dve.tensor_tensor(state[:, pair, :], state[:, pair, :], spread(weights[:, 3, ch * MH + 2 * x:ch * MH + 2 * x + 2], MD + 1), ALU.mult))
                        step(dve.tensor_tensor(state[:, pair, :], state[:, pair, :], two(6 + x), ALU.add))
                    else:
                        step(dve.tensor_copy(a[:, pair, :], two(2 + x)))
                        step(dve.tensor_copy(state[:, pair, :], two(6 + x)))
                dve.sem_inc(state_ready, 1)
                dve.sem_inc(out_read, 1)
                d = den[:, ch % 2, :, :]
                step(dve.tensor_scalar(d[:, 0, :], a[:, :, MD], -1.0, None, ALU.mult))
                step(dve.tensor_tensor(d[:, 0, :], d[:, 0, :], a[:, :, MD], ALU.max))
                step(dve.tensor_tensor(d[:, 1, :], d[:, 0, :], weights[:, 1, mine], ALU.max))
                step(dve.reciprocal(d[:, 2, :], d[:, 1, :]))
                dve.tensor_tensor(mixed[:, ch, GH:, :], a[:, :, 0:MD], spread(d[:, 2, :], MD), ALU.mult)
            m.keep(step)


class HeadNormTurn(PlainTurn):

    def __init__(self, m, c, name, mixed, gate, gains, gains_loaded, square, turned, banks):
        super().__init__(m, c, name, mixed.rearrange("p t h d -> p t (h d)"), turned, TT, D, banks)
        self.mixed, self.gate, self.gains, self.gains_loaded, self.square = mixed, gate, gains, gains_loaded, square
        self.stat = c.enter_context(m.nc.sbuf_tensor(name + "_stat", [P, 3, TT * (GH + MH)], F32))
        self.mean_ready, self.rstd_ready, self.done = (m.sem(c, name + x) for x in ("_mean", "_rstd", "_done"))

    def vector(self, dve, step):
        st, n = self.stat, GH + MH
        flat = lambda ap: ap.rearrange("p t h d -> p (t h) d")
        step(dve.tensor_tensor(flat(self.square), flat(self.mixed), flat(self.mixed), ALU.mult))
        step(dve.tensor_reduce(st[:, 0, :], flat(self.square), AX.X, ALU.add))
        step(dve.tensor_scalar(st[:, 1, :], st[:, 0, :], 1.0 / GD, EPS, ALU.mult, ALU.add))
        dve.reciprocal(st[:, 2, :], st[:, 1, :]).then_inc(self.mean_ready, 1)
        dve.wait_ge(self.gains_loaded, 16)
        for t in range(TT):
            step(dve.tensor_tensor(self.gate[:, t, :], self.gate[:, t, :], self.gains, ALU.mult))
        dve.wait_ge(self.rstd_ready, 1)
        for t in range(TT):
            step(dve.tensor_tensor(self.mixed[:, t, :, :], self.mixed[:, t, :, :], spread(st[:, 0, t * n:(t + 1) * n], GD), ALU.mult))
            dve.tensor_tensor(self.src[:, t, :], self.src[:, t, :], self.gate[:, t, :], ALU.mult).then_inc(self.done, 1)

    def scalar_rstd(self, act):
        act.wait_ge(self.mean_ready, 1)
        act.activation(self.stat[:, 0, :], self.stat[:, 2, :], ACT.Sqrt).then_inc(self.rstd_ready, 1)

    def tensor(self, pe):
        pe.wait_ge(self.done, TT)
        super().tensor(pe)


def hybrid_out(m, mixed, gate, conved):
    nc = m.nc
    with ExitStack() as c:
        gains = c.enter_context(nc.sbuf_tensor("hyb_gains", [P, D], F32))
        gains_loaded = m.sem(c, "hyb_gains_loaded")
        square = conved[:, 0:8, :].rearrange("p (t a) (b d) -> p t (a b) d", t=TT, d=GD)
        turned = [c.enter_context(nc.sbuf_tensor(f"hyb_turned_{x}", [P, DT, SEQ], F32R)) for x in ("high", "low")]
        turn = HeadNormTurn(m, c, "hyb_hnorm", mixed[:, :, :, :], gate, gains[:, :], gains_loaded, square,
                            turned, m.banks[0:2])
        project_and_add(m, c, "hyb_o", turn, turned, DT, None, None,
                        load=lambda sp: sp.dma_start(gains[:, :], m.row("hyb_gains", D)).then_inc(gains_loaded, 16))



MT = MEM // P


def copy_columns(m, act, n, u0, free, dst, banks, width):
    act.sem_inc(free, RING)
    with act.Fori(0, n // RING) as i:
        for b in range(RING):
            act.wait_ge(m.w_used, i * RING + (u0 + b + 1))
            act.activation(dst[:, i * RING + b, :], banks[b][:, 0:width], ACT.Copy).then_inc(free, 1)


def cross_attention(m):
    nc = m.nc
    with ExitStack() as c:
        sb = lambda n, s, d=F32: c.enter_context(nc.sbuf_tensor(n, s, d))
        q_ch = sb("xa_q", [P, DT, SEQ])
        k_ch = sb("xa_k", [P, DT, MEM])
        v_tok = sb("xa_v", [P, MT, D])
        cross_in(m, q_ch, k_ch, v_tok)
        o_ch = [sb(f"xa_o_{x}", [P, DT, SEQ], F32R) for x in ("high", "low")]
        cross_core(m, q_ch, k_ch, v_tok, o_ch)
        with ExitStack() as c2:
            project_and_add(m, c2, "xa_out", None, o_ch, DT, None, None)


def cross_in(m, q_ch, k_ch, v_tok):
    nc, ins = m.nc, m.ins
    with ExitStack() as c:
        sb = lambda n, s, d=F32: c.enter_context(nc.sbuf_tensor(n, s, d))
        sem = lambda n: m.sem(c, n)
        mem = sb("xa_mem", [P, MT, D])
        mem_scaled = sb("xa_mem_scaled", [P, MT, D])
        mem_h = [sb(f"xa_mem_h_{x}", [P, DT, MEM], F32R) for x in ("high", "low")]
        h = [sb(f"xa_h_{x}", [P, DT, SEQ], F32R) for x in ("high", "low")]
        m.open_parts(c)
        scaled = sb("xa_scaled", [P, TT, D])
        norm_m = NormTurn(m, c, "xa_mnorm", mem, mem_scaled, mem_h, lambda k: m.col("norm_mem", k), MT, D, m.banks[2:4])
        norm = NormTurn(m, c, "xa_norm", m.resid, scaled, h, lambda k: m.col("norm_xa", k), TT, D, m.banks[0:2])
        mem_loaded, q_copied, k_copied, v_done, v_copied = (sem("xa_mem_loaded"), sem("xa_q_copied"), sem("xa_k_copied"),
                                                           sem("xa_v_done"), sem("xa_v_copied"))
        u_q = m.unit
        u_k = u_q + DT
        u_v = u_k + DT
        block = c.enter_context(nc.Block())

        @block.sync
        def _(sp):
            sp.dma_start(mem[:, :, :], ins["mem"].rearrange("(t p) d -> p t d", p=P)).then_inc(mem_loaded, 16)
            stream_weights(m, sp, 2 * DT + 2 * DT // 2)

        @block.gpsimd
        def _(pool):
            split_weights(m, pool, 2 * DT + 2 * DT // 2)

        @block.tensor
        def _(pe):
            norm.tensor(pe)
            norm_m.tensor(pe)
            pe.wait_ge(norm.turned_ready, DT)
            columns_out(m, pe, DT, h, SEQ, q_copied, 1, m.banks[4:8])
            pe.wait_ge(norm_m.turned_ready, DT)
            pe.wait_ge(q_copied, RING + DT)
            columns_out(m, pe, DT, mem_h, MEM, k_copied, 1, m.banks[4:8])
            tokens_out(m, pe, 2, DT, mem_h, MT, v_done, lambda ch, t: None, lambda ch, t: m.banks[MT * ch + t])

        @block.vector
        def _(dve):
            step = m.steps(dve, m.dve_step)
            norm.vector(dve, step)
            dve.wait_ge(mem_loaded, 16)
            norm_m.vector(dve, step)
            norm.vector_turned(dve)
            norm_m.vector_turned(dve)
            m.keep(step)

        @block.scalar
        def _(act):
            norm.scalar_rstd(act)
            norm_m.scalar_rstd(act)
            norm.scalar_turned(act)
            norm_m.scalar_turned(act)
            copy_columns(m, act, DT, u_q, q_copied, q_ch, m.banks[4:8], SEQ)
            copy_columns(m, act, DT, u_k, k_copied, k_ch, m.banks[4:8], MEM)
            for ch in range(2):
                for t in range(MT):
                    wait_tokens(m, act, u_v, DT, MT, v_done, ch, t)
                    act.activation(v_tok[:, t, ch * 512:(ch + 1) * 512], m.banks[MT * ch + t][:, :], ACT.Copy)\
                       .then_inc(v_copied, 1)


def cross_core(m, q_ch, k_ch, v_tok, o_ch):
    nc = m.nc
    HT = XD // P
    SCALE = XD ** -0.5
    units = [(t, pair) for t in range(TT) for pair in range(XH // 2)]
    N = len(units)
    with ExitStack() as c:
        sb = lambda n, s, d=F32: c.enter_context(nc.sbuf_tensor(n, s, d))
        sem = lambda n: m.sem(c, n)
        p = sb("xa_p", [P, 2, 2, MEM])
        pt = sb("xa_pt", [P, XH, MT, SEQ])
        stat = sb("xa_stat", [P, 2, 4, 2])
        high_ready = sem("xa_o_high_ready")
        scores_done, max_ready, exp_done, p_ready, turned, turn_read, out_done = (
            sem("xa_scores_done"), sem("xa_max_ready"), sem("xa_exp_done"), sem("xa_p_ready"), sem("xa_turned"),
            sem("xa_turn_read"), sem("xa_out_done"))
        block = c.enter_context(nc.Block())

        @block.tensor
        def _(pe):
            for i in range(N + 1):
                if i < N:
                    t, pair = units[i]
                    if i >= 2:
                        pe.wait_ge(exp_done, i - 1)
                    for x in range(2):
                        for k in range(HT):
                            j = (2 * pair + x) * HT + k
                            mm = pe.matmul(m.banks[i % 2][:, x * MEM:(x + 1) * MEM], q_ch[:, j, t * P:(t + 1) * P],
                                           k_ch[:, j, :], start=(k == 0), stop=(k == HT - 1))
                    mm.then_inc(scores_done, 1)
                if i >= 1:
                    u = i - 1
                    pe.wait_ge(p_ready, u + 1)
                    if u >= 2:
                        pe.wait_ge(turn_read, u - 1)
                    for x in range(2):
                        for half in range(MT):
                            n = MT * x + half
                            mm = pe.transpose(m.banks[2 + u % 2][:, n * P:(n + 1) * P],
                                              p[:, u % 2, x, half * P:(half + 1) * P], m.ident[:, :])
                    mm.then_inc(turned, 1)
            pe.wait_ge(turn_read, N)
            for j in range(DT):
                for half in range(MT):
                    mm = pe.matmul(m.banks[(4 + j) % 8][:, :], v_tok[:, half, j * P:(j + 1) * P],
                                   pt[:, j // HT, half, :], start=(half == 0), stop=(half == MT - 1))
                mm.then_inc(out_done, 1)

        @block.vector
        def _(dve):
            step = m.steps(dve, m.dve_step)
            for i in range(N):
                st = stat[:, i % 2, :, :]
                dve.wait_ge(scores_done, i + 1)
                step(dve.tensor_reduce(st[:, 0, :], m.banks[i % 2][:, :].rearrange("p (x k) -> p x k", x=2), AX.X, ALU.max))
                dve.tensor_scalar(st[:, 1, :], st[:, 0, :], -SCALE, None, ALU.mult).then_inc(max_ready, 1)
                dve.wait_ge(exp_done, i + 1)
                step(dve.reciprocal(st[:, 3, :], st[:, 2, :]))
                for x in range(2):
                    mul = dve.tensor_scalar(p[:, i % 2, x, :], p[:, i % 2, x, :], st[:, 3, x:x + 1], None, ALU.mult)
                mul.then_inc(p_ready, 1)
            for j in range(DT):
                dve.wait_ge(high_ready, j + 1)
                dve.tensor_tensor(o_ch[1][:, j, :], m.banks[(4 + j) % 8][:, :], o_ch[0][:, j, :], ALU.subtract)
            m.keep(step)

        @block.scalar
        def _(act):
            for i in range(N + 1):
                if i < N:
                    st = stat[:, i % 2, :, :]
                    act.wait_ge(max_ready, i + 1)
                    if i >= 2:
                        act.wait_ge(turned, i - 1)
                    for x in range(2):
                        e = act.activation(p[:, i % 2, x, :], m.banks[i % 2][:, x * MEM:(x + 1) * MEM], ACT.Exp,
                                           bias=st[:, 1, x:x + 1], scale=SCALE, accum_out=st[:, 2, x:x + 1])
                    e.then_inc(exp_done, 1)
                if i >= 1:
                    u = i - 1
                    t, pair = units[u]
                    act.wait_ge(turned, u + 1)
                    act.activation(pt[:, 2 * pair:2 * pair + 2, :, t * P:(t + 1) * P],
                                   m.banks[2 + u % 2][:, :].rearrange("p (x a n) -> p x a n", x=2, a=MT), ACT.Copy)\
                       .then_inc(turn_read, 1)
            for j in range(DT):
                act.wait_ge(out_done, j + 1)
                act.activation(o_ch[0][:, j, :], m.banks[(4 + j) % 8][:, :], ACT.Copy).then_inc(high_ready, 1)



HP = 2 * PH
SLOTS = PH * TOPK
ROWS = 16
GROUP = 4


def peer(m):
    nc = m.nc
    with ExitStack() as c:
        sb = lambda n, s, d=F32: c.enter_context(nc.sbuf_tensor(n, s, d))
        h_tok = sb("peer_h_tok", [P, TT, D])
        choice = Choice(m, c)
        peer_in(m, h_tok, choice)
        peer_experts(m, h_tok, choice)


PART = PH // 2
PARTS = TT * 2


class Choice:

    def __init__(self, m, c):
        nc = m.nc
        self.m = m
        sb = lambda n, s, d=F32: c.enter_context(nc.sbuf_tensor(n, s, d))
        sem = lambda n: m.sem(c, n)
        self.gates = sb("peer_gates", [P, TT, SLOTS])
        self.ids = sb("peer_ids", [P, TT, SLOTS], U32)
        self.top_v = sb("peer_top_v", [P, TT, HP, TOPK])
        self.top_f = sb("peer_top_f", [P, TT, HP, TOPK])
        self.best_v = sb("peer_best_v", [P, PART, TOPK])
        self.place = sb("peer_place", [P, PART, TOPK], U32)
        self.digit = sb("peer_digit", [P, 2, PART, TOPK], U32)
        self.digit_f = sb("peer_digit_f", [P, 2, PART, TOPK])
        self.chosen = sb("peer_chosen", [P, 2, PART, TOPK])
        self.count = sb("peer_count", [P, TOPK])
        self.soft = sb("peer_soft", [P, PART, TOPK])
        self.total = sb("peer_total", [P, 2, PART])
        self.soft_in, self.soft_out, self.ids_ready, self.count_made = (
            sem("peer_soft_in"), sem("peer_soft_out"), sem("peer_ids_ready"), sem("peer_count_made"))

    def slots(self, k):
        return k // 2, slice((k % 2) * PART * TOPK, (k % 2 + 1) * PART * TOPK)

    def vector(self, dve, step, k, scratch):
        t, at = self.slots(k)
        heads = slice((k % 2) * 2 * PART, (k % 2 + 1) * 2 * PART)
        v4 = self.top_v[:, t, heads, :].rearrange("p (h two) k -> p h two k", two=2)
        f4 = self.top_f[:, t, heads, :].rearrange("p (h two) k -> p h two k", two=2)
        square = [P, PART, TOPK, TOPK]
        cand, left = (x.rearrange("p (h n) -> p h n", h=PART) for x in scratch[0:2])
        picked = scratch[2].rearrange("p (r n) -> p r n", n=TOPK)
        p4 = scratch[2].rearrange("p (h k n) -> p h k n", h=PART, k=TOPK)
        a = v4[:, :, 0, :].rearrange("p h (k o) -> p h k o", o=1).broadcast_to(square)
        b = v4[:, :, 1, :].rearrange("p h (o k) -> p h o k", o=1).broadcast_to(square)
        step(dve.tensor_tensor(cand.rearrange("p h (a b) -> p h a b", a=TOPK), a, b, ALU.add))
        best_16(dve, step, PART, lambda r: cand[:, r, :], lambda r: left[:, r, :], lambda r: self.best_v[:, r, :],
                lambda r: self.place[:, r, :])
        if k > 0:
            dve.wait_ge(self.soft_out, k)
        dve.tensor_tensor(self.soft[:, :, :], self.best_v[:, :, :],
                          self.best_v[:, :, 0:1].broadcast_to([P, PART, TOPK]), ALU.subtract).then_inc(self.soft_in, 1)
        dve.tensor_scalar(self.digit[:, 0, :, :], self.place[:, :, :], 4, None, ALU.logical_shift_right)
        step(dve.tensor_scalar(self.digit[:, 1, :, :], self.place[:, :, :], 15, None, ALU.bitwise_and))
        step(dve.tensor_copy(self.digit_f[:, :, :, :], self.digit[:, :, :, :]))
        for half in range(2):
            which = self.digit_f[:, half, :, :].rearrange("p h k -> p (h k)")
            step(dve.tensor_tensor(picked, spread(which, TOPK), again(self.count[:, :], PART * TOPK), ALU.is_equal))
            step(dve.tensor_tensor(p4, p4, f4[:, :, half, :].rearrange("p h (o k) -> p h o k", o=1).broadcast_to(square),
                                   ALU.mult))
            step(dve.tensor_reduce(self.chosen[:, half, :, :].rearrange("p h k -> p (h k)"), picked, AX.X, ALU.add))
        step(dve.scalar_tensor_tensor(self.chosen[:, 0, :, :], self.chosen[:, 0, :, :], float(KEYS), self.chosen[:, 1, :, :],
                                      ALU.mult, ALU.add))
        dve.tensor_copy(self.ids[:, t, at], self.chosen[:, 0, :, :].rearrange("p h k -> p (h k)"))\
           .then_inc(self.ids_ready, 1)
        dve.wait_ge(self.soft_out, k + 1)
        g3 = self.gates[:, t, at].rearrange("p (h k) -> p h k", h=PART)
        step(dve.tensor_reduce(self.total[:, 0, :], g3, AX.X, ALU.add))
        step(dve.reciprocal(self.total[:, 1, :], self.total[:, 0, :]))
        step(dve.tensor_tensor(g3, g3, spread(self.total[:, 1, :], TOPK), ALU.mult))

    def scalar(self, act, k):
        t, at = self.slots(k)
        act.wait_ge(self.soft_in, k + 1)
        act.activation(self.gates[:, t, at], self.soft[:, :, :].rearrange("p h k -> p (h k)"), ACT.Exp)\
           .then_inc(self.soft_out, 1)


def best_16(dve, step, n, values, left, out_v, out_i, hold=None):
    for pick in range(2):
        of = values if pick == 0 else left
        eight = slice(8 * pick, 8 * pick + 8)
        if hold is not None:
            dve.sem_inc(hold, 1)
        for r in range(n):
            last = dve.max(out_v(r)[:, eight], of(r))
        step(last)
        if hold is not None:
            dve.sem_inc(hold, 1)
        for r in range(n):
            last = dve.max_index(out_i(r)[:, eight], out_v(r)[:, eight], of(r))
        if pick == 0:
            for r in range(n):
                last = dve.match_replace(left(r), out_v(r)[:, eight], values(r), NEG)
        step(last)


def peer_in(m, h_tok, choice):
    nc, ins = m.nc, m.ins
    with ExitStack() as c:
        sb = lambda n, s, d=F32: c.enter_context(nc.sbuf_tensor(n, s, d))
        sem = lambda n: m.sem(c, n)
        h = [sb(f"peer_h_{x}", [P, DT, SEQ], F32R) for x in ("high", "low")]
        m.open_parts(c)
        gain = sb("peer_gain", [P, D])
        keys = sb("peer_keys", [P, HP, KEYS])
        q = sb("peer_q", [P, RING, SEQ])
        sc = sb("peer_sc", [P, RING, TT, KEYS])
        sc2 = sb("peer_sc2", [P, TT, KEYS])
        top = sb("peer_top", [P, TT, TOPK])
        top_i = sb("peer_top_i", [P, TT, TOPK], U32)
        scratch = sb("peer_scratch", [P, 3, PART * TOPK * TOPK])
        norm = NormTurn(m, c, "peer_norm", m.resid, h_tok, h, lambda k: m.col("norm_ffn", k), TT, D, m.banks[0:2])
        gain_loaded, keys_loaded, q_copied, scores_done, scores_read, sc_free = (
            sem("peer_gain_loaded"), sem("peer_keys_loaded"), sem("peer_q_copied"), sem("peer_scores_done"),
            sem("peer_scores_read"), sem("peer_sc_free"))
        held = sem("peer_index_held")
        u0 = m.unit
        m.unit += HP
        ORDER = [("q", 0), ("q", 1), ("s", 0), ("q", 2), ("s", 1), ("q", 3), ("s", 2), ("s", 3)]
        block = c.enter_context(nc.Block())

        @block.sync
        def _(sp):
            sp.dma_start(gain[:, :], m.row("norm_ffn", D)).then_inc(gain_loaded, 16)
            sp.dma_start(keys[:, :, :], ins["peer_keys"]).then_inc(keys_loaded, 16)
            stream_weights(m, sp, HP)

        @block.gpsimd
        def _(pool):
            pool.iota(choice.count[:, :], [[1, TOPK]], base=0, channel_multiplier=0,
                      allow_small_or_imprecise_dtypes=True).then_inc(choice.count_made, 1)
            split_weights(m, pool, HP)

        @block.tensor
        def _(pe):
            norm.tensor(pe)
            pe.wait_ge(norm.turned_ready, DT)
            pe.wait_ge(keys_loaded, 16)
            with pe.Fori(0, HP // RING) as i:
                for what, s in ORDER:
                    if what == "q":
                        pe.wait_ge(m.w_split, i * RING + (u0 + s + 1))
                        pe.wait_ge(q_copied, i * RING + (s + 1))
                        mm = column(m, pe, s, h, m.banks[4 + s][:, :])
                        mm.then_inc(m.w_used, 1)
                    else:
                        pe.wait_ge(q_copied, i * RING + (RING + s + 1))
                        pe.wait_ge(scores_read, i * RING + (s + 1))
                        for t in range(TT):
                            mm = pe.matmul(m.banks[s][:, t * KEYS:(t + 1) * KEYS], q[:, s, t * P:(t + 1) * P],
                                           keys[:, i * RING + s, :], start=True, stop=True)
                        mm.then_inc(scores_done, 1)

        @block.scalar
        def _(act):
            norm.scalar_rstd(act)
            norm.scalar_turned(act)
            act.sem_inc(q_copied, RING)
            act.sem_inc(scores_read, RING)

            def columns(i, first):
                for what, s in ORDER:
                    x = first + s
                    if what == "q":
                        act.wait_ge(m.w_used, i * RING + (u0 + x + 1))
                        act.activation(q[:, s, :], m.banks[4 + s][:, :], ACT.Copy).then_inc(q_copied, 1)
                    else:
                        act.wait_ge(scores_done, i * RING + (x + 1))
                        act.wait_ge(sc_free, i * RING + (x + 1))
                        act.activation(sc[:, s, :, :].rearrange("p t k -> p (t k)"), m.banks[s][:, :], ACT.Copy)\
                           .then_inc(scores_read, 1)

            with act.Fori(0, 2) as i:
                columns(i, 0)
            choice.scalar(act, 0)
            with act.Fori(0, 2) as i:
                columns(i, HP // 2)

        @block.vector
        def _(dve):
            step = m.steps(dve, m.dve_step)
            norm.vector(dve, step)
            norm.vector_turned(dve)
            dve.wait_ge(gain_loaded, 16)
            dve.wait_ge(norm.turned_in_bank, DT)
            for t in range(TT):
                dve.tensor_tensor(h_tok[:, t, :], h_tok[:, t, :], gain[:, :], ALU.mult)
            dve.sem_inc(sc_free, RING)
            dve.wait_ge(choice.count_made, 1)

            def columns(first):
                with dve.Fori(0, 2) as i:
                    step.loop(i, 5 * RING)
                    for s in range(RING):
                        dve.wait_ge(scores_read, i * RING + (RING + first + s + 1))
                        x = i * RING + (first + s)
                        best_16(dve, step, TT, lambda t: sc[:, s, t, :], lambda t: sc2[:, t, :],
                                lambda t: top[:, t, :], lambda t: top_i[:, t, :], held)
                        dve.sem_inc(sc_free, 1)
                        dve.tensor_copy(choice.top_v[:, :, x, :], top[:, :, :])
                        step(dve.tensor_copy(choice.top_f[:, :, x, :], top_i[:, :, :]))
                    step.end_loop(2)

            columns(0)
            choice.vector(dve, step, 0, [scratch[:, n, :] for n in range(3)])
            columns(HP // 2)
            m.keep(step)


def peer_experts(m, h_tok, choice):
    nc, ins = m.nc, m.ins
    gates, ids = choice.gates, choice.ids
    PER_PART = PART * TOPK
    TURNS = PER_PART // ROWS
    NG = ROWS // GROUP
    with ExitStack() as c:
        sb = lambda n, s, d=F32: c.enter_context(nc.sbuf_tensor(n, s, d))
        sem = lambda n: m.sem(c, n)
        rows = sb("peer_rows", [P, ROWS, 2 * D])
        at = sb("peer_at", [P, NG, GROUP], U32)
        dots = sb("peer_dots", [P, NG, GROUP])
        acts = sb("peer_acts", [P, NG, GROUP])
        weight = sb("peer_weight", [P, NG, GROUP])
        diag = sb("peer_diag", [P, 2 * GROUP, P])
        zero = sb("peer_zero", [P, P])
        loaded = [sem(f"peer_loaded{s}") for s in range(ROWS)]
        at_ready, held, dots_ready, acts_ready, weight_ready, diag_ready, row_used, zero_made = (
            sem("peer_at_ready"), sem("peer_held"), sem("peer_dots_ready"), sem("peer_acts_ready"), sem("peer_weight_ready"),
            sem("peer_diag_ready"), sem("peer_row_used"), sem("peer_zero_made"))
        scratch = [m.ring[:, s, 0:PART * TOPK * TOPK] for s in range(3)]
        block = c.enter_context(nc.Block())

        @block.gpsimd
        def _(pool):
            pool.memset(zero[:, :], 0.0).then_inc(zero_made, 1)
            pool.sem_inc(row_used, ROWS)
            for part in range(PARTS):
                t, begin = part // 2, (part % 2) * PER_PART
                pool.wait_ge(choice.ids_ready, part + 1)
                with pool.Fori(0, TURNS) as i:
                    for g in range(NG):
                        pool.wait_ge(row_used, i * ROWS + (part * PER_PART + GROUP * g + 1))
                        pool.sem_inc(held, 1)
                        pool.tensor_copy(at[:, g, :], ids[:, t, bass.ds(i * ROWS + (begin + GROUP * g), GROUP)])\
                            .then_inc(at_ready, 1)
                        pool.wait_ge(at_ready, i * NG + (part * TURNS * NG + g + 1))
                        pool.sem_inc(held, 1)
                        for r in range(GROUP):
                            s = GROUP * g + r
                            if r > 0:
                                pool.wait_ge(row_used, i * ROWS + (part * PER_PART + s + 1))
                                pool.sem_inc(held, 1)
                            pool.indirect_dma_start(rows[:, s, :], None, ins["peer_uv"],
                                                    bass.IndirectOffsetOnAxis(ap=at[:, g, r:r + 1], axis=0))\
                                .then_inc(loaded[s], 16)

        @block.vector
        def _(dve):
            step = m.steps(dve, m.dve_step)

            def turns(part, first, last):
                t, begin = part // 2, (part % 2) * PER_PART
                with dve.Fori(0, last - first) as i:
                    for g in range(NG):
                        for r in range(GROUP):
                            s = GROUP * g + r
                            dve.wait_ge(loaded[s], i * 16 + 16 * (part * TURNS + first + 1))
                            dot = dve.tensor_tensor_reduce(rows[:, s, 0:D], rows[:, s, 0:D], h_tok[:, t, :], 1.0, 0.0,
                                                           ALU.mult, ALU.add, dots[:, g, r:r + 1])
                        dot.then_inc(dots_ready, 1)
                        dve.wait_ge(acts_ready, i * NG + ((part * TURNS + first) * NG + g + 1))
                        dve.tensor_tensor(weight[:, g, :], acts[:, g, :],
                                          gates[:, t, bass.ds(i * ROWS + (begin + first * ROWS + GROUP * g), GROUP)],
                                          ALU.mult).then_inc(weight_ready, 1)

            for part in range(PARTS):
                turns(part, 0, 1)
                if part < PARTS - 1:
                    choice.vector(dve, step, part + 1, scratch)
                turns(part, 1, TURNS)
            for t in range(TT):
                dve.wait_ge(row_used, ROWS + SLOTS * TT)
                for half in range(2):
                    here = m.resid[:, t, half * 512:(half + 1) * 512]
                    dve.tensor_tensor(here, here, m.banks[2 * t + half][:, :], ALU.add)
            m.keep(step)

        @block.scalar
        def _(act):
            def turns(part, first, last):
                with act.Fori(0, last - first) as i:
                    for g in range(NG):
                        n = i * NG + ((part * TURNS + first) * NG + g + 1)
                        act.wait_ge(dots_ready, n)
                        act.activation(acts[:, g, :], dots[:, g, :], ACT.Gelu).then_inc(acts_ready, 1)
                        act.wait_ge(weight_ready, n)
                        for r in range(GROUP):
                            d = GROUP * (g % 2) + r
                            act.wait_ge(row_used, i * ROWS + (part * PER_PART + first * ROWS + GROUP * g + r + 1
                                                              + ROWS - 2 * GROUP))
                            act.activation(diag[:, d, :], m.ident[:, :], ACT.Copy, scale=weight[:, g, r:r + 1])\
                               .then_inc(diag_ready, 1)

            for part in range(PARTS):
                turns(part, 0, 1)
                if part < PARTS - 1:
                    choice.scalar(act, part + 1)
                turns(part, 1, TURNS)

        @block.tensor
        def _(pe):
            pe.wait_ge(zero_made, 1)
            for t in range(TT):
                for half in range(2):
                    pe.matmul(m.banks[2 * t + half][:, :], zero[:, :], h_tok[:, t, 0:512], start=True, stop=False,
                              skip_group_check=True)
                with pe.Fori(0, SLOTS // ROWS) as i:
                    for s in range(ROWS):
                        pe.wait_ge(diag_ready, i * ROWS + (t * SLOTS + s + 1))
                        for half in range(2):
                            mm = pe.matmul(m.banks[2 * t + half][:, :], diag[:, s % (2 * GROUP), :],
                                           rows[:, s, D + half * 512:D + (half + 1) * 512], start=False, stop=False,
                                           skip_group_check=True)
                        mm.then_inc(row_used, 1)


def final_norm(m, out):
    nc = m.nc
    with ExitStack() as c:
        sb = lambda n, s, d=F32: c.enter_context(nc.sbuf_tensor(n, s, d))
        sem = lambda n: m.sem(c, n)
        stat = sb("fin_stat", [P, 3, TT])
        gain = sb("fin_gain", [P, D])
        y = sb("fin_y", [P, TT, D])
        gain_loaded, mean_ready, rstd_ready, y_ready, stored = (sem("fin_gain_loaded"), sem("fin_mean"), sem("fin_rstd"),
                                                                sem("fin_y_ready"), sem("fin_stored"))
        block = c.enter_context(nc.Block())

        @block.sync
        def _(sp):
            sp.dma_start(gain[:, :], m.row("norm_final", D)).then_inc(gain_loaded, 16)
            for t in range(TT):
                sp.wait_ge(y_ready, t + 1)
                sp.dma_start(out[t * P:(t + 1) * P, :], y[:, t, :]).then_inc(stored, 16)
            sp.wait_ge(stored, 16 * TT)

        @block.vector
        def _(dve):
            step = m.steps(dve, m.dve_step)
            for t in range(TT):
                last = dve.tensor_tensor_reduce(y[:, t, :], m.resid[:, t, :], m.resid[:, t, :], 1.0, 0.0, ALU.mult,
                                                ALU.add, stat[:, 0, t:t + 1])
            step(last)
            step(dve.tensor_scalar(stat[:, 1, :], stat[:, 0, :], 1.0 / D, EPS, ALU.mult, ALU.add))
            dve.reciprocal(stat[:, 2, :], stat[:, 1, :]).then_inc(mean_ready, 1)
            dve.wait_ge(rstd_ready, 1)
            dve.wait_ge(gain_loaded, 16)
            for t in range(TT):
                dve.scalar_tensor_tensor(y[:, t, :], m.resid[:, t, :], stat[:, 0, t:t + 1], gain[:, :], ALU.mult,
                                         ALU.mult).then_inc(y_ready, 1)
            m.keep(step)

        @block.scalar
        def _(act):
            act.wait_ge(mean_ready, 1)
            act.activation(stat[:, 0, :], stat[:, 2, :], ACT.Sqrt).then_inc(rstd_ready, 1)



def column_units(w):
    import numpy as np
    kt, n = w.shape[0] // P, w.shape[1] // P
    return np.ascontiguousarray(w.reshape(kt, P, n, P).transpose(2, 1, 0, 3)).reshape(n, P, kt * P)


def token_units(w):
    import numpy as np
    kt, n = w.shape[0] // P, w.shape[1] // 512
    return np.ascontiguousarray(w.reshape(kt // 2, 2, P, n, 512).transpose(3, 0, 2, 1, 4)).reshape(n * kt // 2, P, UNIT)


def lay_out(a):
    import numpy as np
    units, col, row = [], [], []
    col_at, row_at = {}, {}

    def add_cols(name, v):
        col_at[name] = sum(x.shape[1] for x in col)
        col.append(v)

    def add_row(name, v):
        row_at[name] = sum(x.shape[0] for x in row)
        row.append(v.reshape(-1))

    def by_tile(v):
        return v.reshape(-1, P).T

    def taps(w):
        return w.reshape(CONV, -1, P).transpose(2, 1, 0).reshape(P, -1)

    w = a["ssm_w_in"][0]
    units += [token_units(w[:, 0:DI]), column_units(w[:, DI:DI + CM_T * P])]
    arrays = {"ssm_w_dt": w[:, DI + CM_T * P:].reshape(DT, P, HEADS).transpose(1, 0, 2)}
    units += [token_units(a["ssm_w_out"][0])]
    add_cols("pre_norm0", by_tile(a["pre_norm"][0]))
    add_cols("ssm_conv_w", taps(a["ssm_conv_w"][0]))
    add_cols("ssm_conv_b", by_tile(a["ssm_conv_b"][0]))
    add_cols("ssm_gate_norm", by_tile(a["ssm_gate_norm"][0]))
    add_row("ssm_dt_bias", a["ssm_dt_bias"][0])
    add_row("ssm_a_log", a["ssm_a_log"][0])
    add_row("ssm_d", a["ssm_d"][0])
    add_row("post_norm0", a["post_norm"][0])

    heads = lambda w: w.reshape(w.shape[0], QH, AD)[:, HEAD_ORDER].reshape(w.shape[0], QW)
    w = a["att_w_in"][0]
    units += [token_units(np.concatenate([heads(w[:, 0:QW]), w[:, QW:QW + 2 * KVW], heads(w[:, QW + 2 * KVW:])], axis=1))]
    units += [token_units(a["att_w_out"][0].reshape(QH, AD, D)[HEAD_ORDER].reshape(QW, D))]
    add_cols("pre_norm1", by_tile(a["pre_norm"][1]))
    add_row("att_sinks", a["att_sinks"][0][HEAD_ORDER])
    add_row("post_norm1", a["post_norm"][1])
    arrays["positions"] = a["positions"].reshape(TT, P).T

    w = a["w_in_2"][0]
    GW, MW = GH * GD, MH * MD
    cuts = np.cumsum([3 * GW, GW, GH, GH, 2 * MW, MW, MW, MH, MH])
    g_qkv, g_z, g_a, g_b, m_qk, m_v, m_o, m_i, m_f = np.split(w, cuts[:-1], axis=1)
    units += [token_units(np.concatenate([g_z, m_v, m_o], axis=1)), column_units(np.concatenate([g_qkv, m_qk], axis=1))]
    arrays["hyb_w_small"] = np.concatenate([g_a, g_b, m_i, m_f], axis=1).reshape(DT, P, 16).transpose(1, 0, 2)
    units += [token_units(a["w_out_2"][0])]
    add_cols("norm_mix", by_tile(a["norm_mix_w_2"][0]))
    add_cols("hyb_conv_w", taps(np.concatenate([a["gdn_conv_w_2"][0], a["mlstm_conv_w_2"][0]], axis=1)))
    add_row("gdn_dt_bias", a["gdn_dt_bias_2"][0])
    add_row("gdn_a_log", a["gdn_a_log_2"][0])
    add_row("mls_i_bias", a["mlstm_i_bias_2"][0])
    add_row("mls_f_bias", a["mlstm_f_bias_2"][0])
    add_row("hyb_gains", np.concatenate([a["gdn_norm_w_2"][0]] * GH + [a["mlstm_norm_w_2"][0]]))

    units += [column_units(a["xa_wq_2"][0]), column_units(a["xa_wkv_2"][0][:, 0:D]), token_units(a["xa_wkv_2"][0][:, D:])]
    units += [token_units(a["xa_wo_2"][0]), column_units(a["peer_wq_2"][0])]
    arrays["mem"] = a["mem_2"].reshape(MEM, D)
    add_cols("norm_xa", by_tile(a["norm_xa_w_2"][0]))
    add_cols("norm_mem", by_tile(a["norm_mem_w_2"][0]))
    add_cols("norm_ffn", by_tile(a["norm_ffn_w_2"][0]))
    add_row("norm_ffn", a["norm_ffn_w_2"][0])
    add_row("norm_final", a["norm_final_w_2"])
    arrays["peer_keys"] = a["peer_sub_keys_2"][0].reshape(HP, KEYS, P).transpose(2, 0, 1)
    arrays["peer_uv"] = np.concatenate([a["peer_u_2"][0], a["peer_v_2"][0]], axis=1)
    arrays["x"] = a["x"].reshape(SEQ, D)
    arrays["weights"] = np.concatenate(units)
    arrays["cols"] = np.concatenate(col, axis=1)
    arrays["rows"] = np.concatenate(row)[None, :]
    return arrays, col_at, row_at



STAGES = [mamba, attention, hybrid, cross_attention, peer]


def program(nc, ins, out):
    with ExitStack() as ctx:
        m = Machine(nc, ctx, ins)
        set_up(m)
        for stage in STAGES:
            stage(m)
            m.clear_signals()
        final_norm(m, out)



def kernel(**inputs):
    import numpy as np
    from concourse import bacc
    from concourse.bass_utils import run_bass_kernel_spmd

    laid, col_at, row_at = lay_out({k: np.asarray(v) for k, v in inputs.items()})
    nc = bacc.Bacc("TRN2", target_bir_lowering=False, num_devices=1)
    arrays, ins = {}, {"col_at": col_at, "row_at": row_at}
    for name, a in laid.items():
        a = np.ascontiguousarray(a)
        arrays[f"in_{name}"] = a
        ins[name] = nc.dram_tensor(f"in_{name}", a.shape, mybir.dt.from_np(a.dtype), kind="ExternalInput").ap()
    out = nc.dram_tensor("out_0", (SEQ, D), F32, kind="ExternalOutput").ap()
    program(nc, ins, out)
    r = run_bass_kernel_spmd(nc, [arrays], core_ids=[0])
    return r.results[0]["out_0"].reshape(1, SEQ, D)
```

```python
from contextlib import ExitStack

import concourse.bass as bass
from concourse import mybir

F32 = mybir.dt.float32
F32R = mybir.dt.float32r
U32 = mybir.dt.uint32
I32 = mybir.dt.int32
ALU = mybir.AluOpType
ACT = mybir.ActivationFunctionType
AX = mybir.AxisListType

P = 128
SEQ = 512
TT = SEQ // P
D = 1024
DT = D // P
EPS = 1e-6
RING = 4
UNIT = 1024

DI = 2048
HEADS, HD = 32, 64
GROUPS, STATE = 8, 128
HPG = HEADS // GROUPS
CONV = 4
XS_T, BC_T = DI // P, GROUPS * STATE // P
CM_T = XS_T + 2 * BC_T
QH, KVH, AD = 16, 4, 64
QW, KVW = QH * AD, KVH * AD
HEAD_ORDER = [8 * a + 4 * b + i for a in range(2) for i in range(4) for b in range(2)]
ROPE = AD // 4
HALF = ROPE // 2
THETA = 500000.0
GH, GD = 4, 128
MH, MD = 4, 128
MEM = 256
XH, XD = 4, 256
PH, KEYS, TOPK = 8, 128, 16
NEG = -3.0e38


class Steps:

    def __init__(self, eng, sem, start=0):
        self.eng, self.sem, self.n, self.turn = eng, sem, start, None

    def value(self):
        if self.turn is None:
            return self.n
        i, per, base = self.turn
        return i * per + (base + self.n)

    def __call__(self, ins):
        ins.then_inc(self.sem, 1)
        self.n += 1
        self.eng.wait_ge(self.sem, self.value())

    def loop(self, i, per):
        self.turn, self.n = (i, per, self.n), 0

    def end_loop(self, count):
        _, per, base = self.turn
        assert self.n == per
        self.turn, self.n = None, base + count * per


class Machine:

    def __init__(self, nc, ctx, ins, out):
        self.nc, self.ins, self.out = nc, ins, out
        self.spent = []
        self.steps_at = {}
        self.unit = 0
        self.streamed = 0
        self.banks = [ctx.enter_context(nc.psum_tensor(f"bank{i}", [P, 512], F32)) for i in range(8)]
        self.w_loaded = [ctx.enter_context(nc.semaphore(f"w_loaded{i}")) for i in range(RING)]
        self.w_high = ctx.enter_context(nc.semaphore("w_high"))
        self.w_split = ctx.enter_context(nc.semaphore("w_split"))
        self.w_held = ctx.enter_context(nc.semaphore("w_held"))
        self.w_used = ctx.enter_context(nc.semaphore("w_used"))
        self.split = 0
        self.parts = None
        self.dve_step = ctx.enter_context(nc.semaphore("dve_step"))
        self.act_step = ctx.enter_context(nc.semaphore("act_step"))
        self.pool_step = ctx.enter_context(nc.semaphore("pool_step"))
        sb = lambda n, s, d=F32: ctx.enter_context(nc.sbuf_tensor(n, s, d))
        self.ident = sb("ident", [P, P])
        self.ones = sb("ones", [P, P])
        self.zero = sb("zero", [P, 1])
        self.upto = sb("upto", [P, P])
        self.after = sb("after", [P, P])
        self.ring = sb("ring", [P, RING, UNIT])
        self.resid = sb("resid", [P, TT, D])
        self.cols = sb("cols", [P, ins["cols"].shape[1]])

    def sem(self, scope, name):
        handle = self.nc.alloc_semaphore(name)
        scope.callback(self.spent.append, handle)
        return handle

    def clear_signals(self):
        self.nc.clear_and_free_semaphores(self.spent)
        self.nc.all_engine_barrier()
        self.spent = []

    def open_parts(self, scope):
        self.parts = scope.enter_context(self.nc.sbuf_tensor(f"w_parts_{self.unit}", [P, 2, 2, UNIT], F32R))

    def steps(self, eng, sem):
        return Steps(eng, sem, self.steps_at.get(id(sem), 0))

    def keep(self, steps):
        self.steps_at[id(steps.sem)] = steps.n

    def row(self, name, width):
        return self.row_at(self.ins["row_at"][name], width)

    def row_at(self, at, width):
        r = self.ins["rows"]
        return bass.AP(tensor=r.tensor, offset=r.offset + at, ap=[[0, P], [1, width]])

    def col(self, name, i=0, n=1):
        at = self.ins["col_at"][name] + i
        return self.cols[:, at:at + n]



def stream_weights(m, sp, n):
    u0 = m.streamed
    assert u0 % RING == 0 and n % RING == 0
    w = m.ins["weights"]
    total = w.shape[0]
    n = min(n, total - u0)
    m.streamed += n
    if u0 == 0:
        for s in range(RING):
            sp.dma_start(m.ring[:, s, :], w[s]).then_inc(m.w_loaded[s], 16)
        u0, n = RING, n - RING
    if n <= 0:
        return
    with sp.Fori(0, n // RING) as i:
        for s in range(RING):
            sp.wait_ge(m.w_split, i * RING + (u0 - RING + s + 1))
            sp.dma_start(m.ring[:, s, :], w[i * RING + (u0 + s)]).then_inc(m.w_loaded[s], 16)


def split_weights(m, pool, n):
    u0 = m.split
    m.split += n

    zeros = m.zero[:, :].broadcast_to([P, UNIT])

    def four(i, first, fresh):
        for s in range(RING):
            pool.wait_ge(m.w_loaded[s], i * 16 + 16 * (first // RING + 1))
            pool.sem_inc(m.w_held, 1)
            if s >= 2 or not fresh:
                pool.wait_ge(m.w_used, i * RING + (first + s - 1))
                pool.sem_inc(m.w_held, 1)
            high, low = (m.parts[:, s % 2, x, :] for x in range(2))
            pool.tensor_tensor(high, m.ring[:, s, :], zeros, ALU.add).then_inc(m.w_high, 1)
            pool.wait_ge(m.w_high, i * RING + (first + s + 1))
            pool.sem_inc(m.w_held, 1)
            pool.tensor_tensor(low, m.ring[:, s, :], high, ALU.subtract).then_inc(m.w_split, 1)

    if u0 == 0:
        four(0, 0, True)
        u0, n = RING, n - RING
    with pool.Fori(0, n // RING) as i:
        four(i, u0, False)


def high_weight(m, act, u):
    act.wait_ge(m.w_loaded[u % RING], 16 * (u // RING + 1))
    act.wait_ge(m.w_used, u - 1)
    act.activation(m.parts[:, u % 2, 0, :], m.ring[:, u % RING, :], ACT.Copy).then_inc(m.w_high, 1)


def low_weights(m, pool, n):
    for u in range(m.split, m.split + n):
        pool.wait_ge(m.w_high, u + 1)
        pool.tensor_tensor(m.parts[:, u % 2, 1, :], m.ring[:, u % RING, :], m.parts[:, u % 2, 0, :], ALU.subtract)\
            .then_inc(m.w_split, 1)
    m.split += n


PASSES = ((0, 0), (0, 1), (1, 0))


def columns_out(m, pe, n, rhs, width, free, free0, banks):
    u0 = m.unit
    m.unit += n
    with pe.Fori(0, n // RING) as i:
        for s in range(RING):
            pe.wait_ge(m.w_split, i * RING + (u0 + s + 1))
            pe.wait_ge(free, i * RING + (free0 + s))
            mm = column(m, pe, s, rhs, banks[s][:, 0:width])
            mm.then_inc(m.w_used, 1)


def column(m, pe, s, rhs, out):
    for k in range(DT):
        for a, b in PASSES:
            mm = pe.matmul(out, m.parts[:, s % 2, a, k * P:(k + 1) * P], rhs[b][:, k, :],
                           start=(k == 0 and (a, b) == PASSES[0]), stop=(k == DT - 1 and (a, b) == PASSES[-1]))
    return mm


def tokens_out(m, pe, chunks, kt, lhs, tiles, done, before_bank, bank_of):
    for c in range(chunks):
        for kk in range(kt // 2):
            u = m.unit
            m.unit += 1
            pe.wait_ge(m.w_split, u + 1)
            for t in range(tiles):
                if kk == 0:
                    before_bank(c, t)
                for k in (2 * kk, 2 * kk + 1):
                    for a, b in PASSES:
                        mm = pe.matmul(bank_of(c, t)[:, :], lhs[a][:, k, t * P:(t + 1) * P],
                                       m.parts[:, u % 2, b, (k % 2) * 512:(k % 2 + 1) * 512],
                                       start=(k == 0 and (a, b) == PASSES[0]),
                                       stop=(k == kt - 1 and (a, b) == PASSES[-1]), skip_group_check=True)
                if kk == kt // 2 - 1:
                    if t < tiles - 1:
                        mm.then_inc(done, 1)
            mm.then_inc(m.w_used, 1)


def wait_tokens(m, eng, u0, kt, tiles, done, c, t):
    if t < tiles - 1:
        eng.wait_ge(done, (tiles - 1) * c + t + 1)
    else:
        eng.wait_ge(m.w_used, u0 + (c + 1) * kt // 2)



class NormTurn:

    def __init__(self, m, c, name, src, turned, gain, tiles, width, banks):
        self.m, self.src, self.turned = m, src, turned
        self.gain, self.tiles, self.width, self.banks = gain, tiles, width, banks
        nc = m.nc
        self.stat = c.enter_context(nc.sbuf_tensor(name + "_stat", [P, 3, tiles], F32))
        self.squares = c.enter_context(nc.sbuf_tensor(name + "_squares", [P, tiles, width], F32))
        self.diag = c.enter_context(nc.sbuf_tensor(name + "_diag", [P, tiles, P], F32))
        sem = lambda n: m.sem(c, f"{name}_{n}")
        self.sums_ready, self.mean_ready, self.rstd_ready, self.diag_ready = sem("sums"), sem("mean"), sem("rstd"), sem("diag")
        self.turned_in_bank, self.high_ready, self.turned_ready = sem("bank"), sem("high"), sem("turned")

    def scalar_sums(self, act):
        for t in range(self.tiles // 2, self.tiles):
            last = act.activation(self.squares[:, t, :], self.src[:, t, :], ACT.Square, accum_out=self.stat[:, 0, t:t + 1])
        last.then_inc(self.sums_ready, 1)

    def vector(self, dve, step):
        st = self.stat
        for t in range(self.tiles // 2):
            last = dve.tensor_tensor_reduce(self.squares[:, t, :], self.src[:, t, :], self.src[:, t, :], 1.0, 0.0,
                                            ALU.mult, ALU.add, st[:, 0, t:t + 1])
        step(last)
        dve.wait_ge(self.sums_ready, 1)
        step(dve.tensor_scalar(st[:, 1, :], st[:, 0, :], 1.0 / self.width, EPS, ALU.mult, ALU.add))
        dve.reciprocal(st[:, 2, :], st[:, 1, :]).then_inc(self.mean_ready, 1)
        dve.wait_ge(self.rstd_ready, 1)
        for t in range(self.tiles):
            dve.tensor_scalar(self.diag[:, t, :], self.m.ident[:, :], st[:, 0, t:t + 1], None, ALU.mult)\
               .then_inc(self.diag_ready, 1)

    def scalar_rstd(self, act):
        act.wait_ge(self.mean_ready, 1)
        act.activation(self.stat[:, 0, :], self.stat[:, 2, :], ACT.Sqrt).then_inc(self.rstd_ready, 1)

    def tensor(self, pe):
        pe.wait_ge(self.diag_ready, self.tiles)
        for k in range(self.width // P):
            if k >= len(self.banks):
                pe.wait_ge(self.turned_ready, k - len(self.banks) + 1)
            for t in range(self.tiles):
                mm = pe.matmul(self.banks[k % len(self.banks)][:, t * P:(t + 1) * P], self.src[:, t, k * P:(k + 1) * P],
                               self.diag[:, t, :], start=True, stop=True)
            mm.then_inc(self.turned_in_bank, 1)

    def scalar_turned(self, act):
        for k in range(self.width // P):
            act.wait_ge(self.turned_in_bank, k + 1)
            act.activation(self.turned[0][:, k, :], self.banks[k % len(self.banks)][:, 0:self.tiles * P], ACT.Copy,
                           scale=self.gain(k)).then_inc(self.high_ready, 1)

    def vector_turned(self, dve):
        for k in range(self.width // P):
            dve.wait_ge(self.high_ready, k + 1)
            dve.scalar_tensor_tensor(self.turned[1][:, k, :], self.banks[k % len(self.banks)][:, 0:self.tiles * P], self.gain(k),
                                     self.turned[0][:, k, :], ALU.mult, ALU.subtract).then_inc(self.turned_ready, 1)


class PostNorm:

    def __init__(self, m, c, name, y, gain_row, gain_loaded):
        self.m, self.y, self.gain_row, self.gain_loaded = m, y, gain_row, gain_loaded
        self.sums = c.enter_context(m.nc.sbuf_tensor(name + "_sums", [P, 2, TT], F32))
        self.stat = c.enter_context(m.nc.sbuf_tensor(name + "_stat", [P, 3, TT], F32))
        self.squares = c.enter_context(m.nc.sbuf_tensor(name + "_squares", [P, 2, TT, 512], F32))
        self.squared, self.mean_ready, self.rstd_ready = (m.sem(c, name + x) for x in ("_squared", "_mean", "_rstd"))

    def scalar_chunk(self, act, ch, t, bank):
        act.activation(self.squares[:, ch, t, :], bank, ACT.Square, accum_out=self.sums[:, ch, t:t + 1])\
           .then_inc(self.squared, 1)

    def vector(self, dve, step, bank_of):
        st, y = self.stat, self.y
        dve.wait_ge(self.gain_loaded, 16)
        for ch in range(2):
            for t in range(TT):
                here = slice(ch * 512, (ch + 1) * 512)
                dve.wait_ge(self.squared, TT * ch + t + 1)
                last = dve.tensor_tensor(y[:, t, here], bank_of(ch, t)[:, :], self.gain_row[:, here], ALU.mult)
        step(last)
        step(dve.tensor_tensor(st[:, 0, :], self.sums[:, 0, :], self.sums[:, 1, :], ALU.add))
        step(dve.tensor_scalar(st[:, 1, :], st[:, 0, :], 1.0 / D, EPS, ALU.mult, ALU.add))
        dve.reciprocal(st[:, 2, :], st[:, 1, :]).then_inc(self.mean_ready, 1)
        dve.wait_ge(self.rstd_ready, 1)
        for t in range(TT):
            dve.scalar_tensor_tensor(self.m.resid[:, t, :], y[:, t, :], st[:, 0, t:t + 1], self.m.resid[:, t, :],
                                     ALU.mult, ALU.add)

    def scalar(self, act):
        act.wait_ge(self.mean_ready, 1)
        act.activation(self.stat[:, 0, :], self.stat[:, 2, :], ACT.Sqrt).then_inc(self.rstd_ready, 1)



def set_up(m):
    nc = m.nc
    with ExitStack() as c:
        const = m.sem(c, "const")
        loaded = m.sem(c, "loaded")
        block = c.enter_context(nc.Block())

        @block.sync
        def _(sp):
            sp.dma_start(m.resid[:, :, :], m.ins["x"].rearrange("(t p) d -> p t d", p=P)).then_inc(loaded, 16)
            sp.dma_start(m.cols[:, :], m.ins["cols"]).then_inc(loaded, 16)
            stream_weights(m, sp, RING)
            sp.wait_ge(loaded, 32)

        @block.gpsimd
        def _(pool):
            pool.memset(m.zero[:, :], 0.0)
            pool.memset(m.ident[:, :], 0.0).then_inc(const, 1)
            pool.memset(m.ones[:, :], 1.0).then_inc(const, 1)
            pool.wait_ge(const, 2)
            pool.affine_select(out=m.ident[:, :], in_=m.ident[:, :], compare_op=ALU.not_equal, fill=1.0, base=0,
                               pattern=[[-1, P]], channel_multiplier=1)
            pool.affine_select(out=m.upto[:, :], in_=m.ones[:, :], compare_op=ALU.is_ge, fill=0.0, base=0,
                               pattern=[[1, P]], channel_multiplier=-1)
            pool.affine_select(out=m.after[:, :], in_=m.ones[:, :], compare_op=ALU.is_gt, fill=0.0, base=0,
                               pattern=[[-1, P]], channel_multiplier=1)



def mamba(m):
    nc = m.nc
    with ExitStack() as c:
        sb = lambda n, s, d=F32: c.enter_context(nc.sbuf_tensor(n, s, d))
        dt_raw = sb("ssm_dt_raw", [P, TT, HEADS])
        z_gate = sb("ssm_z_gate", [P, TT, DI])
        with ExitStack() as c2:
            conved = c2.enter_context(nc.sbuf_tensor("ssm_conved", [P, CM_T, SEQ], F32))
            mamba_in(m, z_gate, conved, dt_raw)
            xs = c2.enter_context(nc.sbuf_tensor("ssm_xs", [P, TT, DI], F32))
            mamba_scan(m, z_gate, conved, dt_raw, xs)
        mamba_out(m, z_gate)


def convolve(m, dve, step, tiles, u1, taps, bias, acc, silu_done, conv_done):
    tap_at = m.ins["col_at"][taps]
    dve.sem_inc(conv_done, 4)
    with dve.Fori(0, tiles // 4) as i:
        step.loop(i, 12)
        for b in range(4):
            tap = lambda n: m.cols[:, bass.ds(i * 16 + (tap_at + 4 * b + n), 1)]
            bank, half = m.banks[b], acc[:, b % 2, :]
            dve.wait_ge(m.w_used, i * 4 + (u1 + b + 1))
            dve.wait_ge(silu_done, i * 4 + (b + 1))
            if bias:
                shift = m.cols[:, bass.ds(i * 4 + (m.ins["col_at"][bias] + b), 1)]
                step(dve.tensor_scalar(half, bank[:, :], tap(3), shift, ALU.mult, ALU.add))
            else:
                step(dve.tensor_scalar(half, bank[:, :], tap(3), None, ALU.mult))
            for late in (1, 2):
                step(dve.scalar_tensor_tensor(half[:, late:], bank[:, 0:SEQ - late], tap(3 - late),
                                              half[:, late:], ALU.mult, ALU.add))
            dve.scalar_tensor_tensor(half[:, 3:], bank[:, 0:SEQ - 3], tap(0), half[:, 3:],
                                     ALU.mult, ALU.add).then_inc(conv_done, 1)
        step.end_loop(tiles // 4)


def silu_convolved(act, tiles, conved, acc, silu_done, conv_done):
    act.sem_inc(silu_done, 2)
    with act.Fori(0, tiles // 2) as i:
        for b in range(2):
            act.wait_ge(conv_done, i * 2 + (4 + b + 1))
            act.activation(conved[:, i * 2 + b, :], acc[:, b, :], ACT.Silu).then_inc(silu_done, 1)


def split_small(pool, w, parts, loaded, split):
    pool.wait_ge(loaded, 16)
    pool.tensor_copy(parts[:, 0, :, :], w[:, :, :]).then_inc(split, 1)
    pool.wait_ge(split, 1)
    pool.tensor_tensor(parts[:, 1, :, :], w[:, :, :], parts[:, 0, :, :], ALU.subtract).then_inc(split, 1)


class SmallOut:

    def __init__(self, m, c, name, width, banks):
        self.m, self.width, self.banks = m, width, banks
        self.w = c.enter_context(m.nc.sbuf_tensor(name + "_w", [P, DT, width], F32))
        self.parts = c.enter_context(m.nc.sbuf_tensor(name + "_w_parts", [P, 2, DT, width], F32R))
        self.narrow = c.enter_context(m.nc.sbuf_tensor(name + "_narrow", [P, SEQ], F32))
        self.loaded, self.split, self.done, self.copied = (m.sem(c, f"{name}_{n}") for n in
                                                           ("loaded", "split", "done", "copied"))

    def tensor(self, pe, h):
        wide, turned = self.banks
        pe.wait_ge(self.split, 2)
        for k in range(DT):
            for a, b in PASSES:
                mm = pe.matmul(wide[0:self.width, :], self.parts[:, a, k, :], h[b][:, k, :],
                               start=(k == 0 and (a, b) == PASSES[0]), stop=(k == DT - 1 and (a, b) == PASSES[-1]))
        mm.then_inc(self.done, 1)
        pe.wait_ge(self.copied, 1)
        for t in range(TT):
            mm = pe.transpose(turned[:, t * self.width:(t + 1) * self.width], self.narrow[0:self.width, t * P:(t + 1) * P],
                              self.m.ident[0:self.width, 0:self.width])
        mm.then_inc(self.done, 1)

    def scalar(self, act, dst):
        act.wait_ge(self.done, 1)
        act.activation(self.narrow[0:self.width, :], self.banks[0][0:self.width, :], ACT.Copy).then_inc(self.copied, 1)
        act.wait_ge(self.done, 2)
        act.activation(dst, self.banks[1][:, 0:TT * self.width], ACT.Copy)


def mamba_in(m, z_gate, conved, dt_raw):
    nc, ins = m.nc, m.ins
    ZC = DI // 512
    with ExitStack() as c:
        sb = lambda n, s, d=F32: c.enter_context(nc.sbuf_tensor(n, s, d))
        sem = lambda n: m.sem(c, n)
        h = [sb(f"ssm_h_{x}", [P, DT, SEQ], F32R) for x in ("high", "low")]
        m.open_parts(c)
        raw = SmallOut(m, c, "ssm_dt_in", HEADS, m.banks[4:6])
        acc = sb("ssm_acc", [P, 2, SEQ])
        norm = NormTurn(m, c, "ssm_norm", m.resid, h, lambda k: m.col("pre_norm0", k), TT, D, m.banks[0:4])
        z_done, z_read = sem("ssm_z_done"), sem("ssm_z_read")
        conv_done, silu_done = sem("ssm_conv_done"), sem("ssm_silu_done")
        u0 = m.unit
        u1 = u0 + 4 * ZC
        block = c.enter_context(nc.Block())

        @block.sync
        def _(sp):
            sp.dma_start(raw.w[:, :, :], ins["ssm_w_dt"]).then_inc(raw.loaded, 16)
            stream_weights(m, sp, 4 * ZC + CM_T)

        @block.gpsimd
        def _(pool):
            split_small(pool, raw.w, raw.parts, raw.loaded, raw.split)
            split_weights(m, pool, 4 * ZC + CM_T)

        @block.tensor
        def _(pe):
            norm.tensor(pe)
            pe.wait_ge(norm.turned_ready, DT)

            def before_bank(ch, t):
                if ch >= 2:
                    pe.wait_ge(z_read, 4 * (ch - 2) + t + 1)

            tokens_out(m, pe, ZC, DT, h, TT, z_done, before_bank, lambda ch, t: m.banks[4 * (ch % 2) + t])
            pe.wait_ge(z_read, 4 * ZC)
            columns_out(m, pe, CM_T, h, SEQ, conv_done, 1, m.banks[0:4])
            raw.tensor(pe, h)

        @block.vector
        def _(dve):
            step = m.steps(dve, m.dve_step)
            norm.vector(dve, step)
            norm.vector_turned(dve)
            convolve(m, dve, step, CM_T, u1, "ssm_conv_w", "ssm_conv_b", acc, silu_done, conv_done)
            m.keep(step)

        @block.scalar
        def _(act):
            norm.scalar_sums(act)
            norm.scalar_rstd(act)
            norm.scalar_turned(act)
            for ch in range(ZC):
                for t in range(TT):
                    wait_tokens(m, act, u0, DT, TT, z_done, ch, t)
                    act.activation(z_gate[:, t, ch * 512:(ch + 1) * 512], m.banks[4 * (ch % 2) + t][:, :],
                                   ACT.Silu).then_inc(z_read, 1)
            silu_convolved(act, CM_T, conved, acc, silu_done, conv_done)
            raw.scalar(act, dt_raw[:, :, :])


def mamba_scan(m, z_gate, conved, dt_raw, xs):
    nc = m.nc
    GW = HPG * HD
    with ExitStack() as c:
        sb = lambda n, s, d=F32: c.enter_context(nc.sbuf_tensor(n, s, d))
        b_tok = sb("ssm_b_tok", [P, TT, GROUPS * STATE])
        dt = sb("ssm_dt", [P, TT, HEADS])
        dt_end = sb("ssm_dt_end", [P, TT, HEADS])
        a = sb("ssm_a", [P, TT, HEADS])
        grow = sb("ssm_grow", [P, TT, HEADS])
        whole = sb("ssm_whole", [P, TT, HEADS])
        rows = sb("ssm_rows", [P, 3, HEADS])
        b_tiles = conved[:, XS_T:XS_T + BC_T, :]
        c_tiles = conved[:, XS_T + BC_T:, :]
        every = lambda ap: ap.rearrange("p (o h) -> p o h", o=1).broadcast_to([P, TT, HEADS])

        with ExitStack() as cb:
            sem1 = lambda n: m.sem(cb, n)
            rows_loaded, turned, by_act, by_dve = sem1("ssm_rows_loaded"), sem1("ssm_turned"), sem1("ssm_by_act"), sem1("ssm_by_dve")
            dve_dt, act_dt, pe_dt = sem1("ssm_dve_dt"), sem1("ssm_act_dt"), sem1("ssm_pe_dt")
            block = cb.enter_context(nc.Block())
            N_TURN = XS_T + BC_T
            tmp = cb.enter_context(nc.sbuf_tensor("ssm_tmp", [P, 3, TT * HEADS], F32))

            def place(j):
                dst = xs if j < XS_T else b_tok
                jj = j if j < XS_T else j - XS_T
                return dst[:, :, jj * P:(jj + 1) * P]

            @block.sync
            def _(sp):
                for n, name in enumerate(("ssm_dt_bias", "ssm_a_log", "ssm_d")):
                    sp.dma_start(rows[:, n, :], m.row(name, HEADS)).then_inc(rows_loaded, 16)

            @block.tensor
            def _(pe):
                for j in range(N_TURN):
                    if j >= 4:
                        pe.wait_ge(by_act if j % 2 else by_dve, (j - 4) // 2 + 1)
                    for t in range(TT):
                        mm = pe.transpose(m.banks[j % 4][:, t * P:(t + 1) * P], conved[:, j, t * P:(t + 1) * P],
                                          m.ident[:, :])
                    mm.then_inc(turned, 1)
                pe.wait_ge(dve_dt, 3)
                pe.matmul(m.banks[4][:, 0:P], m.upto[:, :], a[:, :, :].rearrange("p t h -> p (t h)"),
                          start=True, stop=True)
                pe.matmul(m.banks[4][:, P:2 * P], m.ones[:, :], a[:, :, :].rearrange("p t h -> p (t h)"),
                          start=True, stop=True).then_inc(pe_dt, 1)

            @block.vector
            def _(dve):
                step = m.steps(dve, m.dve_step)

                def copies(first, last):
                    for j in range(first, last, 2):
                        dve.wait_ge(turned, j + 1)
                        dve.tensor_copy(place(j), m.banks[j % 4][:, :].rearrange("p (t n) -> p t n", t=TT))\
                           .then_inc(by_dve, 1)

                copies(0, 8)
                dve.wait_ge(rows_loaded, 48)
                dve.tensor_tensor(dt[:, :, :], dt_raw[:, :, :], every(rows[:, 0, :]), ALU.add).then_inc(dve_dt, 1)
                copies(8, 16)
                dve.wait_ge(act_dt, 1)
                step(dve.scalar_tensor_tensor(dt[:, :, :], dt[:, :, :], 0.0,
                                              tmp[:, 0, :].rearrange("p (t h) -> p t h", t=TT), ALU.max, ALU.add))
                dve.scalar_tensor_tensor(a[:, :, :], dt[:, :, :], -1.0, every(rows[:, 1, :]), ALU.mult, ALU.mult)\
                   .then_inc(dve_dt, 2)
                copies(16, N_TURN)
                dve.wait_ge(act_dt, 2)
                dve.tensor_tensor(tmp[:, 2, :], m.banks[4][:, P:2 * P], tmp[:, 1, :], ALU.subtract).then_inc(dve_dt, 1)
                dve.wait_ge(act_dt, 3)
                step(dve.tensor_tensor(dt_end[:, :, :], dt[:, :, :], dt_end[:, :, :], ALU.mult))
                m.keep(step)

            @block.scalar
            def _(act):
                step = m.steps(act, m.act_step)

                def copies(first, last):
                    for j in range(first + 1, last, 2):
                        act.wait_ge(turned, j + 1)
                        act.activation(place(j), m.banks[j % 4][:, :].rearrange("p (t n) -> p t n", t=TT), ACT.Copy)\
                           .then_inc(by_act, 1)

                copies(0, 8)
                act.wait_ge(dve_dt, 1)
                u = tmp[:, 0, :]
                step(act.activation(u, dt[:, :, :].rearrange("p t h -> p (t h)"), ACT.Abs))
                step(act.activation(u, u, ACT.Exp, scale=-1.0))
                act.activation(rows[:, 1, :], rows[:, 1, :], ACT.Exp)
                act.activation(u, u, ACT.Ln, bias=1.0).then_inc(act_dt, 1)
                copies(8, N_TURN)
                act.wait_ge(pe_dt, 1)
                act.activation(grow[:, :, :].rearrange("p t h -> p (t h)"), m.banks[4][:, 0:P], ACT.Exp)
                act.activation(whole[:, :, :].rearrange("p t h -> p (t h)"), m.banks[4][:, P:2 * P], ACT.Exp)
                act.activation(tmp[:, 1, :], m.banks[4][:, 0:P], ACT.Copy).then_inc(act_dt, 1)
                act.wait_ge(dve_dt, 4)
                act.activation(dt_end[:, :, :].rearrange("p t h -> p (t h)"), tmp[:, 2, :], ACT.Exp).then_inc(act_dt, 1)
                m.keep(step)

        x_dt = conved[:, 0:8, :].rearrange("p (b a) n -> p b (a n)", b=2)
        x_end = conved[:, 8:16, :].rearrange("p (b a) n -> p b (a n)", b=2)
        cut = sb("ssm_cut", [P, 2, HPG, P])
        decay = sb("ssm_decay", [P, 2, HPG, P])
        cb_low = sb("ssm_cb_low", [P, 2, P])
        mix = sb("ssm_mix", [P, 2, HPG, P])
        state = sb("ssm_state", [P, GROUPS, GW])
        part = sb("ssm_part", [P, 2, GW])
        units = [(ch, g) for ch in range(TT) for g in range(GROUPS)]
        N = len(units)
        with ExitStack() as cb:
            sem1 = lambda n: m.sem(cb, n)
            cut_ready, seg_done, decay_ready = sem1("ssm_cut_ready"), sem1("ssm_seg_done"), sem1("ssm_decay_ready")
            mix_ready, y_done, y_read, state_ready = sem1("ssm_mix_ready"), sem1("ssm_y_done"), sem1("ssm_y_read"), sem1("ssm_state_ready")
            faded = sem1("ssm_faded")
            cb_done, xdt_ready, xend_ready, skip_ready = sem1("ssm_cb_done"), sem1("ssm_xdt_ready"), sem1("ssm_xend_ready"), sem1("ssm_skip_ready")
            block = cb.enter_context(nc.Block())
            heads = lambda ap: ap.rearrange("p (h d) -> p h d", d=HD)
            per_head = lambda ap, n: ap.rearrange("p (h o) -> p h o", o=1).broadcast_to([P, n, HD])

            @block.gpsimd
            def _(pool):
                def prepare_end(ch):
                    if ch >= 2:
                        pool.wait_ge(y_done, GROUPS * (ch - 1))
                    pool.tensor_tensor(heads(x_end[:, ch % 2, :]), heads(xs[:, ch, :]),
                                       per_head(dt_end[:, ch, :], HEADS), ALU.mult).then_inc(xend_ready, 1)

                def prepare_skip(ch):
                    pool.wait_ge(xdt_ready, ch + 1)
                    pool.wait_ge(xend_ready, ch + 1)
                    pool.tensor_tensor(heads(xs[:, ch, :]), heads(xs[:, ch, :]), per_head(rows[:, 2, :], HEADS),
                                       ALU.mult).then_inc(skip_ready, 1)

                for i, (ch, g) in enumerate(units):
                    if i == 0:
                        prepare_end(0)
                    if i >= 2:
                        pool.wait_ge(seg_done, i - 1)
                    pool.tensor_tensor(cut[:, i % 2, :, :],
                                       m.upto[:, :].rearrange("p (o l) -> p o l", o=1).broadcast_to([P, HPG, P]),
                                       a[:, ch, g * HPG:(g + 1) * HPG].rearrange("p (h o) -> p h o", o=1)
                                       .broadcast_to([P, HPG, P]), ALU.mult).then_inc(cut_ready, 1)
                    if i == 0:
                        prepare_skip(0)
                    elif g == 3 and ch < TT - 1:
                        prepare_end(ch + 1)
                    elif g == 5 and ch < TT - 1:
                        prepare_skip(ch + 1)

            @block.tensor
            def _(pe):
                for i in range(N + 1):
                    if i < N:
                        ch, g = units[i]
                        pe.wait_ge(cut_ready, i + 1)
                        if i >= 2:
                            pe.wait_ge(decay_ready, i - 1)
                            pe.wait_ge(mix_ready, i - 1)
                        pe.matmul(m.banks[i % 2][:, :], m.after[:, :],
                                  cut[:, i % 2, :, :].rearrange("p h l -> p (h l)"), start=True, stop=True)\
                          .then_inc(seg_done, 1)
                        at = slice(ch * P, (ch + 1) * P)
                        pe.matmul(m.banks[2 + i % 2][:, 0:P], b_tiles[:, g, at], c_tiles[:, g, at],
                                  start=True, stop=True).then_inc(cb_done, 1)
                    if i >= 1:
                        j = i - 1
                        ch, g = units[j]
                        at = slice(ch * P, (ch + 1) * P)
                        yb, sbk = m.banks[4 + j % 2], m.banks[6 + j % 2]
                        pe.wait_ge(mix_ready, j + 1)
                        pe.wait_ge(xdt_ready, ch + 1)
                        pe.wait_ge(xend_ready, ch + 1)
                        if j >= 2:
                            pe.wait_ge(y_read, j - 1)
                            pe.wait_ge(state_ready, j - 1)
                        for r in range(HPG):
                            h0 = (g * HPG + r) * HD
                            pe.matmul(yb[:, r * HD:(r + 1) * HD], mix[:, j % 2, r, :], x_dt[:, ch % 2, h0:h0 + HD],
                                      start=True, stop=True)
                        if ch > 0:
                            pe.matmul(yb[:, GW:2 * GW], c_tiles[:, g, at], state[:, g, :], start=True, stop=True)
                        pe.matmul(sbk[:, 0:GW], b_tok[:, ch, g * STATE:(g + 1) * STATE],
                                  x_end[:, ch % 2, g * GW:(g + 1) * GW], start=True, stop=True).then_inc(y_done, 1)

            @block.scalar
            def _(act):
                def fade_state(j):
                    ch, g = units[j]
                    if ch > 0:
                        act.wait_ge(y_done, j + 1)
                        for r in range(HPG):
                            here = state[:, g, r * HD:(r + 1) * HD]
                            h = g * HPG + r
                            last = act.activation(here, here, ACT.Copy, scale=whole[:, ch, h:h + 1])
                        last.then_inc(faded, 1)

                for i in range(N):
                    act.wait_ge(seg_done, i + 1)
                    if i >= 2:
                        act.wait_ge(mix_ready, i - 1)
                    act.activation(decay[:, i % 2, :, :].rearrange("p h l -> p (h l)"), m.banks[i % 2][:, :],
                                   ACT.Exp).then_inc(decay_ready, 1)
                    if i >= 1:
                        fade_state(i - 1)
                fade_state(N - 1)

            @block.vector
            def _(dve):
                step = m.steps(dve, m.dve_step)

                def prepare_dt(ch):
                    if ch >= 2:
                        dve.wait_ge(y_done, GROUPS * (ch - 1))
                    dve.tensor_tensor(heads(x_dt[:, ch % 2, :]), heads(xs[:, ch, :]),
                                      per_head(dt[:, ch, :], HEADS), ALU.mult).then_inc(xdt_ready, 1)

                for i in range(N + 1):
                    if i < N:
                        ch, g = units[i]
                        if i == 0:
                            prepare_dt(0)
                        elif g == 3 and ch < TT - 1:
                            prepare_dt(ch + 1)
                        dve.wait_ge(cb_done, i + 1)
                        step(dve.tensor_tensor(cb_low[:, i % 2, :], m.banks[2 + i % 2][:, 0:P], m.upto[:, :], ALU.mult))
                        dve.wait_ge(decay_ready, i + 1)
                        if i >= 2:
                            dve.wait_ge(y_done, i - 1)
                        dve.tensor_tensor(mix[:, i % 2, :, :], decay[:, i % 2, :, :],
                                          cb_low[:, i % 2, :].rearrange("p (o l) -> p o l", o=1)
                                          .broadcast_to([P, HPG, P]), ALU.mult).then_inc(mix_ready, 1)
                    if i >= 1:
                        j = i - 1
                        ch, g = units[j]
                        yb, sbk = m.banks[4 + j % 2], m.banks[6 + j % 2]
                        here = slice(g * GW, (g + 1) * GW)
                        y = part[:, j % 2, :]
                        dve.wait_ge(y_done, j + 1)
                        gated = z_gate[:, ch, here]
                        dve.wait_ge(skip_ready, ch + 1)
                        if ch > 0:
                            step(dve.tensor_tensor(heads(y), heads(yb[:, GW:2 * GW]),
                                                   per_head(grow[:, ch, g * HPG:(g + 1) * HPG], HPG), ALU.mult))
                            step(dve.tensor_tensor(y, y, xs[:, ch, here], ALU.add))
                            dve.tensor_tensor(y, yb[:, 0:GW], y, ALU.add).then_inc(y_read, 1)
                        else:
                            dve.tensor_tensor(y, yb[:, 0:GW], xs[:, ch, here], ALU.add).then_inc(y_read, 1)
                        if ch == 0:
                            dve.tensor_copy(state[:, g, :], sbk[:, 0:GW]).then_inc(state_ready, 1)
                        else:
                            dve.wait_ge(faded, j - GROUPS + 1)
                            dve.tensor_tensor(state[:, g, :], state[:, g, :], sbk[:, 0:GW], ALU.add)\
                               .then_inc(state_ready, 1)
                        dve.wait_ge(y_read, j + 1)
                        dve.tensor_tensor(gated, gated, y, ALU.mult)
                m.keep(step)


def mamba_out(m, y):
    nc = m.nc
    with ExitStack() as c:
        turned = [c.enter_context(nc.sbuf_tensor(f"ssm_y_{x}", [P, XS_T, SEQ], F32R)) for x in ("high", "low")]
        norm = NormTurn(m, c, "ssm_gnorm", y, turned, lambda k: m.col("ssm_gate_norm", k), TT, DI, m.banks[0:4])
        project_and_add(m, c, "ssm_o", norm, turned, DI // P, y[:, :, 0:D], "post_norm0")


def project_and_add(m, c, name, norm, turned, kt, y, gain):
    nc = m.nc
    sem = lambda n: m.sem(c, f"{name}_{n}")
    out_done = sem("out_done")
    bank_of = lambda ch, t: m.banks[(4 * ch + t + 2) % 8]
    if gain:
        gain_row = c.enter_context(nc.sbuf_tensor(name + "_gain", [P, D], F32))
        gain_loaded = sem("gain_loaded")
        post = PostNorm(m, c, name + "_post", y, gain_row, gain_loaded)
    m.open_parts(c)
    u0 = m.unit
    block = c.enter_context(nc.Block())

    @block.sync
    def _(sp):
        if gain:
            sp.dma_start(gain_row[:, :], m.row(gain, D)).then_inc(gain_loaded, 16)
        stream_weights(m, sp, 2 * kt // 2)

    @block.gpsimd
    def _(pool):
        split_weights(m, pool, 2 * kt // 2)

    @block.tensor
    def _(pe):
        if norm:
            norm.tensor(pe)
            pe.wait_ge(norm.turned_ready, kt)
        tokens_out(m, pe, 2, kt, turned, TT, out_done, lambda ch, t: None, bank_of)

    @block.vector
    def _(dve):
        step = m.steps(dve, m.dve_step)
        if norm:
            norm.vector(dve, step)
            norm.vector_turned(dve)
        if gain:
            post.vector(dve, step, bank_of)
        else:
            for ch in range(2):
                for t in range(TT):
                    wait_tokens(m, dve, u0, kt, TT, out_done, ch, t)
                    here = m.resid[:, t, ch * 512:(ch + 1) * 512]
                    dve.tensor_tensor(here, here, bank_of(ch, t)[:, :], ALU.add)
        m.keep(step)

    @block.scalar
    def _(act):
        if norm:
            norm.scalar_sums(act)
            norm.scalar_rstd(act)
            norm.scalar_turned(act)
        if gain:
            for ch in range(2):
                for t in range(TT):
                    wait_tokens(m, act, u0, kt, TT, out_done, ch, t)
                    post.scalar_chunk(act, ch, t, bank_of(ch, t)[:, :])
            post.scalar(act)



class PlainTurn:

    def __init__(self, m, c, name, src, turned, tiles, width, banks):
        self.m, self.src, self.turned, self.tiles, self.width, self.banks = m, src, turned, tiles, width, banks
        self.turned_in_bank = m.sem(c, name + "_bank")
        self.high_ready = m.sem(c, name + "_high")
        self.turned_ready = m.sem(c, name + "_turned")

    def vector(self, dve, step):
        pass

    def scalar_sums(self, act):
        pass

    def scalar_rstd(self, act):
        pass

    def tensor(self, pe):
        for k in range(self.width // P):
            if k >= len(self.banks):
                pe.wait_ge(self.turned_ready, k - len(self.banks) + 1)
            for t in range(self.tiles):
                mm = pe.transpose(self.banks[k % len(self.banks)][:, t * P:(t + 1) * P], self.src[:, t, k * P:(k + 1) * P],
                                  self.m.ident[:, :])
            mm.then_inc(self.turned_in_bank, 1)

    def scalar_turned(self, act):
        for k in range(self.width // P):
            act.wait_ge(self.turned_in_bank, k + 1)
            act.activation(self.turned[0][:, k, :], self.banks[k % len(self.banks)][:, 0:self.tiles * P], ACT.Copy)\
               .then_inc(self.high_ready, 1)

    def vector_turned(self, dve):
        for k in range(self.width // P):
            dve.wait_ge(self.high_ready, k + 1)
            dve.tensor_tensor(self.turned[1][:, k, :], self.banks[k % len(self.banks)][:, 0:self.tiles * P], self.turned[0][:, k, :],
                              ALU.subtract).then_inc(self.turned_ready, 1)


def attention(m):
    nc = m.nc
    with ExitStack() as c:
        sb = lambda n, s, d=F32: c.enter_context(nc.sbuf_tensor(n, s, d))
        qk = sb("att_qk", [P, TT, QW + KVW])
        v = sb("att_v", [P, TT, KVW])
        gate = sb("att_gate", [P, TT, QW])
        attention_in(m, qk, v, gate)
        turned = sb("att_turned", [P, (QW + KVW) // P, SEQ])
        attention_core(m, qk, v, gate, turned)
        with ExitStack() as c2:
            parts = [c2.enter_context(nc.sbuf_tensor(f"att_turned_{x}", [P, DT, SEQ], F32R)) for x in ("high", "low")]
            turn = PlainTurn(m, c2, "att_oturn", gate, parts, TT, QW, m.banks[0:4])
            project_and_add(m, c2, "att_o", turn, parts, DT, qk[:, :, 0:D], "post_norm1")


def attention_in(m, qk, v, gate):
    nc, ins = m.nc, m.ins
    import math
    with ExitStack() as c:
        sb = lambda n, s, d=F32: c.enter_context(nc.sbuf_tensor(n, s, d))
        sem = lambda n: m.sem(c, n)
        h = [sb(f"att_h_{x}", [P, DT, SEQ], F32R) for x in ("high", "low")]
        m.open_parts(c)
        norm = NormTurn(m, c, "att_norm", m.resid, h, lambda k: m.col("pre_norm1", k), TT, D, m.banks[0:4])
        pos_i = sb("att_pos_i", [P, TT], I32)
        pos = sb("att_pos", [P, TT])
        freq = sb("att_freq", [P, HALF])
        ang = sb("att_ang", [P, 5, TT, HALF])
        rot = sb("att_rot", [P, 4, TT, QH + KVH, HALF])
        done, read, pos_loaded, sin_ready, ang_ready = (sem("att_in_done"), sem("att_in_read"), sem("att_pos_loaded"),
                                                        sem("att_sin_ready"), sem("att_ang_ready"))
        u0 = m.unit
        CH = 5
        block = c.enter_context(nc.Block())

        @block.sync
        def _(sp):
            sp.dma_start(pos_i[:, :], ins["positions"]).then_inc(pos_loaded, 16)
            stream_weights(m, sp, CH * DT // 2)

        @block.gpsimd
        def _(pool):
            split_weights(m, pool, CH * DT // 2)

        @block.tensor
        def _(pe):
            norm.tensor(pe)
            pe.wait_ge(norm.turned_ready, DT)

            def before_bank(ch, t):
                if ch >= 2:
                    pe.wait_ge(read, TT * (ch - 2) + t + 1)

            tokens_out(m, pe, CH, DT, h, TT, done, before_bank, lambda ch, t: m.banks[4 * (ch % 2) + t])

        @block.scalar
        def _(act):
            norm.scalar_sums(act)
            norm.scalar_rstd(act)
            norm.scalar_turned(act)
            act.wait_ge(ang_ready, 1)
            act.activation(ang[:, 3:5, :, :], ang[:, 1:3, :, :], ACT.Sin).then_inc(sin_ready, 1)
            for ch in range(CH):
                for t in range(TT):
                    wait_tokens(m, act, u0, DT, TT, done, ch, t)
                    bank = m.banks[4 * (ch % 2) + t]
                    if ch < 2:
                        act.activation(qk[:, t, ch * 512:(ch + 1) * 512], bank[:, :], ACT.Copy).then_inc(read, 1)
                    elif ch == 2:
                        act.activation(qk[:, t, QW:QW + KVW], bank[:, 0:KVW], ACT.Copy)
                        act.activation(v[:, t, :], bank[:, KVW:2 * KVW], ACT.Copy).then_inc(read, 1)
                    else:
                        act.activation(gate[:, t, (ch - 3) * 512:(ch - 2) * 512], bank[:, :], ACT.Silu)\
                           .then_inc(read, 1)

        @block.vector
        def _(dve):
            step = m.steps(dve, m.dve_step)
            norm.vector(dve, step)
            norm.vector_turned(dve)
            for j in range(HALF):
                dve.memset(freq[:, j:j + 1], THETA ** (-2.0 * j / ROPE))
            dve.wait_ge(pos_loaded, 16)
            step(dve.tensor_copy(pos[:, :], pos_i[:, :]))
            x, turns = ang[:, 0, :, :], ang[:, 2, :, :]
            step(dve.tensor_tensor(x, pos[:, :].rearrange("p (t o) -> p t o", o=1).broadcast_to([P, TT, HALF]),
                                   freq[:, :].rearrange("p (o j) -> p o j", o=1).broadcast_to([P, TT, HALF]),
                                   ALU.mult))
            big = 1.5 * 2.0 ** 23
            step(dve.tensor_scalar(turns, x, 1.0 / (2 * math.pi), big, ALU.mult, ALU.add))
            step(dve.tensor_scalar(turns, turns, big, None, ALU.subtract))
            c1 = 6.28125
            c2 = round((2 * math.pi - c1) * 2.0 ** 19) / 2.0 ** 19
            c3 = 2 * math.pi - c1 - c2
            for part in (c1, c2, c3):
                step(dve.scalar_tensor_tensor(x, turns, -part, x, ALU.mult, ALU.add))
            step(dve.tensor_scalar(ang[:, 1, :, :], x, 3.1415925, -3.1415925, ALU.min, ALU.max))
            step(dve.tensor_scalar(ang[:, 2, :, :], ang[:, 1, :, :], -1.0, None, ALU.mult))
            step(dve.tensor_tensor(ang[:, 2, :, :], ang[:, 2, :, :], ang[:, 1, :, :], ALU.min))
            dve.tensor_scalar(ang[:, 2, :, :], ang[:, 2, :, :], math.pi / 2, None, ALU.add).then_inc(ang_ready, 1)
            dve.wait_ge(sin_ready, 1)
            dve.wait_ge(read, 3 * TT)
            n = QH + KVH
            for t in range(TT):
                heads = qk[:, t, :].rearrange("p (h d) -> p h d", d=AD)
                lo, hi = heads[:, :, 0:HALF], heads[:, :, HALF:ROPE]
                every = lambda ap: ap.rearrange("p (o j) -> p o j", o=1).broadcast_to([P, n, HALF])
                sin, cos = every(ang[:, 3, t, :]), every(ang[:, 4, t, :])
                dve.tensor_tensor(rot[:, 0, t, :, :], lo, cos, ALU.mult)
                dve.tensor_tensor(rot[:, 1, t, :, :], hi, sin, ALU.mult)
                dve.tensor_tensor(rot[:, 2, t, :, :], hi, cos, ALU.mult)
                step(dve.tensor_tensor(rot[:, 3, t, :, :], lo, sin, ALU.mult))
                dve.tensor_tensor(lo, rot[:, 0, t, :, :], rot[:, 1, t, :, :], ALU.subtract)
                dve.tensor_tensor(hi, rot[:, 2, t, :, :], rot[:, 3, t, :, :], ALU.add)
            m.keep(step)


def attention_core(m, qk, v, gate, turned):
    nc = m.nc
    NQ = QW // P
    with ExitStack() as c:
        sb = lambda n, s, d=F32: c.enter_context(nc.sbuf_tensor(n, s, d))
        sem = lambda n: m.sem(c, n)
        mask = sb("att_mask", [P, 2 * P])
        sinks = sb("att_sinks", [P, QH])
        s = sb("att_s", [P, 2, 4, 2 * P])
        p = sb("att_p", [P, 2, 4, 2 * P])
        pt = sb("att_pt", [P, 2, 4, 2 * P])
        stat = sb("att_stat", [P, 2, 8, 4])
        rden = sb("att_rden", [P, 4, 4])
        o = sb("att_ov", [P, 2, 4 * AD])
        sink_loaded, mask_made, turn_done, turn_read = (sem("att_sink_loaded"), sem("att_mask_made"),
                                                        sem("att_turn_done"), sem("att_turn_read"))
        scores_done, stat_ready, exp_done, pt_done, pt_ready, pv_done, out_ready = (
            sem("att_scores_done"), sem("att_stat_ready"), sem("att_exp_done"), sem("att_pt_done"),
            sem("att_pt_ready"), sem("att_pv_done"), sem("att_out_ready"))
        units = [(n, jj) for n in range(TT) for jj in range(4)]
        N = len(units)
        NT = (QW + KVW) // P
        lo_of = lambda n: P if n == 0 else 0
        block = c.enter_context(nc.Block())

        @block.sync
        def _(sp):
            sp.dma_start(sinks[:, :], m.row("att_sinks", QH)).then_inc(sink_loaded, 16)

        @block.gpsimd
        def _(pool):
            pool.memset(mask[:, :], 0.0).then_inc(mask_made, 1)
            pool.wait_ge(mask_made, 1)
            pool.affine_select(out=mask[:, 0:P], in_=mask[:, 0:P], compare_op=ALU.is_gt, fill=-1e30, base=0,
                               pattern=[[1, P]], channel_multiplier=-1)
            pool.affine_select(out=mask[:, P:], in_=mask[:, P:], compare_op=ALU.is_ge, fill=-1e30, base=0,
                               pattern=[[-1, P]], channel_multiplier=1).then_inc(mask_made, 1)

        @block.tensor
        def _(pe):
            for j in range(NT):
                if j >= 8:
                    pe.wait_ge(turn_read, j - 7)
                for t in range(TT):
                    mm = pe.transpose(m.banks[j % 8][:, t * P:(t + 1) * P], qk[:, t, j * P:(j + 1) * P], m.ident[:, :])
                mm.then_inc(turn_done, 1)
            pe.wait_ge(turn_read, NT)
            for i in range(N + 2):
                if i < N:
                    n, jj = units[i]
                    if i >= 2:
                        pe.wait_ge(stat_ready, 2 * (i - 1))
                    lo = lo_of(n)
                    for x in range(2):
                        j = 2 * jj + x
                        for b in range(2):
                            part = slice(64 * b, 64 * b + 64)
                            mm = pe.matmul(m.banks[2 * (i % 2) + b][:, x * 256 + lo:(x + 1) * 256],
                                           turned[part, j, n * P:(n + 1) * P],
                                           turned[part, NQ + j // 4, (n - 1) * P + lo:(n + 1) * P],
                                           start=True, stop=True)
                    mm.then_inc(scores_done, 1)
                if 1 <= i <= N:
                    u = i - 1
                    n, jj = units[u]
                    pe.wait_ge(exp_done, u + 1)
                    if u >= 1:
                        pe.wait_ge(pt_ready, u)
                    halves = (1,) if n == 0 else (0, 1)
                    for half in halves:
                        for q in range(4):
                            mm = pe.transpose(m.banks[4 + half][:, q * P:(q + 1) * P],
                                              p[:, u % 2, q, half * P:(half + 1) * P], m.ident[:, :])
                    mm.then_inc(pt_done, 1)
                if i >= 2:
                    u = i - 2
                    n, jj = units[u]
                    pe.wait_ge(pt_ready, u + 1)
                    if u >= 2:
                        pe.wait_ge(out_ready, u - 1)
                    halves = (1,) if n == 0 else (0, 1)
                    for q in range(4):
                        x, b = q // 2, q % 2
                        kv = 2 * ((2 * jj + x) // 4) + b
                        for half in halves:
                            mm = pe.matmul(m.banks[6 + u % 2][:, q * AD:(q + 1) * AD],
                                           pt[:, u % 2, q, half * P:(half + 1) * P],
                                           v[:, n - 1 + half, kv * AD:(kv + 1) * AD],
                                           start=(half == halves[0]), stop=(half == 1))
                    mm.then_inc(pv_done, 1)

        @block.vector
        def _(dve):
            step = m.steps(dve, m.dve_step)
            dve.wait_ge(sink_loaded, 16)
            dve.wait_ge(mask_made, 2)
            for i in range(N + 2):
                if i < N:
                    n, jj = units[i]
                    lo = lo_of(n)
                    w = 2 * P - lo
                    st = stat[:, i % 2, :, :]
                    dve.wait_ge(scores_done, i + 1)
                    if i >= 2:
                        dve.wait_ge(exp_done, i - 1)
                    for b in range(2):
                        bank = m.banks[2 * (i % 2) + b][:, :].rearrange("p (x k) -> p x k", x=2)[:, :, lo:]
                        step(dve.scalar_tensor_tensor(
                            s[:, i % 2, b:4:2, lo:], bank, AD ** -0.5,
                            mask[:, lo:].rearrange("p (o k) -> p o k", o=1).broadcast_to([P, 2, w]),
                            ALU.mult, ALU.add))
                    step(dve.tensor_reduce(st[:, 0, :], s[:, i % 2, :, lo:], AX.X, ALU.max))
                    step(dve.tensor_tensor(st[:, 0, :], st[:, 0, :], sinks[:, 4 * jj:4 * jj + 4], ALU.max))
                    dve.tensor_scalar(st[:, 1, :], st[:, 0, :], -1.0, None, ALU.mult).then_inc(stat_ready, 1)
                    dve.tensor_tensor(st[:, 2, :], sinks[:, 4 * jj:4 * jj + 4], st[:, 0, :], ALU.subtract)\
                       .then_inc(stat_ready, 1)
                if i >= 2:
                    u = i - 2
                    n, jj = units[u]
                    st = stat[:, u % 2, :, :]
                    out = o[:, u % 2, :]
                    per_head = lambda ap: ap.rearrange("p (h o) -> p h o", o=1).broadcast_to([P, 4, AD])
                    dve.wait_ge(pv_done, u + 1)
                    step(dve.tensor_tensor(out.rearrange("p (h d) -> p h d", d=AD),
                                           m.banks[6 + u % 2][:, 0:4 * AD].rearrange("p (h d) -> p h d", d=AD),
                                           per_head(rden[:, u % 4, :]), ALU.mult))
                    here = gate[:, n, 4 * jj * AD:4 * (jj + 1) * AD]
                    dve.tensor_tensor(here, here, out, ALU.mult).then_inc(out_ready, 1)
                if 1 <= i <= N:
                    u = i - 1
                    st = stat[:, u % 2, :, :]
                    dve.wait_ge(exp_done, u + 1)
                    step(dve.tensor_tensor(st[:, 5, :], st[:, 3, :], st[:, 4, :], ALU.add))
                    step(dve.reciprocal(rden[:, u % 4, :], st[:, 5, :]))
            m.keep(step)

        @block.scalar
        def _(act):
            for j in range(NT):
                act.wait_ge(turn_done, j + 1)
                act.activation(turned[:, j, :], m.banks[j % 8][:, :], ACT.Copy).then_inc(turn_read, 1)
            for i in range(N + 1):
                if i < N:
                    n, jj = units[i]
                    lo = lo_of(n)
                    st = stat[:, i % 2, :, :]
                    act.wait_ge(stat_ready, 2 * (i + 1))
                    if i >= 2:
                        act.wait_ge(pt_done, i - 1)
                    for q in range(4):
                        act.activation(p[:, i % 2, q, lo:], s[:, i % 2, q, lo:], ACT.Exp, bias=st[:, 1, q:q + 1],
                                       accum_out=st[:, 3, q:q + 1])
                    act.activation(st[:, 4, :], st[:, 2, :], ACT.Exp).then_inc(exp_done, 1)
                if i >= 1:
                    u = i - 1
                    n, jj = units[u]
                    act.wait_ge(pt_done, u + 1)
                    if u >= 2:
                        act.wait_ge(pv_done, u - 1)
                    halves = (1,) if n == 0 else (0, 1)
                    for half in halves:
                        cp = act.activation(pt[:, u % 2, :, half * P:(half + 1) * P],
                                            m.banks[4 + half][:, :].rearrange("p (q k) -> p q k", q=4), ACT.Copy)
                    cp.then_inc(pt_ready, 1)



HC_T = 3 * GH + 2 * MH


def hybrid(m):
    nc = m.nc
    with ExitStack() as c:
        sb = lambda n, s, d=F32: c.enter_context(nc.sbuf_tensor(n, s, d))
        conved = sb("hyb_conved", [P, HC_T, SEQ])
        gate = sb("hyb_gate", [P, TT, D])
        v_one = sb("hyb_v_one", [P, TT, MH, MD + 1])
        small = sb("hyb_small", [P, TT, 16])
        hybrid_in(m, conved, gate, v_one, small)
        mixed = sb("hyb_mixed", [P, TT, GH + MH, GD])
        gates = Gates(m, c, small)
        with ExitStack() as c2:
            delta_net(m, c2, conved, mixed, small, gates)
        with ExitStack() as c2:
            mlstm(m, c2, conved, mixed, v_one, gates, gate)
        hybrid_out(m, mixed, gate, conved)


def hybrid_in(m, conved, gate, v_one, small):
    nc, ins = m.nc, m.ins
    with ExitStack() as c:
        sb = lambda n, s, d=F32: c.enter_context(nc.sbuf_tensor(n, s, d))
        sem = lambda n: m.sem(c, n)
        h = [sb(f"hyb_h_{x}", [P, DT, SEQ], F32R) for x in ("high", "low")]
        m.open_parts(c)
        raw = SmallOut(m, c, "hyb_small_in", 16, m.banks[4:6])
        acc = sb("hyb_acc", [P, 2, SEQ])
        norm = NormTurn(m, c, "hyb_norm", m.resid, h, lambda k: m.col("norm_mix", k), TT, D, m.banks[0:4])
        done, read = sem("hyb_in_done"), sem("hyb_in_read")
        conv_done, silu_done = sem("hyb_conv_done"), sem("hyb_silu_done")
        CH = 3
        u0 = m.unit
        u1 = u0 + CH * DT // 2
        block = c.enter_context(nc.Block())

        @block.sync
        def _(sp):
            sp.dma_start(raw.w[:, :, :], ins["hyb_w_small"]).then_inc(raw.loaded, 16)
            stream_weights(m, sp, CH * DT // 2 + HC_T)

        @block.gpsimd
        def _(pool):
            split_small(pool, raw.w, raw.parts, raw.loaded, raw.split)
            split_weights(m, pool, CH * DT // 2 + HC_T)

        @block.tensor
        def _(pe):
            norm.tensor(pe)
            pe.wait_ge(norm.turned_ready, DT)

            def before_bank(ch, t):
                if ch >= 2:
                    pe.wait_ge(read, TT * (ch - 2) + t + 1)

            tokens_out(m, pe, CH, DT, h, TT, done, before_bank, lambda ch, t: m.banks[4 * (ch % 2) + t])
            pe.wait_ge(read, TT * CH)
            columns_out(m, pe, HC_T, h, SEQ, conv_done, 1, m.banks[0:4])
            raw.tensor(pe, h)

        @block.vector
        def _(dve):
            step = m.steps(dve, m.dve_step)
            norm.vector(dve, step)
            norm.vector_turned(dve)
            dve.memset(v_one[:, :, :, MD:MD + 1], 1.0)
            convolve(m, dve, step, HC_T, u1, "hyb_conv_w", None, acc, silu_done, conv_done)
            m.keep(step)

        @block.scalar
        def _(act):
            norm.scalar_sums(act)
            norm.scalar_rstd(act)
            norm.scalar_turned(act)
            for ch in range(CH):
                for t in range(TT):
                    wait_tokens(m, act, u0, DT, TT, done, ch, t)
                    bank = m.banks[4 * (ch % 2) + t][:, :]
                    if ch == 0:
                        act.activation(gate[:, t, 0:512], bank, ACT.Silu).then_inc(read, 1)
                    elif ch == 1:
                        act.activation(v_one[:, t, :, 0:MD], bank.rearrange("p (h d) -> p h d", h=MH), ACT.Copy)\
                           .then_inc(read, 1)
                    else:
                        act.activation(gate[:, t, 512:], bank, ACT.Sigmoid).then_inc(read, 1)
            silu_convolved(act, HC_T, conved, acc, silu_done, conv_done)
            raw.scalar(act, small[:, :, :])


def spread(ap, n):
    return ap.rearrange("p (k o) -> p k o", o=1).broadcast_to([ap.shape[0], ap.shape[1], n])


def again(ap, n):
    return ap.rearrange("p (o k) -> p o k", o=1).broadcast_to([ap.shape[0], n, ap.shape[1]])


def delta_net(m, c, conved, mixed, small, gates):
    nc = m.nc
    sb = lambda n, s, d=F32: c.enter_context(nc.sbuf_tensor(n, s, d))
    q_ch, k_ch = conved[:, 0:GH, :], conved[:, GH:2 * GH, :]
    k_tok = sb("gdn_k", [P, TT, GH, GD])
    v_tok = sb("gdn_v", [P, TT, GH, GD])
    k_in = sb("gdn_k_in", [P, TT, GH, GD])
    beta = sb("gdn_beta", [P, TT * GH])
    la = sb("gdn_la", [P, TT * GH])
    grow = sb("gdn_grow", [P, TT * GH])
    whole = sb("gdn_whole", [P, TT * GH])
    to_end = sb("gdn_to_end", [P, TT * GH])
    tmp = sb("gdn_tmp", [P, 4, TT * GH])
    rows = sb("gdn_rows", [P, 2, GH])

    with ExitStack() as cb:
        sem = lambda n: m.sem(cb, n)
        rows_loaded, dve_g, act_g, pe_g = sem("gdn_rows_loaded"), sem("gdn_dve_g"), sem("gdn_act_g"), sem("gdn_pe_g")
        sq_ready, sum_done, root_ready, unit_ready = sem("gdn_sq_ready"), sem("gdn_sum_done"), sem("gdn_root_ready"), sem("gdn_unit_ready")
        turned, turn_read = sem("gdn_turned"), sem("gdn_turn_read")
        square = cb.enter_context(nc.sbuf_tensor("gdn_square", [P, 2 * GH, SEQ], F32))
        eps = cb.enter_context(nc.sbuf_tensor("gdn_eps", [P, 1], F32))
        NL = 2 * GH
        eps_made = sem("gdn_eps_made")
        picks_made, recip_ready, spread_done = sem("gdn_picks_made"), sem("gdn_recip_ready"), sem("gdn_spread_done")
        to_row = cb.enter_context(nc.sbuf_tensor("gdn_to_row", [P, NL, NL], F32))
        from_row = cb.enter_context(nc.sbuf_tensor("gdn_from_row", [NL, NL, P], F32))
        norms = cb.enter_context(nc.sbuf_tensor("gdn_norms", [NL, 2, SEQ], F32))
        ORDER = [*range(GH, 2 * GH), *range(GH)]
        block = cb.enter_context(nc.Block())

        @block.sync
        def _(sp):
            sp.dma_start(rows[:, 0, :], m.row("gdn_dt_bias", GH)).then_inc(rows_loaded, 16)
            sp.dma_start(rows[:, 1, :], m.row("gdn_a_log", GH)).then_inc(rows_loaded, 16)
            gates.sync(sp)

        @block.tensor
        def _(pe):
            pe.wait_ge(picks_made, 2)
            for n, j in enumerate(ORDER):
                pe.wait_ge(sq_ready, n + 1)
                mm = pe.matmul(m.banks[0][0:NL, :], to_row[:, j, :], square[:, j, :], start=(n == 0), stop=(n == NL - 1))
            mm.then_inc(sum_done, 1)

            def turn(j):
                src = 2 * GH + j if j < GH else j
                if j >= GH:
                    pe.wait_ge(unit_ready, j - GH + 1)
                if j >= 2:
                    pe.wait_ge(turn_read, j - 1)
                for t in range(TT):
                    mm = pe.transpose(m.banks[4 + j % 2][:, t * P:(t + 1) * P], conved[:, src, t * P:(t + 1) * P],
                                      m.ident[:, :])
                mm.then_inc(turned, 1)

            pe.wait_ge(dve_g, 3)
            pe.matmul(m.banks[6][:, 0:TT * GH], m.upto[:, :], la[:, :], start=True, stop=True)
            pe.matmul(m.banks[6][:, 16:16 + TT * GH], m.ones[:, :], la[:, :], start=True, stop=True).then_inc(pe_g, 1)
            gates.tensor_cumulate(pe, m.banks[7])
            for j in range(GH):
                turn(j)
            pe.wait_ge(recip_ready, 1)
            for n, j in enumerate(ORDER):
                if n >= 4:
                    pe.wait_ge(unit_ready, n - 3)
                pe.matmul(m.banks[n % 4][:, :], from_row[:, j, :], norms[:, 1, :], start=True, stop=True)\
                  .then_inc(spread_done, 1)
                if n >= GH:
                    turn(n)

        @block.scalar
        def _(act):
            step = m.steps(act, m.act_step)
            for j in ORDER:
                act.activation(square[:, j, :], conved[:, j, :], ACT.Square).then_inc(sq_ready, 1)
            act.wait_ge(dve_g, 1)
            step(act.activation(tmp[:, 1, :], tmp[:, 0, :], ACT.Abs))
            act.activation(beta[:, :], small[:, :, GH:2 * GH], ACT.Sigmoid)
            step(act.activation(tmp[:, 1, :], tmp[:, 1, :], ACT.Exp, scale=-1.0))
            act.activation(rows[:, 1, :], rows[:, 1, :], ACT.Exp)
            gates.scalar_exp(act, step)
            act.activation(tmp[:, 1, :], tmp[:, 1, :], ACT.Ln, bias=1.0).then_inc(act_g, 1)
            gates.scalar_log(act)
            act.wait_ge(eps_made, 1)
            act.wait_ge(sum_done, 1)
            act.activation(norms[:, 0, :], m.banks[0][0:NL, :], ACT.Sqrt, bias=eps[0:NL, 0:1]).then_inc(root_ready, 1)
            act.wait_ge(pe_g, 1)
            act.activation(grow[:, :], m.banks[6][:, 0:TT * GH], ACT.Exp)
            act.activation(whole[:, :], m.banks[6][:, 16:16 + TT * GH], ACT.Exp)
            act.activation(tmp[:, 2, :], m.banks[6][:, 0:TT * GH], ACT.Copy).then_inc(act_g, 1)
            act.wait_ge(dve_g, 4)
            act.activation(to_end[:, :], tmp[:, 3, :], ACT.Exp).then_inc(act_g, 1)
            for j in range(NL):
                act.wait_ge(turned, j + 1)
                dst = v_tok if j < GH else k_tok
                act.activation(dst[:, :, j % GH, :], m.banks[4 + j % 2][:, :].rearrange("p (t n) -> p t n", t=TT),
                               ACT.Copy).then_inc(turn_read, 1)
            m.keep(step)

        @block.vector
        def _(dve):
            step = m.steps(dve, m.dve_step)
            dve.memset(eps[:, :], EPS).then_inc(eps_made, 1)
            dve.wait_ge(rows_loaded, 32)
            t3 = lambda ap: ap.rearrange("p (t h) -> p t h", t=TT)
            dve.tensor_tensor(t3(tmp[:, 0, :]), small[:, :, 0:GH], again(rows[:, 0, :], TT), ALU.add).then_inc(dve_g, 1)
            gates.vector_biases(dve)
            dve.wait_ge(act_g, 1)
            step(dve.scalar_tensor_tensor(tmp[:, 0, :], tmp[:, 0, :], 0.0, tmp[:, 1, :], ALU.max, ALU.add))
            dve.scalar_tensor_tensor(t3(la[:, :]), t3(tmp[:, 0, :]), -1.0, again(rows[:, 1, :], TT), ALU.mult, ALU.mult)\
               .then_inc(dve_g, 2)
            gates.vector_log_f(dve)
            dve.wait_ge(root_ready, 1)
            dve.reciprocal(norms[:, 1, :], norms[:, 0, :]).then_inc(recip_ready, 1)
            dve.wait_ge(act_g, 2)
            dve.tensor_tensor(tmp[:, 3, :], m.banks[6][:, 16:16 + TT * GH], tmp[:, 2, :], ALU.subtract).then_inc(dve_g, 1)
            gates.vector_g(dve, step, m.banks[7])
            for n, j in enumerate(ORDER):
                dve.wait_ge(spread_done, n + 1)
                dve.tensor_tensor(conved[:, j, :], conved[:, j, :], m.banks[n % 4][:, :], ALU.mult).then_inc(unit_ready, 1)
            dve.wait_ge(turn_read, NL)
            dve.wait_ge(act_g, 3)
            step(dve.tensor_tensor(tmp[:, 0, :], beta[:, :], grow[:, :], ALU.mult))
            rows16 = lambda ap: ap.rearrange("p t h d -> p (t h) d")
            dve.tensor_tensor(rows16(v_tok[:, :, :, :]), rows16(v_tok[:, :, :, :]), spread(beta[:, :], GD), ALU.mult)
            dve.tensor_tensor(rows16(k_in[:, :, :, :]), rows16(k_tok[:, :, :, :]), spread(tmp[:, 0, :], GD), ALU.mult)
            m.keep(step)

        @block.gpsimd
        def _(pool):
            pool.memset(to_row[:, :, :], 0.0).then_inc(picks_made, 1)
            pool.wait_ge(picks_made, 1)
            pool.affine_select(out=to_row[:, :, :], in_=to_row[:, :, :], compare_op=ALU.not_equal, fill=1.0, base=0,
                               pattern=[[1, NL], [-1, NL]], channel_multiplier=0)
            pool.tensor_copy(from_row[:, :, :], spread(m.ident[0:NL, 0:NL], P)).then_inc(picks_made, 1)

    mats = lambda n: sb("gdn_" + n, [P, TT, GH * P])
    far_part, qk_t, W1, W2, X2, W3 = (mats(n) for n in ("far_part", "qk_t", "w1", "w2", "x2", "w3"))
    near_part = mixed[:, :, 0:GH, :].rearrange("p t h n -> p t (h n)")
    X1 = mixed[:, :, GH:, :].rearrange("p t h n -> p t (h n)")
    W4 = conved[:, 2 * GH:3 * GH, :]
    before = sb("gdn_before", [P, P])
    near = sb("gdn_near", [P, 4, P])
    first_level = [
        (X2, X1, [("copy", W1)]),
        (X1, X2, [("copy", W2), ("plus", W3)]),
        (W2, W1, [("plus", W4)]),
        (W3, W4, [("copy", W1)]),
        (X2, W1, [("copy", W2)]),
        (W1, X2, [("copy", W3)]),
    ]

    def next_level(L):
        return [
            (W3, L, [("copy", W1)]),
            (L, W3, [("copy", W4), ("minus", X1)]),
            (W1, W4, [("plus", X2)]),
            (X2, W2, [("copy", W1)]),
            (X1, W1, [("copy", W2)]),
            (W1, X1, [("copy", W3)]),
        ]

    inversion = first_level + next_level(near_part) + next_level(far_part)
    per4 = lambda ap: ap.rearrange("p (h n) -> p h n", h=GH)
    with ExitStack() as cb:
        sem = lambda n: m.sem(cb, n)
        made, cut_ready, exp_ready = sem("gdn_made"), sem("gdn_cut_ready"), sem("gdn_exp_ready")
        pe_done, bank_read = sem("gdn_pe_done"), sem("gdn_bank_read")
        a_ready, parts_ready = sem("gdn_a_ready"), sem("gdn_parts_ready")
        block = cb.enter_context(nc.Block())
        blocks = lambda ap, n: ap.rearrange("p (b n) -> p b n", n=n)

        @block.gpsimd
        def _(pool):
            step = m.steps(pool, m.pool_step)
            pool.tensor_tensor(before[:, :], m.upto[:, :], m.ident[:, :], ALU.subtract)
            step(pool.memset(near[:, :, :], 1.0))
            for n, size in enumerate((8, 32)):
                step(pool.affine_select(out=blocks(near[:, n, :], size), in_=blocks(near[:, n, :], size),
                                        compare_op=ALU.is_ge, fill=0.0, base=0,
                                        pattern=[[-size, P // size], [0, size]], channel_multiplier=1))
                step(pool.affine_select(out=blocks(near[:, n, :], size), in_=blocks(near[:, n, :], size),
                                        compare_op=ALU.is_ge, fill=0.0, base=size - 1,
                                        pattern=[[size, P // size], [0, size]], channel_multiplier=-1))
            pool.tensor_tensor(near[:, 2, :], near[:, 1, :], near[:, 0, :], ALU.subtract)
            pool.tensor_tensor(near[:, 3, :], near[:, 3, :], near[:, 1, :], ALU.subtract).then_inc(made, 1)
            for ch in range(TT):
                pool.tensor_tensor(per4(qk_t[:, ch, :]), again(m.upto[:, :], GH), spread(la[:, ch * GH:(ch + 1) * GH], P),
                                   ALU.mult).then_inc(cut_ready, 1)
            k16 = k_tok[:, :, :, :].rearrange("p t h d -> p (t h) d")
            pool.tensor_tensor(k16, k16, spread(to_end[:, :], GD), ALU.mult)
            for ch in range(TT):
                far = far_part[:, ch, :]
                pool.wait_ge(a_ready, ch + 1)
                step(pool.tensor_tensor(per4(near_part[:, ch, :]), per4(far), again(near[:, 2, :], GH), ALU.mult))
                pool.tensor_tensor(per4(far), per4(far), again(near[:, 3, :], GH), ALU.mult).then_inc(parts_ready, 1)
            m.keep(step)

        @block.tensor
        def _(pe):
            def result(stage, ch):
                if stage >= 1:
                    pe.wait_ge(bank_read, TT * (stage - 1) + ch + 1)
                return m.banks[(TT * stage + ch) % 8]

            def four(bank, lhs, rhs):
                for h in range(GH):
                    mm = pe.matmul(bank[:, h * P:(h + 1) * P], lhs(h), rhs(h), start=True, stop=True)
                mm.then_inc(pe_done, 1)

            mat = lambda X, ch: (lambda h: X[:, ch, h * P:(h + 1) * P])
            chunk = lambda X, ch: (lambda h: X[:, h, ch * P:(ch + 1) * P])
            for ch in range(TT):
                pe.wait_ge(cut_ready, ch + 1)
                pe.matmul(result(0, ch)[:, :], m.after[:, :], qk_t[:, ch, :], start=True, stop=True).then_inc(pe_done, 1)
            for ch in range(TT):
                four(result(1, ch), chunk(k_ch, ch), chunk(k_ch, ch))
            for ch in range(TT):
                four(result(2, ch), chunk(k_ch, ch), chunk(q_ch, ch))
            for stage, X in ((3, W2), (4, X1)):
                for ch in range(TT):
                    bank = result(stage, ch)
                    for h in range(GH):
                        mm = pe.transpose(bank[:, h * P:(h + 1) * P], mat(X, ch)(h), m.ident[:, :])
                    mm.then_inc(pe_done, 1)
            stage = 5
            for n, (lhs, rhs, _outs) in enumerate(inversion):
                if n == len(first_level):
                    pe.wait_ge(parts_ready, TT)
                for ch in range(TT):
                    four(result(stage, ch), mat(lhs, ch), mat(rhs, ch))
                stage += 1
            for ch in range(TT):
                four(result(stage, ch), lambda h: k_in[:, ch, h, :], mat(W3, ch))
            for ch in range(TT):
                four(result(stage + 1, ch), mat(W3, ch), lambda h: v_tok[:, ch, h, :])

        @block.scalar
        def _(act):
            for ch in range(TT):
                act.wait_ge(pe_done, ch + 1)
                act.activation(W1[:, ch, :], m.banks[ch][:, :], ACT.Exp).then_inc(exp_ready, 1)

        @block.vector
        def _(dve):
            step = m.steps(dve, m.dve_step)

            def result(stage, ch):
                dve.wait_ge(pe_done, TT * stage + ch + 1)
                return m.banks[(TT * stage + ch) % 8][:, :]

            dve.wait_ge(made, 1)
            for ch in range(TT):
                dve.wait_ge(exp_ready, ch + 1)
                dve.tensor_tensor(per4(W1[:, ch, :]), per4(W1[:, ch, :]), again(m.upto[:, :], GH), ALU.mult)\
                   .then_inc(bank_read, 1)
            for ch in range(TT):
                dve.wait_ge(bank_read, ch + 1)
                step(dve.tensor_tensor(W2[:, ch, :], result(1, ch), W1[:, ch, :], ALU.mult))
                dve.tensor_tensor(per4(W2[:, ch, :]), per4(W2[:, ch, :]), again(before[:, :], GH), ALU.mult)\
                   .then_inc(bank_read, 1)
            for ch in range(TT):
                dve.scalar_tensor_tensor(qk_t[:, ch, :], result(2, ch), GD ** -0.5, W1[:, ch, :], ALU.mult, ALU.mult)\
                   .then_inc(bank_read, 1)
            for ch in range(TT):
                far = far_part[:, ch, :]
                step(dve.tensor_tensor(per4(far), per4(result(3, ch)), spread(beta[:, ch * GH:(ch + 1) * GH], P), ALU.mult))
                step(dve.tensor_tensor(per4(X1[:, ch, :]), per4(far), again(near[:, 0, :], GH), ALU.mult))
                dve.sem_inc(a_ready, 1)
                dve.sem_inc(bank_read, 1)
            for ch in range(TT):
                dve.tensor_copy(X2[:, ch, :], result(4, ch)).then_inc(bank_read, 1)
            stage = 5
            for _lhs, _rhs, outs in inversion:
                for ch in range(TT):
                    bank = result(stage, ch)
                    for kind, X in outs:
                        if kind == "copy":
                            last = dve.tensor_copy(X[:, ch, :], bank)
                        else:
                            last = dve.scalar_tensor_tensor(per4(X[:, ch, :]), per4(bank), 1.0 if kind == "plus" else -1.0,
                                                            again(m.ident[:, :], GH), ALU.mult, ALU.add)
                    if stage == 6:
                        last = dve.scalar_tensor_tensor(per4(X2[:, ch, :]), per4(X2[:, ch, :]), -1.0,
                                                        again(m.ident[:, :], GH), ALU.mult, ALU.add)
                    last.then_inc(bank_read, 1)
                stage += 1
            for X in (W1, W2):
                for ch in range(TT):
                    dve.tensor_copy(X[:, ch, :], result(stage, ch)).then_inc(bank_read, 1)
                stage += 1
            m.keep(step)

    w_t, u = W1, W2
    state = sb("gdn_state", [P, GH * GD])
    carry = sb("gdn_carry", [P, 2, GH * GD])
    with ExitStack() as cb:
        sem = lambda n: m.sem(cb, n)
        old_done, new_ready, new_done, state_ready, out_read = (sem("gdn_old_done"), sem("gdn_new_ready"), sem("gdn_new_done"),
                                                                sem("gdn_state_ready"), sem("gdn_out_read"))
        gates.place(W3, far_part)
        block = cb.enter_context(nc.Block())
        mat = lambda X, ch, h: X[:, ch, h * P:(h + 1) * P]
        head = lambda X, h: X[:, h * P:(h + 1) * P]

        @block.scalar
        def _(act):
            gates.scalar_weights(act, m.banks[3])

        @block.tensor
        def _(pe):
            for ch in range(TT):
                bw, bq, bo, bs = m.banks[4 * (ch % 2):4 * (ch % 2) + 4]
                if ch == 0:
                    gates.tensor_turn(pe, m.banks[4], m.banks[5])
                if ch == 1:
                    pe.wait_ge(gates.dve_p, 4)
                if ch > 0:
                    pe.wait_ge(state_ready, ch)
                    if ch >= 2:
                        pe.wait_ge(out_read, ch - 1)
                    for h in range(GH):
                        pe.matmul(head(bw, h), mat(w_t, ch, h), head(state, h), start=True, stop=True)
                    for h in range(GH):
                        mm = pe.matmul(head(bq, h), q_ch[:, h, ch * P:(ch + 1) * P], head(state, h), start=True, stop=True)
                    mm.then_inc(old_done, 1)
                    pe.wait_ge(new_ready, ch)
                for h in range(GH):
                    pe.matmul(head(bo, h), mat(qk_t, ch, h), mat(u, ch, h), start=True, stop=True)
                for h in range(GH):
                    mm = pe.matmul(head(bs, h), k_tok[:, ch, h, :], mat(u, ch, h), start=True, stop=True)
                mm.then_inc(new_done, 1)
            gates.tensor_weights(pe, m.banks[3])

        @block.vector
        def _(dve):
            step = m.steps(dve, m.dve_step)
            gates.vector_turned(dve, step, m.banks[4], m.banks[5])
            for ch in range(TT):
                bw, bq, bo, bs = m.banks[4 * (ch % 2):4 * (ch % 2) + 4]
                mine = slice(ch * GH, (ch + 1) * GH)
                if ch > 0:
                    dve.wait_ge(old_done, ch)
                    dve.tensor_tensor(u[:, ch, :], u[:, ch, :], bw[:, :], ALU.subtract).then_inc(new_ready, 1)
                    old = carry[:, ch % 2, :]
                    step(dve.tensor_tensor(per4(old), per4(bq[:, :]), spread(grow[:, mine], GD), ALU.mult))
                dve.wait_ge(new_done, ch + 1)
                if ch > 0:
                    step(dve.tensor_tensor(per4(state[:, :]), per4(state[:, :]), spread(whole[:, mine], GD), ALU.mult))
                    dve.tensor_tensor(state[:, :], state[:, :], bs[:, :], ALU.add).then_inc(state_ready, 1)
                    dve.scalar_tensor_tensor(mixed[:, ch, 0:GH, :], per4(old), GD ** -0.5, per4(bo[:, :]), ALU.mult, ALU.add)\
                       .then_inc(out_read, 1)
                else:
                    dve.tensor_copy(state[:, :], bs[:, :]).then_inc(state_ready, 1)
                    dve.tensor_copy(mixed[:, ch, 0:GH, :], per4(bo[:, :])).then_inc(out_read, 1)
                gates.vector_maxima(dve, step, ch)
            gates.vector_rows(dve, step)
            gates.vector_w_end(dve)
            m.keep(step)


class Gates:

    def __init__(self, m, c, small):
        self.m, self.small = m, small
        sb = lambda n, s: c.enter_context(m.nc.sbuf_tensor(n, s, F32))
        self.W = TT * MH
        self.rows = sb("mls_rows", [P, 2, MH])
        self.tmp = sb("mls_tmp", [P, 4, self.W])
        self.g = sb("mls_g", [P, self.W])
        self.at_start = sb("mls_at_start", [MH, TT + 1])
        self.last = sb("mls_last", [MH, TT])
        self.diag = sb("mls_diag", [MH, TT, MH])
        self.M_diag = sb("mls_M_diag", [MH, TT, MH, P])
        self.weights = sb("mls_weights", [P, 4, self.W])
        self.w_end = sb("mls_w_end", [P, self.W])
        self.loaded, self.dve_p, self.act_p, self.pe_p = (m.sem(c, "mls_" + n) for n in ("loaded", "dve_p", "act_p", "pe_p"))

    def place(self, four, two):
        self.G, self.B, self.MX, self.A1 = (four[0:MH, n, :] for n in range(4))
        self.A2, self.A3 = (two[0:MH, n, :] for n in range(2))

    @staticmethod
    def part(ap, ch):
        return ap[:, ch * P:(ch + 1) * P]

    def sync(self, sp):
        sp.dma_start(self.rows[:, 0, :], self.m.row("mls_i_bias", MH)).then_inc(self.loaded, 16)
        sp.dma_start(self.rows[:, 1, :], self.m.row("mls_f_bias", MH)).then_inc(self.loaded, 16)

    def vector_biases(self, dve):
        t3 = lambda ap: ap.rearrange("p (t h) -> p t h", t=TT)
        dve.wait_ge(self.loaded, 32)
        dve.tensor_tensor(t3(self.tmp[:, 0, :]), self.small[:, :, 3 * MH:], again(self.rows[:, 1, :], TT), ALU.add)\
           .then_inc(self.dve_p, 1)
        dve.tensor_tensor(t3(self.g[:, :]), self.small[:, :, 2 * MH:3 * MH], again(self.rows[:, 0, :], TT), ALU.add)

    def scalar_exp(self, act, step):
        u = self.tmp[:, 1, :]
        act.wait_ge(self.dve_p, 1)
        step(act.activation(u, self.tmp[:, 0, :], ACT.Abs))
        step(act.activation(u, u, ACT.Exp, scale=-1.0))

    def scalar_log(self, act):
        u = self.tmp[:, 1, :]
        act.activation(u, u, ACT.Ln, bias=1.0).then_inc(self.act_p, 1)

    def vector_log_f(self, dve):
        dve.wait_ge(self.act_p, 1)
        dve.scalar_tensor_tensor(self.tmp[:, 2, :], self.tmp[:, 0, :], 0.0, self.tmp[:, 1, :], ALU.min, ALU.subtract)\
           .then_inc(self.dve_p, 1)

    def tensor_cumulate(self, pe, bank):
        pe.wait_ge(self.dve_p, 2)
        pe.matmul(bank[:, 0:self.W], self.m.upto[:, :], self.tmp[:, 2, :], start=True, stop=True).then_inc(self.pe_p, 1)

    def vector_g(self, dve, step, bank):
        dve.wait_ge(self.pe_p, 1)
        step(dve.tensor_copy(self.tmp[:, 3, :], bank[:, 0:self.W]))
        dve.tensor_tensor(self.g[:, :], self.g[:, :], self.tmp[:, 3, :], ALU.subtract).then_inc(self.dve_p, 1)

    def tensor_turn(self, pe, bank_g, bank_b):
        pe.wait_ge(self.dve_p, 3)
        for t in range(TT):
            pe.transpose(bank_g[0:MH, t * P:(t + 1) * P], self.g[:, t * MH:(t + 1) * MH], self.m.ident[:, :])
            mm = pe.transpose(bank_b[0:MH, t * P:(t + 1) * P], self.tmp[:, 3, t * MH:(t + 1) * MH], self.m.ident[:, :])
        mm.then_inc(self.pe_p, 1)

    def vector_turned(self, dve, step, bank_g, bank_b):
        dve.wait_ge(self.pe_p, 2)
        dve.tensor_copy(self.G, bank_g[0:MH, :])
        step(dve.tensor_copy(self.B, bank_b[0:MH, :]))
        dve.sem_inc(self.dve_p, 1)

    def vector_maxima(self, dve, step, ch):
        part, at_start, last = self.part, self.at_start, self.last
        G, B, MX, A1, A3 = self.G, self.B, self.MX, self.A1, self.A3
        if ch == 0:
            step(dve.memset(at_start[:, 0:1], 0.0))
        end = (ch + 1) * P - 1
        step(dve.tensor_tensor_scan(part(MX, ch), part(G, ch), part(G, ch), at_start[:, ch:ch + 1], ALU.max, ALU.max))
        step(dve.tensor_tensor(at_start[:, ch + 1:ch + 2], B[:, end:end + 1], MX[:, end:end + 1], ALU.add))
        dve.tensor_scalar(part(A1, ch), part(MX, ch), -1.0, at_start[:, ch:ch + 1], ALU.mult, ALU.add)
        dve.tensor_scalar(part(A3, ch), part(G, ch), MX[:, end:end + 1], None, ALU.subtract)
        dve.tensor_tensor(last[:, ch:ch + 1], at_start[:, ch:ch + 1], MX[:, end:end + 1], ALU.subtract)
        dve.tensor_tensor(self.M_diag[:, ch, :, :], again(part(MX, ch), MH), spread(self.m.ident[0:MH, 0:MH], P), ALU.mult)

    def vector_rows(self, dve, step):
        step(dve.scalar_tensor_tensor(self.A2, self.B, -1.0, self.MX, ALU.mult, ALU.subtract))
        dve.tensor_tensor(self.diag[:, :, :], spread(self.last[:, :], MH), again(self.m.ident[0:MH, 0:MH], TT), ALU.mult)\
           .then_inc(self.dve_p, 1)

    def tensor_weights(self, pe, bank):
        W = self.W
        pe.wait_ge(self.dve_p, 5)
        for n, rowset in enumerate((self.A1, self.A2, self.A3)):
            for t in range(TT):
                pe.transpose(bank[:, n * W + t * MH:n * W + (t + 1) * MH], self.part(rowset, t), self.m.ident[0:MH, 0:MH])
        pe.matmul(bank[:, 3 * W:4 * W], self.m.ones[0:MH, :], self.diag[:, :, :].rearrange("p t h -> p (t h)"),
                  start=True, stop=True).then_inc(self.pe_p, 1)

    def scalar_weights(self, act, bank):
        act.wait_ge(self.pe_p, 3)
        act.activation(self.weights[:, :, :].rearrange("p k w -> p (k w)"), bank[:, 0:4 * self.W], ACT.Exp)\
           .then_inc(self.act_p, 1)

    def vector_w_end(self, dve):
        dve.wait_ge(self.act_p, 2)
        dve.tensor_scalar(self.w_end[:, :], self.weights[:, 2, :], MD ** -0.5, None, ALU.mult)


def mlstm(m, c, conved, mixed, v_one, gates, gate):
    nc = m.nc
    sb = lambda n, s, d=F32: c.enter_context(nc.sbuf_tensor(n, s, d))
    q_ch, k_ch = conved[:, 3 * GH:3 * GH + MH, :], conved[:, 3 * GH + MH:, :]
    k_end = sb("mls_k_end", [P, TT, MH, MD])
    g, weights, M_diag = gates.g, gates.weights, gates.M_diag
    fade = sb("mls_fade", [P, TT, MH, P])
    state = sb("mls_state", [P, MH, MD + 1])
    acc = sb("mls_acc", [P, 2, MH, MD + 1])
    den = sb("mls_den", [P, 2, 3, MH])
    gains = sb("hyb_gains", [P, D])
    with ExitStack() as cb:
        sem = lambda n: m.sem(cb, n)
        m_done, gap_ready, fade_ready, low_ready, qk_done, p_ready = (sem("mls_m_done"), sem("mls_gap_ready"), sem("mls_fade_ready"),
                                                                    sem("mls_low_ready"), sem("mls_qk_done"), sem("mls_p_ready"))
        out_done, out_read, state_ready = sem("mls_out_done"), sem("mls_out_read"), sem("mls_state_ready")
        gains_loaded, turned, turn_read, k_ready = (sem("hyb_gains_loaded"), sem("mls_turned"), sem("mls_turn_read"),
                                                    sem("mls_k_ready"))
        two = lambda n: m.banks[n][:, 0:2 * (MD + 1)].rearrange("p (h d) -> p h d", h=2)
        block = cb.enter_context(nc.Block())

        @block.tensor
        def _(pe):
            for ch in range(TT):
                if ch >= 2:
                    pe.wait_ge(gap_ready, ch - 1)
                pe.matmul(m.banks[ch % 2][:, :], m.ones[0:MH, :], M_diag[:, ch, :, :].rearrange("p h n -> p (h n)"),
                          start=True, stop=True).then_inc(m_done, 1)
            for h in range(MH):
                if h >= 2:
                    pe.wait_ge(turn_read, h - 1)
                for t in range(TT):
                    mm = pe.transpose(m.banks[4 + h % 2][:, t * P:(t + 1) * P], k_ch[:, h, t * P:(t + 1) * P], m.ident[:, :])
                mm.then_inc(turned, 1)
            for ch in range(TT):
                at = slice(ch * P, (ch + 1) * P)
                pe.wait_ge(gap_ready, TT)
                if ch >= 2:
                    pe.wait_ge(p_ready, ch - 1)
                for h in range(MH):
                    mm = pe.matmul(m.banks[ch % 2][:, h * P:(h + 1) * P], k_ch[:, h, at], q_ch[:, h, at], start=True, stop=True)
                mm.then_inc(qk_done, 1)
                if ch > 0:
                    pe.wait_ge(out_read, ch)
                    pe.wait_ge(state_ready, ch)
                    for h in range(MH):
                        pe.matmul(two(4 + h // 2)[:, h % 2, :], q_ch[:, h, at], state[:, h, :], start=True, stop=True)
                if ch == 0:
                    pe.wait_ge(k_ready, 1)
                for h in range(MH):
                    pe.matmul(two(6 + h // 2)[:, h % 2, :], k_end[:, ch, h, :], v_one[:, ch, h, :], start=True, stop=True)
                pe.wait_ge(p_ready, ch + 1)
                for h in range(MH):
                    mm = pe.matmul(two(2 + h // 2)[:, h % 2, :], fade[:, ch, h, :], v_one[:, ch, h, :], start=True, stop=True)
                mm.then_inc(out_done, 1)

        @block.scalar
        def _(act):
            for ch in range(TT):
                act.wait_ge(gap_ready, ch + 1)
                act.activation(fade[:, ch, :, :], fade[:, ch, :, :], ACT.Exp, scale=-1.0).then_inc(fade_ready, 1)
                h = ch
                act.wait_ge(turned, h + 1)
                act.activation(k_end[:, :, h, :], m.banks[4 + h % 2][:, :].rearrange("p (t n) -> p t n", t=TT), ACT.Copy)\
                   .then_inc(turn_read, 1)

        @block.gpsimd
        def _(pool):
            for ch in range(TT):
                pool.wait_ge(fade_ready, ch + 1)
                pool.tensor_tensor(fade[:, ch, :, :], fade[:, ch, :, :], again(m.upto[:, :], MH), ALU.mult).then_inc(low_ready, 1)
            pool.wait_ge(gains_loaded, 16)
            for t in range(TT):
                pool.tensor_tensor(gate[:, t, :], gate[:, t, :], gains[:, :], ALU.mult)

        @block.sync
        def _(sp):
            sp.dma_start(gains[:, :], m.row("hyb_gains", D)).then_inc(gains_loaded, 16)

        @block.vector
        def _(dve):
            step = m.steps(dve, m.dve_step)
            for ch in range(TT):
                dve.wait_ge(m_done, ch + 1)
                for h in range(MH):
                    col = g[:, ch * MH + h:ch * MH + h + 1]
                    gap = dve.tensor_scalar(fade[:, ch, h, :], m.banks[ch % 2][:, h * P:(h + 1) * P], col, 0.0,
                                            ALU.subtract, ALU.max)
                gap.then_inc(gap_ready, 1)
            dve.wait_ge(turn_read, MH)
            k16 = k_end[:, :, :, :].rearrange("p t h d -> p (t h) d")
            dve.tensor_tensor(k16, k16, spread(gates.w_end[:, :], MD), ALU.mult).then_inc(k_ready, 1)
            for ch in range(TT):
                mine = slice(ch * MH, (ch + 1) * MH)
                dve.wait_ge(qk_done, ch + 1)
                dve.wait_ge(low_ready, ch + 1)
                dve.scalar_tensor_tensor(fade[:, ch, :, :], m.banks[ch % 2][:, :].rearrange("p (h n) -> p h n", h=MH),
                                         MD ** -0.5, fade[:, ch, :, :], ALU.mult, ALU.mult).then_inc(p_ready, 1)
                dve.wait_ge(out_done, ch + 1)
                a = acc[:, ch % 2, :, :]
                for x in range(2):
                    pair = slice(2 * x, 2 * x + 2)
                    if ch > 0:
                        step(dve.tensor_tensor(a[:, pair, :], two(4 + x), spread(weights[:, 0, ch * MH + 2 * x:ch * MH + 2 * x + 2], MD + 1), ALU.mult))
                        step(dve.tensor_tensor(a[:, pair, :], a[:, pair, :], two(2 + x), ALU.add))
                        step(dve.tensor_tensor(state[:, pair, :], state[:, pair, :], spread(weights[:, 3, ch * MH + 2 * x:ch * MH + 2 * x + 2], MD + 1), ALU.mult))
                        step(dve.tensor_tensor(state[:, pair, :], state[:, pair, :], two(6 + x), ALU.add))
                    else:
                        step(dve.tensor_copy(a[:, pair, :], two(2 + x)))
                        step(dve.tensor_copy(state[:, pair, :], two(6 + x)))
                dve.sem_inc(state_ready, 1)
                dve.sem_inc(out_read, 1)
                d = den[:, ch % 2, :, :]
                step(dve.tensor_scalar(d[:, 0, :], a[:, :, MD], -1.0, None, ALU.mult))
                step(dve.tensor_tensor(d[:, 0, :], d[:, 0, :], a[:, :, MD], ALU.max))
                step(dve.tensor_tensor(d[:, 1, :], d[:, 0, :], weights[:, 1, mine], ALU.max))
                step(dve.reciprocal(d[:, 2, :], d[:, 1, :]))
                dve.tensor_tensor(mixed[:, ch, GH:, :], a[:, :, 0:MD], spread(d[:, 2, :], MD), ALU.mult)
            m.keep(step)


class HeadNormTurn(PlainTurn):

    def __init__(self, m, c, name, mixed, gate, square, turned, banks):
        super().__init__(m, c, name, mixed.rearrange("p t h d -> p t (h d)"), turned, TT, D, banks)
        self.mixed, self.gate, self.square = mixed, gate, square
        self.stat = c.enter_context(m.nc.sbuf_tensor(name + "_stat", [P, 3, TT * (GH + MH)], F32))
        self.squared, self.mean_ready, self.rstd_ready, self.done = (m.sem(c, name + x) for x in
                                                                     ("_squared", "_mean", "_rstd", "_done"))

    def vector(self, dve, step):
        st, n = self.stat, GH + MH
        for t in range(TT):
            dve.wait_ge(self.squared, t + 1)
            last = dve.tensor_reduce(st[:, 0, t * n:(t + 1) * n], self.square[:, t, :, :], AX.X, ALU.add)
        step(last)
        step(dve.tensor_scalar(st[:, 1, :], st[:, 0, :], 1.0 / GD, EPS, ALU.mult, ALU.add))
        dve.reciprocal(st[:, 2, :], st[:, 1, :]).then_inc(self.mean_ready, 1)
        for t in range(TT):
            last = dve.tensor_tensor(self.src[:, t, :], self.src[:, t, :], self.gate[:, t, :], ALU.mult)
        step(last)
        dve.wait_ge(self.rstd_ready, 1)
        for t in range(TT):
            dve.tensor_tensor(self.mixed[:, t, :, :], self.mixed[:, t, :, :], spread(st[:, 0, t * n:(t + 1) * n], GD), ALU.mult)\
               .then_inc(self.done, 1)

    def scalar_sums(self, act):
        for t in range(TT):
            act.activation(self.square[:, t, :, :], self.mixed[:, t, :, :], ACT.Square).then_inc(self.squared, 1)

    def scalar_rstd(self, act):
        act.wait_ge(self.mean_ready, 1)
        act.activation(self.stat[:, 0, :], self.stat[:, 2, :], ACT.Sqrt).then_inc(self.rstd_ready, 1)

    def tensor(self, pe):
        pe.wait_ge(self.done, TT)
        super().tensor(pe)


def hybrid_out(m, mixed, gate, conved):
    nc = m.nc
    with ExitStack() as c:
        square = conved[:, 0:8, :].rearrange("p (t a) (b d) -> p t (a b) d", t=TT, d=GD)
        turned = [c.enter_context(nc.sbuf_tensor(f"hyb_turned_{x}", [P, DT, SEQ], F32R)) for x in ("high", "low")]
        turn = HeadNormTurn(m, c, "hyb_hnorm", mixed[:, :, :, :], gate, square,
                            turned, m.banks[0:4])
        project_and_add(m, c, "hyb_o", turn, turned, DT, None, None)



MT = MEM // P


def copy_columns(m, act, n, u0, free, dst, banks, width):
    act.sem_inc(free, RING)
    with act.Fori(0, n // RING) as i:
        for b in range(RING):
            act.wait_ge(m.w_used, i * RING + (u0 + b + 1))
            act.activation(dst[:, i * RING + b, :], banks[b][:, 0:width], ACT.Copy).then_inc(free, 1)


def cross_attention(m):
    nc = m.nc
    with ExitStack() as c:
        sb = lambda n, s, d=F32: c.enter_context(nc.sbuf_tensor(n, s, d))
        q_ch = sb("xa_q", [P, DT, SEQ])
        k_ch = sb("xa_k", [P, DT, MEM])
        v_tok = sb("xa_v", [P, MT, D])
        cross_in(m, q_ch, k_ch, v_tok)
        o_ch = [sb(f"xa_o_{x}", [P, DT, SEQ], F32R) for x in ("high", "low")]
        cross_core(m, q_ch, k_ch, v_tok, o_ch)
        with ExitStack() as c2:
            project_and_add(m, c2, "xa_out", None, o_ch, DT, None, None)


def cross_in(m, q_ch, k_ch, v_tok):
    nc, ins = m.nc, m.ins
    with ExitStack() as c:
        sb = lambda n, s, d=F32: c.enter_context(nc.sbuf_tensor(n, s, d))
        sem = lambda n: m.sem(c, n)
        mem = sb("xa_mem", [P, MT, D])
        mem_h = [sb(f"xa_mem_h_{x}", [P, DT, MEM], F32R) for x in ("high", "low")]
        h = [sb(f"xa_h_{x}", [P, DT, SEQ], F32R) for x in ("high", "low")]
        m.open_parts(c)
        norm_m = NormTurn(m, c, "xa_mnorm", mem, mem_h, lambda k: m.col("norm_mem", k), MT, D, m.banks[2:4])
        norm = NormTurn(m, c, "xa_norm", m.resid, h, lambda k: m.col("norm_xa", k), TT, D, m.banks[0:2] + m.banks[4:6])
        mem_loaded, q_copied, k_copied, v_done, v_copied = (sem("xa_mem_loaded"), sem("xa_q_copied"), sem("xa_k_copied"),
                                                           sem("xa_v_done"), sem("xa_v_copied"))
        u_q = m.unit
        u_k = u_q + DT
        u_v = u_k + DT
        block = c.enter_context(nc.Block())

        @block.sync
        def _(sp):
            sp.dma_start(mem[:, :, :], ins["mem"].rearrange("(t p) d -> p t d", p=P)).then_inc(mem_loaded, 16)
            stream_weights(m, sp, 2 * DT + 2 * DT // 2)

        @block.gpsimd
        def _(pool):
            split_weights(m, pool, DT)
            low_weights(m, pool, 2 * DT)

        @block.tensor
        def _(pe):
            norm.tensor(pe)
            norm_m.tensor(pe)
            pe.wait_ge(norm.turned_ready, DT)
            columns_out(m, pe, DT, h, SEQ, q_copied, 1, m.banks[4:8])
            pe.wait_ge(norm_m.turned_ready, DT)
            pe.wait_ge(q_copied, RING + DT)
            columns_out(m, pe, DT, mem_h, MEM, k_copied, 1, m.banks[4:8])
            tokens_out(m, pe, 2, DT, mem_h, MT, v_done, lambda ch, t: None, lambda ch, t: m.banks[MT * ch + t])

        @block.vector
        def _(dve):
            step = m.steps(dve, m.dve_step)
            norm.vector(dve, step)
            dve.wait_ge(mem_loaded, 16)
            norm_m.vector(dve, step)
            norm.vector_turned(dve)
            norm_m.vector_turned(dve)
            m.keep(step)

        @block.scalar
        def _(act):
            norm.scalar_sums(act)
            norm.scalar_rstd(act)
            act.wait_ge(mem_loaded, 16)
            norm_m.scalar_sums(act)
            norm_m.scalar_rstd(act)
            norm.scalar_turned(act)
            norm_m.scalar_turned(act)
            copy_columns(m, act, DT, u_q, q_copied, q_ch, m.banks[4:8], SEQ)
            act.sem_inc(k_copied, RING)
            high_weight(m, act, u_k)
            high_weight(m, act, u_k + 1)
            for k in range(DT):
                high_weight(m, act, u_k + k + 2)
                act.wait_ge(m.w_used, u_k + k + 1)
                act.activation(k_ch[:, k, :], m.banks[4 + k % RING][:, 0:MEM], ACT.Copy).then_inc(k_copied, 1)
            ahead = u_v + 2
            for ch in range(2):
                while ahead < min(u_v + (ch + 1) * DT // 2 + 2, u_v + DT):
                    high_weight(m, act, ahead)
                    ahead += 1
                for t in range(MT):
                    wait_tokens(m, act, u_v, DT, MT, v_done, ch, t)
                    act.activation(v_tok[:, t, ch * 512:(ch + 1) * 512], m.banks[MT * ch + t][:, :], ACT.Copy)\
                       .then_inc(v_copied, 1)


def cross_core(m, q_ch, k_ch, v_tok, o_ch):
    nc = m.nc
    HT = XD // P
    SCALE = XD ** -0.5
    units = [(t, pair) for t in range(TT) for pair in range(XH // 2)]
    N = len(units)
    with ExitStack() as c:
        sb = lambda n, s, d=F32: c.enter_context(nc.sbuf_tensor(n, s, d))
        sem = lambda n: m.sem(c, n)
        p = sb("xa_p", [P, 2, 2, MEM])
        pt = sb("xa_pt", [P, XH, MT, SEQ])
        stat = sb("xa_stat", [P, 2, 4, 2])
        high_ready = sem("xa_o_high_ready")
        scores_done, max_ready, exp_done, p_ready, turned, turn_read, out_done = (
            sem("xa_scores_done"), sem("xa_max_ready"), sem("xa_exp_done"), sem("xa_p_ready"), sem("xa_turned"),
            sem("xa_turn_read"), sem("xa_out_done"))
        block = c.enter_context(nc.Block())

        @block.tensor
        def _(pe):
            for i in range(N + 1):
                if i < N:
                    t, pair = units[i]
                    if i >= 2:
                        pe.wait_ge(exp_done, i - 1)
                    for x in range(2):
                        for k in range(HT):
                            j = (2 * pair + x) * HT + k
                            mm = pe.matmul(m.banks[i % 2][:, x * MEM:(x + 1) * MEM], q_ch[:, j, t * P:(t + 1) * P],
                                           k_ch[:, j, :], start=(k == 0), stop=(k == HT - 1))
                    mm.then_inc(scores_done, 1)
                if i >= 1:
                    u = i - 1
                    pe.wait_ge(p_ready, u + 1)
                    if u >= 2:
                        pe.wait_ge(turn_read, u - 1)
                    for x in range(2):
                        for half in range(MT):
                            n = MT * x + half
                            mm = pe.transpose(m.banks[2 + u % 2][:, n * P:(n + 1) * P],
                                              p[:, u % 2, x, half * P:(half + 1) * P], m.ident[:, :])
                    mm.then_inc(turned, 1)
            pe.wait_ge(turn_read, N)
            for j in range(DT):
                for half in range(MT):
                    mm = pe.matmul(m.banks[(4 + j) % 8][:, :], v_tok[:, half, j * P:(j + 1) * P],
                                   pt[:, j // HT, half, :], start=(half == 0), stop=(half == MT - 1))
                mm.then_inc(out_done, 1)

        @block.vector
        def _(dve):
            step = m.steps(dve, m.dve_step)
            for i in range(N):
                st = stat[:, i % 2, :, :]
                dve.wait_ge(scores_done, i + 1)
                step(dve.tensor_reduce(st[:, 0, :], m.banks[i % 2][:, :].rearrange("p (x k) -> p x k", x=2), AX.X, ALU.max))
                dve.tensor_scalar(st[:, 1, :], st[:, 0, :], -SCALE, None, ALU.mult).then_inc(max_ready, 1)
                dve.wait_ge(exp_done, i + 1)
                step(dve.reciprocal(st[:, 3, :], st[:, 2, :]))
                for x in range(2):
                    mul = dve.tensor_scalar(p[:, i % 2, x, :], p[:, i % 2, x, :], st[:, 3, x:x + 1], None, ALU.mult)
                mul.then_inc(p_ready, 1)
            for j in range(DT):
                dve.wait_ge(high_ready, j + 1)
                dve.tensor_tensor(o_ch[1][:, j, :], m.banks[(4 + j) % 8][:, :], o_ch[0][:, j, :], ALU.subtract)
            m.keep(step)

        @block.scalar
        def _(act):
            for i in range(N + 1):
                if i < N:
                    st = stat[:, i % 2, :, :]
                    act.wait_ge(max_ready, i + 1)
                    if i >= 2:
                        act.wait_ge(turned, i - 1)
                    for x in range(2):
                        e = act.activation(p[:, i % 2, x, :], m.banks[i % 2][:, x * MEM:(x + 1) * MEM], ACT.Exp,
                                           bias=st[:, 1, x:x + 1], scale=SCALE, accum_out=st[:, 2, x:x + 1])
                    e.then_inc(exp_done, 1)
                if i >= 1:
                    u = i - 1
                    t, pair = units[u]
                    act.wait_ge(turned, u + 1)
                    act.activation(pt[:, 2 * pair:2 * pair + 2, :, t * P:(t + 1) * P],
                                   m.banks[2 + u % 2][:, :].rearrange("p (x a n) -> p x a n", x=2, a=MT), ACT.Copy)\
                       .then_inc(turn_read, 1)
            for j in range(DT):
                act.wait_ge(out_done, j + 1)
                act.activation(o_ch[0][:, j, :], m.banks[(4 + j) % 8][:, :], ACT.Copy).then_inc(high_ready, 1)



HP = 2 * PH
SLOTS = PH * TOPK
ROWS = 16
GROUP = 4


def peer(m):
    nc = m.nc
    with ExitStack() as c:
        sb = lambda n, s, d=F32: c.enter_context(nc.sbuf_tensor(n, s, d))
        h_tok = sb("peer_h_tok", [P, TT, D])
        choice = Choice(m, c)
        peer_in(m, h_tok, choice)
        peer_experts(m, h_tok, choice)


PART = PH // 2
PARTS = TT * 2
EARLY = TT - 1
LATE = 4


class Choice:

    def __init__(self, m, c):
        nc = m.nc
        self.m = m
        sb = lambda n, s, d=F32: c.enter_context(nc.sbuf_tensor(n, s, d))
        sem = lambda n: m.sem(c, n)
        self.gates = sb("peer_gates", [P, TT, SLOTS])
        self.ids = sb("peer_ids", [P, TT, SLOTS], U32)
        self.top_v = sb("peer_top_v", [P, TT, HP, TOPK])
        self.top_f = sb("peer_top_f", [P, TT, HP, TOPK])
        self.late = sb("peer_late", [P, HP, KEYS])
        self.late_i = sb("peer_late_i", [P, LATE, TOPK], U32)
        self.best_v = sb("peer_best_v", [P, PART, TOPK])
        self.place = sb("peer_place", [P, PART, TOPK], U32)
        self.digit = sb("peer_digit", [P, 2, PART, TOPK], U32)
        self.digit_f = sb("peer_digit_f", [P, 2, PART, TOPK])
        self.chosen = sb("peer_chosen", [P, 2, PART, TOPK])
        self.count = sb("peer_count", [P, TOPK])
        self.soft = sb("peer_soft", [P, PART, TOPK])
        self.total = sb("peer_total", [P, 2, PART])
        self.soft_in, self.soft_out, self.ids_ready, self.count_made = (
            sem("peer_soft_in"), sem("peer_soft_out"), sem("peer_ids_ready"), sem("peer_count_made"))

    def slots(self, k):
        return k // 2, slice((k % 2) * PART * TOPK, (k % 2 + 1) * PART * TOPK)

    def vector(self, dve, step, k, scratch):
        t, at = self.slots(k)
        heads = slice((k % 2) * 2 * PART, (k % 2 + 1) * 2 * PART)
        v4 = self.top_v[:, t, heads, :].rearrange("p (h two) k -> p h two k", two=2)
        f4 = self.top_f[:, t, heads, :].rearrange("p (h two) k -> p h two k", two=2)
        square = [P, PART, TOPK, TOPK]
        cand, left = (x.rearrange("p (h n) -> p h n", h=PART) for x in scratch[0:2])
        picked = scratch[2].rearrange("p (r n) -> p r n", n=TOPK)
        p4 = scratch[2].rearrange("p (h k n) -> p h k n", h=PART, k=TOPK)
        a = v4[:, :, 0, :].rearrange("p h (k o) -> p h k o", o=1).broadcast_to(square)
        b = v4[:, :, 1, :].rearrange("p h (o k) -> p h o k", o=1).broadcast_to(square)
        step(dve.tensor_tensor(cand.rearrange("p h (a b) -> p h a b", a=TOPK), a, b, ALU.add))
        best_16(dve, step, PART, lambda r: cand[:, r, :], lambda r: left[:, r, :], lambda r: self.best_v[:, r, :],
                lambda r: self.place[:, r, :])
        if k > 0:
            dve.wait_ge(self.soft_out, k)
        dve.tensor_tensor(self.soft[:, :, :], self.best_v[:, :, :],
                          self.best_v[:, :, 0:1].broadcast_to([P, PART, TOPK]), ALU.subtract).then_inc(self.soft_in, 1)
        dve.tensor_scalar(self.digit[:, 0, :, :], self.place[:, :, :], 4, None, ALU.logical_shift_right)
        step(dve.tensor_scalar(self.digit[:, 1, :, :], self.place[:, :, :], 15, None, ALU.bitwise_and))
        step(dve.tensor_copy(self.digit_f[:, :, :, :], self.digit[:, :, :, :]))
        for half in range(2):
            which = self.digit_f[:, half, :, :].rearrange("p h k -> p (h k)")
            step(dve.tensor_tensor(picked, spread(which, TOPK), again(self.count[:, :], PART * TOPK), ALU.is_equal))
            step(dve.tensor_tensor(p4, p4, f4[:, :, half, :].rearrange("p h (o k) -> p h o k", o=1).broadcast_to(square),
                                   ALU.mult))
            step(dve.tensor_reduce(self.chosen[:, half, :, :].rearrange("p h k -> p (h k)"), picked, AX.X, ALU.add))
        step(dve.scalar_tensor_tensor(self.chosen[:, 0, :, :], self.chosen[:, 0, :, :], float(KEYS), self.chosen[:, 1, :, :],
                                      ALU.mult, ALU.add))
        dve.tensor_copy(self.ids[:, t, at], self.chosen[:, 0, :, :].rearrange("p h k -> p (h k)"))\
           .then_inc(self.ids_ready, 1)

    def vector_gates(self, dve, step, k):
        t, at = self.slots(k)
        dve.wait_ge(self.soft_out, k + 1)
        g3 = self.gates[:, t, at].rearrange("p (h k) -> p h k", h=PART)
        step(dve.tensor_reduce(self.total[:, 0, :], g3, AX.X, ALU.add))
        step(dve.reciprocal(self.total[:, 1, :], self.total[:, 0, :]))
        step(dve.tensor_tensor(g3, g3, spread(self.total[:, 1, :], TOPK), ALU.mult))

    def vector_late(self, dve, step, n, scratch):
        columns = slice(n * LATE, (n + 1) * LATE)
        left = scratch.rearrange("p (r n) -> p r n", n=KEYS)
        best_16(dve, step, LATE, lambda r: self.late[:, n * LATE + r, :], lambda r: left[:, r, :],
                lambda r: self.top_v[:, EARLY, n * LATE + r, :], lambda r: self.late_i[:, r, :])
        step(dve.tensor_copy(self.top_f[:, EARLY, columns, :], self.late_i[:, :, :]))

    def scalar(self, act, k):
        t, at = self.slots(k)
        act.wait_ge(self.soft_in, k + 1)
        act.activation(self.gates[:, t, at], self.soft[:, :, :].rearrange("p h k -> p (h k)"), ACT.Exp)\
           .then_inc(self.soft_out, 1)


def best_16(dve, step, n, values, left, out_v, out_i, hold=None):
    for pick in range(2):
        of = values if pick == 0 else left
        eight = slice(8 * pick, 8 * pick + 8)
        if hold is not None:
            dve.sem_inc(hold, 1)
        for r in range(n):
            last = dve.max(out_v(r)[:, eight], of(r))
        step(last)
        if hold is not None:
            dve.sem_inc(hold, 1)
        for r in range(n):
            last = dve.max_index(out_i(r)[:, eight], out_v(r)[:, eight], of(r))
        if pick == 0:
            for r in range(n):
                last = dve.match_replace(left(r), out_v(r)[:, eight], values(r), NEG)
        step(last)


def peer_in(m, h_tok, choice):
    nc, ins = m.nc, m.ins
    with ExitStack() as c:
        sb = lambda n, s, d=F32: c.enter_context(nc.sbuf_tensor(n, s, d))
        sem = lambda n: m.sem(c, n)
        h = [sb(f"peer_h_{x}", [P, DT, SEQ], F32R) for x in ("high", "low")]
        m.open_parts(c)
        gain = sb("peer_gain", [P, D])
        keys = sb("peer_keys", [P, HP, KEYS])
        q = sb("peer_q", [P, RING, SEQ])
        sc = sb("peer_sc", [P, RING, EARLY, KEYS])
        sc2 = sb("peer_sc2", [P, 2, EARLY, KEYS])
        top = sb("peer_top", [P, 2, EARLY, TOPK])
        top_i = sb("peer_top_i", [P, 2, EARLY, TOPK], U32)
        scratch = sb("peer_scratch", [P, 3, PART * TOPK * TOPK])
        norm = NormTurn(m, c, "peer_norm", m.resid, h, lambda k: m.col("norm_ffn", k), TT, D, m.banks[0:4])
        gain_loaded, keys_loaded, q_copied, scores_done, scores_read, sc_free = (
            sem("peer_gain_loaded"), sem("peer_keys_loaded"), sem("peer_q_copied"), sem("peer_scores_done"),
            sem("peer_scores_read"), sem("peer_sc_free"))
        held = sem("peer_index_held")
        u0 = m.unit
        m.unit += HP
        ORDER = [("q", 0), ("q", 1), ("s", 0), ("q", 2), ("s", 1), ("q", 3), ("s", 2), ("s", 3)]
        block = c.enter_context(nc.Block())

        @block.sync
        def _(sp):
            sp.dma_start(gain[:, :], m.row("norm_ffn", D)).then_inc(gain_loaded, 16)
            sp.dma_start(keys[:, :, :], ins["peer_keys"]).then_inc(keys_loaded, 16)
            stream_weights(m, sp, HP)

        @block.gpsimd
        def _(pool):
            pool.iota(choice.count[:, :], [[1, TOPK]], base=0, channel_multiplier=0,
                      allow_small_or_imprecise_dtypes=True).then_inc(choice.count_made, 1)
            split_weights(m, pool, HP)

        @block.tensor
        def _(pe):
            norm.tensor(pe)
            pe.wait_ge(norm.turned_ready, DT)
            pe.wait_ge(keys_loaded, 16)
            with pe.Fori(0, HP // RING) as i:
                for what, s in ORDER:
                    if what == "q":
                        pe.wait_ge(m.w_split, i * RING + (u0 + s + 1))
                        pe.wait_ge(q_copied, i * RING + (s + 1))
                        mm = column(m, pe, s, h, m.banks[4 + s][:, :])
                        mm.then_inc(m.w_used, 1)
                    else:
                        pe.wait_ge(q_copied, i * RING + (RING + s + 1))
                        pe.wait_ge(scores_read, i * RING + (s + 1))
                        for t in range(TT):
                            mm = pe.matmul(m.banks[s][:, t * KEYS:(t + 1) * KEYS], q[:, s, t * P:(t + 1) * P],
                                           keys[:, i * RING + s, :], start=True, stop=True)
                        mm.then_inc(scores_done, 1)

        @block.scalar
        def _(act):
            norm.scalar_sums(act)
            norm.scalar_rstd(act)
            norm.scalar_turned(act)
            act.sem_inc(q_copied, RING)
            act.sem_inc(scores_read, RING)

            def columns(i, first):
                for what, s in ORDER:
                    x = first + s
                    if what == "q":
                        act.wait_ge(m.w_used, i * RING + (u0 + x + 1))
                        act.activation(q[:, s, :], m.banks[4 + s][:, :], ACT.Copy).then_inc(q_copied, 1)
                    else:
                        act.wait_ge(scores_done, i * RING + (x + 1))
                        act.wait_ge(sc_free, i * RING + (x + 1))
                        act.activation(choice.late[:, i * RING + x, :], m.banks[s][:, EARLY * KEYS:], ACT.Copy)
                        act.activation(sc[:, s, :, :].rearrange("p t k -> p (t k)"), m.banks[s][:, 0:EARLY * KEYS], ACT.Copy)\
                           .then_inc(scores_read, 1)

            with act.Fori(0, 2) as i:
                columns(i, 0)
            with act.Fori(0, 2) as i:
                columns(i, HP // 2)
            choice.scalar(act, 0)

        @block.vector
        def _(dve):
            step = m.steps(dve, m.dve_step)
            norm.vector(dve, step)
            norm.vector_turned(dve)
            dve.wait_ge(gain_loaded, 16)
            for t in range(TT):
                dve.scalar_tensor_tensor(h_tok[:, t, :], m.resid[:, t, :], norm.stat[:, 0, t:t + 1], gain[:, :],
                                         ALU.mult, ALU.mult)
            dve.sem_inc(sc_free, RING)
            dve.wait_ge(choice.count_made, 1)

            def columns(first):
                with dve.Fori(0, 2) as i:
                    step.loop(i, 5 * RING // 2)
                    for s in range(0, RING, 2):
                        dve.wait_ge(scores_read, i * RING + (RING + first + s + 2))
                        best_16(dve, step, 2 * EARLY, lambda r: sc[:, s + r // EARLY, r % EARLY, :],
                                lambda r: sc2[:, r // EARLY, r % EARLY, :], lambda r: top[:, r // EARLY, r % EARLY, :],
                                lambda r: top_i[:, r // EARLY, r % EARLY, :], held)
                        dve.sem_inc(sc_free, 2)
                        for j in range(2):
                            x = i * RING + (first + s + j)
                            dve.tensor_copy(choice.top_v[:, 0:EARLY, x, :], top[:, j, :, :])
                            last = dve.tensor_copy(choice.top_f[:, 0:EARLY, x, :], top_i[:, j, :, :])
                        step(last)
                    step.end_loop(2)

            columns(0)
            choice.vector(dve, step, 0, [scratch[:, n, :] for n in range(3)])
            columns(HP // 2)
            choice.vector_gates(dve, step, 0)
            m.keep(step)


def peer_experts(m, h_tok, choice):
    nc, ins = m.nc, m.ins
    gates, ids = choice.gates, choice.ids
    PER_PART = PART * TOPK
    TURNS = PER_PART // ROWS
    NG = ROWS // GROUP
    with ExitStack() as c:
        sb = lambda n, s, d=F32: c.enter_context(nc.sbuf_tensor(n, s, d))
        sem = lambda n: m.sem(c, n)
        rows = sb("peer_rows", [P, ROWS, 2 * D])
        at = sb("peer_at", [P, NG, GROUP], U32)
        dots = sb("peer_dots", [P, NG, GROUP])
        acts = sb("peer_acts", [P, NG, GROUP])
        weight = sb("peer_weight", [P, NG, GROUP])
        diag = sb("peer_diag", [P, 2 * GROUP, P])
        zero = sb("peer_zero", [P, P])
        loaded = [sem(f"peer_loaded{s}") for s in range(ROWS)]
        at_ready, held, dots_ready, acts_ready, weight_ready, diag_ready, row_used, zero_made = (
            sem("peer_at_ready"), sem("peer_held"), sem("peer_dots_ready"), sem("peer_acts_ready"), sem("peer_weight_ready"),
            sem("peer_diag_ready"), sem("peer_row_used"), sem("peer_zero_made"))
        scratch = [m.ring[:, s, 0:PART * TOPK * TOPK] for s in range(3)]
        last_norm = LastNorm(m, c, m.ring[:, 3, :], h_tok, row_used)
        block = c.enter_context(nc.Block())

        @block.sync
        def _(sp):
            last_norm.sync(sp)

        @block.gpsimd
        def _(pool):
            pool.memset(zero[:, :], 0.0).then_inc(zero_made, 1)
            pool.sem_inc(row_used, ROWS)
            for part in range(PARTS):
                t, begin = part // 2, (part % 2) * PER_PART
                pool.wait_ge(choice.ids_ready, part + 1)
                with pool.Fori(0, TURNS) as i:
                    for g in range(NG):
                        pool.wait_ge(row_used, i * ROWS + (part * PER_PART + GROUP * g + 1))
                        pool.sem_inc(held, 1)
                        pool.tensor_copy(at[:, g, :], ids[:, t, bass.ds(i * ROWS + (begin + GROUP * g), GROUP)])\
                            .then_inc(at_ready, 1)
                        pool.wait_ge(at_ready, i * NG + (part * TURNS * NG + g + 1))
                        pool.sem_inc(held, 1)
                        for r in range(GROUP):
                            s = GROUP * g + r
                            if r > 0:
                                pool.wait_ge(row_used, i * ROWS + (part * PER_PART + s + 1))
                                pool.sem_inc(held, 1)
                            pool.indirect_dma_start(rows[:, s, :], None, ins["peer_uv"],
                                                    bass.IndirectOffsetOnAxis(ap=at[:, g, r:r + 1], axis=0))\
                                .then_inc(loaded[s], 16)

        @block.vector
        def _(dve):
            step = m.steps(dve, m.dve_step)

            def turns(part, first, last):
                t, begin = part // 2, (part % 2) * PER_PART
                with dve.Fori(0, last - first) as i:
                    for g in range(NG):
                        for r in range(GROUP):
                            s = GROUP * g + r
                            dve.wait_ge(loaded[s], i * 16 + 16 * (part * TURNS + first + 1))
                            dot = dve.tensor_tensor_reduce(rows[:, s, 0:D], rows[:, s, 0:D], h_tok[:, t, :], 1.0, 0.0,
                                                           ALU.mult, ALU.add, dots[:, g, r:r + 1])
                        dot.then_inc(dots_ready, 1)
                        dve.wait_ge(acts_ready, i * NG + ((part * TURNS + first) * NG + g + 1))
                        dve.tensor_tensor(weight[:, g, :], acts[:, g, :],
                                          gates[:, t, bass.ds(i * ROWS + (begin + first * ROWS + GROUP * g), GROUP)],
                                          ALU.mult).then_inc(weight_ready, 1)

            for part in range(PARTS):
                turns(part, 0, 1)
                if part < PARTS - 1:
                    choice.vector(dve, step, part + 1, scratch)
                    choice.vector_gates(dve, step, part + 1)
                if part % 2 == 0 and part > 0:
                    last_norm.vector(dve, step, part // 2 - 1)
                if part < HP // LATE:
                    turns(part, 1, 3)
                    choice.vector_late(dve, step, part, m.ring[:, 1, 0:LATE * KEYS])
                    turns(part, 3, TURNS)
                else:
                    turns(part, 1, TURNS)
            last_norm.vector(dve, step, TT - 1)
            m.keep(step)

        @block.scalar
        def _(act):
            def turns(part, first, last):
                with act.Fori(0, last - first) as i:
                    for g in range(NG):
                        n = i * NG + ((part * TURNS + first) * NG + g + 1)
                        act.wait_ge(dots_ready, n)
                        act.activation(acts[:, g, :], dots[:, g, :], ACT.Gelu).then_inc(acts_ready, 1)
                        act.wait_ge(weight_ready, n)
                        for r in range(GROUP):
                            d = GROUP * (g % 2) + r
                            act.wait_ge(row_used, i * ROWS + (part * PER_PART + first * ROWS + GROUP * g + r + 1
                                                              + ROWS - 2 * GROUP))
                            act.activation(diag[:, d, :], m.ident[:, :], ACT.Copy, scale=weight[:, g, r:r + 1])\
                               .then_inc(diag_ready, 1)

            for part in range(PARTS):
                turns(part, 0, 1)
                if part < PARTS - 1:
                    choice.scalar(act, part + 1)
                if part % 2 == 0 and part > 0:
                    last_norm.scalar(act, part // 2 - 1)
                turns(part, 1, TURNS)
            last_norm.scalar(act, TT - 1)

        @block.tensor
        def _(pe):
            pe.wait_ge(zero_made, 1)
            for t in range(TT):
                for half in range(2):
                    pe.matmul(m.banks[2 * t + half][:, :], zero[:, :], h_tok[:, t, 0:512], start=True, stop=False,
                              skip_group_check=True)
                with pe.Fori(0, SLOTS // ROWS) as i:
                    for s in range(ROWS):
                        pe.wait_ge(diag_ready, i * ROWS + (t * SLOTS + s + 1))
                        for half in range(2):
                            mm = pe.matmul(m.banks[2 * t + half][:, :], diag[:, s % (2 * GROUP), :],
                                           rows[:, s, D + half * 512:D + (half + 1) * 512], start=False, stop=False,
                                           skip_group_check=True)
                        mm.then_inc(row_used, 1)


class LastNorm:

    def __init__(self, m, c, gain, junk, row_used):
        self.m, self.gain, self.junk, self.row_used = m, gain, junk, row_used
        self.stat = c.enter_context(m.nc.sbuf_tensor("last_stat", [P, 3, TT], F32))
        self.gain_loaded, self.mean_ready, self.rstd_ready, self.ready, self.stored = (
            m.sem(c, "last_" + n) for n in ("gain_loaded", "mean", "rstd", "ready", "stored"))

    def sync(self, sp):
        sp.dma_start(self.gain, self.m.row("norm_final", D)).then_inc(self.gain_loaded, 16)
        for t in range(TT):
            sp.wait_ge(self.ready, t + 1)
            sp.dma_start(self.m.out[t * P:(t + 1) * P, :], self.m.resid[:, t, :]).then_inc(self.stored, 16)
            sp.wait_ge(self.stored, 16 * (t + 1))

    def vector(self, dve, step, t):
        m, st = self.m, self.stat
        dve.wait_ge(self.row_used, ROWS + SLOTS * (t + 1))
        for half in range(2):
            here = m.resid[:, t, half * 512:(half + 1) * 512]
            last = dve.tensor_tensor(here, here, m.banks[2 * t + half][:, :], ALU.add)
        step(last)
        step(dve.tensor_tensor_reduce(self.junk[:, t, :], m.resid[:, t, :], m.resid[:, t, :], 1.0, 0.0, ALU.mult, ALU.add,
                                      st[:, 0, t:t + 1]))
        step(dve.tensor_scalar(st[:, 1, t:t + 1], st[:, 0, t:t + 1], 1.0 / D, EPS, ALU.mult, ALU.add))
        dve.reciprocal(st[:, 2, t:t + 1], st[:, 1, t:t + 1]).then_inc(self.mean_ready, 1)
        dve.wait_ge(self.rstd_ready, t + 1)
        dve.wait_ge(self.gain_loaded, 16)
        dve.scalar_tensor_tensor(m.resid[:, t, :], m.resid[:, t, :], st[:, 0, t:t + 1], self.gain, ALU.mult, ALU.mult)\
           .then_inc(self.ready, 1)

    def scalar(self, act, t):
        act.wait_ge(self.mean_ready, t + 1)
        act.activation(self.stat[:, 0, t:t + 1], self.stat[:, 2, t:t + 1], ACT.Sqrt).then_inc(self.rstd_ready, 1)



def column_units(w):
    import numpy as np
    kt, n = w.shape[0] // P, w.shape[1] // P
    return np.ascontiguousarray(w.reshape(kt, P, n, P).transpose(2, 1, 0, 3)).reshape(n, P, kt * P)


def token_units(w):
    import numpy as np
    kt, n = w.shape[0] // P, w.shape[1] // 512
    return np.ascontiguousarray(w.reshape(kt // 2, 2, P, n, 512).transpose(3, 0, 2, 1, 4)).reshape(n * kt // 2, P, UNIT)


def lay_out(a):
    import numpy as np
    units, col, row = [], [], []
    col_at, row_at = {}, {}

    def add_cols(name, v):
        col_at[name] = sum(x.shape[1] for x in col)
        col.append(v)

    def add_row(name, v):
        row_at[name] = sum(x.shape[0] for x in row)
        row.append(v.reshape(-1))

    def by_tile(v):
        return v.reshape(-1, P).T

    def taps(w):
        return w.reshape(CONV, -1, P).transpose(2, 1, 0).reshape(P, -1)

    w = a["ssm_w_in"][0]
    units += [token_units(w[:, 0:DI]), column_units(w[:, DI:DI + CM_T * P])]
    arrays = {"ssm_w_dt": w[:, DI + CM_T * P:].reshape(DT, P, HEADS).transpose(1, 0, 2)}
    units += [token_units(a["ssm_w_out"][0])]
    add_cols("pre_norm0", by_tile(a["pre_norm"][0]))
    add_cols("ssm_conv_w", taps(a["ssm_conv_w"][0]))
    add_cols("ssm_conv_b", by_tile(a["ssm_conv_b"][0]))
    add_cols("ssm_gate_norm", by_tile(a["ssm_gate_norm"][0]))
    add_row("ssm_dt_bias", a["ssm_dt_bias"][0])
    add_row("ssm_a_log", a["ssm_a_log"][0])
    add_row("ssm_d", a["ssm_d"][0])
    add_row("post_norm0", a["post_norm"][0])

    heads = lambda w: w.reshape(w.shape[0], QH, AD)[:, HEAD_ORDER].reshape(w.shape[0], QW)
    w = a["att_w_in"][0]
    units += [token_units(np.concatenate([heads(w[:, 0:QW]), w[:, QW:QW + 2 * KVW], heads(w[:, QW + 2 * KVW:])], axis=1))]
    units += [token_units(a["att_w_out"][0].reshape(QH, AD, D)[HEAD_ORDER].reshape(QW, D))]
    add_cols("pre_norm1", by_tile(a["pre_norm"][1]))
    add_row("att_sinks", a["att_sinks"][0][HEAD_ORDER])
    add_row("post_norm1", a["post_norm"][1])
    arrays["positions"] = a["positions"].reshape(TT, P).T

    w = a["w_in_2"][0]
    GW, MW = GH * GD, MH * MD
    cuts = np.cumsum([3 * GW, GW, GH, GH, 2 * MW, MW, MW, MH, MH])
    g_qkv, g_z, g_a, g_b, m_qk, m_v, m_o, m_i, m_f = np.split(w, cuts[:-1], axis=1)
    units += [token_units(np.concatenate([g_z, m_v, m_o], axis=1)), column_units(np.concatenate([g_qkv, m_qk], axis=1))]
    arrays["hyb_w_small"] = np.concatenate([g_a, g_b, m_i, m_f], axis=1).reshape(DT, P, 16).transpose(1, 0, 2)
    units += [token_units(a["w_out_2"][0])]
    add_cols("norm_mix", by_tile(a["norm_mix_w_2"][0]))
    add_cols("hyb_conv_w", taps(np.concatenate([a["gdn_conv_w_2"][0], a["mlstm_conv_w_2"][0]], axis=1)))
    add_row("gdn_dt_bias", a["gdn_dt_bias_2"][0])
    add_row("gdn_a_log", a["gdn_a_log_2"][0])
    add_row("mls_i_bias", a["mlstm_i_bias_2"][0])
    add_row("mls_f_bias", a["mlstm_f_bias_2"][0])
    add_row("hyb_gains", np.concatenate([a["gdn_norm_w_2"][0]] * GH + [a["mlstm_norm_w_2"][0]]))

    units += [column_units(a["xa_wq_2"][0]), column_units(a["xa_wkv_2"][0][:, 0:D]), token_units(a["xa_wkv_2"][0][:, D:])]
    units += [token_units(a["xa_wo_2"][0]), column_units(a["peer_wq_2"][0])]
    arrays["mem"] = a["mem_2"].reshape(MEM, D)
    add_cols("norm_xa", by_tile(a["norm_xa_w_2"][0]))
    add_cols("norm_mem", by_tile(a["norm_mem_w_2"][0]))
    add_cols("norm_ffn", by_tile(a["norm_ffn_w_2"][0]))
    add_row("norm_ffn", a["norm_ffn_w_2"][0])
    add_row("norm_final", a["norm_final_w_2"])
    arrays["peer_keys"] = a["peer_sub_keys_2"][0].reshape(HP, KEYS, P).transpose(2, 0, 1)
    arrays["peer_uv"] = np.concatenate([a["peer_u_2"][0], a["peer_v_2"][0]], axis=1)
    arrays["x"] = a["x"].reshape(SEQ, D)
    arrays["weights"] = np.concatenate(units)
    arrays["cols"] = np.concatenate(col, axis=1)
    arrays["rows"] = np.concatenate(row)[None, :]
    return arrays, col_at, row_at



STAGES = [mamba, attention, hybrid, cross_attention, peer]


def program(nc, ins, out):
    with ExitStack() as ctx:
        m = Machine(nc, ctx, ins, out)
        set_up(m)
        for stage in STAGES:
            stage(m)
            m.clear_signals()



def kernel(**inputs):
    import numpy as np
    from concourse import bacc
    from concourse.bass_utils import run_bass_kernel_spmd

    laid, col_at, row_at = lay_out({k: np.asarray(v) for k, v in inputs.items()})
    nc = bacc.Bacc("TRN2", target_bir_lowering=False, num_devices=1)
    arrays, ins = {}, {"col_at": col_at, "row_at": row_at}
    for name, a in laid.items():
        a = np.ascontiguousarray(a)
        arrays[f"in_{name}"] = a
        ins[name] = nc.dram_tensor(f"in_{name}", a.shape, mybir.dt.from_np(a.dtype), kind="ExternalInput").ap()
    out = nc.dram_tensor("out_0", (SEQ, D), F32, kind="ExternalOutput").ap()
    program(nc, ins, out)
    r = run_bass_kernel_spmd(nc, [arrays], core_ids=[0])
    return r.results[0]["out_0"].reshape(1, SEQ, D)
```
